# Optimizing a Trainium2 kernel written in Bass

```python
import math
import jax, jax.numpy as jnp
from jax import lax
import numpy as np

D_MODEL = 1024
BATCH = 1
SEQ = 512
DEPTH = 1

CHUNK = 64
QBLK = 128
MEM_LEN = 256
EPS = 1e-6

POOL_WIDTH = D_MODEL // 4
POOL_GROUPS = 4
POOL_GDIM = POOL_WIDTH // POOL_GROUPS
POOL_WINDOWS = (2, 4, 8, 16)

RWKV_WIDTH = D_MODEL // 4
RWKV_HEAD = 64
RWKV_HEADS = RWKV_WIDTH // RWKV_HEAD
D_DECAY_LORA = 64
D_AAA_LORA = 64
D_GATE_LORA = 128
RWKV_COLS = 3 * RWKV_WIDTH + D_DECAY_LORA + D_AAA_LORA + D_GATE_LORA
RWKV_SPLITS = tuple(int(i) for i in np.cumsum(
    [RWKV_WIDTH, RWKV_WIDTH, RWKV_WIDTH, D_DECAY_LORA, D_AAA_LORA]))
RWKV_GN_EPS = 64e-5

DIFF_WIDTH = D_MODEL // 2
DIFF_HEADS = 4
DIFF_VDIM = DIFF_WIDTH // DIFF_HEADS
DIFF_QK = DIFF_VDIM // 2
DIFF_COLS = 3 * DIFF_WIDTH

P_IN = POOL_WIDTH + RWKV_COLS + DIFF_COLS

XA_HEADS = 4
XA_HEAD = D_MODEL // XA_HEADS
D_FF = 2816
CONV_W = 3


F32 = jnp.float32

def rms_normalize(x, eps=EPS):
    xf = x.astype(F32)
    return xf * lax.rsqrt(jnp.mean(xf * xf, axis=-1, keepdims=True) + eps)

def rmsnorm(x, g):
    return (rms_normalize(x) * g.astype(F32)).astype(x.dtype)

def shift_right(x, n=1):
    return jnp.pad(x, ((0, 0), (n, 0), (0, 0)))[:, :x.shape[1]]

def alibi_slopes(n_heads):
    return jnp.asarray(2.0 ** (-8.0 * (np.arange(n_heads) + 1) / n_heads), dtype=F32)

def pool_mixer(u, w_grp, scale):
    B, S, _ = u.shape
    ug = u.astype(F32).reshape(B, S, POOL_GROUPS, POOL_GDIM)
    t = jnp.arange(S)
    outs = []
    for gi, w in enumerate(POOL_WINDOWS):
        c = jnp.cumsum(ug[:, :, gi], axis=1)
        win_sum = c - shift_right(c, w)
        count = jnp.minimum(t + 1, w).astype(F32)[None, :, None]
        outs.append(win_sum / count - ug[:, :, gi])
    d = jnp.stack(outs, axis=2)
    y = jnp.einsum('bsgc,gcd->bsgd', d, w_grp.astype(F32))
    return (y.reshape(B, S, POOL_WIDTH) * scale.astype(F32)).astype(u.dtype)

def wkv7_scan(r, decay, k, v, a_vec, b_vec):
    B, S, H, N = r.shape

    def step(s, inp):
        r_t, w_t, k_t, v_t, a_t, b_t = inp
        sa = jnp.einsum('bhvk,bhk->bhv', s, a_t)
        s = (s * w_t[:, :, None, :] + sa[..., None] * b_t[:, :, None, :]
             + v_t[..., None] * k_t[:, :, None, :])
        y = jnp.einsum('bhvk,bhk->bhv', s, r_t)
        return s, y

    seq_first = lambda a: jnp.moveaxis(a, 1, 0)
    s0 = jnp.zeros((B, H, N, N), F32)
    _, ys = lax.scan(step, s0, (seq_first(r), seq_first(decay), seq_first(k),
                                seq_first(v), seq_first(a_vec), seq_first(b_vec)))
    return jnp.moveaxis(ys, 0, 1)

def rwkv7_mixer(z, mu, w0, w2, a0, a2, g2, k_k, k_a, r_k, ln_w, ln_b):
    B, S, _ = z.shape
    H, N = RWKV_HEADS, RWKV_HEAD
    zf = z.astype(F32)
    zm = zf + mu.astype(F32) * (shift_right(zf) - zf)
    r, k, v, wd, ad, gd = jnp.split(zm, RWKV_SPLITS, axis=-1)
    w = -jax.nn.softplus(-(w0 + jnp.tanh(wd) @ w2)) - 0.5
    a = jax.nn.sigmoid(a0 + ad @ a2)
    g = jax.nn.sigmoid(gd) @ g2
    heads = lambda t: t.reshape(B, S, H, N)
    r, w, k, v, a = heads(r), heads(w), heads(k), heads(v), heads(a)
    kk = k * k_k.astype(F32).reshape(H, N)
    kk = kk / jnp.maximum(jnp.sqrt(jnp.sum(kk * kk, -1, keepdims=True)), 1e-12)
    k = k * (1.0 + (a - 1.0) * k_a.astype(F32).reshape(H, N))
    decay = jnp.exp(-jnp.exp(w))
    y = wkv7_scan(r, decay, k, v, -kk, kk * a)
    mean = jnp.mean(y, -1, keepdims=True)
    var = jnp.mean(jnp.square(y - mean), -1, keepdims=True)
    y = ((y - mean) * lax.rsqrt(var + RWKV_GN_EPS)).reshape(B, S, RWKV_WIDTH)
    y = y * ln_w.astype(F32) + ln_b.astype(F32)
    bonus = jnp.sum(r * k * r_k.astype(F32), -1, keepdims=True) * v
    y = y + bonus.reshape(B, S, RWKV_WIDTH)
    return (y * g).astype(z.dtype)

def diff_attention(z, q_norm, k_norm, lq1, lk1, lq2, lk2, subln, lambda_init):
    B, S, _ = z.shape
    H = DIFF_HEADS
    q, k, v = jnp.split(z.astype(F32), 3, axis=-1)
    q = rms_normalize(q.reshape(B, S, H, 2, DIFF_QK)) * q_norm.astype(F32)
    k = rms_normalize(k.reshape(B, S, H, 2, DIFF_QK)) * k_norm.astype(F32)
    v = v.reshape(B, S, H, DIFF_VDIM)
    lam = (jnp.exp(jnp.sum(lq1.astype(F32) * lk1.astype(F32)))
           - jnp.exp(jnp.sum(lq2.astype(F32) * lk2.astype(F32))) + lambda_init)
    slopes = alibi_slopes(H)
    nblk = S // QBLK
    qb = q.reshape(B, nblk, QBLK, H, 2, DIFF_QK).transpose(1, 0, 2, 3, 4, 5)
    kpos = jnp.arange(S)
    kchunk = kpos // CHUNK
    scale = DIFF_QK ** -0.5

    def block(args):
        q_blk, start = args
        qpos = start + jnp.arange(QBLK)
        s = jnp.einsum('bqhcd,bkhcd->bhcqk', q_blk, k) * scale
        dist = jnp.abs(qpos[:, None] - kpos[None, :]).astype(F32)
        bias = -slopes[:, None, None, None] * dist
        visible = kchunk[None, :] <= (qpos // CHUNK)[:, None]
        s = jnp.where(visible, s + bias, -jnp.inf)
        p = jax.nn.softmax(s, axis=-1)
        p = p[:, :, 0] - lam * p[:, :, 1]
        return jnp.einsum('bhqk,bkhd->bqhd', p, v)

    starts = jnp.arange(nblk) * QBLK
    o = lax.map(block, (qb, starts))
    o = jnp.moveaxis(o, 0, 1).reshape(B, S, H, DIFF_VDIM)
    o = rms_normalize(o) * subln.astype(F32) * (1.0 - lambda_init)
    return o.reshape(B, S, DIFF_WIDTH).astype(z.dtype)

def memory_cross_attention(xn, memn, wq, wk, wv, wo, q_norm, k_norm):
    B, S, _ = xn.shape
    M = memn.shape[1]
    q = rms_normalize((xn @ wq).reshape(B, S, XA_HEADS, XA_HEAD)) * q_norm.astype(F32)
    k = rms_normalize((memn @ wk).reshape(B, M, XA_HEADS, XA_HEAD)) * k_norm.astype(F32)
    v = (memn @ wv).reshape(B, M, XA_HEADS, XA_HEAD).astype(F32)
    s = jnp.einsum('bshd,bmhd->bhsm', q, k) * (XA_HEAD ** -0.5)
    p = jax.nn.softmax(s, axis=-1)
    o = jnp.einsum('bhsm,bmhd->bshd', p, v).reshape(B, S, D_MODEL).astype(xn.dtype)
    return o @ wo

def conv_ffn(xn, w_up, conv_w, conv_b, w_down):
    h = xn @ w_up
    a, b = jnp.split(h, 2, axis=-1)
    rhs = conv_w.reshape(CONV_W, 1, D_FF).astype(a.dtype)
    c = lax.conv_general_dilated(a, rhs, window_strides=(1,), padding=[(CONV_W - 1, 0)],
                                 dimension_numbers=('NWC', 'WIO', 'NWC'),
                                 feature_group_count=D_FF) + conv_b
    return (jax.nn.gelu(c, approximate=False) * b) @ w_down

def first_inputs(seed: int = 0) -> dict:
    key = jax.random.key(seed)
    ks = iter(jax.random.split(key, 40))
    nrm = lambda shape, s: jax.random.normal(next(ks), shape, F32) * s
    gain = lambda shape: 1.0 + 0.02 * jax.random.normal(next(ks), shape, F32)
    L = DEPTH
    return {
        "x": nrm((BATCH, SEQ, D_MODEL), 1.0),
        "mem": nrm((BATCH, MEM_LEN, D_MODEL), 1.0),
        "mix_norm_g": gain((L, D_MODEL)),
        "w_in": nrm((L, D_MODEL, P_IN), D_MODEL ** -0.5),
        "pool_w": nrm((L, POOL_GROUPS, POOL_GDIM, POOL_GDIM), POOL_GDIM ** -0.5),
        "pool_scale": gain((L, POOL_WIDTH)),
        "rwkv_mu": jax.random.uniform(next(ks), (L, RWKV_COLS), F32),
        "rwkv_w0": jax.random.uniform(next(ks), (L, RWKV_WIDTH), F32, -5.0, -1.0),
        "rwkv_w2": nrm((L, D_DECAY_LORA, RWKV_WIDTH), 0.5 * D_DECAY_LORA ** -0.5),
        "rwkv_a0": nrm((L, RWKV_WIDTH), 0.1),
        "rwkv_a2": nrm((L, D_AAA_LORA, RWKV_WIDTH), 0.5 * D_AAA_LORA ** -0.5),
        "rwkv_g2": nrm((L, D_GATE_LORA, RWKV_WIDTH), D_GATE_LORA ** -0.5),
        "rwkv_k_k": 0.85 + nrm((L, RWKV_WIDTH), 0.05),
        "rwkv_k_a": 1.0 + nrm((L, RWKV_WIDTH), 0.05),
        "rwkv_r_k": nrm((L, RWKV_HEADS, RWKV_HEAD), 0.1),
        "rwkv_ln_w": gain((L, RWKV_WIDTH)),
        "rwkv_ln_b": nrm((L, RWKV_WIDTH), 0.02),
        "diff_q_norm": gain((L, 2, DIFF_QK)),
        "diff_k_norm": gain((L, 2, DIFF_QK)),
        "diff_lq1": nrm((L, DIFF_QK), 0.1),
        "diff_lk1": nrm((L, DIFF_QK), 0.1),
        "diff_lq2": nrm((L, DIFF_QK), 0.1),
        "diff_lk2": nrm((L, DIFF_QK), 0.1),
        "diff_subln": gain((L, DIFF_VDIM)),
        "w_out": nrm((L, D_MODEL, D_MODEL), D_MODEL ** -0.5),
        "xa_norm_g": gain((L, D_MODEL)),
        "mem_norm_g": gain((L, D_MODEL)),
        "xa_wq": nrm((L, D_MODEL, D_MODEL), D_MODEL ** -0.5),
        "xa_wk": nrm((L, D_MODEL, D_MODEL), D_MODEL ** -0.5),
        "xa_wv": nrm((L, D_MODEL, D_MODEL), D_MODEL ** -0.5),
        "xa_wo": nrm((L, D_MODEL, D_MODEL), D_MODEL ** -0.5),
        "xa_q_norm": gain((L, XA_HEAD)),
        "xa_k_norm": gain((L, XA_HEAD)),
        "ffn_norm_g": gain((L, D_MODEL)),
        "ffn_w_up": nrm((L, D_MODEL, 2 * D_FF), D_MODEL ** -0.5),
        "ffn_conv_w": nrm((L, CONV_W, D_FF), CONV_W ** -0.5),
        "ffn_conv_b": nrm((L, D_FF), 0.02),
        "ffn_w_down": nrm((L, D_FF, D_MODEL), D_FF ** -0.5),
    }

def first_block(x, mem, mix_norm_g, w_in, pool_w, pool_scale,
              rwkv_mu, rwkv_w0, rwkv_w2, rwkv_a0, rwkv_a2, rwkv_g2,
              rwkv_k_k, rwkv_k_a, rwkv_r_k, rwkv_ln_w, rwkv_ln_b,
              diff_q_norm, diff_k_norm, diff_lq1, diff_lk1, diff_lq2, diff_lk2, diff_subln,
              w_out, xa_norm_g, mem_norm_g, xa_wq, xa_wk, xa_wv, xa_wo, xa_q_norm, xa_k_norm,
              ffn_norm_g, ffn_w_up, ffn_conv_w, ffn_conv_b, ffn_w_down):
    h = x
    for l in range(DEPTH):
        lambda_init = 0.8 - 0.6 * math.exp(-0.3 * l)
        z = rmsnorm(h, mix_norm_g[l]) @ w_in[l]
        z_pool = z[..., :POOL_WIDTH]
        z_rwkv = z[..., POOL_WIDTH:POOL_WIDTH + RWKV_COLS]
        z_diff = z[..., POOL_WIDTH + RWKV_COLS:]
        y_pool = pool_mixer(z_pool, pool_w[l], pool_scale[l])
        y_rwkv = rwkv7_mixer(z_rwkv, rwkv_mu[l], rwkv_w0[l], rwkv_w2[l], rwkv_a0[l],
                             rwkv_a2[l], rwkv_g2[l], rwkv_k_k[l], rwkv_k_a[l],
                             rwkv_r_k[l], rwkv_ln_w[l], rwkv_ln_b[l])
        y_diff = diff_attention(z_diff, diff_q_norm[l], diff_k_norm[l], diff_lq1[l],
                                diff_lk1[l], diff_lq2[l], diff_lk2[l], diff_subln[l],
                                lambda_init)
        y = jnp.concatenate([y_pool, y_rwkv, y_diff], axis=-1)
        h = h + y @ w_out[l]
        h = h + memory_cross_attention(rmsnorm(h, xa_norm_g[l]), rmsnorm(mem, mem_norm_g[l]),
                                       xa_wq[l], xa_wk[l], xa_wv[l], xa_wo[l],
                                       xa_q_norm[l], xa_k_norm[l])
        h = h + conv_ffn(rmsnorm(h, ffn_norm_g[l]), ffn_w_up[l], ffn_conv_w[l],
                         ffn_conv_b[l], ffn_w_down[l])
    return h


SGU_CHUNK = 128
SGU_GROUPS = 4
SGU_GROUP_DIM = 128
SGU_WIDTH = SGU_GROUPS * SGU_GROUP_DIM
N_HEADS = 8
HEAD_DIM = 64
ATTN_WIDTH = N_HEADS * HEAD_DIM
IDX_HEADS = 8
IDX_DIM = 64
TOPK_MAX = 256
Q_BLOCK = 128
ROPE_THETA = 10000.0
D_FF_2 = 4 * D_MODEL
N_BRANCHES = 2

IN_SIZES = (SGU_WIDTH, SGU_WIDTH, ATTN_WIDTH, ATTN_WIDTH, ATTN_WIDTH,
            IDX_HEADS * IDX_DIM, IDX_DIM, IDX_HEADS, N_BRANCHES * D_MODEL)
D_IN = 2 * SGU_WIDTH + 3 * ATTN_WIDTH + IDX_HEADS * IDX_DIM + IDX_DIM + IDX_HEADS + N_BRANCHES * D_MODEL


def rmsnorm_2(x, g):
    xf = x.astype(jnp.float32)
    y = xf * lax.rsqrt(jnp.mean(xf * xf, axis=-1, keepdims=True) + EPS)
    return (y * g.astype(jnp.float32)).astype(x.dtype)

def layernorm(x, g, b):
    xf = x.astype(jnp.float32)
    mu = jnp.mean(xf, axis=-1, keepdims=True)
    xc = xf - mu
    y = xc * lax.rsqrt(jnp.mean(xc * xc, axis=-1, keepdims=True) + EPS)
    return (y * g.astype(jnp.float32) + b.astype(jnp.float32)).astype(x.dtype)

def rope_tables(seq_len, dim, dtype):
    pos = jnp.arange(seq_len, dtype=jnp.float32)
    inv_freq = ROPE_THETA ** (-jnp.arange(0, dim, 2, dtype=jnp.float32) / dim)
    ang = pos[:, None] * inv_freq[None, :]
    return jnp.cos(ang).astype(dtype)[:, None, :], jnp.sin(ang).astype(dtype)[:, None, :]

def apply_rope(x, cos, sin):
    x1, x2 = jnp.split(x, 2, axis=-1)
    return jnp.concatenate([x1 * cos - x2 * sin, x2 * cos + x1 * sin], axis=-1)

def split_cols(t, sizes):
    out, start = [], 0
    for s in sizes:
        out.append(t[..., start:start + s])
        start += s
    return out

def sgu_mixer(u, v, w_s, b_s, ln_g, ln_b):
    B, S, _ = u.shape
    n_chunks = S // SGU_CHUNK
    v = layernorm(v, ln_g, ln_b)
    vc = v.reshape(B, n_chunks, SGU_CHUNK, SGU_GROUPS, SGU_GROUP_DIM)
    causal = jnp.tril(jnp.ones((SGU_CHUNK, SGU_CHUNK), dtype=bool))
    ws = jnp.where(causal[None], w_s, jnp.zeros((), w_s.dtype))
    s = jnp.einsum('gts,bcsgd->bctgd', ws, vc) + b_s.T[:, :, None]
    return u * s.reshape(B, S, SGU_WIDTH)

def dsa_attention(q, k, v, q_idx, k_idx, w_idx):
    B, S = q.shape[0], q.shape[1]
    topk = min(TOPK_MAX, S // 4)
    n_blocks = S // Q_BLOCK
    key_pos = jnp.arange(S)
    idx_scale = (IDX_DIM ** -0.5) * (IDX_HEADS ** -0.5)
    attn_scale = HEAD_DIM ** -0.5
    k_idx32 = k_idx.astype(jnp.float32)

    def block(i):
        start = i * Q_BLOCK
        qb = lax.dynamic_slice_in_dim(q, start, Q_BLOCK, axis=1)
        qib = lax.dynamic_slice_in_dim(q_idx, start, Q_BLOCK, axis=1)
        wib = lax.dynamic_slice_in_dim(w_idx, start, Q_BLOCK, axis=1)
        q_pos = start + jnp.arange(Q_BLOCK)
        logits = jnp.einsum('bthd,bsd->bths', qib.astype(jnp.float32), k_idx32)
        score = jnp.einsum('bth,bths->bts', wib.astype(jnp.float32) * idx_scale, jax.nn.relu(logits))
        causal = key_pos[None, :] <= q_pos[:, None]
        score = jnp.where(causal[None], score, -jnp.inf)
        _, sel = lax.top_k(score, topk)
        k_sel = jax.vmap(lambda kk, ii: kk[ii])(k, sel)
        v_sel = jax.vmap(lambda vv, ii: vv[ii])(v, sel)
        valid = sel <= q_pos[None, :, None]
        att = jnp.einsum('bthd,btkhd->bthk', qb, k_sel).astype(jnp.float32) * attn_scale
        att = jnp.where(valid[:, :, None, :], att, -jnp.inf)
        p = jax.nn.softmax(att, axis=-1).astype(v.dtype)
        return jnp.einsum('bthk,btkhd->bthd', p, v_sel)

    out = lax.map(block, jnp.arange(n_blocks))
    return out.transpose(1, 0, 2, 3, 4).reshape(B, S, ATTN_WIDTH)

def second_inputs(seed: int = 0) -> dict:
    key = jax.random.key(seed)
    ks = jax.random.split(key, 16)
    f32 = jnp.float32
    n = lambda k, shape, scale: jax.random.normal(k, shape, f32) * scale
    return {
        "x": n(ks[0], (BATCH, SEQ, D_MODEL), 1.0),
        "norm1_g": 1.0 + n(ks[1], (DEPTH, D_MODEL), 0.02),
        "w_in": n(ks[2], (DEPTH, D_MODEL, D_IN), D_MODEL ** -0.5),
        "w_s": n(ks[3], (DEPTH, SGU_GROUPS, SGU_CHUNK, SGU_CHUNK), SGU_CHUNK ** -0.5),
        "b_s": 1.0 + n(ks[4], (DEPTH, SGU_GROUPS, SGU_CHUNK), 0.02),
        "sgu_ln_g": 1.0 + n(ks[5], (DEPTH, SGU_WIDTH), 0.02),
        "sgu_ln_b": n(ks[6], (DEPTH, SGU_WIDTH), 0.02),
        "w_out_a": n(ks[7], (DEPTH, SGU_WIDTH, D_MODEL), SGU_WIDTH ** -0.5),
        "w_out_b": n(ks[8], (DEPTH, ATTN_WIDTH, D_MODEL), ATTN_WIDTH ** -0.5),
        "w_o": n(ks[9], (DEPTH, D_MODEL, D_MODEL), D_MODEL ** -0.5),
        "norm2_g": 1.0 + n(ks[10], (DEPTH, D_MODEL), 0.02),
        "w_ff_in": n(ks[11], (DEPTH, D_MODEL, D_FF_2), D_MODEL ** -0.5),
        "w_ff_out": n(ks[12], (DEPTH, D_FF_2, D_MODEL), D_FF_2 ** -0.5),
        "norm_f_g": 1.0 + n(ks[13], (D_MODEL,), 0.02),
    }

def second_block(x, norm1_g, w_in, w_s, b_s, sgu_ln_g, sgu_ln_b, w_out_a, w_out_b, w_o,
              norm2_g, w_ff_in, w_ff_out, norm_f_g):
    B, S, _ = x.shape
    cos, sin = rope_tables(S, HEAD_DIM, x.dtype)
    for layer in range(DEPTH):
        h = rmsnorm_2(x, norm1_g[layer])
        proj = h @ w_in[layer]
        u, v_g, q, k, v, q_idx, k_idx, w_idx, gates = split_cols(proj, IN_SIZES)
        u = jax.nn.gelu(u)
        v_g = jax.nn.gelu(v_g)
        y_a = sgu_mixer(u, v_g, w_s[layer], b_s[layer], sgu_ln_g[layer], sgu_ln_b[layer])
        q = apply_rope(q.reshape(B, S, N_HEADS, HEAD_DIM), cos, sin)
        k = apply_rope(k.reshape(B, S, N_HEADS, HEAD_DIM), cos, sin)
        v = v.reshape(B, S, N_HEADS, HEAD_DIM)
        q_idx = apply_rope(q_idx.reshape(B, S, IDX_HEADS, IDX_DIM), cos, sin)
        k_idx = apply_rope(k_idx[:, :, None, :], cos, sin)[:, :, 0, :]
        y_b = dsa_attention(q, k, v, q_idx, k_idx, w_idx)
        g = jax.nn.sigmoid(gates.reshape(B, S, N_BRANCHES, D_MODEL))
        merged = g[:, :, 0, :] * (y_a @ w_out_a[layer]) + g[:, :, 1, :] * (y_b @ w_out_b[layer])
        x = x + merged @ w_o[layer]
        h2 = rmsnorm_2(x, norm2_g[layer])
        x = x + jnp.square(jax.nn.relu(h2 @ w_ff_in[layer])) @ w_ff_out[layer]
    return rmsnorm_2(x, norm_f_g)


_first_inputs = second_inputs


def second_inputs(seed=0):
    import zlib

    import numpy as np

    out = dict(_first_inputs(seed))
    spreads = {}
    factors = {'norm1_g': 3.518,
     'b_s': 28.215,
     'sgu_ln_g': 37.973,
     'sgu_ln_b': 37.661,
     'norm2_g': 12.602,
     'norm_f_g': 7.541}
    for name, (base, spread) in spreads.items():
        noise = np.random.default_rng([zlib.crc32(name.encode()), seed]).standard_normal(out[name].shape)
        drawn = base * np.exp(spread * noise) if base else spread * noise
        out[name] = __import__('jax').numpy.asarray(drawn.astype(out[name].dtype))
    for name, factor in factors.items():
        out[name] = (out[name] * factor).astype(out[name].dtype)
    return out


_narrow_inputs = second_inputs


def second_inputs(seed=0):

    out = dict(_narrow_inputs(seed))
    wider = {'b_s': 4.14, 'sgu_ln_g': 4.22, 'sgu_ln_b': 4.21, 'norm_f_g': 3.09}
    for name, times in wider.items():
        mean = out[name].mean()
        out[name] = (mean + times * (out[name] - mean)).astype(out[name].dtype)
    return out


N_META = 16
META_PAD = CHUNK - N_META
FOX_HEADS = 8
FOX_HEAD_DIM = 64
FOX_WIDTH = FOX_HEADS * FOX_HEAD_DIM
GDN_HEADS = 8
GDN_HEAD_DIM = 64
GDN_WIDTH = GDN_HEADS * GDN_HEAD_DIM
GDN_CONV = 4
FFN_CONV = 3
IN_SPLITS = (3 * FOX_WIDTH, FOX_HEADS, 3 * GDN_WIDTH, GDN_WIDTH, GDN_HEADS, GDN_HEADS, 2 * D_MODEL)
IN_WIDTH = 3 * FOX_WIDTH + FOX_HEADS + 4 * GDN_WIDTH + 2 * GDN_HEADS + 2 * D_MODEL
RMS_EPS = 1e-6
NEG_INF = -1e30


def rms_norm(x, gain):
    xf = x.astype(jnp.float32)
    y = xf * lax.rsqrt(jnp.mean(xf * xf, axis=-1, keepdims=True) + RMS_EPS)
    return (y * gain.astype(jnp.float32)).astype(x.dtype)

def l2_norm(x):
    return x * lax.rsqrt(jnp.sum(x * x, axis=-1, keepdims=True) + RMS_EPS)

def causal_dwconv(x, w, b=None):
    k_width, ch = w.shape
    y = lax.conv_general_dilated(
        x, w[:, None, :].astype(x.dtype), window_strides=(1,), padding=[(k_width - 1, 0)],
        dimension_numbers=('NWC', 'WIO', 'NWC'), feature_group_count=ch)
    if b is not None:
        y = y + b.astype(x.dtype)
    return y

def split_cols_3(a, sizes):
    idx = []
    acc = 0
    for s in sizes[:-1]:
        acc += s
        idx.append(acc)
    return jnp.split(a, idx, axis=-1)

def forgetting_attention(q, k, v, log_f):
    bn, seq_len, heads, dh = q.shape
    lp = -(-seq_len // Q_BLOCK) * Q_BLOCK
    pad = lp - seq_len
    q, k, v = [jnp.pad(a, ((0, 0), (0, pad), (0, 0), (0, 0))) for a in (q, k, v)]
    c = jnp.cumsum(jnp.pad(log_f, ((0, 0), (0, pad), (0, 0))), axis=1).transpose(0, 2, 1)
    nblk = lp // Q_BLOCK
    qb = q.reshape(bn, nblk, Q_BLOCK, heads, dh).transpose(1, 0, 3, 2, 4)
    cb = c.reshape(bn, heads, nblk, Q_BLOCK).transpose(2, 0, 1, 3)
    kpos = jnp.arange(lp)
    scale = dh ** -0.5

    def block(args):
        q_i, c_i, i = args
        s = jnp.einsum('bhqd,bkhd->bhqk', q_i, k, preferred_element_type=jnp.float32) * scale
        s = s + c_i[..., None] - c[:, :, None, :]
        qpos = i * Q_BLOCK + jnp.arange(Q_BLOCK)
        s = jnp.where(kpos[None, :] <= qpos[:, None], s, NEG_INF)
        p = jax.nn.softmax(s, axis=-1).astype(v.dtype)
        return jnp.einsum('bhqk,bkhd->bqhd', p, v)

    o = lax.map(block, (qb, cb, jnp.arange(nblk)))
    return o.transpose(1, 0, 2, 3, 4).reshape(bn, lp, heads * dh)[:, :seq_len]

def gated_delta_rule(q, k, v, beta, g):
    bn, seq_len, heads, dk = q.shape
    dv = v.shape[-1]
    q = l2_norm(q.astype(jnp.float32)) * (dk ** -0.5)
    k = l2_norm(k.astype(jnp.float32))
    v = v.astype(jnp.float32)
    total = META_PAD + seq_len
    back = (-total) % CHUNK
    total = total + back
    n_chunks = total // CHUNK
    pad4 = ((0, 0), (META_PAD, back), (0, 0), (0, 0))
    pad3 = ((0, 0), (META_PAD, back), (0, 0))
    q, k, v = [jnp.pad(a, pad4).reshape(bn, n_chunks, CHUNK, heads, -1).transpose(0, 3, 1, 2, 4)
               for a in (q, k, v)]
    beta, g = [jnp.pad(a, pad3).reshape(bn, n_chunks, CHUNK, heads).transpose(0, 3, 1, 2)
               for a in (beta, g)]
    gc = jnp.cumsum(g, axis=-1)
    tril = jnp.tril(jnp.ones((CHUNK, CHUNK), dtype=bool))
    strict = jnp.tril(jnp.ones((CHUNK, CHUNK), dtype=bool), -1)
    decay = jnp.exp(jnp.where(tril, gc[..., :, None] - gc[..., None, :], NEG_INF))
    kb = k * beta[..., None]
    vb = v * beta[..., None]
    lmat = jnp.where(strict, jnp.einsum('bhncd,bhnsd->bhncs', kb, k) * decay, 0.0)
    eye = jnp.eye(CHUNK, dtype=jnp.float32)
    rhs = jnp.concatenate([vb, kb * jnp.exp(gc)[..., None]], axis=-1)
    sol = lax.linalg.triangular_solve(lmat + eye, rhs, left_side=True, lower=True, unit_diagonal=True)
    value, k_cumdecay = sol[..., :dv], sol[..., dv:]
    attn_intra = jnp.einsum('bhncd,bhnsd->bhncs', q, k) * decay
    q_dec = q * jnp.exp(gc)[..., None]
    k_tail = k * jnp.exp(gc[..., -1:] - gc)[..., None]
    chunk_decay = jnp.exp(gc[..., -1])

    def step(state, xs):
        value_n, kcd_n, attn_n, qd_n, kt_n, cd_n = xs
        v_new = value_n - jnp.einsum('bhcd,bhdv->bhcv', kcd_n, state)
        o_n = jnp.einsum('bhcd,bhdv->bhcv', qd_n, state) + jnp.einsum('bhcs,bhsv->bhcv', attn_n, v_new)
        state = state * cd_n[..., None, None] + jnp.einsum('bhcd,bhcv->bhdv', kt_n, v_new)
        return state, o_n

    xs = tuple(jnp.moveaxis(a, 2, 0) for a in (value, k_cumdecay, attn_intra, q_dec, k_tail, chunk_decay))
    state0 = jnp.zeros((bn, heads, dk, dv), jnp.float32)
    _, o = lax.scan(step, state0, xs)
    o = o.transpose(1, 0, 3, 2, 4).reshape(bn, total, heads, dv)
    return o[:, META_PAD:META_PAD + seq_len]

def hybrid_mixer(h, w_in, fgt_bias, gdn_conv_w, gdn_a_log, gdn_dt_bias, gdn_norm_w, gate_bias,
                 w_branch_fox, w_branch_gdn, w_out):
    bn, seq_len, _ = h.shape
    proj = h @ w_in.astype(h.dtype)
    fox_qkv, fox_f, gdn_qkv, gdn_z, gdn_b, gdn_a, gates = split_cols_3(proj, IN_SPLITS)
    fox_qkv = fox_qkv.reshape(bn, seq_len, 3, FOX_HEADS, FOX_HEAD_DIM)
    log_f = jax.nn.log_sigmoid(fox_f.astype(jnp.float32) + fgt_bias.astype(jnp.float32))
    o_fox = forgetting_attention(fox_qkv[:, :, 0], fox_qkv[:, :, 1], fox_qkv[:, :, 2], log_f)
    gdn_qkv = jax.nn.silu(causal_dwconv(gdn_qkv, gdn_conv_w))
    gdn_qkv = gdn_qkv.reshape(bn, seq_len, 3, GDN_HEADS, GDN_HEAD_DIM)
    beta = jax.nn.sigmoid(gdn_b.astype(jnp.float32))
    g = -jnp.exp(gdn_a_log.astype(jnp.float32)) * jax.nn.softplus(
        gdn_a.astype(jnp.float32) + gdn_dt_bias.astype(jnp.float32))
    o_gdn = gated_delta_rule(gdn_qkv[:, :, 0], gdn_qkv[:, :, 1], gdn_qkv[:, :, 2], beta, g)
    z = gdn_z.reshape(bn, seq_len, GDN_HEADS, GDN_HEAD_DIM).astype(jnp.float32)
    o_gdn = (rms_norm(o_gdn, gdn_norm_w) * jax.nn.silu(z)).astype(h.dtype).reshape(bn, seq_len, GDN_WIDTH)
    y_fox = o_fox @ w_branch_fox.astype(h.dtype)
    y_gdn = o_gdn @ w_branch_gdn.astype(h.dtype)
    gate = jax.nn.sigmoid(gates.astype(jnp.float32) + gate_bias.astype(jnp.float32)).astype(h.dtype)
    g_fox, g_gdn = gate[..., :D_MODEL], gate[..., D_MODEL:]
    return (g_fox * y_fox + g_gdn * y_gdn) @ w_out.astype(h.dtype)

def conv_ffn_3(h, w_up, conv_w, conv_b, w_down):
    u = causal_dwconv(h @ w_up.astype(h.dtype), conv_w, conv_b)
    gate, up = u[..., :D_FF], u[..., D_FF:]
    return (jax.nn.silu(gate) * up) @ w_down.astype(h.dtype)

def third_inputs(seed: int = 0) -> dict:
    key = jax.random.key(seed)
    ks = jax.random.split(key, 20)
    f32 = jnp.float32

    def nrm(k, shape, scale):
        return jax.random.normal(k, shape, f32) * scale

    dt = jnp.exp(jax.random.uniform(ks[5], (DEPTH, GDN_HEADS), f32, np.log(1e-3), np.log(1e-1)))
    return {
        "x": nrm(ks[0], (BATCH, SEQ, D_MODEL), 1.0),
        "meta_tokens": nrm(ks[1], (N_META, D_MODEL), 1.0),
        "w_in": nrm(ks[2], (DEPTH, D_MODEL, IN_WIDTH), D_MODEL ** -0.5),
        "fgt_bias": 2.0 + nrm(ks[3], (DEPTH, FOX_HEADS), 0.5),
        "gdn_conv_w": nrm(ks[4], (DEPTH, GDN_CONV, 3 * GDN_WIDTH), GDN_CONV ** -0.5),
        "gdn_a_log": jnp.log(jax.random.uniform(ks[6], (DEPTH, GDN_HEADS), f32, 1.0, 16.0)),
        "gdn_dt_bias": dt + jnp.log(-jnp.expm1(-dt)),
        "gdn_norm_w": 1.0 + nrm(ks[7], (DEPTH, GDN_HEAD_DIM), 0.01),
        "gate_bias": nrm(ks[8], (DEPTH, 2 * D_MODEL), 0.01),
        "w_branch_fox": nrm(ks[9], (DEPTH, FOX_WIDTH, D_MODEL), FOX_WIDTH ** -0.5),
        "w_branch_gdn": nrm(ks[10], (DEPTH, GDN_WIDTH, D_MODEL), GDN_WIDTH ** -0.5),
        "w_out": nrm(ks[11], (DEPTH, D_MODEL, D_MODEL), D_MODEL ** -0.5),
        "norm_mix_w": 1.0 + nrm(ks[12], (DEPTH, D_MODEL), 0.01),
        "norm_ffn_w": 1.0 + nrm(ks[13], (DEPTH, D_MODEL), 0.01),
        "ffn_w_up": nrm(ks[14], (DEPTH, D_MODEL, 2 * D_FF), D_MODEL ** -0.5),
        "ffn_conv_w": nrm(ks[15], (DEPTH, FFN_CONV, 2 * D_FF), FFN_CONV ** -0.5),
        "ffn_conv_b": nrm(ks[16], (DEPTH, 2 * D_FF), 0.01),
        "ffn_w_down": nrm(ks[17], (DEPTH, D_FF, D_MODEL), D_FF ** -0.5),
        "norm_final_w": 1.0 + nrm(ks[18], (D_MODEL,), 0.01),
    }

def third_block(x, meta_tokens, w_in, fgt_bias, gdn_conv_w, gdn_a_log, gdn_dt_bias, gdn_norm_w,
              gate_bias, w_branch_fox, w_branch_gdn, w_out, norm_mix_w, norm_ffn_w, ffn_w_up,
              ffn_conv_w, ffn_conv_b, ffn_w_down, norm_final_w):
    bn = x.shape[0]
    meta = jnp.broadcast_to(meta_tokens[None].astype(x.dtype), (bn, N_META, D_MODEL))
    h = jnp.concatenate([meta, x], axis=1)
    for layer in range(DEPTH):
        h = h + hybrid_mixer(rms_norm(h, norm_mix_w[layer]), w_in[layer], fgt_bias[layer],
                             gdn_conv_w[layer], gdn_a_log[layer], gdn_dt_bias[layer],
                             gdn_norm_w[layer], gate_bias[layer], w_branch_fox[layer],
                             w_branch_gdn[layer], w_out[layer])
        h = h + conv_ffn_3(rms_norm(h, norm_ffn_w[layer]), ffn_w_up[layer], ffn_conv_w[layer],
                         ffn_conv_b[layer], ffn_w_down[layer])
    return rms_norm(h, norm_final_w)[:, N_META:]


_first_inputs_3 = third_inputs


def third_inputs(seed=0):
    import zlib

    import numpy as np

    out = dict(_first_inputs_3(seed))
    spreads = {}
    factors = {'gdn_norm_w': 8.0,
     'gate_bias': 8.0,
     'norm_mix_w': 7.61,
     'norm_ffn_w': 7.585,
     'ffn_conv_b': 7.949,
     'norm_final_w': 5.798}
    for name, (base, spread) in spreads.items():
        noise = np.random.default_rng([zlib.crc32(name.encode()), seed]).standard_normal(out[name].shape)
        drawn = base * np.exp(spread * noise) if base else spread * noise
        out[name] = __import__('jax').numpy.asarray(drawn.astype(out[name].dtype))
    for name, factor in factors.items():
        out[name] = (out[name] * factor).astype(out[name].dtype)
    return out


_narrow_inputs_3 = third_inputs


def third_inputs(seed=0):

    out = dict(_narrow_inputs_3(seed))
    wider = {'gdn_norm_w': 4.96,
     'gate_bias': 4.43,
     'norm_ffn_w': 5.23,
     'ffn_conv_b': 5.05,
     'norm_final_w': 6.51}
    for name, times in wider.items():
        mean = out[name].mean()
        out[name] = (mean + times * (out[name] - mean)).astype(out[name].dtype)
    return out


def setup_inputs(seed=0):
    out = dict(first_inputs(seed))
    for name, value in second_inputs(seed + 1).items():
        if name != "x":
            out[name + "_2"] = value
    for name, value in third_inputs(seed + 2).items():
        if name != "x":
            out[name + "_3"] = value
    return out


def reference(
    x, mem, mix_norm_g, w_in, pool_w, pool_scale, rwkv_mu, rwkv_w0, rwkv_w2, rwkv_a0, rwkv_a2,
    rwkv_g2, rwkv_k_k, rwkv_k_a, rwkv_r_k, rwkv_ln_w, rwkv_ln_b, diff_q_norm, diff_k_norm,
    diff_lq1, diff_lk1, diff_lq2, diff_lk2, diff_subln, w_out, xa_norm_g, mem_norm_g, xa_wq,
    xa_wk, xa_wv, xa_wo, xa_q_norm, xa_k_norm, ffn_norm_g, ffn_w_up, ffn_conv_w, ffn_conv_b,
    ffn_w_down, norm1_g_2, w_in_2, w_s_2, b_s_2, sgu_ln_g_2, sgu_ln_b_2, w_out_a_2, w_out_b_2,
    w_o_2, norm2_g_2, w_ff_in_2, w_ff_out_2, norm_f_g_2, meta_tokens_3, w_in_3, fgt_bias_3,
    gdn_conv_w_3, gdn_a_log_3, gdn_dt_bias_3, gdn_norm_w_3, gate_bias_3, w_branch_fox_3,
    w_branch_gdn_3, w_out_3, norm_mix_w_3, norm_ffn_w_3, ffn_w_up_3, ffn_conv_w_3, ffn_conv_b_3,
    ffn_w_down_3, norm_final_w_3,
):
    x = first_block(
        x, mem, mix_norm_g, w_in, pool_w, pool_scale, rwkv_mu, rwkv_w0, rwkv_w2, rwkv_a0,
        rwkv_a2, rwkv_g2, rwkv_k_k, rwkv_k_a, rwkv_r_k, rwkv_ln_w, rwkv_ln_b, diff_q_norm,
        diff_k_norm, diff_lq1, diff_lk1, diff_lq2, diff_lk2, diff_subln, w_out, xa_norm_g,
        mem_norm_g, xa_wq, xa_wk, xa_wv, xa_wo, xa_q_norm, xa_k_norm, ffn_norm_g, ffn_w_up,
        ffn_conv_w, ffn_conv_b, ffn_w_down,
    )
    x = second_block(
        x, norm1_g_2, w_in_2, w_s_2, b_s_2, sgu_ln_g_2, sgu_ln_b_2, w_out_a_2, w_out_b_2, w_o_2,
        norm2_g_2, w_ff_in_2, w_ff_out_2, norm_f_g_2,
    )
    return third_block(
        x, meta_tokens_3, w_in_3, fgt_bias_3, gdn_conv_w_3, gdn_a_log_3, gdn_dt_bias_3,
        gdn_norm_w_3, gate_bias_3, w_branch_fox_3, w_branch_gdn_3, w_out_3, norm_mix_w_3,
        norm_ffn_w_3, ffn_w_up_3, ffn_conv_w_3, ffn_conv_b_3, ffn_w_down_3, norm_final_w_3,
    )


_drawn_inputs = setup_inputs


def setup_inputs(seed=0):
    import zlib

    import numpy as np

    out = dict(_drawn_inputs(seed))
    spreads = {}
    factors = {'xa_norm_g': 4.752, 'mem_norm_g': 3.297, 'xa_q_norm': 3.771, 'xa_k_norm': 4.059}
    for name, (base, spread) in spreads.items():
        noise = np.random.default_rng([zlib.crc32(name.encode()), seed]).standard_normal(out[name].shape)
        drawn = base * np.exp(spread * noise) if base else spread * noise
        out[name] = __import__('jax').numpy.asarray(drawn.astype(out[name].dtype))
    for name, factor in factors.items():
        out[name] = (out[name] * factor).astype(out[name].dtype)
    return out
```

```python
from contextlib import ExitStack, contextmanager

import numpy as np

import concourse.bass as bass
from concourse import mybir

F32 = mybir.dt.float32
ALU = mybir.AluOpType
ACT = mybir.ActivationFunctionType
AX = mybir.AxisListType.X

P = 128
D = 1024
KT = D // P
S = 512
META = 16
T3 = S + META
MEM = 256
FF = 2816
FT = FF // P
FF2 = 4096
CH = 64
NCH = S // CH
HD = 64
C3 = 88
NC3 = T3 // C3
SLOTS = 8
EPS = 1e-6
GN_EPS = 64e-5
LAMBDA_INIT = 0.2
SUBLN = (1.0 - LAMBDA_INIT) ** -2
TOPK = 128
NEG = -1.0e30
LOWEST = -3.0e38
HALVES = [(0, T3 // 2), (T3 // 2, T3)]

VEC_COLS = {}


def _vec(name, n):
    VEC_COLS[name] = (sum(c for _, c in VEC_COLS.values()), n)


for _n, _c in [("mix_norm_g", KT), ("pool_scale", 2), ("rwkv_mu", 8), ("rwkv_w0", 2), ("rwkv_a0", 2),
               ("rwkv_k_k", 2), ("rwkv_k_a", 2), ("rwkv_r_k", 2), ("rwkv_ln_w", 2), ("rwkv_ln_b", 2),
               ("diff_q_norm", 1), ("diff_k_norm", 1), ("diff_subln", 1), ("xa_norm_g", KT),
               ("mem_norm_g", KT), ("xa_q_norm", 2), ("xa_k_norm", 2), ("ffn_norm_g", KT),
               ("ffn_conv_w", 3 * FT), ("ffn_conv_b", FT),
               ("norm1_g_2", KT), ("norm2_g_2", KT), ("norm_f_g_2", KT),
               ("fgt_bias_3", 1), ("gdn_a_log_3", 1), ("gdn_dt_bias_3", 1), ("gdn_conv_w_3", 4 * 12),
               ("gdn_norm_w_3", 1), ("gate_bias_3", 16), ("norm_mix_w_3", KT), ("norm_ffn_w_3", KT),
               ("ffn_conv_w_3", 3 * 2 * FT), ("ffn_conv_b_3", 2 * FT), ("norm_final_w_3", KT)]:
    _vec(_n, _c)
NVEC = sum(c for _, c in VEC_COLS.values())

LEVELS_R = 6
LEVELS_G = 7


def shape_constants():
    i = np.arange(P)
    ident = np.eye(P)
    ones = np.ones((P, P))
    blk = (i[:, None] // HD == i[None, :] // HD) * 1.0
    half = HD // 2
    rot = np.zeros((P, P))
    for p in range(P):
        if p % HD < half:
            rot[p + half, p] = -1.0
        else:
            rot[p - half, p] = 1.0
    upper = (i[:, None] <= i[None, :]) * 1.0
    sq = np.concatenate([ident, ones, blk, rot, upper], axis=1)

    def level(n, l):
        a = np.arange(n)
        return ((a[:, None] >> (l + 1) == a[None, :] >> (l + 1)) & (a[:, None] >> l & 1 == 1)
                & (a[None, :] >> l & 1 == 0)) * 1.0

    lr = np.zeros((P, LEVELS_R + 5, CH))
    c = np.arange(CH)
    for l in range(LEVELS_R):
        lr[:CH, l] = level(CH, l)
    lr[:CH, LEVELS_R] = level(CH, 0).T
    lr[:CH, LEVELS_R + 1] = np.eye(CH)
    lr[:CH, LEVELS_R + 2] = c[:, None] > c[None, :]
    lr[:CH, LEVELS_R + 3] = c[:, None] < c[None, :]
    lr[:CH, LEVELS_R + 4] = c[:, None] <= c[None, :]
    lg = np.zeros((P, LEVELS_G + 5, C3))
    c = np.arange(C3)
    for l in range(LEVELS_G):
        lg[:C3, l] = level(C3, l)
    lg[:C3, LEVELS_G] = level(C3, 0).T
    lg[:C3, LEVELS_G + 1] = np.eye(C3)
    lg[:C3, LEVELS_G + 2] = c[:, None] > c[None, :]
    lg[:C3, LEVELS_G + 3] = c[:, None] < c[None, :]
    lg[:C3, LEVELS_G + 4] = c[:, None] <= c[None, :]
    t = np.arange(S)
    win = np.array([2, 4, 8, 16])[(np.arange(256) // 64)]
    recip_count = (1.0 / np.minimum(t[None, :] + 1, win[:, None])).reshape(2, P, S).transpose(1, 0, 2)
    chunk_keep = np.broadcast_to((t % CH != 0) * 1.0, (P, S))
    gdn_keep = np.broadcast_to((np.arange(T3) % C3 != 0) * 1.0, (P, T3))
    j = np.arange(S) - 3 * P
    dist = np.abs(i[:, None] - j[None, :]).astype(np.float64)
    dist[(j[None, :] // 64) > (i[:, None] // 64)] = 1.0e32
    pos = np.arange(S, dtype=np.float32)
    inv = np.float32(10000.0) ** (-np.arange(0, HD, 2, dtype=np.float32) / np.float32(HD))
    ang = (pos[None, :] * inv[:, None]).astype(np.float32)
    cos, sin = (np.tile(f(ang), (4, 1)) for f in (np.cos, np.sin))
    causal = np.where(i[None, :] <= i[:, None], 0.0, NEG)
    causal88 = np.zeros((P, 2 * C3))
    causal88[:C3, :C3] = np.where(np.arange(C3)[None, :] <= np.arange(C3)[:, None], 0.0, NEG)
    parts = {"c_square": sq, "c_levels_r": lr, "c_levels_g": lg, "c_recip_count": recip_count,
             "c_chunk_keep": chunk_keep, "c_gdn_keep": gdn_keep, "c_dist": dist, "c_cos": cos, "c_sin": sin,
             "c_causal": causal, "c_causal88": causal88}
    return {k: np.ascontiguousarray(v, dtype=np.float32) for k, v in parts.items()}


class Slabs:

    def __init__(self, nc, ctx, stream, total):
        self.ring = ctx.enter_context(nc.sbuf_tensor("ring", [P, SLOTS, D], F32))
        self.loaded = [ctx.enter_context(nc.semaphore(f"slab_loaded_{j}")) for j in range(SLOTS)]
        self.used = ctx.enter_context(nc.semaphore("slabs_used"))
        self.stream, self.total, self.n = stream, total, 0

    def slot(self, n):
        return self.ring[:, n % SLOTS, :]

    def wait_loaded(self, eng, n, turn=0):
        eng.wait_ge(self.loaded[n % SLOTS], turn * 16 + 16 * (n // SLOTS + 1))

    def first(self, sp):
        for n in range(SLOTS):
            sp.dma_start(self.slot(n), self.stream[n]).then_inc(self.loaded[n], 16)

    def refill(self, sp, first, count):
        count = min(count, self.total - SLOTS - first)
        turns = count // SLOTS
        if turns > 1:
            with sp.Fori(0, turns) as turn:
                for j in range(SLOTS):
                    n = first + j
                    sp.wait_ge(self.used, turn * SLOTS + (n + 1))
                    sp.dma_start(self.ring[:, n % SLOTS:n % SLOTS + 1, :],
                                 self.stream[bass.ds(turn * SLOTS + (n + SLOTS), 1)].rearrange("o p n -> p o n")
                                 ).then_inc(self.loaded[n % SLOTS], 16)
        else:
            turns = 0
        for n in range(first + turns * SLOTS, first + count):
            sp.wait_ge(self.used, n + 1)
            sp.dma_start(self.slot(n), self.stream[n + SLOTS]).then_inc(self.loaded[n % SLOTS], 16)


class Chain:

    def __init__(self, eng, sem):
        self.eng, self.sem, self.n = eng, sem, 0

    def __call__(self, ins):
        self.n += 1
        ins.then_inc(self.sem, 1)
        self.eng.wait_ge(self.sem, self.n)


class Core:

    def __init__(self, nc, ctx, stream, total):
        self.nc, self.ctx = nc, ctx
        self.ps = ctx.enter_context(nc.psum_tensor("ps", [P, 8, 512], F32))
        self.slabs = Slabs(nc, ctx, stream, total)
        self.vecs = ctx.enter_context(nc.sbuf_tensor("vecs", [P, NVEC], F32))
        self.sq = ctx.enter_context(nc.sbuf_tensor("square_constants", [P, 5 * P], F32))
        self.h = ctx.enter_context(nc.sbuf_tensor("h", [P, KT, T3], F32))
        self.xn = ctx.enter_context(nc.sbuf_tensor("xn", [P, KT, T3], F32))
        self.eps = ctx.enter_context(nc.sbuf_tensor("eps", [P, 6], F32))
        self.ident, self.ones, self.blk, self.rot, self.upper = (self.sq[:, n * P:(n + 1) * P] for n in range(5))
        self.eps_col, self.gn_eps_col, self.one_col = self.eps[:, 0:1], self.eps[:, 1:2], self.eps[:, 2:3]
        self.eps_times = {1: self.eps_col, HD: self.eps[:, 3:4], 4 * HD: self.eps[:, 4:5], SUBLN: self.eps[:, 5:6]}
        self.count, self.in_use, self.cleared = 0, [], []

    def sem(self, name):
        self.count += 1
        self.in_use.append(self.nc.alloc_semaphore(name=f"{name}_{self.count}"))
        return self.in_use[-1]

    @contextmanager
    def stage(self):
        with self.nc.Block() as block:
            yield block
        for s in self.cleared:
            self.nc.release_semaphore(s)
        for s in self.in_use:
            self.nc.sync.sem_clear(s)
        self.cleared, self.in_use = self.in_use, []

    def vec(self, name, n=0):
        c = VEC_COLS[name][0] + n
        return self.vecs[:, c:c + 1]

    def pick(self, h, n):
        return self.ident[0:8, h:h + 1].to_broadcast((8, n))

    def buf(self, ctx, name, shape):
        self.count += 1
        return ctx.enter_context(self.nc.sbuf_tensor(f"{name}_{self.count}", shape, F32))


def load_stage(K, ins):
    nc = K.nc
    arrived, set_up = K.sem("inputs_arrived"), K.sem("eps_set")
    with K.stage() as block:
        @block.sync
        def _(sp):
            sp.dma_start(K.h[:, :, 0:S], ins["x"]).then_inc(arrived, 16)
            sp.dma_start(K.sq[:], ins["c_square"]).then_inc(arrived, 16)
            sp.dma_start(K.vecs[:], ins["vecs"]).then_inc(arrived, 16)
            K.slabs.first(sp)
            sp.wait_ge(arrived, 48)

        @block.vector
        def _(dve):
            nc.vector.memset(K.eps[:, 0:1], EPS).then_inc(set_up, 1)
            nc.vector.memset(K.eps[:, 1:2], GN_EPS).then_inc(set_up, 1)
            nc.vector.memset(K.eps[:, 2:3], 1.0).then_inc(set_up, 1)
            nc.vector.memset(K.eps[:, 3:4], EPS * HD).then_inc(set_up, 1)
            nc.vector.memset(K.eps[:, 4:5], EPS * 4 * HD).then_inc(set_up, 1)
            nc.vector.memset(K.eps[:, 5:6], EPS * SUBLN).then_inc(set_up, 1)


def norm_stage(K, src, dst, gain, cols):
    nc = K.nc
    lo0, hi0 = cols[0][0], cols[-1][1]
    with ExitStack() as local:
        square = K.buf(local, "norm_square", [P, KT, hi0 - lo0])
        rstd = K.buf(local, "norm_rstd", [P, hi0 - lo0])
        squared, summed, rooted, chain = (K.sem(n) for n in ("squared", "summed", "rooted", "norm_chain"))
        with K.stage() as block:
            @block.scalar
            def _(act):
                for k in range(KT):
                    nc.scalar.activation(square[:, k, :], src(k)[:, lo0:hi0], ACT.Square).then_inc(squared, 1)
                act.wait_ge(summed, 1)
                for c, (lo, hi) in enumerate(cols):
                    nc.scalar.activation(rstd[:, lo - lo0:hi - lo0], K.ps[:, c, 0:hi - lo], ACT.Sqrt,
                                         bias=K.eps_col, scale=1.0 / D).then_inc(rooted, 1)

            @block.tensor
            def _(pe):
                for k in range(KT):
                    pe.wait_ge(squared, k + 1)
                    for c, (lo, hi) in enumerate(cols):
                        last = nc.tensor.matmul(K.ps[:, c, 0:hi - lo], K.ones, square[:, k, lo - lo0:hi - lo0],
                                                start=k == 0, stop=k == KT - 1)
                last.then_inc(summed, 1)

            @block.vector
            def _(dve):
                link = Chain(dve, chain)
                dve.wait_ge(rooted, len(cols))
                link(nc.vector.reciprocal(rstd[:], rstd[:]))
                for k in range(KT):
                    nc.vector.scalar_tensor_tensor(out=dst(k)[:, lo0:hi0], in0=src(k)[:, lo0:hi0],
                                                   scalar=K.vec(gain, k), in1=rstd[:],
                                                   op0=ALU.mult, op1=ALU.mult)


class Group:

    def __init__(self, K, banks, slabs, filled, first=None, filled_before=0):
        self.K, self.banks, self.slabs, self.filled = K, banks, slabs, filled
        self.n0 = K.slabs.n if first is None else first
        self.before = filled_before

    def bank_ready(self, eng, b, turn=0):
        if b < self.banks - 1:
            eng.wait_ge(self.filled, turn * (self.banks - 1) + (self.before + b + 1))
        else:
            eng.wait_ge(self.K.slabs.used, turn * self.slabs + (self.n0 + self.slabs))

    def products(self, pe, product, drained=None, turn=0):
        for j in range(self.slabs):
            self.K.slabs.wait_loaded(pe, self.n0 + j, turn)
            for b in range(self.banks):
                if j == 0 and drained is not None:
                    drained(pe, b)
                mm = product(j, b, j == 0, j == self.slabs - 1)
                if b == self.banks - 1:
                    mm.then_inc(self.K.slabs.used, 1)
                elif j == self.slabs - 1:
                    mm.then_inc(self.filled, 1)


def residual_stage(K, rhs, slabs, cols=(0, S), dst=None):
    nc, (lo, hi) = K.nc, cols
    dst = dst or (lambda m: K.h[:, m, lo:hi])
    filled = K.sem("out_filled")
    group = Group(K, KT, slabs, filled)
    K.slabs.n += slabs
    with K.stage() as block:
        @block.sync
        def _(sp):
            K.slabs.refill(sp, group.n0, slabs)

        @block.tensor
        def _(pe):
            group.products(pe, lambda j, b, start, stop: nc.tensor.matmul(
                K.ps[:, b, 0:hi - lo], K.slabs.slot(group.n0 + j)[:, b * P:(b + 1) * P], rhs(j), start=start, stop=stop))

        @block.vector
        def _(dve):
            for m in range(KT):
                group.bank_ready(dve, m)
                nc.vector.tensor_tensor(dst(m), K.ps[:, m, 0:hi - lo], dst(m), ALU.add)


def project_stage(K, dst, rhs, cols):
    nc = K.nc
    filled = K.sem("projection_filled")
    group = Group(K, KT, KT, filled)
    K.slabs.n += KT
    with K.stage() as block:
        @block.sync
        def _(sp):
            K.slabs.refill(sp, group.n0, KT)

        @block.tensor
        def _(pe):
            group.products(pe, lambda j, b, start, stop: nc.tensor.matmul(
                K.ps[:, b, 0:cols], K.slabs.slot(group.n0 + j)[:, b * P:(b + 1) * P], rhs(j), start=start, stop=stop))

        @block.scalar
        def _(act):
            for m in range(KT):
                group.bank_ready(act, m)
                nc.scalar.activation(dst(m), K.ps[:, m, 0:cols], ACT.Copy)


def token_major_stage(K, dst, lhs, tiles):
    nc = K.nc
    filled = K.sem("token_major_filled")
    group = Group(K, 2 * tiles, KT, filled)
    K.slabs.n += KT
    with K.stage() as block:
        @block.sync
        def _(sp):
            K.slabs.refill(sp, group.n0, KT)

        @block.tensor
        def _(pe):
            group.products(pe, lambda j, b, start, stop: nc.tensor.matmul(
                K.ps[:, b, :], lhs(j, b // 2), K.slabs.slot(group.n0 + j)[:, (b % 2) * 512:(b % 2 + 1) * 512],
                start=start, stop=stop))

        @block.scalar
        def _(act):
            for b in range(2 * tiles):
                group.bank_ready(act, b)
                nc.scalar.activation(dst(b // 2, b % 2), K.ps[:, b, :], ACT.Copy)


def mix_in_stage(K, pool_u, rwkv_z, diff_qk, diff_v):
    nc = K.nc
    filled, drained = K.sem("z_filled"), K.sem("z_drained")
    g0 = Group(K, 8, KT, filled)
    g1 = Group(K, 8, KT, filled, g0.n0 + KT, 7)
    g2 = Group(K, 6, KT, filled, g0.n0 + 2 * KT, 14)
    K.slabs.n += 3 * KT

    def place(i):
        if i < 2:
            return pool_u[:, i, 16:16 + S]
        if i < 10:
            return rwkv_z[:, i - 2, 1:1 + S]
        return diff_qk[:, i - 10, :]

    with K.stage() as block:
        @block.sync
        def _(sp):
            K.slabs.refill(sp, g0.n0, 3 * KT)

        @block.tensor
        def _(pe):
            def features(g):
                return lambda j, b, start, stop: nc.tensor.matmul(
                    K.ps[:, b, :], K.slabs.slot(g.n0 + j)[:, b * P:(b + 1) * P], K.xn[:, j, 0:S],
                    start=start, stop=stop)

            def last(j, b, start, stop):
                if b < 2:
                    return features(g2)(j, b, start, stop)
                return nc.tensor.matmul(K.ps[:, b, :], K.xn[:, j, (b - 2) * P:(b - 1) * P],
                                        K.slabs.slot(g2.n0 + j)[:, 2 * P:2 * P + 512], start=start, stop=stop)

            g0.products(pe, features(g0))
            g1.products(pe, features(g1), lambda e, b: e.wait_ge(drained, b + 1))
            g2.products(pe, last, lambda e, b: e.wait_ge(drained, 8 + b + 1))

        @block.scalar
        def _(act):
            for g, group in enumerate((g0, g1, g2)):
                for b in range(group.banks):
                    group.bank_ready(act, b)
                    to = place(8 * g + b) if 8 * g + b < 18 else diff_v[:, b - 2, :]
                    nc.scalar.activation(to, K.ps[:, b, :], ACT.Copy).then_inc(drained, 1)

        @block.vector
        def _(dve):
            nc.vector.memset(pool_u[:, :, 0:16], 0.0)
            nc.vector.memset(rwkv_z[:, :, 0:1], 0.0)


def pool_stage(K, pool_u, y, ins):
    nc = K.nc
    with ExitStack() as local:
        recip = K.buf(local, "pool_recip", [P, 2, S])
        w = K.buf(local, "pool_w", [P, 2, P])
        sums = K.buf(local, "pool_sums", [P, 2, 2, 16 + S])
        diff = K.buf(local, "pool_diff", [P, 2, S])
        arrived, chain, ready, filled = (K.sem(n) for n in ("pool_arrived", "pool_chain", "pool_ready", "pool_filled"))
        with K.stage() as block:
            @block.sync
            def _(sp):
                sp.dma_start(recip[:], ins["c_recip_count"]).then_inc(arrived, 16)
                sp.dma_start(w[:], ins["pool_w"]).then_inc(arrived, 16)

            @block.vector
            def _(dve):
                link = Chain(dve, chain)
                src = pool_u
                link(nc.vector.memset(sums[:, :, :, 0:16], 0.0))
                dve.wait_ge(arrived, 32)
                for n, shift in enumerate((1, 2, 4, 8)):
                    s = sums[:, n % 2]
                    link(nc.vector.tensor_tensor(s[:, :, 16:16 + S], src[:, :, 16:16 + S],
                                                 src[:, :, 16 - shift:16 - shift + S], ALU.add))
                    part, tile = (n % 2) * HD, n // 2
                    rows = slice(part, part + HD)
                    link(nc.vector.tensor_tensor(diff[rows, tile, :], s[rows, tile, 16:16 + S], recip[rows, tile, :], ALU.mult))
                    src = s
                nc.vector.tensor_tensor(diff[:], diff[:], pool_u[:, :, 16:16 + S], ALU.subtract).then_inc(ready, 1)
                for t in range(2):
                    dve.wait_ge(filled, t + 1)
                    nc.vector.tensor_scalar(y[:, t, :], K.ps[:, t, :], K.vec("pool_scale", t), None, ALU.mult)

            @block.tensor
            def _(pe):
                pe.wait_ge(ready, 1)
                pe.wait_ge(arrived, 32)
                for t in range(2):
                    nc.tensor.matmul(K.ps[:, t, :], w[:, t, :], diff[:, t, :], start=True, stop=True).then_inc(filled, 1)


def rwkv_prepare_stage(K, z, zm, V, ins):
    nc = K.nc
    (gate, a_t, b_t, k_t, r_t, bonus, p_end) = V
    with ExitStack() as local:
        lora = K.buf(local, "rwkv_lora", [P, 2, 256])
        keep = K.buf(local, "rwkv_keep", [P, S])
        diff = K.xn[:, :, 0:S]
        tanh_w = K.buf(local, "rwkv_tanh", [P, S])
        sig_g = K.buf(local, "rwkv_sig_g", [P, S])
        logw, iclr, kk, cum, p_now, p_before, p_inv, k2 = (
            K.buf(local, n, [P, 2, S]) for n in ("logw", "iclr", "kk", "cum", "p_now", "p_before", "p_inv", "k2"))
        arrived, mixed, gates_in, filled, sig_ready, kk_sq, kk_sum, kk_root, cum_ready, less_ready, decays, chain, \
            rk_ready, rk_sum = (K.sem(n) for n in (
                "rwkv_arrived", "mixed", "gates_in", "lora_filled", "sig_ready", "kk_sq", "kk_sum", "kk_root",
                "cum_ready", "less_ready", "decays", "rwkv_chain", "rk_ready", "rk_sum"))
        with K.stage() as block:
            @block.sync
            def _(sp):
                sp.dma_start(lora[:], ins["rwkv_lora"]).then_inc(arrived, 16)
                sp.dma_start(keep[:], ins["c_chunk_keep"]).then_inc(arrived, 16)

            @block.vector
            def _(dve):
                link = Chain(dve, chain)
                link(nc.vector.tensor_tensor(diff, z[:, :, 0:S], z[:, :, 1:1 + S], ALU.subtract))
                for i in (6, 7, 0, 1, 2, 3, 4, 5):
                    nc.vector.scalar_tensor_tensor(out=zm[:, i, :], in0=diff[:, i, :], scalar=K.vec("rwkv_mu", i),
                                                   in1=z[:, i, 1:1 + S], op0=ALU.mult, op1=ALU.add).then_inc(mixed, 1)
                dve.wait_ge(mixed, 8)
                r, k, v = zm[:, 0:2, :], zm[:, 2:4, :], zm[:, 4:6, :]
                for t in range(2):
                    link(nc.vector.tensor_scalar(kk[:, t, :], k[:, t, :], K.vec("rwkv_k_k", t), None, ALU.mult))
                nc.vector.tensor_tensor(k2[:], kk[:], kk[:], ALU.mult).then_inc(kk_sq, 1)
                dve.wait_ge(kk_root, 2)
                link(nc.vector.tensor_scalar(p_inv[:], p_inv[:], 1e-12, None, ALU.max))
                link(nc.vector.reciprocal(p_inv[:], p_inv[:]))
                link(nc.vector.tensor_tensor(kk[:], kk[:], p_inv[:], ALU.mult))
                dve.wait_ge(sig_ready, 2)
                dve.wait_ge(arrived, 32)
                link(nc.vector.tensor_scalar(logw[:], logw[:], -float(np.exp(-0.5)), None, ALU.mult))
                for t in range(2):
                    nc.vector.tensor_tensor_scan(cum[:, t, :], keep[:], logw[:, t, :], 0.0, ALU.mult, ALU.add).then_inc(cum_ready, 1)
                dve.wait_ge(cum_ready, 2)
                nc.vector.tensor_tensor(p_before[:], cum[:], logw[:], ALU.subtract).then_inc(less_ready, 1)
                dve.wait_ge(sig_ready, 4)
                for t in range(2):
                    link(nc.vector.tensor_scalar(k2[:, t, :], iclr[:, t, :], -1.0, K.vec("rwkv_k_a", t), ALU.add, ALU.mult))
                    link(nc.vector.scalar_tensor_tensor(out=k2[:, t, :], in0=k2[:, t, :], scalar=1.0, in1=k[:, t, :],
                                                        op0=ALU.add, op1=ALU.mult))
                    nc.vector.scalar_tensor_tensor(out=diff[:, t, :], in0=r[:, t, :], scalar=K.vec("rwkv_r_k", t),
                                                   in1=k2[:, t, :], op0=ALU.mult, op1=ALU.mult).then_inc(rk_ready, 1)
                link(nc.vector.tensor_tensor(b_t[:], kk[:], iclr[:], ALU.mult))
                dve.wait_ge(decays, 3)
                nc.vector.scalar_tensor_tensor(out=a_t[:], in0=kk[:], scalar=-1.0, in1=p_before[:], op0=ALU.mult, op1=ALU.mult)
                nc.vector.tensor_tensor(b_t[:], b_t[:], p_inv[:], ALU.mult)
                nc.vector.tensor_tensor(k_t[:], k2[:], p_inv[:], ALU.mult)
                nc.vector.tensor_tensor(r_t[:], r, p_now[:], ALU.mult)
                nc.vector.tensor_copy(p_end[:], p_now[:].rearrange("p t (c i) -> p t c i", i=CH)[:, :, :, CH - 1])
                for t in range(2):
                    dve.wait_ge(rk_sum, t + 1)
                    nc.vector.tensor_tensor(bonus[:, t, :], K.ps[:, t, :], v[:, t, :], ALU.mult)

            @block.scalar
            def _(act):
                act.wait_ge(mixed, 2)
                nc.scalar.activation(tanh_w[0:64, :], zm[0:64, 6, :], ACT.Tanh).then_inc(gates_in, 1)
                nc.scalar.activation(sig_g[:], zm[:, 7, :], ACT.Sigmoid).then_inc(gates_in, 1)
                for t in range(2):
                    act.wait_ge(filled, t + 1)
                    nc.scalar.activation(logw[:, t, :], K.ps[:, t, :], ACT.Sigmoid, bias=K.vec("rwkv_w0", t)).then_inc(sig_ready, 1)
                for t in range(2):
                    act.wait_ge(filled, 2 + t + 1)
                    nc.scalar.activation(iclr[:, t, :], K.ps[:, 2 + t, :], ACT.Sigmoid, bias=K.vec("rwkv_a0", t)).then_inc(sig_ready, 1)
                for t in range(2):
                    act.wait_ge(filled, 4 + t + 1)
                    nc.scalar.activation(gate[:, t, :], K.ps[:, 4 + t, :], ACT.Copy)
                for t in range(2):
                    act.wait_ge(kk_sum, t + 1)
                    nc.scalar.activation(p_inv[:, t, :], K.ps[:, 6 + t, :], ACT.Sqrt).then_inc(kk_root, 1)
                act.wait_ge(cum_ready, 2)
                nc.scalar.activation(p_now[:], cum[:], ACT.Exp).then_inc(decays, 1)
                act.wait_ge(less_ready, 1)
                nc.scalar.activation(p_before[:], p_before[:], ACT.Exp).then_inc(decays, 1)
                nc.scalar.activation(p_inv[:], cum[:], ACT.Exp, scale=-1.0).then_inc(decays, 1)

            @block.tensor
            def _(pe):
                pe.wait_ge(arrived, 32)
                pe.wait_ge(gates_in, 2)
                for t in range(2):
                    nc.tensor.matmul(K.ps[:, t, :], lora[0:64, 0, t * P:(t + 1) * P], tanh_w[0:64, :], start=True, stop=True).then_inc(filled, 1)
                for t in range(2):
                    nc.tensor.matmul(K.ps[:, 2 + t, :], lora[64:128, 0, t * P:(t + 1) * P], zm[64:128, 6, :], start=True, stop=True).then_inc(filled, 1)
                for t in range(2):
                    nc.tensor.matmul(K.ps[:, 4 + t, :], lora[:, 1, t * P:(t + 1) * P], sig_g[:], start=True, stop=True).then_inc(filled, 1)
                pe.wait_ge(kk_sq, 1)
                for t in range(2):
                    nc.tensor.matmul(K.ps[:, 6 + t, :], K.blk, k2[:, t, :], start=True, stop=True).then_inc(kk_sum, 1)
                pe.wait_ge(sig_ready, 2)
                for t in range(2):
                    pe.wait_ge(rk_ready, t + 1)
                    nc.tensor.matmul(K.ps[:, t, :], K.blk, diff[:, t, :], start=True, stop=True).then_inc(rk_sum, 1)


def token_tiles_stage(K, jobs, rows, tiles):
    nc = K.nc
    ready, drained = K.sem("turned"), K.sem("turned_out")
    lots = [(src, place, t, min(4, tiles - t)) for src, place in jobs for t in range(0, tiles, 4)]
    with K.stage() as block:
        @block.tensor
        def _(pe):
            for n, (src, place, t0, k) in enumerate(lots):
                if n >= 8:
                    pe.wait_ge(drained, n - 7)
                for i in range(k):
                    last = nc.tensor.transpose(K.ps[0:rows, n % 8, i * P:(i + 1) * P],
                                               src[:, (t0 + i) * rows:(t0 + i + 1) * rows], K.ident)
                last.then_inc(ready, 1)

        @block.scalar
        def _(act):
            for n, (src, place, t0, k) in enumerate(lots):
                act.wait_ge(ready, n + 1)
                nc.scalar.activation(place(t0, k), K.ps[0:rows, n % 8, 0:k * P].rearrange("p (i c) -> p i c", c=P),
                                     ACT.Copy).then_inc(drained, 1)


def rwkv_chunk_stage(K, V, tok, out, ins):
    nc = K.nc
    (_, a_t, b_t, k_t, r_t, _, _) = V
    (a_tok, v_tok) = tok
    (x1, x2, rb, rk) = out
    H = 4
    with ExitStack() as local:
        masks_in = K.buf(local, "rwkv_masks", [CH, LEVELS_R + 5, CH])
        inv, invT = (K.buf(local, n, [CH, H, NCH, CH]) for n in ("rwkv_inv", "rwkv_invT"))
        spare = K.xn[:].rearrange("p k t -> p (k t)")
        amat, prod = (spare[0:CH, n * H * S:(n + 1) * H * S].rearrange("p (h c i) -> p h c i", h=H, c=NCH) for n in range(2))
        amask = K.buf(local, "rwkv_A_level", [CH, 2, NCH, CH])
        akT = K.buf(local, "rwkv_akT", [CH, 2, NCH, CH])
        arrived, filled, chain, masked, z_filled, z_out, d_filled, d_added, drained = (K.sem(n) for n in (
            "masks_arrived", "pairs_filled", "chunk_chain", "level_masked", "z_filled", "z_out", "d_filled", "d_added", "pairs_out"))
        w_filled, w_out, x_filled, x_out = (K.sem(n) for n in ("w_filled", "w_out", "x_filled", "x_out"))
        masks = [masks_in[:, n:n + 1, :].to_broadcast((CH, NCH, CH)) for n in range(LEVELS_R + 5)]
        m_strict, m_strictT, m_lowerT = (masks[LEVELS_R + 2 + i] for i in range(3))
        m_first, m_firstT, m_eye = masks[0], masks[LEVELS_R], masks[LEVELS_R + 1]

        def head(t, h, c):
            return t[(h % 2) * HD:(h % 2 + 1) * HD, h // 2, c * CH:(c + 1) * CH]

        def bank(b):
            return K.ps[0:CH, b, :].rearrange("p (c i) -> p c i", i=CH)

        pairs = ((a_t, b_t), (b_t, a_t), (k_t, a_t), (b_t, r_t), (k_t, r_t))
        with K.stage() as block:
            @block.sync
            def _(sp):
                sp.dma_start(masks_in[:], ins["c_levels_r"]).then_inc(arrived, 16)

            @block.tensor
            def _(pe):
                for h in range(H):
                    for n, (lhs, rhs) in enumerate(pairs):
                        at = 5 * h + n
                        if at >= 8:
                            pe.wait_ge(drained, at - 7)
                        for c in range(NCH):
                            last = nc.tensor.matmul(bank(at % 8)[:, c, :], head(lhs, h, c), head(rhs, h, c), start=True, stop=True)
                        last.then_inc(filled, 1)
                    pe.wait_ge(drained, 5 * h + 3)
                    pe.wait_ge(drained, 5 * h + 5)
                    at = 5 * h + 5
                    for c in range(NCH):
                        last = nc.tensor.matmul(bank(at % 8)[:, c, :], akT[:, h % 2, c, :], v_tok[:, c, h * HD:(h + 1) * HD], start=True, stop=True)
                    last.then_inc(w_filled, 1)
                    pe.wait_ge(w_out, h + 1)
                pe.wait_ge(drained, 5 * H)
                n = 0
                for l in range(1, LEVELS_R):
                    for h in range(H):
                        zb, b1, b2 = (n % 2) * 4, (n % 2) * 4 + 1, (n % 2) * 4 + 2
                        pe.wait_ge(masked, n + 1)
                        if n >= 2:
                            pe.wait_ge(d_added, 2 * (n - 1))
                        if l > 1:
                            pe.wait_ge(d_added, 2 * (n - H + 1))
                        for c in range(NCH):
                            last = nc.tensor.matmul(bank(zb)[:, c, :], amask[:, n % 2, c, :], invT[:, h, c, :], start=True, stop=True)
                        last.then_inc(z_filled, 1)
                        pe.wait_ge(z_out, n + 1)
                        for c in range(NCH):
                            nc.tensor.matmul(bank(b1)[:, c, :], prod[:, h, c, :], inv[:, h, c, :], start=True, stop=True)
                        for c in range(NCH):
                            last = nc.tensor.matmul(bank(b2)[:, c, :], inv[:, h, c, :], prod[:, h, c, :], start=True, stop=True)
                        last.then_inc(d_filled, 1)
                        n += 1
                pe.wait_ge(d_added, 2 * n)
                for h in range(H):
                    for c in range(NCH):
                        last = nc.tensor.matmul(bank(2 * h % 8)[:, c, :], a_tok[:, c, h * HD:(h + 1) * HD], invT[:, h, c, :], start=True, stop=True)
                    last.then_inc(x_filled, 1)
                    for c in range(NCH):
                        last = nc.tensor.matmul(bank((2 * h + 1) % 8)[:, c, :], invT[:, h, c, :], x2[:, h, c, :], start=True, stop=True)
                    last.then_inc(x_filled, 1)

            @block.vector
            def _(dve):
                link = Chain(dve, chain)
                dve.wait_ge(arrived, 16)
                for h in range(H):
                    at = 5 * h
                    dve.wait_ge(filled, at + 1)
                    nc.vector.tensor_tensor(amat[:, h], bank(at % 8), m_strict, ALU.mult).then_inc(drained, 1)
                    dve.wait_ge(filled, at + 2)
                    nc.vector.tensor_tensor(invT[:, h], bank((at + 1) % 8), m_firstT, ALU.mult).then_inc(drained, 1)
                    dve.wait_ge(filled, at + 3)
                    nc.vector.tensor_tensor(akT[:, h % 2], bank((at + 2) % 8), m_strictT, ALU.mult).then_inc(drained, 1)
                    dve.wait_ge(filled, at + 4)
                    nc.vector.tensor_tensor(rb[:, h], bank((at + 3) % 8), m_lowerT, ALU.mult).then_inc(drained, 1)
                    dve.wait_ge(filled, at + 5)
                    nc.vector.tensor_tensor(rk[:, h], bank((at + 4) % 8), m_lowerT, ALU.mult).then_inc(drained, 1)
                    dve.wait_ge(drained, at + 5)
                    link(nc.vector.tensor_tensor(inv[:, h], amat[:, h], m_first, ALU.mult))
                    link(nc.vector.tensor_tensor(inv[:, h], inv[:, h], m_eye, ALU.add))
                    link(nc.vector.tensor_tensor(invT[:, h], invT[:, h], m_eye, ALU.add))
                    dve.wait_ge(w_filled, h + 1)
                    nc.vector.tensor_copy(x2[:, h], bank((at + 5) % 8)).then_inc(w_out, 1)
                steps = [(l, h) for l in range(1, LEVELS_R) for h in range(H)]
                for n in range(len(steps) + 1):
                    if n < len(steps):
                        l, h = steps[n]
                        if n >= 2:
                            dve.wait_ge(z_filled, n - 1)
                        nc.vector.tensor_tensor(amask[:, n % 2], amat[:, h], masks[l], ALU.mult).then_inc(masked, 1)
                    if n >= 1:
                        h = steps[n - 1][1]
                        at = ((n - 1) % 2) * 4
                        dve.wait_ge(d_filled, n)
                        nc.vector.tensor_tensor(inv[:, h], bank(at + 1), inv[:, h], ALU.add).then_inc(d_added, 1)
                        nc.vector.tensor_tensor(invT[:, h], bank(at + 2), invT[:, h], ALU.add).then_inc(d_added, 1)

            @block.scalar
            def _(act):
                steps = [(l, h) for l in range(1, LEVELS_R) for h in range(H)]
                for n, (l, h) in enumerate(steps):
                    act.wait_ge(z_filled, n + 1)
                    if n >= H:
                        act.wait_ge(d_filled, n - H + 1)
                    nc.scalar.activation(prod[:, h], bank((n % 2) * 4), ACT.Copy).then_inc(z_out, 1)
                for h in range(H):
                    act.wait_ge(x_filled, 2 * h + 1)
                    nc.scalar.activation(x1[:, h], bank(2 * h % 8), ACT.Copy)
                    act.wait_ge(x_filled, 2 * h + 2)
                    nc.scalar.activation(x2[:, h], bank((2 * h + 1) % 8), ACT.Copy)


def rwkv_scan_stage(K, V, tok, mats, y):
    nc = K.nc
    (gate, _, _, _, r_t, bonus, p_end) = V
    (b_tok, k_tok, v_tok) = tok
    (x1, x2, rb, rk) = mats
    H = 4
    with ExitStack() as local:
        state = K.buf(local, "rwkv_state", [HD, 2, H, HD])
        u = K.buf(local, "rwkv_u", [CH, 2, H, HD])
        kept = K.buf(local, "rwkv_kept", [HD, H, HD])
        pe_ = K.buf(local, "rwkv_p_end", [HD, H, NCH])
        r0 = K.buf(local, "rwkv_r0", [HD, H, S])
        yraw = K.buf(local, "rwkv_y", [P, 2, S])
        ysq = K.buf(local, "rwkv_ysq", [P, 2, S])
        var = K.buf(local, "rwkv_var", [P, 2, S])
        u_filled, u_ready, s_filled, s_ready, y_filled, y_out, moved, chain, cleared = (K.sem(n) for n in (
            "u_filled", "u_ready", "s_filled", "s_ready", "y_filled", "y_out", "r_moved", "scan_chain", "state_cleared"))
        mean_filled, centred, var_filled, rooted = (K.sem(n) for n in ("mean_filled", "centred", "var_filled", "rwkv_rooted"))

        def grid(b):
            return K.ps[0:HD, b, 0:H * HD].rearrange("p (h i) -> p h i", i=HD)

        with K.stage() as block:
            @block.scalar
            def _(act):
                for h in range(H):
                    rows = slice((h % 2) * HD, (h % 2 + 1) * HD)
                    nc.scalar.activation(r0[:, h, :], r_t[rows, h // 2, :], ACT.Copy).then_inc(moved, 1)
                    nc.scalar.activation(pe_[:, h, :], p_end[rows, h // 2, :], ACT.Copy).then_inc(moved, 1)
                for c in range(NCH):
                    act.wait_ge(y_filled, c + 1)
                    for h in range(H):
                        rows = slice((h % 2) * HD, (h % 2 + 1) * HD)
                        nc.scalar.activation(yraw[rows, h // 2, c * CH:(c + 1) * CH], grid(4 + c % 2)[:, h, :], ACT.Copy).then_inc(y_out, 1)
                for t in range(2):
                    act.wait_ge(var_filled, t + 1)
                    nc.scalar.activation(var[:, t, :], K.ps[:, 6 + t, :], ACT.Sqrt, bias=K.gn_eps_col, scale=1.0 / HD).then_inc(rooted, 1)

            @block.tensor
            def _(pe):
                pe.wait_ge(cleared, 1)
                pe.wait_ge(moved, 2 * H)
                for c in range(NCH):
                    s = state[:, c % 2]
                    if c:
                        pe.wait_ge(s_ready, c)
                    for h in range(H):
                        last = nc.tensor.matmul(grid(c % 2)[:, h, :], x1[:, h, c, :], s[:, h, :], start=True, stop=True)
                    last.then_inc(u_filled, 1)
                    pe.wait_ge(u_ready, c + 1)
                    for h in range(H):
                        nc.tensor.matmul(grid(2 + c % 2)[:, h, :], b_tok[:, c, h * HD:(h + 1) * HD], u[:, c % 2, h, :], start=True, stop=False)
                        last = nc.tensor.matmul(grid(2 + c % 2)[:, h, :], k_tok[:, c, h * HD:(h + 1) * HD], v_tok[:, c, h * HD:(h + 1) * HD], start=False, stop=True)
                    last.then_inc(s_filled, 1)
                    if c >= 2:
                        pe.wait_ge(y_out, H * (c - 1))
                    for h in range(H):
                        to = grid(4 + c % 2)[:, h, :]
                        nc.tensor.matmul(to, s[:, h, :], r0[:, h, c * CH:(c + 1) * CH], start=True, stop=False)
                        nc.tensor.matmul(to, u[:, c % 2, h, :], rb[:, h, c, :], start=False, stop=False)
                        last = nc.tensor.matmul(to, v_tok[:, c, h * HD:(h + 1) * HD], rk[:, h, c, :], start=False, stop=True)
                    last.then_inc(y_filled, 1)
                pe.wait_ge(y_out, H * NCH)
                for t in range(2):
                    nc.tensor.matmul(K.ps[:, t, :], K.blk, yraw[:, t, :], start=True, stop=True).then_inc(mean_filled, 1)
                for t in range(2):
                    pe.wait_ge(centred, t + 1)
                    nc.tensor.matmul(K.ps[:, 6 + t, :], K.blk, ysq[:, t, :], start=True, stop=True).then_inc(var_filled, 1)

            @block.vector
            def _(dve):
                link = Chain(dve, chain)
                nc.vector.memset(state[:, 0], 0.0).then_inc(cleared, 1)
                dve.wait_ge(cleared, 1)
                dve.wait_ge(moved, 2 * H)
                for c in range(NCH):
                    dve.wait_ge(u_filled, c + 1)
                    nc.vector.tensor_tensor(u[:, c % 2], grid(c % 2), x2[:, :, c, :], ALU.add).then_inc(u_ready, 1)
                    dve.wait_ge(s_filled, c + 1)
                    if c >= 1:
                        dve.wait_ge(y_filled, c)
                    link(nc.vector.tensor_tensor(kept[:], grid(2 + c % 2), state[:, c % 2], ALU.add))
                    for h in range(H):
                        ins = nc.vector.tensor_scalar(state[:, (c + 1) % 2, h, :], kept[:, h, :], pe_[:, h, c:c + 1], None, ALU.mult)
                        if h == H - 1:
                            ins.then_inc(s_ready, 1)
                    dve.wait_ge(s_ready, c + 1)
                for t in range(2):
                    dve.wait_ge(mean_filled, t + 1)
                    link(nc.vector.scalar_tensor_tensor(out=yraw[:, t, :], in0=K.ps[:, t, :], scalar=-1.0 / HD, in1=yraw[:, t, :], op0=ALU.mult, op1=ALU.add))
                    nc.vector.tensor_tensor(ysq[:, t, :], yraw[:, t, :], yraw[:, t, :], ALU.mult).then_inc(centred, 1)
                for t in range(2):
                    dve.wait_ge(rooted, t + 1)
                    link(nc.vector.reciprocal(var[:, t, :], var[:, t, :]))
                    link(nc.vector.tensor_tensor(yraw[:, t, :], yraw[:, t, :], var[:, t, :], ALU.mult))
                    link(nc.vector.tensor_scalar(yraw[:, t, :], yraw[:, t, :], K.vec("rwkv_ln_w", t), K.vec("rwkv_ln_b", t), ALU.mult, ALU.add))
                    link(nc.vector.tensor_tensor(yraw[:, t, :], yraw[:, t, :], bonus[:, t, :], ALU.add))
                    nc.vector.tensor_tensor(y[:, 2 + t, :], yraw[:, t, :], gate[:, t, :], ALU.mult)


def head_norm_stage(K, groups):
    nc = K.nc
    most = max(len(g[0]) for g in groups)
    wide = max(g[0][0][0].shape[-1] for g in groups)
    with ExitStack() as local:
        square = K.buf(local, "head_square", [P, 2, most, wide])
        rstd = K.buf(local, "head_rstd", [P, 2, wide])
        squared, summed, rooted, chain, applied = (K.sem(n) for n in ("head_squared", "head_summed", "head_rooted", "head_chain", "head_applied"))
        with K.stage() as block:
            @block.gpsimd
            def _(pool):
                for n, (tiles, matrix, width, times) in enumerate(groups):
                    if n >= 2:
                        pool.wait_ge(summed, n - 1)
                    for i, (src, _, _) in enumerate(tiles):
                        ins = nc.gpsimd.tensor_tensor(square[:, n % 2, i, 0:src.shape[-1]], src, src, ALU.mult)
                        if i == len(tiles) - 1:
                            ins.then_inc(squared, 1)

            @block.tensor
            def _(pe):
                for n, (tiles, matrix, width, times) in enumerate(groups):
                    pe.wait_ge(squared, n + 1)
                    if n >= 8:
                        pe.wait_ge(rooted, n - 7)
                    for i, (src, _, _) in enumerate(tiles):
                        w = src.shape[-1]
                        last = nc.tensor.matmul(K.ps[:, n % 8, 0:w], matrix, square[:, n % 2, i, 0:w], start=i == 0, stop=i == len(tiles) - 1)
                    last.then_inc(summed, 1)

            @block.scalar
            def _(act):
                for n, (tiles, matrix, width, times) in enumerate(groups):
                    w = tiles[0][0].shape[-1]
                    act.wait_ge(summed, n + 1)
                    if n >= 2:
                        act.wait_ge(applied, n - 1)
                    nc.scalar.activation(rstd[:, n % 2, 0:w], K.ps[:, n % 8, 0:w], ACT.Sqrt, bias=K.eps_times[times], scale=times / width).then_inc(rooted, 1)

            @block.vector
            def _(dve):
                link = Chain(dve, chain)
                for n, (tiles, matrix, width, times) in enumerate(groups):
                    w = tiles[0][0].shape[-1]
                    dve.wait_ge(rooted, n + 1)
                    link(nc.vector.reciprocal(rstd[:, n % 2, 0:w], rstd[:, n % 2, 0:w]))
                    for i, (src, dst, gain) in enumerate(tiles):
                        if gain is None:
                            ins = nc.vector.tensor_tensor(dst, src, rstd[:, n % 2, 0:w], ALU.mult)
                        else:
                            ins = nc.vector.scalar_tensor_tensor(out=dst, in0=src, scalar=gain, in1=rstd[:, n % 2, 0:w], op0=ALU.mult, op1=ALU.mult)
                        if i == len(tiles) - 1:
                            ins.then_inc(applied, 1)


def attention_stage(K, units, rows, scores, value, place, bias=None, diagonal=None, parts=1, minus_lambda=None, before=None, width=HD):
    nc = K.nc
    U = len(units)
    kmax = max(u[2] for u in units)
    flat = K.ps[:].rearrange("p b n -> p (b n)")
    dts = (width + P - 1) // P
    drows = min(width, P)
    with ExitStack() as local:
        p = K.buf(local, "probs", [P, 2, parts, kmax * rows])
        s = K.buf(local, "scores", [P, 2, parts, kmax * rows]) if bias else None
        pT = K.buf(local, "probsT", [P, 2, kmax, rows])
        stat = K.buf(local, "softmax_stats", [P, 2, parts, 4])
        scored, maxed, exped, inverted, p_ready, turned, pT_out, o_filled, o_out, chain, pool_chain, bias_ready = (K.sem(n) for n in (
            "scored", "maxed", "exped", "inverted", "p_ready", "p_turned", "pT_out", "o_filled", "o_out", "att_chain", "att_pool_chain", "bias_ready"))

        def bank(u, part, n):
            lo = (u % 2) * 1024 + part * 512
            return flat[0:rows, lo:lo + n]

        def turned_at(i):
            lo = 2048 + (i // 4) * 512 + (i % 4) * rows
            return flat[0:rows, lo:lo + rows]

        with K.stage() as block:
            @block.tensor
            def _(pe):
                for n in range(U + 1):
                    if n < U:
                        keys = units[n][2] * rows
                        if n >= 2:
                            pe.wait_ge(exped, parts * (n - 1))
                        if bias is None and before is not None and n == 0:
                            before(pe)
                        for part in range(parts):
                            for lo in range(0, keys, 512):
                                hi = min(keys, lo + 512)
                                last = scores(units[n], part, lo, hi, bank(n, part, keys)[:, lo:hi])
                        last.then_inc(scored, 1)
                    if n >= 1:
                        u = n - 1
                        h, i, kt = units[u]
                        pe.wait_ge(p_ready, u + 1)
                        if u >= 1:
                            pe.wait_ge(pT_out, u)
                        for t in range(kt):
                            last = nc.tensor.transpose(turned_at(t), p[0:rows, u % 2, 0, t * rows:(t + 1) * rows], K.ident[0:rows, 0:rows])
                        last.then_inc(turned, 1)
                        pe.wait_ge(pT_out, u + 1)
                        if u >= 2:
                            pe.wait_ge(o_out, u - 1)
                        for d in range(dts):
                            for t in range(kt):
                                last = nc.tensor.matmul(K.ps[0:drows, 6 + u % 2, d * rows:(d + 1) * rows], value(h, t, d), pT[0:rows, u % 2, t, :], start=t == 0, stop=t == kt - 1)
                        last.then_inc(o_filled, 1)

            @block.vector
            def _(dve):
                link = Chain(dve, chain)
                for n in range(U + 1):
                    if n < U:
                        keys = units[n][2] * rows
                        if bias is not None and n >= 2:
                            dve.wait_ge(exped, parts * (n - 1))
                        dve.wait_ge(scored, n + 1)
                        for part in range(parts):
                            top = stat[0:rows, n % 2, part, 0:1]
                            src = bank(n, part, keys)
                            if bias is not None:
                                link(nc.vector.tensor_tensor(s[0:rows, n % 2, part, 0:keys], src, bias(units[n]), ALU.add))
                                src = s[0:rows, n % 2, part, 0:keys]
                            if diagonal is not None:
                                link(nc.vector.tensor_tensor(src[:, keys - rows:keys], src[:, keys - rows:keys], diagonal, ALU.add))
                            link(nc.vector.tensor_reduce(top, src, AX, ALU.max))
                            nc.vector.tensor_scalar(stat[0:rows, n % 2, part, 1:2], top, -1.0, None, ALU.mult).then_inc(maxed, 1)
                    if n >= 1:
                        u = n - 1
                        dve.wait_ge(exped, parts * (u + 1))
                        for part in range(parts):
                            ins = nc.vector.reciprocal(stat[0:rows, u % 2, part, 3:4], stat[0:rows, u % 2, part, 2:3])
                            if part == 1:
                                link(ins)
                                ins = nc.vector.tensor_tensor(stat[0:rows, u % 2, 1, 3:4], stat[0:rows, u % 2, 1, 3:4], minus_lambda[0:rows, :], ALU.mult)
                            ins.then_inc(inverted, 1)

            @block.scalar
            def _(act):
                def out(u):
                    act.wait_ge(o_filled, u + 1)
                    for d in range(dts):
                        ins = nc.scalar.activation(place(units[u], d), K.ps[0:drows, 6 + u % 2, d * rows:(d + 1) * rows], ACT.Copy)
                    ins.then_inc(o_out, 1)

                for n in range(U + 1):
                    if n < U:
                        keys = units[n][2] * rows
                        if n >= 2:
                            act.wait_ge(turned, n - 1)
                        for part in range(parts):
                            act.wait_ge(maxed, parts * n + part + 1)
                            src = s[0:rows, n % 2, part, 0:keys] if bias is not None else bank(n, part, keys)
                            nc.scalar.activation(p[0:rows, n % 2, part, 0:keys], src, ACT.Exp, bias=stat[0:rows, n % 2, part, 1:2],
                                                 accum_out=stat[0:rows, n % 2, part, 2:3]).then_inc(exped, 1)
                    if n >= 2:
                        out(n - 2)
                    if n >= 1:
                        u = n - 1
                        kt = units[u][2]
                        act.wait_ge(turned, u + 1)
                        for lo in range(0, kt, 4):
                            k = min(4, kt - lo)
                            ins = nc.scalar.activation(pT[0:rows, u % 2, lo:lo + k, :].rearrange("p t q -> p (t q)"),
                                                       flat[0:rows, 2048 + lo * 128:2048 + lo * 128 + k * rows], ACT.Copy)
                        ins.then_inc(pT_out, 1)
                out(U - 1)

            @block.gpsimd
            def _(pool):
                link = Chain(pool, pool_chain)
                for u in range(U):
                    keys = units[u][2] * rows
                    pool.wait_ge(inverted, parts * (u + 1))
                    pp = p[0:rows, u % 2]
                    if parts == 1:
                        nc.gpsimd.tensor_scalar(pp[:, 0, 0:keys], pp[:, 0, 0:keys], stat[0:rows, u % 2, 0, 3:4], None, ALU.mult).then_inc(p_ready, 1)
                    else:
                        for part in range(2):
                            link(nc.gpsimd.tensor_scalar(pp[:, part, 0:keys], pp[:, part, 0:keys], stat[0:rows, u % 2, part, 3:4], None, ALU.mult))
                        nc.gpsimd.tensor_tensor(pp[:, 0, 0:keys], pp[:, 0, 0:keys], pp[:, 1, 0:keys], ALU.add).then_inc(p_ready, 1)


def diff_tables_stage(K, biases, minus_lambda, ins):
    nc = K.nc
    with ExitStack() as local:
        dist = K.buf(local, "dist", [P, S])
        lv = K.buf(local, "lambda_vectors", [P, 4, HD])
        ls = K.buf(local, "lambda_sums", [P, 2])
        le = K.buf(local, "lambda_exps", [P, 2])
        prod = K.buf(local, "lambda_products", [P, HD])
        arrived, summed, exped, chain = (K.sem(n) for n in ("dist_arrived", "lambda_summed", "lambda_exped", "lambda_chain"))
        with K.stage() as block:
            @block.sync
            def _(sp):
                sp.dma_start(dist[:], ins["c_dist"]).then_inc(arrived, 16)
                sp.dma_start(lv[:], ins["diff_lambda"]).then_inc(arrived, 16)

            @block.vector
            def _(dve):
                link = Chain(dve, chain)
                dve.wait_ge(arrived, 32)
                for n in range(2):
                    link(nc.vector.tensor_tensor(prod[:], lv[:, 2 * n, :], lv[:, 2 * n + 1, :], ALU.mult))
                    nc.vector.tensor_reduce(ls[:, n:n + 1], prod[:], AX, ALU.add).then_inc(summed, 1)
                    dve.wait_ge(summed, n + 1)
                for h in range(4):
                    nc.vector.tensor_scalar(biases[:, h, :], dist[:], -float(2.0 ** (-8.0 * (h + 1) / 4)), None, ALU.mult)
                dve.wait_ge(exped, 1)
                link(nc.vector.tensor_tensor(minus_lambda[:], le[:, 1:2], le[:, 0:1], ALU.subtract))
                nc.vector.tensor_scalar(minus_lambda[:], minus_lambda[:], -LAMBDA_INIT, None, ALU.add)

            @block.scalar
            def _(act):
                act.wait_ge(summed, 2)
                nc.scalar.activation(le[:], ls[:], ACT.Exp).then_inc(exped, 1)


def mixer_1(K, ins):
    nc = K.nc
    with ExitStack() as mix:
        y = K.buf(mix, "mix_y", [P, KT, S])
        rwkv_z = K.buf(mix, "rwkv_z", [P, 8, 1 + S])
        with ExitStack() as early:
            pool_u = K.buf(early, "pool_u", [P, 2, 16 + S])
            diff_qk = K.buf(early, "diff_qk", [P, 8, S])
            diff_v = K.buf(early, "diff_v", [P, 4, S])
            mix_in_stage(K, pool_u, rwkv_z, diff_qk, diff_v)
            pool_stage(K, pool_u, y, ins)
            with ExitStack() as att:
                biases = K.buf(att, "diff_bias", [P, 4, S])
                minus_lambda = K.buf(att, "minus_lambda", [P, 1])
                diff_tables_stage(K, biases, minus_lambda, ins)
                head_norm_stage(K, [([(diff_qk[:, i, :], diff_qk[:, i, :], K.vec("diff_q_norm" if i < 4 else "diff_k_norm"))],
                                     K.blk, HD, HD if i < 4 else 1) for i in range(8)])
                units = [(h, i, i + 1) for h in range(4) for i in range(4)]

                def scores(unit, part, lo, hi, to):
                    h, i, _ = unit
                    rows = slice(part * HD, (part + 1) * HD)
                    return nc.tensor.matmul(to, diff_qk[rows, h, i * P:(i + 1) * P], diff_qk[rows, 4 + h, lo:hi], start=True, stop=True)

                attention_stage(K, units, P, scores, lambda h, t, d: diff_v[:, t, h * P:(h + 1) * P],
                                lambda unit, d: y[:, 4 + unit[0], unit[1] * P:(unit[1] + 1) * P],
                                bias=lambda unit: biases[:, unit[0], (3 - unit[1]) * P:4 * P],
                                parts=2, minus_lambda=minus_lambda, width=P)
                head_norm_stage(K, [([(y[:, 4 + h, :], y[:, 4 + h, :], K.vec("diff_subln"))], K.ones, P, SUBLN) for h in range(4)])
        with ExitStack() as rec:
            V = [K.buf(rec, n, [P, 2, S]) for n in ("rwkv_gate", "rwkv_a", "rwkv_b", "rwkv_k", "rwkv_r", "rwkv_bonus")]
            V.append(K.buf(rec, "rwkv_p_ends", [P, 2, NCH]))
            zm = rwkv_z[:, :, 1:1 + S]
            rwkv_prepare_stage(K, rwkv_z, zm, V, ins)
            toks = [K.buf(rec, n, [CH, NCH, 256]) for n in ("a_tok", "b_tok", "k_tok", "v_tok")]
            jobs = [(src[:, t, :], (lambda c, n, tok=tok, t=t: tok[:, c:c + n, t * P:(t + 1) * P]))
                    for src, tok in zip((V[1], V[2], V[3], zm[:, 4:6, :]), toks) for t in range(2)]
            token_tiles_stage(K, jobs, CH, NCH)
            spare = rwkv_z[:].rearrange("p k t -> p (k t)")
            mats = [spare[0:CH, n * 4 * S:(n + 1) * 4 * S].rearrange("p (h c i) -> p h c i", h=4, c=NCH) for n in range(2)]
            mats += [K.buf(rec, n, [CH, 4, NCH, CH]) for n in ("rbT", "rkT")]
            rwkv_chunk_stage(K, V, (toks[0], toks[3]), mats, ins)
            rwkv_scan_stage(K, V, toks[1:], mats, y)
        residual_stage(K, lambda j: y[:, j, :], KT)


def cross_attention(K, ins):
    nc = K.nc
    with ExitStack() as xa:
        mem = K.buf(xa, "mem", [P, KT, MEM])
        memn = K.buf(xa, "memn", [P, KT, MEM])
        q = K.buf(xa, "xa_q", [P, KT, S])
        k = K.buf(xa, "xa_k", [P, KT, MEM])
        v = K.buf(xa, "xa_v", [P, 2, D])
        o = K.buf(xa, "xa_o", [P, KT, S])
        arrived = K.sem("mem_arrived")
        with K.stage() as block:
            @block.sync
            def _(sp):
                sp.dma_start(mem[:], ins["mem"]).then_inc(arrived, 16)
                sp.wait_ge(arrived, 16)
        norm_stage(K, lambda i: mem[:, i, :], lambda i: memn[:, i, :], "mem_norm_g", [(0, MEM)])
        norm_stage(K, lambda i: K.h[:, i, 0:S], lambda i: K.xn[:, i, 0:S], "xa_norm_g", [(0, S)])
        project_stage(K, lambda m: q[:, m, :], lambda j: K.xn[:, j, 0:S], S)
        project_stage(K, lambda m: k[:, m, :], lambda j: memn[:, j, :], MEM)
        token_major_stage(K, lambda i, half: v[:, i, half * 512:(half + 1) * 512], lambda j, i: memn[:, j, i * P:(i + 1) * P], 2)
        head_norm_stage(K, [([(t[:, 2 * h + i, :], t[:, 2 * h + i, :], K.vec(gain, i)) for i in range(2)], K.ones, 4 * HD, times)
                            for t, gain, times in ((q, "xa_q_norm", 4 * HD), (k, "xa_k_norm", 1)) for h in range(4)])

        def scores(unit, part, lo, hi, to):
            h, i, _ = unit
            nc.tensor.matmul(to, q[:, 2 * h, i * P:(i + 1) * P], k[:, 2 * h, lo:hi], start=True, stop=False)
            return nc.tensor.matmul(to, q[:, 2 * h + 1, i * P:(i + 1) * P], k[:, 2 * h + 1, lo:hi], start=False, stop=True)

        attention_stage(K, [(h, i, 2) for h in range(4) for i in range(4)], P, scores,
                        lambda h, t, d: v[:, t, h * 256 + d * P:h * 256 + (d + 1) * P],
                        lambda unit, d: o[:, 2 * unit[0] + d, unit[1] * P:(unit[1] + 1) * P], width=256)
        residual_stage(K, lambda j: o[:, j, :], KT)


def conv_ffn_1(K):
    nc = K.nc
    with ExitStack() as ffn:
        hidden = K.buf(ffn, "ffn_hidden", [P, FT, S])
        a = K.buf(ffn, "ffn_a", [P, 4, 2 + S])
        c = K.buf(ffn, "ffn_c", [P, 4, S])
        filled, drained, a_ready, conv, gelu, chain = (K.sem(n) for n in ("up_filled", "up_drained", "a_ready", "conv_done", "gelu_done", "conv_chain"))
        sizes = [4] * (FT // 4) + [FT % 4] * (FT % 4 > 0)
        groups, before = [], 0
        n0 = K.slabs.n
        for g, n in enumerate(sizes):
            groups.append(Group(K, 2 * n, KT, filled, n0 + KT * g, before))
            before += 2 * n - 1
        K.slabs.n += KT * len(sizes)
        starts = [sum(sizes[:g]) for g in range(len(sizes))]
        with K.stage() as block:
            @block.sync
            def _(sp):
                K.slabs.refill(sp, n0, KT * len(sizes))

            @block.tensor
            def _(pe):
                done = 0
                for g, n in enumerate(sizes):
                    def free(e, b, g=g, n=n):
                        if g:
                            e.wait_ge(a_ready if b < n else drained, starts[g - 1] + (b % n) + 1)
                    if g and n < 4:
                        def free(e, b, g=g, n=n):
                            e.wait_ge(a_ready, starts[g])
                            e.wait_ge(drained, starts[g])
                    groups[g].products(pe, lambda j, b, start, stop, g=g: nc.tensor.matmul(
                        K.ps[:, b, :], K.slabs.slot(groups[g].n0 + j)[:, b * P:(b + 1) * P], K.xn[:, j, 0:S], start=start, stop=stop), free)

            @block.scalar
            def _(act):
                for g, n in enumerate(sizes):
                    for i in range(n):
                        f = starts[g] + i
                        groups[g].bank_ready(act, i)
                        if f >= 4:
                            act.wait_ge(conv, f - 3)
                        nc.scalar.activation(a[:, f % 4, 2:2 + S], K.ps[:, i, :], ACT.Copy).then_inc(a_ready, 1)
                    for i in range(n):
                        f = starts[g] + i
                        act.wait_ge(conv, f + 1)
                        nc.scalar.activation(hidden[:, f, :], c[:, f % 4, :], ACT.Gelu).then_inc(gelu, 1)

            @block.vector
            def _(dve):
                link = Chain(dve, chain)
                link(nc.vector.memset(a[:, :, 0:2], 0.0))
                for g, n in enumerate(sizes):
                    for i in range(n):
                        f = starts[g] + i
                        dve.wait_ge(a_ready, f + 1)
                        if f >= 4:
                            dve.wait_ge(gelu, f - 3)
                        at, to = a[:, f % 4, :], c[:, f % 4, :]
                        link(nc.vector.tensor_scalar(to, at[:, 0:S], K.vec("ffn_conv_w", f), K.vec("ffn_conv_b", f), ALU.mult, ALU.add))
                        link(nc.vector.scalar_tensor_tensor(out=to, in0=at[:, 1:1 + S], scalar=K.vec("ffn_conv_w", FT + f), in1=to, op0=ALU.mult, op1=ALU.add))
                        nc.vector.scalar_tensor_tensor(out=to, in0=at[:, 2:2 + S], scalar=K.vec("ffn_conv_w", 2 * FT + f), in1=to, op0=ALU.mult, op1=ALU.add).then_inc(conv, 1)
                    for i in range(n):
                        f = starts[g] + i
                        dve.wait_ge(gelu, f + 1)
                        groups[g].bank_ready(dve, n + i)
                        nc.vector.tensor_tensor(hidden[:, f, :], K.ps[:, n + i, :], hidden[:, f, :], ALU.mult).then_inc(drained, 1)
        residual_stage(K, lambda j: hidden[:, j, :], FT)


def block_1(K, ins):
    norm_stage(K, lambda k: K.h[:, k, 0:S], lambda k: K.xn[:, k, 0:S], "mix_norm_g", [(0, S)])
    mixer_1(K, ins)
    cross_attention(K, ins)
    norm_stage(K, lambda k: K.h[:, k, 0:S], lambda k: K.xn[:, k, 0:S], "ffn_norm_g", [(0, S)])
    conv_ffn_1(K)


def block_2_slabs(a):
    w = a["w_in_2"]
    parts = [wide(w, [(0, 1024)]), wide(w, [(1024, 1536), (2048, 2560)]), wide(w, [(1536, 2048), (2560, 3072)]),
             wide(w, [(3144, 4168)]), wide(w, [(4168, 5192)]), wide(a["w_out_a_2"], [(0, D)]),
             wide(a["w_out_b_2"], [(0, D)]), wide(a["w_o_2"], [(0, D)])]
    parts += [wide(a["w_ff_in_2"], [(f, f + D)]) for f in range(0, FF2, D)]
    return parts + [wide(a["w_ff_out_2"], [(0, D)])]


def block_2_inputs(i):
    w = i["w_in_2"][0]
    index = np.concatenate([w[:, 3072:3136], w[:, 3072:3136], w[:, 3136:3144]], axis=1)
    return dict(
        index_w=np.ascontiguousarray(index.reshape(KT, P, -1).transpose(1, 0, 2)),
        sgu_w=np.ascontiguousarray(i["w_s_2"][0].transpose(2, 0, 1)),
        sgu_b=np.ascontiguousarray(np.broadcast_to(np.tile(i["b_s_2"][0], (1, 4)), (P, 4, S))),
        sgu_ln=np.ascontiguousarray(np.broadcast_to(np.stack([i["sgu_ln_g_2"][0], i["sgu_ln_b_2"][0]]), (P, 2, S))))


def mix_in_2_stage(K, u, vg, q, v, k, qi, ki, wi, gates, ins):
    nc = K.nc
    filled, drained, arrived, index_filled = K.sem("proj_filled"), K.sem("proj_drained"), K.sem("index_w_arrived"), K.sem("index_filled")
    groups = [Group(K, 8, KT, filled, K.slabs.n + g * KT, 7 * g) for g in range(5)]
    K.slabs.n += 5 * KT
    with ExitStack() as local:
        w = K.buf(local, "index_w", [P, KT, 2 * HD + 8])
        with K.stage() as block:
            @block.sync
            def _(sp):
                sp.dma_start(w[:], ins["index_w"]).then_inc(arrived, 16)
                K.slabs.refill(sp, groups[0].n0, 5 * KT)

            @block.tensor
            def _(pe):
                for g, group in enumerate(groups):
                    def product(j, b, start, stop, g=g, group=group):
                        slab = K.slabs.slot(group.n0 + j)
                        if g < 2 and b >= 4:
                            return nc.tensor.matmul(K.ps[:, b, :], K.xn[:, j, (b - 4) * P:(b - 3) * P], slab[:, 512:1024], start=start, stop=stop)
                        return nc.tensor.matmul(K.ps[:, b, :], slab[:, b * P:(b + 1) * P], K.xn[:, j, 0:S], start=start, stop=stop)
                    group.products(pe, product, (lambda e, b, g=g: e.wait_ge(drained, 8 * (g - 1) + b + 1)) if g else None)
                pe.wait_ge(arrived, 16)
                pe.wait_ge(drained, 8 * 4 + 2)
                for j in range(KT):
                    last = nc.tensor.matmul(K.ps[:, 0, :], w[:, j, 0:P], K.xn[:, j, 0:S], start=j == 0, stop=j == KT - 1)
                last.then_inc(index_filled, 1)
                for i in range(4):
                    for j in range(KT):
                        last = nc.tensor.matmul(K.ps[:, 1, i * 8:(i + 1) * 8], K.xn[:, j, i * P:(i + 1) * P], w[:, j, P:P + 8], start=j == 0, stop=j == KT - 1)
                last.then_inc(index_filled, 1)

            @block.scalar
            def _(act):
                places = [(u, vg), (q, v), (k, qi), (gates[:, 0:4], gates[:, 4:8]), (gates[:, 8:12], gates[:, 12:16])]
                for g, group in enumerate(groups):
                    func = ACT.Gelu_apprx_tanh if g == 0 else ACT.Sigmoid if g >= 3 else ACT.Copy
                    for b in range(8):
                        group.bank_ready(act, b)
                        nc.scalar.activation(places[g][b // 4][:, b % 4, :], K.ps[:, b, :], func).then_inc(drained, 1)
                act.wait_ge(index_filled, 2)
                nc.scalar.activation(ki[:], K.ps[:, 0, :], ACT.Copy)
                nc.scalar.activation(wi[:].rearrange("p i h -> p (i h)"), K.ps[:, 1, 0:32], ACT.Copy, scale=float(64.0 ** -0.5 * 8.0 ** -0.5))


def sgu_stage(K, u, vg, ya, ins):
    nc = K.nc
    with ExitStack() as local:
        w = K.buf(local, "sgu_w", [P, 4, P])
        b = K.buf(local, "sgu_b", [P, 4, S])
        ln = K.buf(local, "sgu_ln", [P, 2, S])
        stats = K.buf(local, "sgu_stats", [P, 4, 6])
        moments = K.buf(local, "sgu_moments", [P, 4, 2])
        arrived, chain, rooted, v_ready, w_ready, filled = (K.sem(n) for n in ("sgu_arrived", "sgu_chain", "sgu_rooted", "sgu_v_ready", "sgu_w_ready", "sgu_filled"))
        moments_ready, rstd_ready = K.sem("moments_ready"), K.sem("sgu_rstd_ready")
        with K.stage() as block:
            @block.sync
            def _(sp):
                for to, src in ((w, "sgu_w"), (b, "sgu_b"), (ln, "sgu_ln")):
                    sp.dma_start(to[:], ins[src]).then_inc(arrived, 16)

            @block.vector
            def _(dve):
                link = Chain(dve, chain)
                for c in range(4):
                    link(nc.vector.bn_stats(stats[:, c, :], vg[:, c, :]))
                    link(nc.vector.bn_aggr(moments[:, c, :], stats[:, c, :]))
                nc.vector.tensor_copy(stats[:, :, 0:1], moments[:, :, 1:2]).then_inc(moments_ready, 1)
                dve.wait_ge(arrived, 48)
                nc.vector.tensor_tensor(w[:], w[:], K.upper.unsqueeze(1).to_broadcast((P, 4, P)), ALU.mult).then_inc(w_ready, 1)
                dve.wait_ge(rooted, 1)
                nc.vector.reciprocal(stats[:, :, 2:3], stats[:, :, 1:2]).then_inc(rstd_ready, 1)
                dve.wait_ge(rstd_ready, 1)
                for c in range(4):
                    link(nc.vector.tensor_scalar(vg[:, c, :], vg[:, c, :], moments[:, c, 0:1], stats[:, c, 2:3], ALU.subtract, ALU.mult))
                    link(nc.vector.tensor_tensor(vg[:, c, :], vg[:, c, :], ln[:, 0, :], ALU.mult))
                    nc.vector.tensor_tensor(vg[:, c, :], vg[:, c, :], ln[:, 1, :], ALU.add).then_inc(v_ready, 1)
                for g in range(4):
                    dve.wait_ge(filled, g + 1)
                    link(nc.vector.tensor_tensor(ya[:, g, :], K.ps[:, g, :], b[:, g, :], ALU.add))
                    nc.vector.tensor_tensor(ya[:, g, :], ya[:, g, :], u[:, g, :], ALU.mult)

            @block.scalar
            def _(act):
                act.wait_ge(moments_ready, 1)
                nc.scalar.activation(stats[:, :, 1:2], stats[:, :, 0:1], ACT.Sqrt, bias=K.eps_col).then_inc(rooted, 1)

            @block.tensor
            def _(pe):
                pe.wait_ge(w_ready, 1)
                pe.wait_ge(v_ready, 4)
                for g in range(4):
                    for c in range(4):
                        last = nc.tensor.matmul(K.ps[:, g, c * P:(c + 1) * P], vg[:, c, g * P:(g + 1) * P], w[:, g, :], start=True, stop=True)
                    last.then_inc(filled, 1)


def rope_stage(K, tiles, ins):
    nc = K.nc
    with ExitStack() as local:
        table = K.buf(local, "rope_table", [P, 2, 2, S])
        part = K.buf(local, "rope_part", [P, 2, S])
        arrived, scaled, turned, chain, cos_done, drained = (K.sem(n) for n in ("rope_arrived", "rope_scaled", "rope_turned", "rope_chain", "rope_cos_done", "rope_drained"))
        with K.stage() as block:
            @block.sync
            def _(sp):
                sp.dma_start(table[:, 0, 0, :], ins["c_cos"]).then_inc(arrived, 16)
                sp.dma_start(table[:, 0, 1, :], ins["c_sin"]).then_inc(arrived, 16)

            @block.tensor
            def _(pe):
                for n, (x, _) in enumerate(tiles):
                    if n >= 8:
                        pe.wait_ge(drained, n - 7)
                    nc.tensor.matmul(K.ps[:, n % 8, :], K.rot, x, start=True, stop=True).then_inc(turned, 1)

            @block.gpsimd
            def _(pool):
                pool.wait_ge(scaled, 1)
                for n, (x, small) in enumerate(tiles):
                    pool.wait_ge(turned, n + 1)
                    nc.gpsimd.tensor_tensor(x, x, table[:, small, 0, :], ALU.mult).then_inc(cos_done, 1)

            @block.vector
            def _(dve):
                link = Chain(dve, chain)
                dve.wait_ge(arrived, 32)
                nc.vector.tensor_scalar(table[:, 1], table[:, 0], HD ** -0.5, None, ALU.mult).then_inc(scaled, 1)
                dve.wait_ge(scaled, 1)
                for n, (x, small) in enumerate(tiles):
                    dve.wait_ge(turned, n + 1)
                    nc.vector.tensor_tensor(part[:, n % 2, :], K.ps[:, n % 8, :], table[:, small, 1, :], ALU.mult).then_inc(drained, 1)
                    dve.wait_ge(drained, n + 1)
                    dve.wait_ge(cos_done, n + 1)
                    link(nc.vector.tensor_tensor(x, x, part[:, n % 2, :], ALU.add))


def select_stage(K, qi, ki, wi, mask, ins):
    nc = K.nc
    heads = 8
    with ExitStack() as local:
        causal = K.buf(local, "causal", [P, P])
        pos = K.buf(local, "relu_logits", [P, 2, S])
        score = K.buf(local, "index_score", [P, S])
        work = K.buf(local, "index_work", [P, S])
        top = K.buf(local, "index_top", [P, 8])
        above = K.buf(local, "index_above", [P, S])
        equal = K.buf(local, "index_equal", [P, S])
        count = K.buf(local, "index_count", [P, 2])
        one = K.buf(local, "index_ones", [P, S])
        arrived, chain, filled, relu, summed = (K.sem(n) for n in ("causal_arrived", "select_chain", "logits_filled", "logits_relu", "logits_summed"))
        with K.stage() as block:
            @block.sync
            def _(sp):
                sp.dma_start(causal[:], ins["c_causal"]).then_inc(arrived, 16)

            @block.tensor
            def _(pe):
                for n in range(3 * heads):
                    i, h = 1 + n // heads, n % heads
                    keys = (i + 1) * P
                    rows = slice((h % 2) * HD, (h % 2 + 1) * HD)
                    if n >= 8:
                        pe.wait_ge(relu, n - 7)
                    nc.tensor.matmul(K.ps[:, n % 8, 0:keys], qi[rows, h // 2, i * P:(i + 1) * P], ki[rows, 0:keys], start=True, stop=True).then_inc(filled, 1)

            @block.scalar
            def _(act):
                for n in range(3 * heads):
                    keys = (2 + n // heads) * P
                    act.wait_ge(filled, n + 1)
                    if n >= 2:
                        act.wait_ge(summed, n - 1)
                    nc.scalar.activation(pos[:, n % 2, 0:keys], K.ps[:, n % 8, 0:keys], ACT.Relu).then_inc(relu, 1)

            @block.vector
            def _(dve):
                link = Chain(dve, chain)
                link(nc.vector.memset(one[:], 1.0))
                dve.wait_ge(arrived, 16)
                nc.vector.tensor_copy(mask[:, 0, 0:P], causal[:])
                for i in range(1, 4):
                    keys = (i + 1) * P
                    sc, wk = score[:, 0:keys], work[:, 0:keys]
                    for h in range(heads):
                        n = (i - 1) * heads + h
                        dve.wait_ge(relu, n + 1)
                        if h == 0:
                            ins_ = nc.vector.tensor_scalar(sc, pos[:, n % 2, 0:keys], wi[:, i, 0:1], None, ALU.mult)
                        else:
                            ins_ = nc.vector.scalar_tensor_tensor(out=sc, in0=pos[:, n % 2, 0:keys], scalar=wi[:, i, h:h + 1], in1=sc, op0=ALU.mult, op1=ALU.add)
                        ins_.then_inc(summed, 1)
                        dve.wait_ge(summed, n + 1)
                    link(nc.vector.tensor_tensor(score[:, i * P:keys], score[:, i * P:keys], causal[:], ALU.add))
                    for n in range(TOPK // 8):
                        link(nc.vector.max(top[:], sc if n == 0 else wk))
                        if n < TOPK // 8 - 1:
                            link(nc.vector.match_replace(wk, top[:], sc if n == 0 else wk, LOWEST))
                    last = top[:, 7:8]
                    link(nc.vector.tensor_scalar(above[:, 0:keys], sc, last, 0.0, ALU.is_gt, ALU.add, accum_out=count[:, 0:1]))
                    link(nc.vector.tensor_scalar(equal[:, 0:keys], sc, last, None, ALU.is_equal))
                    link(nc.vector.tensor_scalar(count[:, 1:2], count[:, 0:1], -1.0, float(TOPK), ALU.mult, ALU.add))
                    link(nc.vector.tensor_tensor_scan(wk, one[:, 0:keys], equal[:, 0:keys], 0.0, ALU.mult, ALU.add))
                    link(nc.vector.scalar_tensor_tensor(out=wk, in0=wk, scalar=count[:, 1:2], in1=equal[:, 0:keys], op0=ALU.is_le, op1=ALU.mult))
                    link(nc.vector.tensor_tensor(wk, wk, above[:, 0:keys], ALU.add))
                    link(nc.vector.tensor_scalar(mask[:, i, 0:keys], wk, -NEG, NEG, ALU.mult, ALU.add))


def merge_stage(K, ya, yb, gates, merged):
    nc = K.nc
    filled, drained, chain = K.sem("merge_filled"), K.sem("merge_drained"), K.sem("merge_chain")
    groups = [Group(K, KT, 4, filled, K.slabs.n + 4 * g, 7 * g) for g in range(2)]
    K.slabs.n += KT
    with ExitStack() as local:
        part = K.buf(local, "merge_part", [P, 2, S])
        with K.stage() as block:
            @block.sync
            def _(sp):
                K.slabs.refill(sp, groups[0].n0, KT)

            @block.tensor
            def _(pe):
                for g, (group, y) in enumerate(zip(groups, (ya, yb))):
                    group.products(pe, lambda j, b, start, stop, group=group, y=y: nc.tensor.matmul(
                        K.ps[:, b, :], K.slabs.slot(group.n0 + j)[:, b * P:(b + 1) * P], y[:, j, :], start=start, stop=stop),
                        (lambda e, b: e.wait_ge(drained, b + 1)) if g else None)

            @block.vector
            def _(dve):
                link = Chain(dve, chain)
                for m in range(KT):
                    groups[0].bank_ready(dve, m)
                    nc.vector.tensor_tensor(merged(m), K.ps[:, m, :], gates[:, m, :], ALU.mult).then_inc(drained, 1)
                dve.wait_ge(drained, KT)
                for m in range(KT):
                    groups[1].bank_ready(dve, m)
                    link(nc.vector.tensor_tensor(part[:, m % 2, :], K.ps[:, m, :], gates[:, KT + m, :], ALU.mult))
                    nc.vector.tensor_tensor(merged(m), merged(m), part[:, m % 2, :], ALU.add)


def ffn_2(K):
    nc = K.nc
    turns = FF2 // D
    with ExitStack() as ffn:
        hidden = K.buf(ffn, "ff_hidden", [P, FF2 // P, S])
        filled, drained = K.sem("ff_filled"), K.sem("ff_drained")
        group = Group(K, KT, KT, filled)
        K.slabs.n += turns * KT
        with K.stage() as block:
            @block.sync
            def _(sp):
                K.slabs.refill(sp, group.n0, turns * KT)

            @block.tensor
            def _(pe):
                def product(j, b, start, stop):
                    return nc.tensor.matmul(K.ps[:, b, :], K.slabs.slot(group.n0 + j)[:, b * P:(b + 1) * P], K.xn[:, j, 0:S], start=start, stop=stop)

                group.products(pe, product)
                with pe.Fori(1, turns) as turn:
                    group.products(pe, product, lambda e, b: e.wait_ge(drained, turn * KT), turn)

            @block.scalar
            def _(act):
                with act.Fori(0, turns) as turn:
                    for m in range(KT):
                        group.bank_ready(act, m, turn)
                        nc.scalar.activation(hidden[:, bass.ds(turn * KT + m, 1), :], K.ps[:, m:m + 1, :], ACT.Relu).then_inc(drained, 1)

            @block.gpsimd
            def _(pool):
                with pool.Fori(0, turns) as turn:
                    for m in range(KT):
                        pool.wait_ge(drained, turn * KT + (m + 1))
                        at = hidden[:, bass.ds(turn * KT + m, 1), :]
                        nc.gpsimd.tensor_tensor(at, at, at, ALU.mult)
        residual_stage(K, lambda j: hidden[:, j, :], FF2 // P)


def block_2(K, ins):
    norm_stage(K, lambda k: K.h[:, k, 0:S], lambda k: K.xn[:, k, 0:S], "norm1_g_2", [(0, S)])
    with ExitStack() as mix:
        ya, yb, u, vg, q, v, k, qi = (K.buf(mix, n, [P, 4, S]) for n in ("sgu_y", "dsa_y", "sgu_u", "sgu_v", "dsa_q", "dsa_v", "dsa_k", "index_q"))
        ki = K.buf(mix, "index_k", [P, S])
        wi = K.buf(mix, "index_weights", [P, 4, 8])
        gates = K.buf(mix, "branch_gates", [P, 16, S])
        mix_in_2_stage(K, u, vg, q, v, k, qi, ki, wi, gates, ins)
        sgu_stage(K, u, vg, ya, ins)
        rope_stage(K, [(x[:, t, :], s) for x, s in ((qi, 0), (k, 0), (q, 1)) for t in range(4)] + [(ki[:], 0)], ins)
        with ExitStack() as att:
            mask = K.buf(att, "dsa_mask", [P, 4, S])
            select_stage(K, qi, ki, wi, mask, ins)

            def scores(unit, part, lo, hi, to):
                h, i, _ = unit
                rows = slice((h % 2) * HD, (h % 2 + 1) * HD)
                return K.nc.tensor.matmul(to, q[rows, h // 2, i * P:(i + 1) * P], k[rows, h // 2, lo:hi], start=True, stop=True)

            attention_stage(K, [(h, i, i + 1) for h in range(8) for i in range(4)], P, scores,
                            lambda h, t, d: v[:, t, h * HD:(h + 1) * HD],
                            lambda unit, d: yb[(unit[0] % 2) * HD:(unit[0] % 2 + 1) * HD, unit[0] // 2, unit[1] * P:(unit[1] + 1) * P],
                            bias=lambda unit: mask[:, unit[1], 0:unit[2] * P])
        merge_stage(K, ya, yb, gates, lambda m: K.xn[:, m, 0:S])
    residual_stage(K, lambda j: K.xn[:, j, 0:S], KT)
    norm_stage(K, lambda k: K.h[:, k, 0:S], lambda k: K.xn[:, k, 0:S], "norm2_g_2", [(0, S)])
    ffn_2(K)
    norm_stage(K, lambda k: K.h[:, k, 0:S], lambda k: K.xn[:, k, META:T3], "norm_f_g_2", [(0, S)])
    K.h, K.xn = K.xn, K.h


FOX_HEADS = 8
GDN_HEADS = 8
QUAD = 4


def block_3_slabs(a):
    w = a["w_in_3"]
    parts = [paired(w, [(lo, lo + 512)]) for lo in (0, 512, 1024, 1544, 2056, 2568, 3080, 3608, 4120, 4632, 5144)]
    for lo in (0, 512):
        parts += [paired(a["w_branch_fox_3"], [(lo, lo + 512)]), paired(a["w_branch_gdn_3"], [(lo, lo + 512)])]
    parts += [paired(a["w_out_3"], [(lo, lo + 512)]) for lo in (0, 512)]
    parts += [paired(a["ffn_w_up_3"], [(f, f + 256), (FF + f, FF + f + 256)]) for f in range(0, FF, 256)]
    return parts + [wide(a["ffn_w_down_3"], [(0, D)])]


def block_3_inputs(i):
    w = i["w_in_3"][0]
    small = np.concatenate([w[:, 1536:1544], w[:, 3592:3600], w[:, 3600:3608]], axis=1)
    return dict(head_w=np.ascontiguousarray(small.reshape(KT, P, 24).transpose(1, 0, 2)))


def half_group(K, filled, n0, slabs, before):
    return Group(K, 8, slabs, filled, n0, before)


def half_product(K, group, rhs):
    def product(j, b, start, stop):
        slab, (lo, hi) = K.slabs.slot(group.n0 + j), HALVES[b % 2]
        for k in range(2):
            at = k * 512 + (b // 2) * P
            mm = K.nc.tensor.matmul(K.ps[:, b, 0:hi - lo], slab[:, at:at + P], rhs(2 * j + k)[:, lo:hi], start=start and k == 0, stop=stop and k == 1)
        return mm
    return product


def mix_in_3_stage(K, fq, fk, fv, gin, heads, ins):
    nc = K.nc
    filled, drained, arrived, head_filled = K.sem("proj3_filled"), K.sem("proj3_drained"), K.sem("head_w_arrived"), K.sem("heads_filled")
    groups, before, n0 = [], 0, K.slabs.n
    for g in range(6):
        groups.append(Group(K, NC3 if g == 2 else 8, 4, filled, n0 + 4 * g, before))
        before += groups[-1].banks - 1
    K.slabs.n += 24
    out_before = [sum(x.banks for x in groups[:g]) for g in range(7)]
    with ExitStack() as local:
        w = K.buf(local, "head_w", [P, KT, 24])
        with K.stage() as block:
            @block.sync
            def _(sp):
                sp.dma_start(w[:], ins["head_w"]).then_inc(arrived, 16)
                K.slabs.refill(sp, n0, 24)

            @block.tensor
            def _(pe):
                for g, group in enumerate(groups):
                    def token_major(j, b, start, stop, group=group):
                        for k in range(2):
                            mm = nc.tensor.matmul(K.ps[0:C3, b, :], K.xn[:, 2 * j + k, b * C3:(b + 1) * C3],
                                                  K.slabs.slot(group.n0 + j)[:, k * 512:(k + 1) * 512], start=start and k == 0, stop=stop and k == 1)
                        return mm

                    def free(e, b, g=g):
                        if g:
                            e.wait_ge(drained, out_before[g - 1] + min(b + 1, groups[g - 1].banks))
                    group.products(pe, token_major if g == 2 else half_product(K, group, lambda j: K.xn[:, j, :]), free)
                pe.wait_ge(arrived, 16)
                pe.wait_ge(drained, out_before[6])
                for n in range(3):
                    for c, (lo, hi) in enumerate(HALVES):
                        for j in range(KT):
                            last = nc.tensor.matmul(K.ps[0:8, 2 * n + c, 0:hi - lo], w[:, j, n * 8:(n + 1) * 8], K.xn[:, j, lo:hi], start=j == 0, stop=j == KT - 1)
                last.then_inc(head_filled, 1)

            @block.scalar
            def _(act):
                def place(g, t, lo, hi):
                    if g < 2:
                        return (fq, fk)[g][:, t, lo:hi]
                    return gin[:, 4 * (g - 3) + t, 3 + lo:3 + hi]

                for g, group in enumerate(groups):
                    for b in range(group.banks):
                        group.bank_ready(act, b)
                        if g == 2:
                            ins_ = nc.scalar.activation(fv[:, b, :], K.ps[0:C3, b, :], ACT.Copy)
                        else:
                            (lo, hi), t = HALVES[b % 2], b // 2
                            to, src = place(g, t, lo, hi), K.ps[:, b, 0:hi - lo]
                            if g == 0:
                                ins_ = nc.scalar.activation(to, src, ACT.Copy, scale=HD ** -0.5)
                            else:
                                ins_ = nc.scalar.activation(to, src, ACT.Copy)
                        ins_.then_inc(drained, 1)
                act.wait_ge(head_filled, 1)
                for n in range(3):
                    for c, (lo, hi) in enumerate(HALVES):
                        nc.scalar.activation(heads[:, n, lo:hi], K.ps[0:8, 2 * n + c, 0:hi - lo], ACT.Copy)

            @block.vector
            def _(dve):
                nc.vector.memset(gin[:, :, 0:3], 0.0)


def gate_3_stage(K, z, gates):
    nc = K.nc
    filled, drained = K.sem("gates3_filled"), K.sem("gates3_drained")
    groups = [Group(K, 8, 4, filled, K.slabs.n + 4 * g, 7 * g) for g in range(5)]
    K.slabs.n += 20
    with K.stage() as block:
        @block.sync
        def _(sp):
            K.slabs.refill(sp, groups[0].n0, 20)

        @block.tensor
        def _(pe):
            for g, group in enumerate(groups):
                group.products(pe, half_product(K, group, lambda j: K.xn[:, j, :]),
                               (lambda e, b, g=g: e.wait_ge(drained, 8 * (g - 1) + b + 1)) if g else None)

        @block.scalar
        def _(act):
            for g, group in enumerate(groups):
                for b in range(8):
                    group.bank_ready(act, b)
                    (lo, hi), t = HALVES[b % 2], b // 2
                    src = K.ps[:, b, 0:hi - lo]
                    if g == 0:
                        nc.scalar.activation(z[:, t, lo:hi], src, ACT.Silu).then_inc(drained, 1)
                    else:
                        m = 4 * (g - 1) + t
                        nc.scalar.activation(gates[:, m, lo:hi], src, ACT.Sigmoid, bias=K.vec("gate_bias_3", m)).then_inc(drained, 1)


def head_rates_stage(K, heads, keep):
    nc = K.nc
    with ExitStack() as local:
        x = K.buf(local, "rate_x", [8, 2, T3])
        e = K.buf(local, "rate_e", [8, 2, T3])
        rate = K.buf(local, "gdn_rate", [8, 2])
        chain, e_ready, log_ready, rate_ready, summed = (K.sem(n) for n in ("rate_chain", "e_ready", "log_ready", "rate_ready", "gc_summed"))
        with K.stage() as block:
            @block.vector
            def _(dve):
                link = Chain(dve, chain)
                link(nc.vector.tensor_scalar(x[:, 0, :], heads[:, 0, :], K.vec("fgt_bias_3")[0:8, :], None, ALU.add))
                link(nc.vector.tensor_scalar(x[:, 1, :], heads[:, 2, :], K.vec("gdn_dt_bias_3")[0:8, :], None, ALU.add))
                link(nc.vector.tensor_scalar(e[:], x[:], -1.0, None, ALU.mult))
                nc.vector.tensor_tensor(e[:], e[:], x[:], ALU.min).then_inc(e_ready, 1)
                dve.wait_ge(e_ready, 1)
                dve.wait_ge(log_ready, 1)
                link(nc.vector.tensor_scalar(heads[:, 3, :], x[:, 0, :], 0.0, None, ALU.min))
                link(nc.vector.tensor_tensor(x[:, 0, :], e[:, 0, :], heads[:, 3, :], ALU.subtract))
                link(nc.vector.memset(heads[:, 3, :], 1.0))
                link(nc.vector.tensor_tensor_scan(heads[:, 0, :], heads[:, 3, :], x[:, 0, :], 0.0, ALU.mult, ALU.add))
                link(nc.vector.scalar_tensor_tensor(out=x[:, 1, :], in0=x[:, 1, :], scalar=0.0, in1=e[:, 1, :], op0=ALU.max, op1=ALU.add))
                dve.wait_ge(rate_ready, 1)
                link(nc.vector.tensor_scalar(x[:, 1, :], x[:, 1, :], rate[:, 0:1], -1.0, ALU.mult, ALU.mult))
                nc.vector.tensor_tensor_scan(heads[:, 2, :], keep, x[:, 1, :], 0.0, ALU.mult, ALU.add).then_inc(summed, 1)

            @block.scalar
            def _(act):
                nc.scalar.activation(rate[:, 0:1], K.vec("gdn_a_log_3")[0:8, :], ACT.Exp).then_inc(rate_ready, 1)
                act.wait_ge(e_ready, 1)
                nc.scalar.activation(e[:], e[:], ACT.Exp).then_inc(e_ready, 1)
                act.wait_ge(e_ready, 2)
                nc.scalar.activation(e[:], e[:], ACT.Ln, bias=K.one_col[0:8, :]).then_inc(log_ready, 1)
                act.wait_ge(summed, 1)
                nc.scalar.activation(heads[:, 3, :], heads[:, 2, :], ACT.Exp)
                nc.scalar.activation(heads[:, 1, :], heads[:, 1, :], ACT.Sigmoid)


def conv_silu_stage(K, gin):
    nc = K.nc
    with ExitStack() as local:
        c = K.buf(local, "gdn_conv", [P, 2, T3])
        conv, done, chain = K.sem("gdn_conv_done"), K.sem("gdn_silu_done"), K.sem("gdn_conv_chain")
        with K.stage() as block:
            @block.vector
            def _(dve):
                link = Chain(dve, chain)
                for t in range(12):
                    to = c[:, t % 2, :]
                    if t >= 2:
                        dve.wait_ge(done, t - 1)
                    link(nc.vector.tensor_scalar(to, gin[:, t, 0:T3], K.vec("gdn_conv_w_3", t), None, ALU.mult))
                    for tap in range(1, 4):
                        ins = nc.vector.scalar_tensor_tensor(out=to, in0=gin[:, t, tap:tap + T3], scalar=K.vec("gdn_conv_w_3", 12 * tap + t), in1=to, op0=ALU.mult, op1=ALU.add)
                        if tap < 3:
                            link(ins)
                    ins.then_inc(conv, 1)

            @block.scalar
            def _(act):
                for t in range(12):
                    act.wait_ge(conv, t + 1)
                    nc.scalar.activation(gin[:, t, 3:3 + T3], c[:, t % 2, :], ACT.Silu).then_inc(done, 1)


def gdn_rates_stage(K, heads, q, q0, tok, last_decay):
    nc = K.nc
    with ExitStack() as local:
        turned, turned_out, spread, chain, exped, q_filled, q_out, last_in = (K.sem(n) for n in ("rates_turned", "rates_out", "rates_spread", "rates_chain", "rates_exped", "q_filled", "q_out", "last_in"))
        last_sum = K.buf(local, "last_sum", [8, NC3])
        with K.stage() as block:
            @block.tensor
            def _(pe):
                for n, row in enumerate((1, 2, 3)):
                    for c in range(NC3):
                        last = nc.tensor.transpose(K.ps[0:C3, n, c * 8:(c + 1) * 8], heads[:, row, c * C3:(c + 1) * C3], K.ident[0:8, 0:8])
                last.then_inc(turned, 1)
                pe.wait_ge(last_in, 1)
                for h in range(GDN_HEADS):
                    last = nc.tensor.matmul(K.ps[:, 3, h * NC3:(h + 1) * NC3], K.pick(h, P), last_sum[:], start=True, stop=True)
                last.then_inc(spread, 1)
                for h in range(GDN_HEADS):
                    for c, (lo, hi) in enumerate(HALVES):
                        n = 2 * h + c
                        if n >= 4:
                            pe.wait_ge(q_out, n - 3)
                        nc.tensor.matmul(K.ps[:, 4 + n % 4, 0:hi - lo], K.pick(h, P), heads[:, 3, lo:hi], start=True, stop=True).then_inc(q_filled, 1)

            @block.vector
            def _(dve):
                link = Chain(dve, chain)
                nc.vector.tensor_copy(last_sum[:], heads[:, 2, :].rearrange("h (c i) -> h c i", i=C3)[:, :, C3 - 1]).then_inc(last_in, 1)
                dve.wait_ge(turned, 1)
                flat = tok[:].rearrange("p n c h -> p n (c h)")
                for n in range(3):
                    link(nc.vector.tensor_copy(flat[:, n, :], K.ps[0:C3, n, 0:NC3 * 8]))
                link(nc.vector.tensor_tensor(flat[:, 2, :], flat[:, 2, :], flat[:, 0, :], ALU.mult))
                dve.wait_ge(spread, 1)
                sums = K.ps[0:C3, 3, 0:NC3 * 8].rearrange("p (h c) -> p c h", c=NC3)
                nc.vector.tensor_tensor(tok[:, 3], sums, tok[:, 1], ALU.subtract).then_inc(turned_out, 1)
                for h in range(GDN_HEADS):
                    rows = slice((h % 2) * HD, (h % 2 + 1) * HD)
                    for c, (lo, hi) in enumerate(HALVES):
                        n = 2 * h + c
                        dve.wait_ge(q_filled, n + 1)
                        nc.vector.tensor_tensor(q0[:, h, lo:hi], K.ps[rows, 4 + n % 4, 0:hi - lo], q[rows, h // 2, lo:hi], ALU.mult).then_inc(q_out, 1)

            @block.scalar
            def _(act):
                act.wait_ge(turned_out, 1)
                nc.scalar.activation(tok[:, 3], tok[:, 3], ACT.Exp)
                nc.scalar.activation(last_decay[:].rearrange("p h c -> p (h c)"), K.ps[0:HD, 3, 0:NC3 * 8], ACT.Exp)


def gdn_chunk_stage(K, gin, heads, tok, k_tok, v_tok, out, ins):
    nc = K.nc
    (kcdT, value, attnT) = out
    U = NC3 * 2
    SH = [C3, QUAD, C3]
    with ExitStack() as local:
        masks_in = K.buf(local, "gdn_masks", [C3, LEVELS_G + 5, C3])
        prod, amask = (K.buf(local, n, [C3, 2, QUAD, C3]) for n in ("gdn_prod", "gdn_A_level"))
        amat, inv, invT, up, down = (K.buf(local, n, [C3, 1, QUAD, C3]) for n in ("gdn_A", "gdn_inv", "gdn_invT", "gdn_up", "gdn_down"))
        bv, bk = (K.buf(local, n, [C3, 2, QUAD, HD]) for n in ("gdn_beta_v", "gdn_beta_k"))
        arrived, chain, sums_filled, split, exped, pairs_filled, first, invT_filled, masked, z_filled, z_out, d_filled, d_added, x_filled, x_out, rhs_ready, attn_out, pool_chain = (
            K.sem(n) for n in ("gdn_masks_arrived", "gdn_chain", "sums_filled", "split", "decays_exped", "gdn_pairs_filled", "inv_first",
                               "invT_filled", "gdn_masked", "gdn_z_filled", "gdn_z_out", "gdn_d_filled", "gdn_d_added", "gdn_x_filled",
                               "gdn_x_out", "rhs_ready", "attn_out", "gdn_pool_chain"))

        def mask(n):
            return masks_in[:, n:n + 1, :].to_broadcast(SH)

        def over(n, c, q, width):
            return tok[:, n, c, q:GDN_HEADS:2].unsqueeze(2).to_broadcast((C3, QUAD, width))

        def own(t, c, q):
            return t[:, c, q:GDN_HEADS:2, :]

        def bank(b):
            return K.ps[0:C3, b, 0:QUAD * C3].rearrange("p (h i) -> p h i", i=C3)

        def head(base, h, c):
            rows = slice((h % 2) * HD, (h % 2 + 1) * HD)
            return gin[rows, base + h // 2, 3 + c * C3:3 + (c + 1) * C3]

        units = [(c, q) for c in range(NC3) for q in range(2)]
        LV = LEVELS_G - 1
        with K.stage() as block:
            @block.sync
            def _(sp):
                sp.dma_start(masks_in[:], ins["c_levels_g"][0:C3]).then_inc(arrived, 16)

            @block.tensor
            def _(pe):
                for u, (c, q) in enumerate(units):
                    if u:
                        pe.wait_ge(attn_out, u)
                        pe.wait_ge(first, u)
                    for i in range(QUAD):
                        last = nc.tensor.matmul(bank(0)[:, i, :], K.pick(2 * i + q, C3), heads[:, 2, c * C3:(c + 1) * C3], start=True, stop=True)
                    last.then_inc(sums_filled, 1)
                    for i in range(QUAD):
                        h = 2 * i + q
                        nc.tensor.matmul(bank(1)[:, i, :], head(4, h, c), head(4, h, c), start=True, stop=True)
                    for i in range(QUAD):
                        h = 2 * i + q
                        last = nc.tensor.matmul(bank(2)[:, i, :], head(4, h, c), head(0, h, c), start=True, stop=True)
                    last.then_inc(pairs_filled, 1)
                    pe.wait_ge(first, u + 1)
                    for i in range(QUAD):
                        last = nc.tensor.transpose(bank(3)[:, i, :], inv[:, 0, i, :], K.ident[0:C3, 0:C3])
                    last.then_inc(invT_filled, 1)
                    for l in range(LV):
                        n = u * LV + l
                        pe.wait_ge(masked, n + 1)
                        pe.wait_ge(d_added, 2 * n + u + 1)
                        for i in range(QUAD):
                            last = nc.tensor.matmul(bank(4)[:, i, :], amask[:, l % 2, i, :], invT[:, 0, i, :], start=True, stop=True)
                        last.then_inc(z_filled, 1)
                        pe.wait_ge(z_out, n + 1)
                        if l < LV - 1:
                            for i in range(QUAD):
                                nc.tensor.matmul(bank(5)[:, i, :], prod[:, l % 2, i, :], inv[:, 0, i, :], start=True, stop=True)
                        for i in range(QUAD):
                            last = nc.tensor.matmul(bank(6)[:, i, :], inv[:, 0, i, :], prod[:, l % 2, i, :], start=True, stop=True)
                        last.then_inc(d_filled, 1)
                    pe.wait_ge(d_added, 2 * LV * (u + 1) + u + 1)
                    pe.wait_ge(rhs_ready, u + 1)
                    for i in range(QUAD):
                        nc.tensor.matmul(K.ps[0:HD, 7, i * C3:(i + 1) * C3], bk[:, u % 2, i, :], invT[:, 0, i, :], start=True, stop=True)
                    for i in range(QUAD):
                        last = nc.tensor.matmul(K.ps[0:C3, 3, i * HD:(i + 1) * HD], invT[:, 0, i, :], bv[:, u % 2, i, :], start=True, stop=True)
                    last.then_inc(x_filled, 1)
                    pe.wait_ge(x_out, 2 * (u + 1))

            @block.vector
            def _(dve):
                link = Chain(dve, chain)
                dve.wait_ge(arrived, 16)
                for u, (c, q) in enumerate(units):
                    w = 0
                    dve.wait_ge(sums_filled, u + 1)
                    link(nc.vector.tensor_tensor(amask[:, 0], bank(0), over(1, c, q, C3), ALU.subtract))
                    nc.vector.tensor_scalar(down[:, w], amask[:, 0], 0.0, None, ALU.max).then_inc(split, 1)
                    nc.vector.tensor_scalar(up[:, w], amask[:, 0], 0.0, None, ALU.min).then_inc(split, 1)
                    dve.wait_ge(pairs_filled, u + 1)
                    dve.wait_ge(exped, 2 * u + 1)
                    link(nc.vector.tensor_tensor(amat[:, w], bank(1), down[:, w], ALU.mult))
                    link(nc.vector.scalar_tensor_tensor(out=amat[:, w], in0=amat[:, w], scalar=-1.0, in1=over(0, c, q, C3), op0=ALU.mult, op1=ALU.mult))
                    link(nc.vector.tensor_tensor(amat[:, w], amat[:, w], mask(LEVELS_G + 2), ALU.mult))
                    link(nc.vector.tensor_tensor(inv[:, w], amat[:, w], mask(0), ALU.mult))
                    nc.vector.tensor_tensor(inv[:, w], inv[:, w], mask(LEVELS_G + 1), ALU.add).then_inc(first, 1)
                    dve.wait_ge(exped, 2 * u + 2)
                    link(nc.vector.tensor_tensor(up[:, w], bank(2), up[:, w], ALU.mult))
                    at = own(attnT, c, q)
                    nc.vector.tensor_tensor(at, up[:, w], mask(LEVELS_G + 4), ALU.mult).then_inc(attn_out, 1)
                    dve.wait_ge(invT_filled, u + 1)
                    nc.vector.tensor_copy(invT[:, w], bank(3)).then_inc(d_added, 1)
                    for l in range(LV):
                        n = u * LV + l
                        nc.vector.tensor_tensor(amask[:, l % 2], amat[:, w], mask(l + 1), ALU.mult).then_inc(masked, 1)
                        dve.wait_ge(d_filled, n + 1)
                        if l < LV - 1:
                            nc.vector.tensor_tensor(inv[:, w], bank(5), inv[:, w], ALU.add).then_inc(d_added, 1)
                        else:
                            nc.vector.tensor_copy(inv[:, w, 0, 0:1], inv[:, w, 0, 0:1]).then_inc(d_added, 1)
                        nc.vector.tensor_tensor(invT[:, w], bank(6), invT[:, w], ALU.add).then_inc(d_added, 1)
                        dve.wait_ge(d_added, 2 * (n + 1) + u + 1)

            @block.scalar
            def _(act):
                for u, (c, q) in enumerate(units):
                    w = 0
                    act.wait_ge(split, 2 * u + 1)
                    nc.scalar.activation(down[:, w], down[:, w], ACT.Exp, scale=-1.0).then_inc(exped, 1)
                    act.wait_ge(split, 2 * u + 2)
                    nc.scalar.activation(up[:, w], up[:, w], ACT.Exp).then_inc(exped, 1)
                    for l in range(LV):
                        n = u * LV + l
                        act.wait_ge(z_filled, n + 1)
                        nc.scalar.activation(prod[:, l % 2], bank(4), ACT.Copy).then_inc(z_out, 1)
                    act.wait_ge(x_filled, u + 1)
                    nc.scalar.activation(own(kcdT, c, q), K.ps[0:HD, 7, 0:QUAD * C3].rearrange("p (h i) -> p h i", i=C3), ACT.Copy).then_inc(x_out, 1)
                    nc.scalar.activation(own(value, c, q), K.ps[0:C3, 3, 0:QUAD * HD].rearrange("p (h i) -> p h i", i=HD), ACT.Copy).then_inc(x_out, 1)

            @block.gpsimd
            def _(pool):
                link = Chain(pool, pool_chain)
                for u, (c, q) in enumerate(units):
                    if u >= 2:
                        pool.wait_ge(x_filled, u - 1)
                    keys, values = (own(t[:].rearrange("p c (h i) -> p c h i", i=HD), c, q) for t in (k_tok, v_tok))
                    link(nc.gpsimd.tensor_tensor(bv[:, u % 2], values, over(0, c, q, HD), ALU.mult))
                    link(nc.gpsimd.tensor_tensor(bk[:, u % 2], keys, over(2, c, q, HD), ALU.mult))
                    nc.gpsimd.tensor_tensor(keys, keys, over(3, c, q, HD), ALU.mult).then_inc(rhs_ready, 1)


def gdn_scan_stage(K, mats, k_tail, q0, last_decay, y):
    nc = K.nc
    (kcdT, value, attnT) = mats
    H = GDN_HEADS
    with ExitStack() as local:
        state = K.buf(local, "gdn_state", [HD, 2, H, HD])
        kept = K.buf(local, "gdn_kept", [HD, H, HD])
        vn = K.buf(local, "gdn_new_values", [C3, 2, H, HD])
        cleared, v_filled, v_ready, s_filled, s_ready, y_filled, y_out, chain = (K.sem(n) for n in (
            "gdn_cleared", "gdn_v_filled", "gdn_v_ready", "gdn_s_filled", "gdn_s_ready", "gdn_y_filled", "gdn_y_out", "gdn_scan_chain"))

        def grid(rows, b, i):
            return K.ps[0:rows, b, 0:H * HD].rearrange("p (h i) -> p h i", i=i)

        with K.stage() as block:
            @block.tensor
            def _(pe):
                pe.wait_ge(cleared, 1)
                for c in range(NC3):
                    s = state[:, c % 2]
                    if c:
                        pe.wait_ge(s_ready, c)
                    for h in range(H):
                        last = nc.tensor.matmul(grid(C3, c % 2, HD)[:, h, :], kcdT[:, c, h, :], s[:, h, :], start=True, stop=True)
                    last.then_inc(v_filled, 1)
                    pe.wait_ge(v_ready, c + 1)
                    for h in range(H):
                        last = nc.tensor.matmul(grid(HD, 2 + c % 2, HD)[:, h, :], k_tail[:, c, h * HD:(h + 1) * HD], vn[:, c % 2, h, :], start=True, stop=True)
                    last.then_inc(s_filled, 1)
                    if c >= 2:
                        pe.wait_ge(y_out, 4 * (c - 1))
                    for h in range(H):
                        b = 4 + 2 * (c % 2) + h // QUAD
                        to = K.ps[0:HD, b, (h % QUAD) * C3:(h % QUAD + 1) * C3]
                        nc.tensor.matmul(to, s[:, h, :], q0[:, h, c * C3:(c + 1) * C3], start=True, stop=False)
                        last = nc.tensor.matmul(to, vn[:, c % 2, h, :], attnT[:, c, h, :], start=False, stop=True)
                    last.then_inc(y_filled, 1)

            @block.vector
            def _(dve):
                link = Chain(dve, chain)
                nc.vector.memset(state[:, 0], 0.0).then_inc(cleared, 1)
                dve.wait_ge(cleared, 1)
                for c in range(NC3):
                    dve.wait_ge(v_filled, c + 1)
                    if c >= 2:
                        dve.wait_ge(y_filled, c - 1)
                    nc.vector.scalar_tensor_tensor(out=vn[:, c % 2], in0=grid(C3, c % 2, HD), scalar=-1.0, in1=value[:, c], op0=ALU.mult, op1=ALU.add).then_inc(v_ready, 1)
                    link(nc.vector.tensor_tensor(kept[:], state[:, c % 2], last_decay[:, :, c:c + 1].to_broadcast((HD, H, HD)), ALU.mult))
                    dve.wait_ge(s_filled, c + 1)
                    if c:
                        dve.wait_ge(y_filled, c)
                    nc.vector.tensor_tensor(state[:, (c + 1) % 2], grid(HD, 2 + c % 2, HD), kept[:], ALU.add).then_inc(s_ready, 1)
                    dve.wait_ge(s_ready, c + 1)

            @block.scalar
            def _(act):
                for c in range(NC3):
                    act.wait_ge(y_filled, c + 1)
                    for half in range(2):
                        src = K.ps[0:HD, 4 + 2 * (c % 2) + half, 0:QUAD * C3].rearrange("p (t o i) -> p t o i", o=2, i=C3)
                        for odd in range(2):
                            nc.scalar.activation(y[odd * HD:(odd + 1) * HD, 2 * half:2 * half + 2, c * C3:(c + 1) * C3], src[:, :, odd, :], ACT.Copy).then_inc(y_out, 1)


def multiply_stage(K, dst, other):
    with K.stage() as block:
        @block.vector
        def _(dve):
            K.nc.vector.tensor_tensor(dst, dst, other, ALU.mult)


def merge_3_stage(K, yf, yg, gates, merged):
    nc = K.nc
    filled, drained, chain = K.sem("merge3_filled"), K.sem("merge3_drained"), K.sem("merge3_chain")
    groups = [Group(K, 8, 2, filled, K.slabs.n + 2 * g, 7 * g) for g in range(4)]
    K.slabs.n += 8
    with ExitStack() as local:
        part = K.buf(local, "merge3_part", [P, 2, T3 // 2])
        with K.stage() as block:
            @block.sync
            def _(sp):
                K.slabs.refill(sp, groups[0].n0, 8)

            @block.tensor
            def _(pe):
                for g, group in enumerate(groups):
                    group.products(pe, half_product(K, group, lambda j, y=(yf, yg)[g % 2]: y[:, j, :]),
                                   (lambda e, b, g=g: e.wait_ge(drained, 8 * (g - 1) + b + 1)) if g else None)

            @block.vector
            def _(dve):
                link = Chain(dve, chain)
                for g, group in enumerate(groups):
                    for b in range(8):
                        (lo, hi), m = HALVES[b % 2], 4 * (g // 2) + b // 2
                        group.bank_ready(dve, b)
                        gate, src = gates[:, KT * (g % 2) + m, lo:hi], K.ps[:, b, 0:hi - lo]
                        if g % 2 == 0:
                            nc.vector.tensor_tensor(merged(m)[:, lo:hi], src, gate, ALU.mult).then_inc(drained, 1)
                        else:
                            nc.vector.tensor_tensor(part[:, b % 2, :], src, gate, ALU.mult).then_inc(drained, 1)
                            dve.wait_ge(drained, 8 * g + b + 1)
                            link(nc.vector.tensor_tensor(merged(m)[:, lo:hi], merged(m)[:, lo:hi], part[:, b % 2, :], ALU.add))


def residual_3_stage(K, rhs):
    nc = K.nc
    filled, drained = K.sem("out3_filled"), K.sem("out3_drained")
    groups = [Group(K, 8, 4, filled, K.slabs.n + 4 * g, 7 * g) for g in range(2)]
    K.slabs.n += 8
    with K.stage() as block:
        @block.sync
        def _(sp):
            K.slabs.refill(sp, groups[0].n0, 8)

        @block.tensor
        def _(pe):
            for g, group in enumerate(groups):
                group.products(pe, half_product(K, group, rhs), (lambda e, b: e.wait_ge(drained, b + 1)) if g else None)

        @block.vector
        def _(dve):
            for g, group in enumerate(groups):
                for b in range(8):
                    (lo, hi), m = HALVES[b % 2], 4 * g + b // 2
                    group.bank_ready(dve, b)
                    nc.vector.tensor_tensor(K.h[:, m, lo:hi], K.ps[:, b, 0:hi - lo], K.h[:, m, lo:hi], ALU.add).then_inc(drained, 1)


def conv_ffn_3(K):
    nc = K.nc
    with ExitStack() as ffn:
        hidden = K.buf(ffn, "ffn3_hidden", [P, FT, S])
        raw = K.buf(ffn, "ffn3_raw", [P, 2, 4, T3])
        c = K.buf(ffn, "ffn3_conv", [P, 2, 4, S])
        filled, drained, conv, silu, chain, multiplied = (K.sem(n) for n in ("up3_filled", "up3_drained", "conv3_done", "silu_done", "conv3_chain", "ffn3_multiplied"))
        G = FT // 2
        groups = [Group(K, 8, 4, filled, K.slabs.n + 4 * g, 7 * g) for g in range(G)]
        K.slabs.n += 4 * G
        with K.stage() as block:
            @block.sync
            def _(sp):
                K.slabs.refill(sp, groups[0].n0, 4 * G)

            @block.tensor
            def _(pe):
                for g, group in enumerate(groups):
                    group.products(pe, half_product(K, group, lambda j: K.xn[:, j, :]),
                                   (lambda e, b, g=g: e.wait_ge(drained, 8 * (g - 1) + b + 1)) if g else None)

            @block.scalar
            def _(act):
                for g, group in enumerate(groups):
                    if g >= 2:
                        act.wait_ge(conv, 4 * (g - 1))
                    for b in range(8):
                        lo, hi = HALVES[b % 2]
                        group.bank_ready(act, b)
                        nc.scalar.activation(raw[:, g % 2, b // 2, lo:hi], K.ps[:, b, 0:hi - lo], ACT.Copy).then_inc(drained, 1)
                    for i in range(2):
                        act.wait_ge(conv, 4 * g + i + 1)
                        nc.scalar.activation(hidden[:, 2 * g + i, :], c[:, g % 2, i, :], ACT.Silu).then_inc(silu, 1)

            @block.vector
            def _(dve):
                link = Chain(dve, chain)
                for g in range(G):
                    for i in range(4):
                        f = 2 * g + i if i < 2 else FT + 2 * g + i - 2
                        dve.wait_ge(drained, 8 * g + 2 * i + 2)
                        if g >= 2:
                            dve.wait_ge(silu, 2 * (g - 1))
                            dve.wait_ge(multiplied, 2 * (g - 1))
                        x, to = raw[:, g % 2, i, :], c[:, g % 2, i, :]
                        link(nc.vector.tensor_scalar(to, x[:, META - 2:T3 - 2], K.vec("ffn_conv_w_3", f), K.vec("ffn_conv_b_3", f), ALU.mult, ALU.add))
                        link(nc.vector.scalar_tensor_tensor(out=to, in0=x[:, META - 1:T3 - 1], scalar=K.vec("ffn_conv_w_3", 2 * FT + f), in1=to, op0=ALU.mult, op1=ALU.add))
                        nc.vector.scalar_tensor_tensor(out=to, in0=x[:, META:T3], scalar=K.vec("ffn_conv_w_3", 4 * FT + f), in1=to, op0=ALU.mult, op1=ALU.add).then_inc(conv, 1)

            @block.gpsimd
            def _(pool):
                for g in range(G):
                    for i in range(2):
                        pool.wait_ge(silu, 2 * g + i + 1)
                        pool.wait_ge(conv, 4 * g + 2 + i + 1)
                        at = hidden[:, 2 * g + i, :]
                        nc.gpsimd.tensor_tensor(at, at, c[:, g % 2, 2 + i, :], ALU.mult).then_inc(multiplied, 1)
        residual_stage(K, lambda j: hidden[:, j, :], FT, (META, T3))


def load_meta_stage(K, ins, keep, causal):
    nc = K.nc
    arrived = K.sem("meta_arrived")
    with K.stage() as block:
        @block.sync
        def _(sp):
            sp.dma_start(K.h[:, :, 0:META], ins["meta"]).then_inc(arrived, 16)
            sp.dma_start(keep[:], ins["c_gdn_keep"][0:8, :]).then_inc(arrived, 16)
            sp.dma_start(causal[:], ins["c_causal88"][0:C3, 0:C3]).then_inc(arrived, 16)
            sp.wait_ge(arrived, 48)


def block_3(K, ins):
    with ExitStack() as mix:
        heads = K.buf(mix, "head_rates", [8, 4, T3])
        yf = K.buf(mix, "fox_y", [P, 4, T3])
        gin = K.buf(mix, "gdn_in", [P, 12, 3 + T3])
        yg = gin[:, 0:4, 3:3 + T3]
        with ExitStack() as fox:
            keep = K.buf(fox, "gdn_keep", [8, T3])
            causal = K.buf(fox, "causal88", [C3, C3])
            load_meta_stage(K, ins, keep, causal)
            norm_stage(K, lambda k: K.h[:, k, :], lambda k: K.xn[:, k, :], "norm_mix_w_3", HALVES)
            fq, fk = (K.buf(fox, n, [P, 4, T3]) for n in ("fox_q", "fox_k"))
            fv = K.buf(fox, "fox_v", [C3, NC3, 512])
            mix_in_3_stage(K, fq, fk, fv, gin, heads, ins)
            head_rates_stage(K, heads, keep[:])

            def scores(unit, part, lo, hi, to):
                h, i, _ = unit
                rows = slice((h % 2) * HD, (h % 2 + 1) * HD)
                K.nc.tensor.matmul(to, fq[rows, h // 2, i * C3:(i + 1) * C3], fk[rows, h // 2, lo:hi], start=True, stop=False)
                return K.nc.tensor.matmul(to, K.pick(h, C3), heads[:, 0, lo:hi], start=False, stop=True)

            attention_stage(K, [(h, i, i + 1) for h in range(FOX_HEADS) for i in range(NC3)], C3, scores,
                            lambda h, t, d: fv[:, t, h * HD:(h + 1) * HD],
                            lambda unit, d: yf[(unit[0] % 2) * HD:(unit[0] % 2 + 1) * HD, unit[0] // 2, unit[1] * C3:(unit[1] + 1) * C3],
                            diagonal=causal[:])
        conv_silu_stage(K, gin)
        head_norm_stage(K, [([(gin[:, t, 3 + lo:3 + hi], gin[:, t, 3 + lo:3 + hi], None)], K.blk, 1, HD if t < 4 else 1)
                            for t in range(8) for lo, hi in HALVES])
        with ExitStack() as gdn:
            q0 = K.buf(gdn, "gdn_q0", [HD, GDN_HEADS, T3])
            tok = K.buf(gdn, "gdn_tok_rates", [C3, 4, NC3, 8])
            last_decay = K.buf(gdn, "gdn_last_decay", [HD, GDN_HEADS, NC3])
            k_tok, v_tok = (K.buf(gdn, n, [C3, NC3, 512]) for n in ("gdn_k_tok", "gdn_v_tok"))
            kcdT = K.buf(gdn, "gdn_kcdT", [HD, NC3, GDN_HEADS, C3])
            value = v_tok[:].rearrange("p c (h i) -> p c h i", i=HD)
            gdn_rates_stage(K, heads, gin[:, 0:4, 3:3 + T3], q0, tok, last_decay)
            token_tiles_stage(K, [(gin[:, b + t, 3:3 + T3], (lambda c, n, to=to, t=t: to[:, c:c + n, t * P:(t + 1) * P]))
                                  for b, to in ((4, k_tok), (8, v_tok)) for t in range(4)], C3, NC3)
            attnT = K.buf(gdn, "gdn_attnT", [C3, NC3, GDN_HEADS, C3])
            mats = (kcdT, value, attnT)
            gdn_chunk_stage(K, gin, heads, tok, k_tok, v_tok, mats, ins)
            gdn_scan_stage(K, mats, k_tok, q0, last_decay, yg)
        head_norm_stage(K, [([(yg[:, t, lo:hi], yg[:, t, lo:hi], K.vec("gdn_norm_w_3"))], K.blk, HD, 1) for t in range(4) for lo, hi in HALVES])
        gates = K.buf(mix, "branch3_gates", [P, 16, T3])
        z = K.buf(mix, "gdn_z", [P, 4, T3])
        gate_3_stage(K, z, gates)
        multiply_stage(K, yg, z[:])
        merge_3_stage(K, yf, yg, gates, lambda m: K.xn[:, m, :])
    residual_3_stage(K, lambda j: K.xn[:, j, :])
    norm_stage(K, lambda k: K.h[:, k, :], lambda k: K.xn[:, k, :], "norm_ffn_w_3", HALVES)
    conv_ffn_3(K)
    norm_stage(K, lambda k: K.h[:, k, :], lambda k: K.xn[:, k, :], "norm_final_w_3", [(META, T3)])


def device_inputs(i):
    vec = {}
    for name, (at, n) in VEC_COLS.items():
        v = i[name]
        if v.size < HD:
            vec[name] = short_column(v)
        elif v.size == HD:
            vec[name] = columns(np.concatenate([v.reshape(-1)] * 2))
        else:
            vec[name] = columns(v)
    arrays = shape_constants()
    arrays["c_levels_r"] = np.ascontiguousarray(arrays["c_levels_r"][:CH])
    pool_w = np.zeros((P, 2, P), np.float32)
    for g in range(4):
        r = slice((g % 2) * HD, (g % 2 + 1) * HD)
        pool_w[r, g // 2, r] = i["pool_w"][0, g]
    lora = np.stack([np.concatenate([i["rwkv_w2"][0], i["rwkv_a2"][0]]), i["rwkv_g2"][0]], axis=1)
    lam = np.stack([i[n][0] for n in ("diff_lq1", "diff_lk1", "diff_lq2", "diff_lk2")])
    arrays.update(
        stream=weight_stream(i), x=features(i["x"][0]), mem=features(i["mem"][0]), meta=features(i["meta_tokens_3"]),
        vecs=np.ascontiguousarray(np.concatenate([vec[n] for n in VEC_COLS], axis=1)),
        pool_w=pool_w, rwkv_lora=np.ascontiguousarray(lora),
        diff_lambda=np.ascontiguousarray(np.broadcast_to(lam, (P, 4, HD))))
    arrays.update(block_2_inputs(i))
    arrays.update(block_3_inputs(i))
    return arrays


def build(nc, ins, out, total):
    with ExitStack() as ctx:
        K = Core(nc, ctx, ins["stream"], total)
        load_stage(K, ins)
        block_1(K, ins)
        block_2(K, ins)
        block_3(K, ins)
        store_stage(K, out)


def store_stage(K, out):
    nc = K.nc
    stored = K.sem("stored")
    with K.stage() as block:
        @block.sync
        def _(sp):
            sp.dma_start(out, K.xn[:, :, META:T3]).then_inc(stored, 16)
            sp.wait_ge(stored, 16)


def features(a):
    a = a.reshape(a.shape[-2], -1)
    return np.ascontiguousarray(a.T.reshape(-1, P, a.shape[0]).transpose(1, 0, 2))


def columns(a):
    return a.reshape(-1, P).T


def short_column(a):
    out = np.zeros((P, 1), a.dtype)
    out[:a.size, 0] = a.reshape(-1)
    return out


def wide(w, cols):
    w = np.concatenate([w[:, lo:hi] for lo, hi in cols], axis=1)
    w = w.reshape(-1, P, w.shape[1])
    if w.shape[2] == D:
        return w
    out = np.zeros((w.shape[0], P, D), w.dtype)
    out[:, :, :w.shape[2]] = w
    return out


def paired(w, cols):
    w = np.concatenate([w[:, lo:hi] for lo, hi in cols], axis=1)
    n = w.shape[1]
    if n < 512:
        w = np.concatenate([w, np.zeros((w.shape[0], 512 - n), w.dtype)], axis=1)
    return np.ascontiguousarray(w.reshape(-1, 2, P, 512).transpose(0, 2, 1, 3)).reshape(-1, P, D)


def weight_stream(i):
    a = {k: v[0] for k, v in i.items() if v.ndim == 3}
    w = a["w_in"]
    parts = [wide(w, [(0, 1024)]), wide(w, [(1024, 2048)]), wide(w, [(2048, 2816)]), wide(a["w_out"], [(0, D)]),
             wide(a["xa_wq"], [(0, D)]), wide(a["xa_wk"], [(0, D)]), wide(a["xa_wv"], [(0, D)]), wide(a["xa_wo"], [(0, D)])]
    for f in range(0, FF, 512):
        e = min(FF, f + 512)
        parts.append(wide(a["ffn_w_up"], [(f, e), (FF + f, FF + e)]))
    parts.append(wide(a["ffn_w_down"], [(0, D)]))
    parts += block_2_slabs(a) + block_3_slabs(a)
    return np.concatenate(parts)


def kernel(**inputs):
    import concourse.bacc as bacc
    from concourse.bass_utils import run_bass_kernel_spmd

    i = {k: np.asarray(v) for k, v in inputs.items()}
    arrays = device_inputs(i)
    nc = bacc.Bacc("TRN2", target_bir_lowering=False, num_devices=1)
    aps = {k: nc.dram_tensor(f"in_{k}", v.shape, F32, kind="ExternalInput").ap() for k, v in arrays.items()}
    out = nc.dram_tensor("out_features", (P, KT, S), F32, kind="ExternalOutput").ap()
    build(nc, aps, out, arrays["stream"].shape[0])
    r = run_bass_kernel_spmd(nc, [{f"in_{k}": v for k, v in arrays.items()}], core_ids=[0])
    got = r.results[0]["out_features"]
    return np.ascontiguousarray(got.transpose(1, 0, 2).reshape(D, S).T).reshape(1, S, D)
```

```python
from contextlib import ExitStack, contextmanager

import numpy as np

import concourse.bass as bass
from concourse import mybir

F32 = mybir.dt.float32
F32R = mybir.dt.float32r
ALU = mybir.AluOpType
ACT = mybir.ActivationFunctionType
AX = mybir.AxisListType.X

P = 128
D = 1024
KT = D // P
S = 512
META = 16
T3 = S + META
MEM = 256
FF = 2816
FT = FF // P
FF2 = 4096
CH = 64
NCH = S // CH
HD = 64
C3 = 88
NC3 = T3 // C3
SLOTS = 4
PARTS = 2
EPS = 1e-6
GN_EPS = 64e-5
LAMBDA_INIT = 0.2
SUBLN = (1.0 - LAMBDA_INIT) ** -2
TOPK = 128
NEG = -1.0e30
LOWEST = -3.0e38
HALVES = [(0, T3 // 2), (T3 // 2, T3)]

VEC_COLS = {}


def _vec(name, n):
    VEC_COLS[name] = (sum(c for _, c in VEC_COLS.values()), n)


for _n, _c in [("mix_norm_g", KT), ("pool_scale", 2), ("rwkv_mu", 8), ("rwkv_w0", 2), ("rwkv_a0", 2),
               ("rwkv_k_k", 2), ("rwkv_k_a", 2), ("rwkv_r_k", 2), ("rwkv_ln_w", 2), ("rwkv_ln_b", 2),
               ("diff_q_norm", 1), ("diff_k_norm", 1), ("diff_subln", 1), ("xa_norm_g", KT),
               ("mem_norm_g", KT), ("xa_q_norm", 2), ("xa_k_norm", 2), ("ffn_norm_g", KT),
               ("ffn_conv_w", 3 * FT), ("ffn_conv_b", FT),
               ("norm1_g_2", KT), ("norm2_g_2", KT), ("norm_f_g_2", KT),
               ("fgt_bias_3", 1), ("gdn_a_log_3", 1), ("gdn_dt_bias_3", 1), ("gdn_conv_w_3", 4 * 12),
               ("gdn_norm_w_3", 1), ("gate_bias_3", 16), ("norm_mix_w_3", KT), ("norm_ffn_w_3", KT),
               ("ffn_conv_w_3", 3 * 2 * FT), ("ffn_conv_b_3", 2 * FT), ("norm_final_w_3", KT)]:
    _vec(_n, _c)
NVEC = sum(c for _, c in VEC_COLS.values())

LEVELS_R = 6
LEVELS_G = 7


def shape_constants():
    i = np.arange(P)
    ident = np.eye(P)
    ones = np.ones((P, P))
    blk = (i[:, None] // HD == i[None, :] // HD) * 1.0
    half = HD // 2
    rot = np.zeros((P, P))
    for p in range(P):
        if p % HD < half:
            rot[p + half, p] = -1.0
        else:
            rot[p - half, p] = 1.0
    upper = (i[:, None] <= i[None, :]) * 1.0
    sq = np.concatenate([ident, ones, blk, rot, upper], axis=1)

    def level(n, l):
        a = np.arange(n)
        return ((a[:, None] >> (l + 1) == a[None, :] >> (l + 1)) & (a[:, None] >> l & 1 == 1)
                & (a[None, :] >> l & 1 == 0)) * 1.0

    c = np.arange(CH)
    pair = [c[:, None] > c[None, :], c[:, None] < c[None, :], c[:, None] <= c[None, :], level(CH, 0).T]
    lr = np.concatenate([np.tile(m, (2, 1)) for m in pair] + [np.kron(np.eye(2), level(CH, l)) for l in range(1, LEVELS_R)], axis=1)
    lg = np.zeros((P, LEVELS_G + 5, C3))
    c = np.arange(C3)
    for l in range(LEVELS_G):
        lg[:C3, l] = level(C3, l)
    lg[:C3, LEVELS_G] = level(C3, 0).T
    lg[:C3, LEVELS_G + 1] = np.eye(C3)
    lg[:C3, LEVELS_G + 2] = c[:, None] > c[None, :]
    lg[:C3, LEVELS_G + 3] = c[:, None] < c[None, :]
    lg[:C3, LEVELS_G + 4] = c[:, None] <= c[None, :]
    t = np.arange(S)
    win = np.array([2, 4, 8, 16])[(np.arange(256) // 64)]
    recip_count = (1.0 / np.minimum(t[None, :] + 1, win[:, None])).reshape(2, P, S).transpose(1, 0, 2)
    chunk_keep = np.broadcast_to((t % CH != 0) * 1.0, (P, S))
    gdn_keep = np.broadcast_to((np.arange(T3) % C3 != 0) * 1.0, (P, T3))
    j = np.arange(S) - 3 * P
    dist = np.abs(i[:, None] - j[None, :]).astype(np.float64)
    dist[(j[None, :] // 64) > (i[:, None] // 64)] = 1.0e32
    pos = np.arange(S, dtype=np.float32)
    inv = np.float32(10000.0) ** (-np.arange(0, HD, 2, dtype=np.float32) / np.float32(HD))
    ang = (pos[None, :] * inv[:, None]).astype(np.float32)
    cos, sin = (np.tile(f(ang), (4, 1)) for f in (np.cos, np.sin))
    causal = np.where(i[None, :] <= i[:, None], 0.0, NEG)
    causal88 = np.zeros((P, 2 * C3))
    causal88[:C3, :C3] = np.where(np.arange(C3)[None, :] <= np.arange(C3)[:, None], 0.0, NEG)
    parts = {"c_square": sq, "c_levels_r": lr, "c_levels_g": lg, "c_recip_count": recip_count,
             "c_chunk_keep": chunk_keep, "c_gdn_keep": gdn_keep, "c_dist": dist, "c_cos": cos, "c_sin": sin,
             "c_causal": causal, "c_causal88": causal88}
    return {k: np.ascontiguousarray(v, dtype=np.float32) for k, v in parts.items()}


class Slabs:

    def __init__(self, nc, ctx, stream, total):
        self.nc = nc
        self.ring = ctx.enter_context(nc.sbuf_tensor("ring", [P, SLOTS, D], F32))
        self.hi = ctx.enter_context(nc.sbuf_tensor("slab_hi", [P, PARTS, D], F32R))
        self.lo = ctx.enter_context(nc.sbuf_tensor("slab_lo", [P, PARTS, D], F32R))
        self.loaded = [ctx.enter_context(nc.semaphore(f"slab_loaded_{j}")) for j in range(SLOTS)]
        self.hi_ready, self.lo_ready, self.used = (ctx.enter_context(nc.semaphore(f"slabs_{n}"))
                                                   for n in ("hi_ready", "lo_ready", "used"))
        self.stream, self.total, self.n = stream, total, 0

    def parts(self, n):
        return self.hi[:, n % PARTS, :], self.lo[:, n % PARTS, :]

    def first(self, sp):
        for n in range(SLOTS):
            sp.dma_start(self.ring[:, n, :], self.stream[n]).then_inc(self.loaded[n], 16)

    def split_hi(self, act, n, turn=0):
        if n >= PARTS:
            act.wait_ge(self.used, turn * KT + (n - PARTS + 1))
        act.wait_ge(self.loaded[n % SLOTS], turn * (16 * KT // SLOTS) + 16 * (n // SLOTS + 1))
        self.nc.scalar.activation(self.hi[:, n % PARTS, :], self.ring[:, n % SLOTS, :], ACT.Copy).then_inc(self.hi_ready, 1)

    def split_lo(self, dve, n, turn=0):
        dve.wait_ge(self.hi_ready, turn * KT + (n + 1))
        self.nc.vector.tensor_tensor(self.lo[:, n % PARTS, :], self.ring[:, n % SLOTS, :], self.hi[:, n % PARTS, :].bitcast(F32),
                                     ALU.subtract).then_inc(self.lo_ready, 1)

    def refill(self, sp, first, count):
        count = min(count, self.total - SLOTS - first)
        turns = count // SLOTS
        if turns > 1:
            with sp.Fori(0, turns) as turn:
                for j in range(SLOTS):
                    n = first + j
                    sp.wait_ge(self.lo_ready, turn * SLOTS + (n + 1))
                    sp.dma_start(self.ring[:, n % SLOTS:n % SLOTS + 1, :],
                                 self.stream[bass.ds(turn * SLOTS + (n + SLOTS), 1)].rearrange("o p n -> p o n")
                                 ).then_inc(self.loaded[n % SLOTS], 16)
        else:
            turns = 0
        for n in range(first + turns * SLOTS, first + count):
            sp.wait_ge(self.lo_ready, n + 1)
            sp.dma_start(self.ring[:, n % SLOTS, :], self.stream[n + SLOTS]).then_inc(self.loaded[n % SLOTS], 16)


class Feed:

    def __init__(self, K, ctx, steps, rows, shape, norm=None):
        self.norm, self.tiles = norm, shape[0] if len(shape) > 1 else 1
        self.nc, self.slabs, self.rows, self.steps, self.n0 = K.nc, K.slabs, rows, steps, K.slabs.n
        K.slabs.n += steps
        self.hi, self.lo = (K.buf(ctx, f"rows_{n}", [P, PARTS] + shape, F32R) for n in ("hi", "lo"))
        self.hi_ready, self.lo_ready = K.sem("rows_hi_ready"), K.sem("rows_lo_ready")

    def slab(self, i):
        return self.slabs.parts(self.n0 + i)

    def acts(self, i):
        return self.hi[:, i % PARTS], self.lo[:, i % PARTS]

    def refill(self, sp):
        self.slabs.refill(sp, self.n0 + 1, self.steps)

    def _rows_hi(self, act, i, turn=0):
        if i >= PARTS:
            act.wait_ge(self.slabs.used, turn * KT + (self.n0 + i - PARTS + 1))
        if self.norm and (i + 1) * self.tiles <= KT:
            act.wait_ge(self.norm.normed, (i + 1) * self.tiles)
        self.nc.scalar.activation(self.hi[:, i % PARTS], self.rows(i), ACT.Copy).then_inc(self.hi_ready, 1)

    def _rows_lo(self, dve, i, turn=0):
        dve.wait_ge(self.hi_ready, turn * KT + (i + 1))
        self.nc.vector.tensor_tensor(self.lo[:, i % PARTS], self.rows(i), self.hi[:, i % PARTS].bitcast(F32),
                                     ALU.subtract).then_inc(self.lo_ready, 1)

    def start_hi(self, act):
        if self.norm:
            self.norm.scalar(act)
        self._rows_hi(act, 0)
        self.slabs.split_hi(act, self.n0 + 1)
        self._rows_hi(act, 1)

    def start_lo(self, dve):
        if self.norm:
            self.norm.vector(dve, range(2 * self.tiles))
        self._rows_lo(dve, 0)
        self.slabs.split_lo(dve, self.n0 + 1)
        self._rows_lo(dve, 1)
        if self.norm:
            self.norm.vector(dve, range(2 * self.tiles, KT))

    def ahead_hi(self, act, steps, turn=0):
        for i in steps:
            if i + 2 <= self.steps and self.n0 + i + 2 < self.slabs.total:
                self.slabs.split_hi(act, self.n0 + i + 2, turn)
            if i + 2 < self.steps:
                self._rows_hi(act, i + 2, turn)

    def ahead_lo(self, dve, steps, turn=0):
        for i in steps:
            if i + 2 <= self.steps and self.n0 + i + 2 < self.slabs.total:
                self.slabs.split_lo(dve, self.n0 + i + 2, turn)
            if i + 2 < self.steps:
                self._rows_lo(dve, i + 2, turn)

    def wait(self, pe, i, turn=0):
        pe.wait_ge(self.slabs.lo_ready, turn * KT + (self.n0 + i + 1))
        pe.wait_ge(self.lo_ready, turn * KT + (i + 1))


def cut(pair, lo, hi):
    return tuple(part[:, lo:hi] for part in pair)


def exact(nc, to, lhsT, rhs, start, stop):
    nc.tensor.matmul(to, lhsT[0], rhs[0], start=start, stop=False)
    nc.tensor.matmul(to, lhsT[0], rhs[1], start=False, stop=False)
    return nc.tensor.matmul(to, lhsT[1], rhs[0], start=False, stop=stop)


class Chain:

    def __init__(self, eng, sem):
        self.eng, self.sem, self.n = eng, sem, 0

    def __call__(self, ins):
        self.n += 1
        ins.then_inc(self.sem, 1)
        self.eng.wait_ge(self.sem, self.n)


class Core:

    def __init__(self, nc, ctx, stream, total):
        self.nc, self.ctx = nc, ctx
        self.ps = ctx.enter_context(nc.psum_tensor("ps", [P, 8, 512], F32))
        self.slabs = Slabs(nc, ctx, stream, total)
        self.vecs = ctx.enter_context(nc.sbuf_tensor("vecs", [P, NVEC], F32))
        self.sq = ctx.enter_context(nc.sbuf_tensor("square_constants", [P, 5 * P], F32))
        self.h = ctx.enter_context(nc.sbuf_tensor("h", [P, KT, T3], F32))
        self.xn = ctx.enter_context(nc.sbuf_tensor("xn", [P, KT, T3], F32))
        self.eps = ctx.enter_context(nc.sbuf_tensor("eps", [P, 6], F32))
        self.ident, self.ones, self.blk, self.rot, self.upper = (self.sq[:, n * P:(n + 1) * P] for n in range(5))
        self.eps_col, self.gn_eps_col, self.one_col = self.eps[:, 0:1], self.eps[:, 1:2], self.eps[:, 2:3]
        self.eps_times = {1: self.eps_col, HD: self.eps[:, 3:4], 4 * HD: self.eps[:, 4:5], SUBLN: self.eps[:, 5:6]}
        self.count, self.in_use, self.cleared = 0, [], []

    def sem(self, name):
        self.count += 1
        self.in_use.append(self.nc.alloc_semaphore(name=f"{name}_{self.count}"))
        return self.in_use[-1]

    @contextmanager
    def stage(self):
        with self.nc.Block() as block:
            yield block
        for s in self.cleared:
            self.nc.release_semaphore(s)
        for s in self.in_use:
            self.nc.sync.sem_clear(s)
        self.cleared, self.in_use = self.in_use, []

    def vec(self, name, n=0):
        c = VEC_COLS[name][0] + n
        return self.vecs[:, c:c + 1]

    def pick(self, h, n, rows=8):
        return self.ident[0:rows, h:h + 1].to_broadcast((rows, n))

    def buf(self, ctx, name, shape, dtype=F32):
        self.count += 1
        return ctx.enter_context(self.nc.sbuf_tensor(f"{name}_{self.count}", shape, dtype))


def load_stage(K, ins):
    nc = K.nc
    arrived, set_up = K.sem("inputs_arrived"), K.sem("eps_set")
    with K.stage() as block:
        @block.sync
        def _(sp):
            sp.dma_start(K.h[:, :, 0:S], ins["x"]).then_inc(arrived, 16)
            sp.dma_start(K.sq[:], ins["c_square"]).then_inc(arrived, 16)
            sp.dma_start(K.vecs[:], ins["vecs"]).then_inc(arrived, 16)
            K.slabs.first(sp)
            K.slabs.refill(sp, 0, 1)
            sp.wait_ge(arrived, 48)

        @block.scalar
        def _(act):
            K.slabs.split_hi(act, 0)

        @block.vector
        def _(dve):
            K.slabs.split_lo(dve, 0)
            nc.vector.memset(K.eps[:, 0:1], EPS).then_inc(set_up, 1)
            nc.vector.memset(K.eps[:, 1:2], GN_EPS).then_inc(set_up, 1)
            nc.vector.memset(K.eps[:, 2:3], 1.0).then_inc(set_up, 1)
            nc.vector.memset(K.eps[:, 3:4], EPS * HD).then_inc(set_up, 1)
            nc.vector.memset(K.eps[:, 4:5], EPS * 4 * HD).then_inc(set_up, 1)
            nc.vector.memset(K.eps[:, 5:6], EPS * SUBLN).then_inc(set_up, 1)


class Norm:

    def __init__(self, K, ctx, src, dst, gain, cols):
        self.K, self.src, self.dst, self.gain, (self.lo, self.hi) = K, src, dst, gain, cols
        self.n = self.hi - self.lo
        self.tiles = [(a, min(a + P, self.n)) for a in range(0, self.n, P)]
        self.square = K.buf(ctx, "norm_square", [P, KT, self.n])
        self.rstd = K.buf(ctx, "norm_rstd", [P, len(self.tiles)])
        self.squared, self.added, self.summed, self.rooted, self.inverted, self.spread, self.normed = (
            K.sem(n) for n in ("squared", "added", "summed", "rooted", "inverted", "spread", "normed"))
        full = self.n // P
        self.lots = [(P, 0, full)] + ([(self.n % P, full, full + 1)] if self.n % P else [])

    def scalar(self, act):
        K, nc = self.K, self.K.nc
        for k in range(KT):
            nc.scalar.activation(self.square[:, k, :], self.src(k)[:, self.lo:self.hi], ACT.Square).then_inc(self.squared, 1)
        act.wait_ge(self.summed, 1)
        for rows, a, b in self.lots:
            nc.scalar.activation(self.rstd[0:rows, a:b], K.ps[0:rows, 3 + a:3 + b, 0], ACT.Sqrt, bias=K.eps_col[0:rows, :], scale=1.0 / D).then_inc(self.rooted, 1)

    def tensor(self, pe):
        K, nc = self.K, self.K.nc
        pe.wait_ge(self.added, KT - 1)
        for i, (a, b) in enumerate(self.tiles):
            last = nc.tensor.matmul(K.ps[0:b - a, 3 + i, 0:1], self.square[:, 0, a:b], K.ones[:, 0:1], start=True, stop=True)
        last.then_inc(self.summed, 1)
        pe.wait_ge(self.inverted, len(self.lots))
        for i, (a, b) in enumerate(self.tiles):
            last = nc.tensor.matmul(K.ps[:, 6 + a // 512, a % 512:a % 512 + b - a], self.rstd[0:b - a, i:i + 1].to_broadcast((b - a, P)),
                                    K.ident[0:b - a, 0:b - a], start=True, stop=True)
        last.then_inc(self.spread, 1)

    def vector(self, dve, ks):
        K, nc = self.K, self.K.nc
        spread = K.ps[:].rearrange("p b n -> p (b n)")[:, 6 * 512:6 * 512 + self.n]
        for k in ks:
            if k == 0:
                for j in range(1, KT):
                    dve.wait_ge(self.squared, j + 1)
                    nc.vector.tensor_tensor(self.square[:, 0, :], self.square[:, 0, :], self.square[:, j, :], ALU.add).then_inc(self.added, 1)
                    dve.wait_ge(self.added, j)
                dve.wait_ge(self.rooted, len(self.lots))
                for rows, a, b in self.lots:
                    nc.vector.reciprocal(self.rstd[0:rows, a:b], self.rstd[0:rows, a:b]).then_inc(self.inverted, 1)
                dve.wait_ge(self.spread, 1)
            nc.vector.scalar_tensor_tensor(out=self.dst(k)[:, self.lo:self.hi], in0=self.src(k)[:, self.lo:self.hi], scalar=K.vec(self.gain, k),
                                           in1=spread, op0=ALU.mult, op1=ALU.mult).then_inc(self.normed, 1)

    def free(self, e, b):
        if b >= 6:
            e.wait_ge(self.normed, KT)


def norm_stage(K, src, dst, gain, cols):
    with ExitStack() as local:
        norm = Norm(K, local, src, dst, gain, cols)
        with K.stage() as block:
            @block.scalar
            def _(act):
                norm.scalar(act)

            @block.tensor
            def _(pe):
                norm.tensor(pe)

            @block.vector
            def _(dve):
                norm.vector(dve, range(KT))


def residual_norm(K, ctx, gain, cols):
    return Norm(K, ctx, lambda k: K.h[:, k, :], lambda k: K.xn[:, k, :], gain, cols)


class Group:

    def __init__(self, feed, banks, first, steps, filled, filled_before=0):
        self.feed, self.banks, self.first, self.steps, self.filled = feed, banks, first, steps, filled
        self.before = filled_before
        self.body = range(first, first + steps - 1)
        self.end = range(first + steps - 1, first + steps)

    def bank_ready(self, eng, b, turn=0):
        if b < self.banks - 1:
            eng.wait_ge(self.filled, turn * (self.banks - 1) + (self.before + b + 1))
        else:
            eng.wait_ge(self.feed.slabs.used, turn * self.steps + (self.feed.n0 + self.first + self.steps))

    def products(self, pe, product, drained=None, turn=0):
        if self.first == 0 and self.feed.norm and drained is None:
            drained = self.feed.norm.free
            self.feed.norm.tensor(pe)
        for j in range(self.steps):
            self.feed.wait(pe, self.first + j, turn)
            for b in range(self.banks):
                if j == 0 and drained is not None:
                    drained(pe, b)
                mm = product(self.first + j, b, j == 0, j == self.steps - 1)
                if b == self.banks - 1:
                    mm.then_inc(self.feed.slabs.used, 1)
                elif j == self.steps - 1:
                    mm.then_inc(self.filled, 1)


def features_product(K, feed, cols):
    return lambda i, b, start, stop: exact(K.nc, K.ps[:, b, 0:cols], cut(feed.slab(i), b * P, (b + 1) * P), feed.acts(i), start, stop)


def residual_stage(K, rhs, steps, cols=(0, S)):
    nc, (lo, hi) = K.nc, cols
    filled = K.sem("out_filled")
    with ExitStack() as local:
        feed = Feed(K, local, steps, rhs, [hi - lo])
        group = Group(feed, KT, 0, steps, filled)
        with K.stage() as block:
            @block.sync
            def _(sp):
                feed.refill(sp)

            @block.tensor
            def _(pe):
                group.products(pe, features_product(K, feed, hi - lo))

            @block.scalar
            def _(act):
                feed.start_hi(act)
                feed.ahead_hi(act, group.body)

            @block.vector
            def _(dve):
                feed.start_lo(dve)
                feed.ahead_lo(dve, group.body)
                for m in range(KT):
                    group.bank_ready(dve, m)
                    nc.vector.tensor_tensor(K.h[:, m, lo:hi], K.ps[:, m, 0:hi - lo], K.h[:, m, lo:hi], ALU.add)


def project_stage(K, dst, rhs, cols, gain=None):
    nc = K.nc
    filled = K.sem("projection_filled")
    with ExitStack() as local:
        feed = Feed(K, local, KT, rhs, [cols], residual_norm(K, local, gain, (0, cols)) if gain else None)
        group = Group(feed, KT, 0, KT, filled)
        with K.stage() as block:
            @block.sync
            def _(sp):
                feed.refill(sp)

            @block.tensor
            def _(pe):
                group.products(pe, features_product(K, feed, cols))

            @block.scalar
            def _(act):
                feed.start_hi(act)
                feed.ahead_hi(act, group.body)
                for m in range(KT):
                    group.bank_ready(act, m)
                    nc.scalar.activation(dst(m), K.ps[:, m, 0:cols], ACT.Copy)

            @block.vector
            def _(dve):
                feed.start_lo(dve)
                feed.ahead_lo(dve, group.body)


def token_major_stage(K, dst, rows, tiles):
    nc = K.nc
    filled = K.sem("token_major_filled")
    with ExitStack() as local:
        feed = Feed(K, local, KT, rows, [tiles * P])
        group = Group(feed, 2 * tiles, 0, KT, filled)
        with K.stage() as block:
            @block.sync
            def _(sp):
                feed.refill(sp)

            @block.tensor
            def _(pe):
                group.products(pe, lambda i, b, start, stop: exact(
                    nc, K.ps[:, b, :], cut(feed.acts(i), b // 2 * P, (b // 2 + 1) * P),
                    cut(feed.slab(i), (b % 2) * 512, (b % 2 + 1) * 512), start, stop))

            @block.scalar
            def _(act):
                feed.start_hi(act)
                feed.ahead_hi(act, group.body)
                for b in range(2 * tiles):
                    group.bank_ready(act, b)
                    nc.scalar.activation(dst(b // 2, b % 2), K.ps[:, b, :], ACT.Copy)

            @block.vector
            def _(dve):
                feed.start_lo(dve)
                feed.ahead_lo(dve, group.body)


def mix_in_stage(K, pool_u, rwkv_z, diff_qk, diff_v):
    nc = K.nc
    filled, drained = K.sem("z_filled"), K.sem("z_drained")

    def place(i):
        if i < 2:
            return pool_u[:, i, 16:16 + S]
        if i < 10:
            return rwkv_z[:, i - 2, 1:1 + S]
        return diff_qk[:, i - 10, :]

    with ExitStack() as local:
        feed = Feed(K, local, 3 * KT, lambda i: K.xn[:, i % KT, 0:S], [S], residual_norm(K, local, "mix_norm_g", (0, S)))
        groups = [Group(feed, banks, g * KT, KT, filled, 7 * g) for g, banks in enumerate((8, 8, 6))]
        with K.stage() as block:
            @block.sync
            def _(sp):
                feed.refill(sp)

            @block.tensor
            def _(pe):
                features = features_product(K, feed, S)

                def last(i, b, start, stop):
                    if b < 2:
                        return features(i, b, start, stop)
                    return exact(nc, K.ps[:, b, :], cut(feed.acts(i), (b - 2) * P, (b - 1) * P),
                                 cut(feed.slab(i), 2 * P, 2 * P + 512), start, stop)

                groups[0].products(pe, features)
                groups[1].products(pe, features, lambda e, b: e.wait_ge(drained, b + 1))
                groups[2].products(pe, last, lambda e, b: e.wait_ge(drained, 8 + b + 1))

            @block.scalar
            def _(act):
                feed.start_hi(act)
                for g, group in enumerate(groups):
                    feed.ahead_hi(act, group.body)
                    for b in range(group.banks):
                        group.bank_ready(act, b)
                        to = place(8 * g + b) if 8 * g + b < 18 else diff_v[:, b - 2, :]
                        nc.scalar.activation(to, K.ps[:, b, :], ACT.Copy).then_inc(drained, 1)
                    feed.ahead_hi(act, group.end)

            @block.vector
            def _(dve):
                nc.vector.memset(pool_u[:, :, 0:16], 0.0)
                nc.vector.memset(rwkv_z[:, :, 0:1], 0.0)
                feed.start_lo(dve)
                feed.ahead_lo(dve, range(3 * KT))


def pool_stage(K, pool_u, y, ins):
    nc = K.nc
    with ExitStack() as local:
        recip = K.buf(local, "pool_recip", [P, 2, S])
        w = K.buf(local, "pool_w", [P, 2, P])
        sums = K.buf(local, "pool_sums", [P, 2, 2, 16 + S])
        diff = K.buf(local, "pool_diff", [P, 2, S])
        arrived, chain, ready, filled = (K.sem(n) for n in ("pool_arrived", "pool_chain", "pool_ready", "pool_filled"))
        with K.stage() as block:
            @block.sync
            def _(sp):
                sp.dma_start(recip[:], ins["c_recip_count"]).then_inc(arrived, 16)
                sp.dma_start(w[:], ins["pool_w"]).then_inc(arrived, 16)

            @block.vector
            def _(dve):
                link = Chain(dve, chain)
                src = pool_u
                link(nc.vector.memset(sums[:, :, :, 0:16], 0.0))
                dve.wait_ge(arrived, 32)
                for n, shift in enumerate((1, 2, 4, 8)):
                    s = sums[:, n % 2]
                    link(nc.vector.tensor_tensor(s[:, :, 16:16 + S], src[:, :, 16:16 + S],
                                                 src[:, :, 16 - shift:16 - shift + S], ALU.add))
                    part, tile = (n % 2) * HD, n // 2
                    rows = slice(part, part + HD)
                    link(nc.vector.tensor_tensor(diff[rows, tile, :], s[rows, tile, 16:16 + S], recip[rows, tile, :], ALU.mult))
                    src = s
                nc.vector.tensor_tensor(diff[:], diff[:], pool_u[:, :, 16:16 + S], ALU.subtract).then_inc(ready, 1)
                for t in range(2):
                    dve.wait_ge(filled, t + 1)
                    nc.vector.tensor_scalar(y[:, t, :], K.ps[:, t, :], K.vec("pool_scale", t), None, ALU.mult)

            @block.tensor
            def _(pe):
                pe.wait_ge(ready, 1)
                pe.wait_ge(arrived, 32)
                for t in range(2):
                    nc.tensor.matmul(K.ps[:, t, :], w[:, t, :], diff[:, t, :], start=True, stop=True).then_inc(filled, 1)


def rwkv_prepare_stage(K, z, zm, V, ins):
    nc = K.nc
    (gate, a_t, b_t, k_t, r_t, bonus, p_end) = V
    with ExitStack() as local:
        lora = K.buf(local, "rwkv_lora", [P, 2, 256])
        keep = K.buf(local, "rwkv_keep", [P, S])
        diff = K.xn[:, :, 0:S]
        tanh_w = K.buf(local, "rwkv_tanh", [P, S])
        sig_g = K.buf(local, "rwkv_sig_g", [P, S])
        logw, iclr, kk, cum, p_now, p_before, p_inv, k2 = (
            K.buf(local, n, [P, 2, S]) for n in ("logw", "iclr", "kk", "cum", "p_now", "p_before", "p_inv", "k2"))
        arrived, mixed, gates_in, filled, sig_ready, kk_sq, kk_sum, kk_root, cum_ready, less_ready, decays, chain, \
            rk_ready, rk_sum = (K.sem(n) for n in (
                "rwkv_arrived", "mixed", "gates_in", "lora_filled", "sig_ready", "kk_sq", "kk_sum", "kk_root",
                "cum_ready", "less_ready", "decays", "rwkv_chain", "rk_ready", "rk_sum"))
        with K.stage() as block:
            @block.sync
            def _(sp):
                sp.dma_start(lora[:], ins["rwkv_lora"]).then_inc(arrived, 16)
                sp.dma_start(keep[:], ins["c_chunk_keep"]).then_inc(arrived, 16)

            @block.vector
            def _(dve):
                link = Chain(dve, chain)
                link(nc.vector.tensor_tensor(diff, z[:, :, 0:S], z[:, :, 1:1 + S], ALU.subtract))
                for i in (6, 7, 0, 1, 2, 3, 4, 5):
                    nc.vector.scalar_tensor_tensor(out=zm[:, i, :], in0=diff[:, i, :], scalar=K.vec("rwkv_mu", i),
                                                   in1=z[:, i, 1:1 + S], op0=ALU.mult, op1=ALU.add).then_inc(mixed, 1)
                dve.wait_ge(mixed, 8)
                r, k, v = zm[:, 0:2, :], zm[:, 2:4, :], zm[:, 4:6, :]
                for t in range(2):
                    link(nc.vector.tensor_scalar(kk[:, t, :], k[:, t, :], K.vec("rwkv_k_k", t), None, ALU.mult))
                nc.vector.tensor_tensor(k2[:], kk[:], kk[:], ALU.mult).then_inc(kk_sq, 1)
                dve.wait_ge(kk_root, 2)
                link(nc.vector.tensor_scalar(p_inv[:], p_inv[:], 1e-12, None, ALU.max))
                link(nc.vector.reciprocal(p_inv[:], p_inv[:]))
                link(nc.vector.tensor_tensor(kk[:], kk[:], p_inv[:], ALU.mult))
                dve.wait_ge(sig_ready, 2)
                dve.wait_ge(arrived, 32)
                link(nc.vector.tensor_scalar(logw[:], logw[:], -float(np.exp(-0.5)), None, ALU.mult))
                for t in range(2):
                    nc.vector.tensor_tensor_scan(cum[:, t, :], keep[:], logw[:, t, :], 0.0, ALU.mult, ALU.add).then_inc(cum_ready, 1)
                dve.wait_ge(cum_ready, 2)
                nc.vector.tensor_tensor(p_before[:], cum[:], logw[:], ALU.subtract).then_inc(less_ready, 1)
                dve.wait_ge(sig_ready, 4)
                for t in range(2):
                    link(nc.vector.tensor_scalar(k2[:, t, :], iclr[:, t, :], -1.0, K.vec("rwkv_k_a", t), ALU.add, ALU.mult))
                    link(nc.vector.scalar_tensor_tensor(out=k2[:, t, :], in0=k2[:, t, :], scalar=1.0, in1=k[:, t, :],
                                                        op0=ALU.add, op1=ALU.mult))
                    nc.vector.scalar_tensor_tensor(out=diff[:, t, :], in0=r[:, t, :], scalar=K.vec("rwkv_r_k", t),
                                                   in1=k2[:, t, :], op0=ALU.mult, op1=ALU.mult).then_inc(rk_ready, 1)
                link(nc.vector.tensor_tensor(b_t[:], kk[:], iclr[:], ALU.mult))
                dve.wait_ge(decays, 3)
                nc.vector.scalar_tensor_tensor(out=a_t[:], in0=kk[:], scalar=-1.0, in1=p_before[:], op0=ALU.mult, op1=ALU.mult)
                nc.vector.tensor_tensor(b_t[:], b_t[:], p_inv[:], ALU.mult)
                nc.vector.tensor_tensor(k_t[:], k2[:], p_inv[:], ALU.mult)
                nc.vector.tensor_tensor(r_t[:], r, p_now[:], ALU.mult)
                nc.vector.tensor_copy(p_end[:], p_now[:].rearrange("p t (c i) -> p t c i", i=CH)[:, :, :, CH - 1])
                for t in range(2):
                    dve.wait_ge(rk_sum, t + 1)
                    nc.vector.tensor_tensor(bonus[:, t, :], K.ps[:, t, :], v[:, t, :], ALU.mult)

            @block.scalar
            def _(act):
                act.wait_ge(mixed, 2)
                nc.scalar.activation(tanh_w[0:64, :], zm[0:64, 6, :], ACT.Tanh).then_inc(gates_in, 1)
                nc.scalar.activation(sig_g[:], zm[:, 7, :], ACT.Sigmoid).then_inc(gates_in, 1)
                for t in range(2):
                    act.wait_ge(filled, t + 1)
                    nc.scalar.activation(logw[:, t, :], K.ps[:, t, :], ACT.Sigmoid, bias=K.vec("rwkv_w0", t)).then_inc(sig_ready, 1)
                for t in range(2):
                    act.wait_ge(filled, 2 + t + 1)
                    nc.scalar.activation(iclr[:, t, :], K.ps[:, 2 + t, :], ACT.Sigmoid, bias=K.vec("rwkv_a0", t)).then_inc(sig_ready, 1)
                for t in range(2):
                    act.wait_ge(filled, 4 + t + 1)
                    nc.scalar.activation(gate[:, t, :], K.ps[:, 4 + t, :], ACT.Copy)
                for t in range(2):
                    act.wait_ge(kk_sum, t + 1)
                    nc.scalar.activation(p_inv[:, t, :], K.ps[:, 6 + t, :], ACT.Sqrt).then_inc(kk_root, 1)
                act.wait_ge(cum_ready, 2)
                nc.scalar.activation(p_now[:], cum[:], ACT.Exp).then_inc(decays, 1)
                act.wait_ge(less_ready, 1)
                nc.scalar.activation(p_before[:], p_before[:], ACT.Exp).then_inc(decays, 1)
                nc.scalar.activation(p_inv[:], cum[:], ACT.Exp, scale=-1.0).then_inc(decays, 1)

            @block.tensor
            def _(pe):
                pe.wait_ge(arrived, 32)
                pe.wait_ge(gates_in, 2)
                for t in range(2):
                    nc.tensor.matmul(K.ps[:, t, :], lora[0:64, 0, t * P:(t + 1) * P], tanh_w[0:64, :], start=True, stop=True).then_inc(filled, 1)
                for t in range(2):
                    nc.tensor.matmul(K.ps[:, 2 + t, :], lora[64:128, 0, t * P:(t + 1) * P], zm[64:128, 6, :], start=True, stop=True).then_inc(filled, 1)
                for t in range(2):
                    nc.tensor.matmul(K.ps[:, 4 + t, :], lora[:, 1, t * P:(t + 1) * P], sig_g[:], start=True, stop=True).then_inc(filled, 1)
                pe.wait_ge(kk_sq, 1)
                for t in range(2):
                    nc.tensor.matmul(K.ps[:, 6 + t, :], K.blk, k2[:, t, :], start=True, stop=True).then_inc(kk_sum, 1)
                pe.wait_ge(sig_ready, 2)
                for t in range(2):
                    pe.wait_ge(rk_ready, t + 1)
                    nc.tensor.matmul(K.ps[:, t, :], K.blk, diff[:, t, :], start=True, stop=True).then_inc(rk_sum, 1)


def token_tiles_stage(K, jobs, rows, tiles):
    nc = K.nc
    ready, drained = K.sem("turned"), K.sem("turned_out")
    lots = [(src, place, t, min(4, tiles - t)) for src, place in jobs for t in range(0, tiles, 4)]
    with K.stage() as block:
        @block.tensor
        def _(pe):
            for n, (src, place, t0, k) in enumerate(lots):
                if n >= 8:
                    pe.wait_ge(drained, n - 7)
                for i in range(k):
                    last = nc.tensor.transpose(K.ps[0:rows, n % 8, i * P:(i + 1) * P],
                                               src[:, (t0 + i) * rows:(t0 + i + 1) * rows], K.ident)
                last.then_inc(ready, 1)

        @block.scalar
        def _(act):
            for n, (src, place, t0, k) in enumerate(lots):
                act.wait_ge(ready, n + 1)
                nc.scalar.activation(place(t0, k), K.ps[0:rows, n % 8, 0:k * P].rearrange("p (i c) -> p i c", c=P),
                                     ACT.Copy).then_inc(drained, 1)


def rwkv_chunk_stage(K, V, tok, out, ins):
    nc = K.nc
    (_, a_t, b_t, k_t, r_t, _, _) = V
    (a_tok, v_tok) = tok
    (x1, x2, rb, rk) = out
    H, PAIRS, LV = 4, 2, LEVELS_R - 1
    with ExitStack() as local:
        masks_in = K.buf(local, "rwkv_masks", [P, 4 * CH + LV * P])
        spare = K.xn[:].rearrange("p k t -> p (k t)")
        amat, prod = (spare[:, n * PAIRS * NCH * P:(n + 1) * PAIRS * NCH * P].rearrange("p (q c i) -> p q c i", q=PAIRS, c=NCH) for n in range(2))
        inv, invT, amask = (K.buf(local, n, [P, PAIRS, NCH, P]) for n in ("rwkv_inv", "rwkv_invT", "rwkv_A_level"))
        a_blocks, b_blocks, k_blocks = prod, amask, inv
        akT = K.buf(local, "rwkv_akT", [CH, 2, NCH, CH])
        low = [amat[0:CH, q].rearrange("p c i -> p (c i)").rearrange("p (o c i) -> p o c i", o=2, c=NCH) for q in range(PAIRS)]
        arrived, zeroed, zeroed_too, chain, a_ready, b_ready, k_ready = (K.sem(n) for n in (
            "masks_arrived", "blocks_zeroed", "A_zeroed", "chunk_chain", "a_blocks_ready", "b_blocks_ready", "k_blocks_ready"))
        filled, drained, w_filled, w_out, firstT, masked, turned, inv_out, z_filled, z_out, d_filled, d_added, x_filled = (
            [K.sem(f"rwkv_{n}_{q}") for q in range(PAIRS)] for n in (
                "pairs_filled", "pairs_drained", "w_filled", "w_out", "firstT", "masked", "turned", "inv_out", "z_filled", "z_out", "d_filled", "d_added", "x_filled"))
        half = [slice(o * CH, (o + 1) * CH) for o in range(2)]

        def mask(n, o):
            return masks_in[half[o], n * CH:(n + 1) * CH].unsqueeze(1).to_broadcast((CH, NCH, CH))

        def level(l):
            return masks_in[:, 4 * CH + l * P:4 * CH + (l + 1) * P].unsqueeze(1).to_broadcast((P, NCH, P))

        def bank(q, b):
            return K.ps[:, 4 * q + b, :].rearrange("p (c i) -> p c i", i=CH)

        def two_banks(q, b):
            return K.ps[:, 4 * q + b:4 * q + b + 2, :].rearrange("p b (c i) -> p (b c) i", i=P)

        def blocks(t, q, o):
            return t[half[o], q, :, half[o]]

        def vectors(t, q, o):
            return t[half[o], q, :].rearrange("p (c i) -> p c i", i=CH)

        products = ((a_blocks, b_t, a_ready), (b_blocks, a_t, b_ready), (k_blocks, a_t, k_ready), (b_blocks, r_t, b_ready), (k_blocks, r_t, k_ready))
        with K.stage() as block:
            @block.sync
            def _(sp):
                sp.dma_start(masks_in[:], ins["c_levels_r"]).then_inc(arrived, 16)

            @block.gpsimd
            def _(pool):
                nc.gpsimd.memset(a_blocks, 0.0).then_inc(zeroed, 1)
                nc.gpsimd.memset(k_blocks[:], 0.0).then_inc(zeroed, 1)
                nc.gpsimd.memset(invT[:], 0.0).then_inc(zeroed, 1)

            @block.tensor
            def _(pe):
                for q in range(PAIRS):
                    for n, (lhs, rhs, ready) in enumerate(products):
                        pe.wait_ge(ready, 2 * (q + 1))
                        if n == 4:
                            pe.wait_ge(drained[q], 2)
                        for c in range(NCH):
                            last = nc.tensor.matmul(bank(q, n % 4)[:, c, :], lhs[:, q, c, :], rhs[:, q, c * CH:(c + 1) * CH], start=True, stop=True)
                        last.then_inc(filled[q], 1)
                for q in range(PAIRS):
                    pe.wait_ge(drained[q], 8)
                    for o in range(2):
                        h = 2 * q + o
                        for c in range(NCH):
                            last = nc.tensor.matmul(bank(q, 1 + 2 * o)[0:CH, c, :], akT[:, o, c, :], v_tok[:, c, h * HD:(h + 1) * HD], start=True, stop=True)
                        last.then_inc(w_filled[q], 1)
                    pe.wait_ge(firstT[q], 1)
                    pe.wait_ge(drained[q], 10)
                    pe.wait_ge(w_out[q], 2)
                for l in range(LV):
                    for q in range(PAIRS):
                        if l:
                            pe.wait_ge(d_added[q], l)
                        for c in range(NCH):
                            last = nc.tensor.transpose(two_banks(q, 2)[:, c, :], invT[:, q, c, :], K.ident)
                        last.then_inc(turned[q], 1)
                        pe.wait_ge(masked[q], l + 1)
                        for c in range(NCH):
                            last = nc.tensor.matmul(two_banks(q, 0)[:, c, :], amask[:, q, c, :], invT[:, q, c, :], start=True, stop=True)
                        last.then_inc(z_filled[q], 1)
                    for q in range(PAIRS):
                        pe.wait_ge(z_out[q], l + 1)
                        pe.wait_ge(inv_out[q], l + 1)
                        for c in range(NCH):
                            last = nc.tensor.matmul(two_banks(q, 0)[:, c, :], inv[:, q, c, :], prod[:, q, c, :], start=True, stop=True)
                        last.then_inc(d_filled[q], 1)
                for q in range(PAIRS):
                    pe.wait_ge(d_added[q], LV + 1)
                    for o in range(2):
                        h = 2 * q + o
                        for c in range(NCH):
                            last = nc.tensor.matmul(bank(q, 2 * o)[0:CH, c, :], a_tok[:, c, h * HD:(h + 1) * HD], low[q][:, o, c, :], start=True, stop=True)
                        last.then_inc(x_filled[q], 1)
                        for c in range(NCH):
                            last = nc.tensor.matmul(bank(q, 2 * o + 1)[0:CH, c, :], low[q][:, o, c, :], x2[:, h, c, :], start=True, stop=True)
                        last.then_inc(x_filled[q], 1)

            @block.vector
            def _(dve):
                link = Chain(dve, chain)
                nc.vector.memset(b_blocks[:], 0.0).then_inc(zeroed_too, 1)
                nc.vector.memset(amat, 0.0).then_inc(zeroed_too, 1)
                dve.wait_ge(zeroed_too, 2)
                dve.wait_ge(zeroed, 3)
                dve.wait_ge(arrived, 16)
                for q in range(PAIRS):
                    for n, m in enumerate((0, 3, 1, 2, 2)):
                        dve.wait_ge(filled[q], n + 1)
                        if n == 2 and q:
                            dve.wait_ge(w_filled[q - 1], 2)
                        for o in range(2):
                            to = (blocks(amat, q, o), blocks(invT, q, o), akT[:, o], rb[:, 2 * q + o], rk[:, 2 * q + o])[n]
                            nc.vector.tensor_tensor(to, bank(q, n % 4)[half[o]], mask(m, o), ALU.mult).then_inc(drained[q], 1)
                    dve.wait_ge(drained[q], 10)
                    nc.vector.tensor_tensor(invT[:, q], invT[:, q], K.ident.unsqueeze(1).to_broadcast((P, NCH, P)), ALU.add).then_inc(firstT[q], 1)
                    nc.vector.tensor_tensor(amask[:, q], amat[:, q], level(0), ALU.mult).then_inc(masked[q], 1)
                for l in range(LV):
                    for q in range(PAIRS):
                        if l < LV - 1:
                            dve.wait_ge(z_filled[q], l + 1)
                            nc.vector.tensor_tensor(amask[:, q], amat[:, q], level(l + 1), ALU.mult).then_inc(masked[q], 1)
                    for q in range(PAIRS):
                        dve.wait_ge(d_filled[q], l + 1)
                        dve.wait_ge(firstT[q], 1)
                        if l < LV - 1:
                            nc.vector.tensor_tensor(invT[:, q], two_banks(q, 0), invT[:, q], ALU.add).then_inc(d_added[q], 1)
                        else:
                            for o in range(2):
                                nc.vector.tensor_tensor(low[q][:, o], two_banks(q, 0)[half[o], :, half[o]], blocks(invT, q, o), ALU.add).then_inc(d_added[q], 1)

            @block.scalar
            def _(act):
                for to, src, ready, zero, count in ((a_blocks, a_t, a_ready, zeroed, 1), (b_blocks, b_t, b_ready, zeroed_too, 1), (k_blocks, k_t, k_ready, zeroed, 2)):
                    act.wait_ge(zero, count)
                    for q in range(PAIRS):
                        for o in range(2):
                            nc.scalar.activation(blocks(to, q, o), vectors(src, q, o), ACT.Copy).then_inc(ready, 1)
                for q in range(PAIRS):
                    for o in range(2):
                        act.wait_ge(w_filled[q], o + 1)
                        nc.scalar.activation(x2[:, 2 * q + o], bank(q, 1 + 2 * o)[0:CH], ACT.Copy).then_inc(w_out[q], 1)
                for l in range(LV):
                    for q in range(PAIRS):
                        act.wait_ge(turned[q], l + 1)
                        nc.scalar.activation(inv[:, q], two_banks(q, 2), ACT.Copy).then_inc(inv_out[q], 1)
                        act.wait_ge(z_filled[q], l + 1)
                        nc.scalar.activation(prod[:, q], two_banks(q, 0), ACT.Copy).then_inc(z_out[q], 1)
                for q in range(PAIRS):
                    for o in range(2):
                        act.wait_ge(x_filled[q], 2 * o + 1)
                        nc.scalar.activation(x1[:, 2 * q + o], bank(q, 2 * o)[0:CH], ACT.Copy)
                        act.wait_ge(x_filled[q], 2 * o + 2)
                        nc.scalar.activation(x2[:, 2 * q + o], bank(q, 2 * o + 1)[0:CH], ACT.Copy)


def rwkv_scan_stage(K, V, tok, mats, y):
    nc = K.nc
    (gate, _, _, _, r_t, bonus, p_end) = V
    (b_tok, k_tok, v_tok) = tok
    (x1, x2, rb, rk) = mats
    H = 4
    with ExitStack() as local:
        state = K.buf(local, "rwkv_state", [HD, 2, H, HD])
        u = K.buf(local, "rwkv_u", [CH, 2, H, HD])
        kept = K.buf(local, "rwkv_kept", [HD, H, HD])
        pe_ = K.buf(local, "rwkv_p_end", [HD, H, NCH])
        r0 = K.buf(local, "rwkv_r0", [HD, H, S])
        yraw = K.buf(local, "rwkv_y", [P, 2, S])
        ysq = K.buf(local, "rwkv_ysq", [P, 2, S])
        var = K.buf(local, "rwkv_var", [P, 2, S])
        u_filled, u_ready, s_filled, s_ready, y_filled, y_out, moved, chain, cleared = (K.sem(n) for n in (
            "u_filled", "u_ready", "s_filled", "s_ready", "y_filled", "y_out", "r_moved", "scan_chain", "state_cleared"))
        mean_filled, centred, var_filled, rooted = (K.sem(n) for n in ("mean_filled", "centred", "var_filled", "rwkv_rooted"))

        def grid(b):
            return K.ps[0:HD, b, 0:H * HD].rearrange("p (h i) -> p h i", i=HD)

        with K.stage() as block:
            @block.scalar
            def _(act):
                for h in range(H):
                    rows = slice((h % 2) * HD, (h % 2 + 1) * HD)
                    nc.scalar.activation(r0[:, h, :], r_t[rows, h // 2, :], ACT.Copy).then_inc(moved, 1)
                    nc.scalar.activation(pe_[:, h, :], p_end[rows, h // 2, :], ACT.Copy).then_inc(moved, 1)
                for c in range(NCH):
                    act.wait_ge(y_filled, c + 1)
                    for h in range(H):
                        rows = slice((h % 2) * HD, (h % 2 + 1) * HD)
                        nc.scalar.activation(yraw[rows, h // 2, c * CH:(c + 1) * CH], grid(4 + c % 2)[:, h, :], ACT.Copy).then_inc(y_out, 1)
                for t in range(2):
                    act.wait_ge(var_filled, t + 1)
                    nc.scalar.activation(var[:, t, :], K.ps[:, 6 + t, :], ACT.Sqrt, bias=K.gn_eps_col, scale=1.0 / HD).then_inc(rooted, 1)

            @block.tensor
            def _(pe):
                pe.wait_ge(cleared, 1)
                pe.wait_ge(moved, 2 * H)
                for c in range(NCH):
                    s = state[:, c % 2]
                    if c:
                        pe.wait_ge(s_ready, c)
                    for h in range(H):
                        last = nc.tensor.matmul(grid(c % 2)[:, h, :], x1[:, h, c, :], s[:, h, :], start=True, stop=True)
                    last.then_inc(u_filled, 1)
                    pe.wait_ge(u_ready, c + 1)
                    for h in range(H):
                        nc.tensor.matmul(grid(2 + c % 2)[:, h, :], b_tok[:, c, h * HD:(h + 1) * HD], u[:, c % 2, h, :], start=True, stop=False)
                        last = nc.tensor.matmul(grid(2 + c % 2)[:, h, :], k_tok[:, c, h * HD:(h + 1) * HD], v_tok[:, c, h * HD:(h + 1) * HD], start=False, stop=True)
                    last.then_inc(s_filled, 1)
                    if c >= 2:
                        pe.wait_ge(y_out, H * (c - 1))
                    for h in range(H):
                        to = grid(4 + c % 2)[:, h, :]
                        nc.tensor.matmul(to, s[:, h, :], r0[:, h, c * CH:(c + 1) * CH], start=True, stop=False)
                        nc.tensor.matmul(to, u[:, c % 2, h, :], rb[:, h, c, :], start=False, stop=False)
                        last = nc.tensor.matmul(to, v_tok[:, c, h * HD:(h + 1) * HD], rk[:, h, c, :], start=False, stop=True)
                    last.then_inc(y_filled, 1)
                pe.wait_ge(y_out, H * NCH)
                for t in range(2):
                    nc.tensor.matmul(K.ps[:, t, :], K.blk, yraw[:, t, :], start=True, stop=True).then_inc(mean_filled, 1)
                for t in range(2):
                    pe.wait_ge(centred, t + 1)
                    nc.tensor.matmul(K.ps[:, 6 + t, :], K.blk, ysq[:, t, :], start=True, stop=True).then_inc(var_filled, 1)

            @block.vector
            def _(dve):
                link = Chain(dve, chain)
                nc.vector.memset(state[:, 0], 0.0).then_inc(cleared, 1)
                dve.wait_ge(cleared, 1)
                dve.wait_ge(moved, 2 * H)
                for c in range(NCH):
                    dve.wait_ge(u_filled, c + 1)
                    nc.vector.tensor_tensor(u[:, c % 2], grid(c % 2), x2[:, :, c, :], ALU.add).then_inc(u_ready, 1)
                    dve.wait_ge(s_filled, c + 1)
                    if c >= 1:
                        dve.wait_ge(y_filled, c)
                    link(nc.vector.tensor_tensor(kept[:], grid(2 + c % 2), state[:, c % 2], ALU.add))
                    for h in range(H):
                        ins = nc.vector.tensor_scalar(state[:, (c + 1) % 2, h, :], kept[:, h, :], pe_[:, h, c:c + 1], None, ALU.mult)
                        if h == H - 1:
                            ins.then_inc(s_ready, 1)
                    dve.wait_ge(s_ready, c + 1)
                for t in range(2):
                    dve.wait_ge(mean_filled, t + 1)
                    link(nc.vector.scalar_tensor_tensor(out=yraw[:, t, :], in0=K.ps[:, t, :], scalar=-1.0 / HD, in1=yraw[:, t, :], op0=ALU.mult, op1=ALU.add))
                    nc.vector.tensor_tensor(ysq[:, t, :], yraw[:, t, :], yraw[:, t, :], ALU.mult).then_inc(centred, 1)
                for t in range(2):
                    dve.wait_ge(rooted, t + 1)
                    link(nc.vector.reciprocal(var[:, t, :], var[:, t, :]))
                    link(nc.vector.tensor_tensor(yraw[:, t, :], yraw[:, t, :], var[:, t, :], ALU.mult))
                    link(nc.vector.tensor_scalar(yraw[:, t, :], yraw[:, t, :], K.vec("rwkv_ln_w", t), K.vec("rwkv_ln_b", t), ALU.mult, ALU.add))
                    link(nc.vector.tensor_tensor(yraw[:, t, :], yraw[:, t, :], bonus[:, t, :], ALU.add))
                    nc.vector.tensor_tensor(y[:, 2 + t, :], yraw[:, t, :], gate[:, t, :], ALU.mult)


def head_norm_stage(K, groups):
    nc = K.nc
    G = len(groups)
    firsts = [sum(len(g[0]) for g in groups[:n]) for n in range(G + 1)]
    tokens = [g[0][0][0].shape[-1] for g in groups]
    most = max(tokens)
    flat = K.ps[:].rearrange("p b n -> p (b n)")

    def token_tiles(n):
        return [(a, min(a + P, tokens[n])) for a in range(0, tokens[n], P)]

    def lots(n):
        full, rest, heads = tokens[n] // P, tokens[n] % P, groups[n][1]
        return [(P, 0, full * heads)] * (full > 0) + [(rest, full * heads, (full + 1) * heads)] * (rest > 0)

    with ExitStack() as local:
        square = K.buf(local, "head_square", [P, firsts[G], most])
        rstd = K.buf(local, "head_rstd", [P, G, 2 * ((most + P - 1) // P)])
        pair = K.buf(local, "head_rstd_rows", [P, 2, (most + P - 1) // P, 2, HD])
        squared, squared_too, summed, rooted, inverted, widened, spread, applied = (K.sem(n) for n in (
            "head_squared", "head_squared_too", "head_summed", "head_rooted", "head_inverted", "head_widened", "head_spread", "head_applied"))
        wide_before = [sum(len(lots(m)) for m in range(n) if groups[m][1] == 2) for n in range(G + 1)]
        sources = [src for g in groups for src, _, _ in g[0]]

        def sums_at(n, rows, a, b):
            return K.ps[0:rows, n % 2, a:b]

        def spread_at(n, a, b):
            lo = (2 + 2 * (n % 3)) * 512
            return flat[:, lo + a:lo + b]

        with K.stage() as block:
            @block.tensor
            def _(pe):
                def sums(n):
                    tiles, heads, _, _ = groups[n]
                    if (firsts[n + 1] + 1) // 2:
                        pe.wait_ge(squared, (firsts[n + 1] + 1) // 2)
                    if firsts[n + 1] // 2:
                        pe.wait_ge(squared_too, firsts[n + 1] // 2)
                    if n >= 2:
                        pe.wait_ge(rooted, sum(len(lots(m)) for m in range(n - 1)))
                    selector = K.ones[:, 0:1] if heads == 1 else K.blk[:, 0:P:HD]
                    for i, (a, b) in enumerate(token_tiles(n)):
                        for j in range(len(tiles)):
                            last = nc.tensor.matmul(sums_at(n, b - a, i * heads, (i + 1) * heads), square[:, firsts[n] + j, a:b], selector, start=j == 0, stop=j == len(tiles) - 1)
                    last.then_inc(summed, 1)

                def spreads(n):
                    heads = groups[n][1]
                    pe.wait_ge(inverted, sum(len(lots(m)) for m in range(n + 1)))
                    if n >= 3:
                        pe.wait_ge(applied, n - 2)
                    if heads == 2:
                        pe.wait_ge(widened, wide_before[n + 1])
                    for i, (a, b) in enumerate(token_tiles(n)):
                        if heads == 1:
                            value = rstd[0:b - a, n, i:i + 1].to_broadcast((b - a, P))
                        else:
                            value = pair[0:b - a, n % 2, i].rearrange("p h r -> p (h r)")
                        last = nc.tensor.matmul(spread_at(n, a, b), value, K.ident[0:b - a, 0:b - a], start=True, stop=True)
                    last.then_inc(spread, 1)

                for n in range(G + 2):
                    if n < G:
                        sums(n)
                    if n >= 2:
                        spreads(n - 2)

            @block.scalar
            def _(act):
                for at in range(0, firsts[G], 2):
                    nc.scalar.activation(square[:, at, 0:sources[at].shape[-1]], sources[at], ACT.Square).then_inc(squared, 1)

                def roots(n):
                    _, _, width, times = groups[n]
                    act.wait_ge(summed, n + 1)
                    for rows, a, b in lots(n):
                        nc.scalar.activation(rstd[0:rows, n, a:b], sums_at(n, rows, a, b), ACT.Sqrt, bias=K.eps_times[times][0:rows, :], scale=times / width).then_inc(rooted, 1)

                def widen(n):
                    act.wait_ge(inverted, sum(len(lots(m)) for m in range(n + 1)))
                    if n >= 2:
                        act.wait_ge(spread, n - 1)
                    for rows, a, b in lots(n):
                        to = pair[0:rows, n % 2, a // 2:b // 2].rearrange("p i h r -> p (i h) r")
                        nc.scalar.activation(to, rstd[0:rows, n, a:b].unsqueeze(2).to_broadcast((rows, b - a, HD)), ACT.Copy).then_inc(widened, 1)

                for n in range(G + 1):
                    if n < G:
                        roots(n)
                    if n and groups[n - 1][1] == 2:
                        widen(n - 1)

            @block.vector
            def _(dve):
                for at in range(1, firsts[G], 2):
                    nc.vector.tensor_tensor(square[:, at, 0:sources[at].shape[-1]], sources[at], sources[at], ALU.mult).then_inc(squared_too, 1)

                def inverses(n):
                    dve.wait_ge(rooted, sum(len(lots(m)) for m in range(n + 1)))
                    for rows, a, b in lots(n):
                        nc.vector.reciprocal(rstd[0:rows, n, a:b], rstd[0:rows, n, a:b]).then_inc(inverted, 1)

                def applications(n):
                    tiles = groups[n][0]
                    dve.wait_ge(spread, n + 1)
                    for i, (src, dst, gain) in enumerate(tiles):
                        if gain is None:
                            ins = nc.vector.tensor_tensor(dst, src, spread_at(n, 0, tokens[n]), ALU.mult)
                        else:
                            ins = nc.vector.scalar_tensor_tensor(out=dst, in0=src, scalar=gain, in1=spread_at(n, 0, tokens[n]), op0=ALU.mult, op1=ALU.mult)
                        if i == len(tiles) - 1:
                            ins.then_inc(applied, 1)

                for n in range(G + 2):
                    if n < G:
                        inverses(n)
                    if n >= 2:
                        applications(n - 2)


def attention_stage(K, units, rows, scores, value, place, bias=None, diagonal=None, parts=1, minus_lambda=None, width=HD, value_rows=None):
    nc = K.nc
    U = len(units)
    units = sorted(units, key=lambda unit: -unit[2])
    kmax = units[0][2]
    value_rows = value_rows or rows
    flat = K.ps[:].rearrange("p b n -> p (b n)")
    dts = (width + P - 1) // P
    drows = min(width, P)
    EXP, NORM, TURN, TURN_OUT, VALUE, OUT = 1, 2, 3, 4, 5, 6
    KEEP = TURN - EXP + 2
    sets = 2 if kmax <= 4 else 1

    def turn(n, lag, step):
        if 0 <= n - lag < U:
            step(n - lag)

    with ExitStack() as local:
        p = K.buf(local, "probs", [P, KEEP, parts, kmax * rows])
        s = K.buf(local, "scores", [P, 2, parts, kmax * rows]) if bias else None
        pT = K.buf(local, "probsT", [P, 2, kmax, rows])
        stat = K.buf(local, "softmax_stats", [P, KEEP, parts, 4])
        padded, scored, maxed, exped, inverted, p_ready, turned, pT_out, o_filled, o_out, chain, pool_chain = (K.sem(n) for n in (
            "att_padded", "scored", "maxed", "exped", "inverted", "p_ready", "p_turned", "pT_out", "o_filled", "o_out", "att_chain", "att_pool_chain"))

        def bank(u, part, n):
            lo = (u % 2) * 1024 + part * 512
            return flat[0:rows, lo:lo + n]

        def turned_at(u, i, n=1):
            lo = 2048 + (u % sets) * 512 + (i // 4) * 512 + (i % 4) * rows
            return flat[0:rows, lo:lo + n * rows]

        with K.stage() as block:
            @block.tensor
            def _(pe):
                def score(u):
                    keys = units[u][2] * rows
                    if u >= 2:
                        pe.wait_ge(exped if bias is None else maxed, parts * (u - 1))
                    for part in range(parts):
                        for lo in range(0, keys, 512):
                            hi = min(keys, lo + 512)
                            last = scores(units[u], part, lo, hi, bank(u, part, keys)[:, lo:hi])
                    last.then_inc(scored, 1)

                def transposes(u):
                    pe.wait_ge(p_ready, u + 1)
                    if u >= sets:
                        pe.wait_ge(pT_out, u - sets + 1)
                    for t in range(units[u][2]):
                        last = nc.tensor.transpose(turned_at(u, t), p[0:rows, u % KEEP, 0, t * rows:(t + 1) * rows], K.ident[0:rows, 0:rows])
                    last.then_inc(turned, 1)

                def values(u):
                    h, i, kt = units[u]
                    pe.wait_ge(pT_out, u + 1)
                    if u >= 2:
                        pe.wait_ge(o_out, u - 1)
                    for d in range(dts):
                        for t in range(kt):
                            last = nc.tensor.matmul(K.ps[0:drows, 6 + u % 2, d * rows:(d + 1) * rows], value(h, t, d), pT[0:value_rows, u % 2, t, :], start=t == 0, stop=t == kt - 1)
                    last.then_inc(o_filled, 1)

                for n in range(U + VALUE):
                    turn(n, 0, score)
                    turn(n, VALUE, values)
                    turn(n, TURN, transposes)

            @block.vector
            def _(dve):
                link = Chain(dve, chain)

                def maxima(u):
                    keys = units[u][2] * rows
                    if u >= 2:
                        dve.wait_ge(exped, parts * (u - 1))
                    dve.wait_ge(scored, u + 1)
                    for part in range(parts):
                        top = stat[0:rows, u % KEEP, part, 0:1]
                        src = bank(u, part, keys)
                        if bias is not None:
                            link(nc.vector.tensor_tensor_reduce(s[0:rows, u % 2, part, 0:keys], src, bias(units[u]), 1.0, LOWEST, ALU.add, ALU.max, accum_out=top))
                        else:
                            if diagonal is not None:
                                link(nc.vector.tensor_tensor(src[:, keys - rows:keys], src[:, keys - rows:keys], diagonal, ALU.add))
                            link(nc.vector.tensor_reduce(top, src, AX, ALU.max))
                        nc.vector.tensor_scalar(stat[0:rows, u % KEEP, part, 1:2], top, -1.0, None, ALU.mult).then_inc(maxed, 1)

                def inverses(u):
                    dve.wait_ge(exped, parts * (u + 1))
                    for part in range(parts):
                        ins = nc.vector.reciprocal(stat[0:rows, u % KEEP, part, 3:4], stat[0:rows, u % KEEP, part, 2:3])
                        if part == 1:
                            link(ins)
                            ins = nc.vector.tensor_tensor(stat[0:rows, u % KEEP, 1, 3:4], stat[0:rows, u % KEEP, 1, 3:4], minus_lambda[0:rows, :], ALU.mult)
                        ins.then_inc(inverted, 1)

                for n in range(U + NORM):
                    turn(n, NORM, inverses)
                    turn(n, 0, maxima)

            @block.scalar
            def _(act):
                def exps(u):
                    keys = units[u][2] * rows
                    if u >= KEEP:
                        act.wait_ge(turned, u - KEEP + 1)
                    for part in range(parts):
                        act.wait_ge(maxed, parts * u + part + 1)
                        src = s[0:rows, u % 2, part, 0:keys] if bias is not None else bank(u, part, keys)
                        nc.scalar.activation(p[0:rows, u % KEEP, part, 0:keys], src, ACT.Exp, bias=stat[0:rows, u % KEEP, part, 1:2],
                                             accum_out=stat[0:rows, u % KEEP, part, 2:3]).then_inc(exped, 1)

                def turned_out(u):
                    kt = units[u][2]
                    act.wait_ge(turned, u + 1)
                    if u >= 2:
                        act.wait_ge(o_filled, u - 1)
                    for lo in range(0, kt, 4):
                        k = min(4, kt - lo)
                        ins = nc.scalar.activation(pT[0:rows, u % 2, lo:lo + k, :].rearrange("p t q -> p (t q)"), turned_at(u, lo, k), ACT.Copy)
                    ins.then_inc(pT_out, 1)

                def out(u):
                    act.wait_ge(o_filled, u + 1)
                    for d in range(dts):
                        ins = nc.scalar.activation(place(units[u], d), K.ps[0:drows, 6 + u % 2, d * rows:(d + 1) * rows], ACT.Copy)
                    ins.then_inc(o_out, 1)

                if value_rows > rows:
                    act.wait_ge(padded, 1)
                for n in range(U + OUT):
                    turn(n, EXP, exps)
                    turn(n, TURN_OUT, turned_out)
                    turn(n, OUT, out)

            @block.gpsimd
            def _(pool):
                link = Chain(pool, pool_chain)
                if value_rows > rows:
                    nc.gpsimd.memset(pT[HD:value_rows], 0.0).then_inc(padded, 1)
                for u in range(U):
                    keys = units[u][2] * rows
                    pool.wait_ge(inverted, parts * (u + 1))
                    pp = p[0:rows, u % KEEP]
                    inv = stat[0:rows, u % KEEP]
                    if parts == 1:
                        nc.gpsimd.tensor_scalar(pp[:, 0, 0:keys], pp[:, 0, 0:keys], inv[:, 0, 3:4], None, ALU.mult).then_inc(p_ready, 1)
                    else:
                        for part in range(2):
                            link(nc.gpsimd.tensor_scalar(pp[:, part, 0:keys], pp[:, part, 0:keys], inv[:, part, 3:4], None, ALU.mult))
                        nc.gpsimd.tensor_tensor(pp[:, 0, 0:keys], pp[:, 0, 0:keys], pp[:, 1, 0:keys], ALU.add).then_inc(p_ready, 1)


def diff_tables_stage(K, biases, minus_lambda, ins):
    nc = K.nc
    with ExitStack() as local:
        dist = K.buf(local, "dist", [P, S])
        lv = K.buf(local, "lambda_vectors", [P, 4, HD])
        ls = K.buf(local, "lambda_sums", [P, 2])
        le = K.buf(local, "lambda_exps", [P, 2])
        prod = K.buf(local, "lambda_products", [P, HD])
        arrived, summed, exped, chain = (K.sem(n) for n in ("dist_arrived", "lambda_summed", "lambda_exped", "lambda_chain"))
        with K.stage() as block:
            @block.sync
            def _(sp):
                sp.dma_start(dist[:], ins["c_dist"]).then_inc(arrived, 16)
                sp.dma_start(lv[:], ins["diff_lambda"]).then_inc(arrived, 16)

            @block.vector
            def _(dve):
                link = Chain(dve, chain)
                dve.wait_ge(arrived, 32)
                for n in range(2):
                    link(nc.vector.tensor_tensor(prod[:], lv[:, 2 * n, :], lv[:, 2 * n + 1, :], ALU.mult))
                    nc.vector.tensor_reduce(ls[:, n:n + 1], prod[:], AX, ALU.add).then_inc(summed, 1)
                    dve.wait_ge(summed, n + 1)
                for h in range(4):
                    nc.vector.tensor_scalar(biases[:, h, :], dist[:], -float(2.0 ** (-8.0 * (h + 1) / 4)), None, ALU.mult)
                dve.wait_ge(exped, 1)
                link(nc.vector.tensor_tensor(minus_lambda[:], le[:, 1:2], le[:, 0:1], ALU.subtract))
                nc.vector.tensor_scalar(minus_lambda[:], minus_lambda[:], -LAMBDA_INIT, None, ALU.add)

            @block.scalar
            def _(act):
                act.wait_ge(summed, 2)
                nc.scalar.activation(le[:], ls[:], ACT.Exp).then_inc(exped, 1)


def mixer_1(K, ins):
    nc = K.nc
    with ExitStack() as mix:
        y = K.buf(mix, "mix_y", [P, KT, S])
        rwkv_z = K.buf(mix, "rwkv_z", [P, 8, 1 + S])
        with ExitStack() as early:
            pool_u = K.buf(early, "pool_u", [P, 2, 16 + S])
            diff_qk = K.buf(early, "diff_qk", [P, 8, S])
            diff_v = K.buf(early, "diff_v", [P, 4, S])
            mix_in_stage(K, pool_u, rwkv_z, diff_qk, diff_v)
            pool_stage(K, pool_u, y, ins)
            with ExitStack() as att:
                biases = K.buf(att, "diff_bias", [P, 4, S])
                minus_lambda = K.buf(att, "minus_lambda", [P, 1])
                diff_tables_stage(K, biases, minus_lambda, ins)
                head_norm_stage(K, [([(diff_qk[:, i, :], diff_qk[:, i, :], K.vec("diff_q_norm" if i < 4 else "diff_k_norm"))],
                                     2, HD, HD if i < 4 else 1) for i in range(8)])
                units = [(h, i, i + 1) for h in range(4) for i in range(4)]

                def scores(unit, part, lo, hi, to):
                    h, i, _ = unit
                    rows = slice(part * HD, (part + 1) * HD)
                    return nc.tensor.matmul(to, diff_qk[rows, h, i * P:(i + 1) * P], diff_qk[rows, 4 + h, lo:hi], start=True, stop=True)

                attention_stage(K, units, P, scores, lambda h, t, d: diff_v[:, t, h * P:(h + 1) * P],
                                lambda unit, d: y[:, 4 + unit[0], unit[1] * P:(unit[1] + 1) * P],
                                bias=lambda unit: biases[:, unit[0], (3 - unit[1]) * P:4 * P],
                                parts=2, minus_lambda=minus_lambda, width=P)
                head_norm_stage(K, [([(y[:, 4 + h, :], y[:, 4 + h, :], K.vec("diff_subln"))], 1, P, SUBLN) for h in range(4)])
        with ExitStack() as rec:
            V = [K.buf(rec, n, [P, 2, S]) for n in ("rwkv_gate", "rwkv_a", "rwkv_b", "rwkv_k", "rwkv_r", "rwkv_bonus")]
            V.append(K.buf(rec, "rwkv_p_ends", [P, 2, NCH]))
            zm = rwkv_z[:, :, 1:1 + S]
            rwkv_prepare_stage(K, rwkv_z, zm, V, ins)
            toks = [K.buf(rec, n, [CH, NCH, 256]) for n in ("a_tok", "b_tok", "k_tok", "v_tok")]
            jobs = [(src[:, t, :], (lambda c, n, tok=tok, t=t: tok[:, c:c + n, t * P:(t + 1) * P]))
                    for src, tok in zip((V[1], V[2], V[3], zm[:, 4:6, :]), toks) for t in range(2)]
            token_tiles_stage(K, jobs, CH, NCH)
            spare = rwkv_z[:].rearrange("p k t -> p (k t)")
            mats = [spare[0:CH, n * 4 * S:(n + 1) * 4 * S].rearrange("p (h c i) -> p h c i", h=4, c=NCH) for n in range(2)]
            mats += [K.buf(rec, n, [CH, 4, NCH, CH]) for n in ("rbT", "rkT")]
            rwkv_chunk_stage(K, V, (toks[0], toks[3]), mats, ins)
            rwkv_scan_stage(K, V, toks[1:], mats, y)
        residual_stage(K, lambda j: y[:, j, :], KT)


def cross_attention(K, ins):
    nc = K.nc
    with ExitStack() as xa:
        mem = K.buf(xa, "mem", [P, KT, MEM])
        memn = K.buf(xa, "memn", [P, KT, MEM])
        q = K.buf(xa, "xa_q", [P, KT, S])
        k = K.buf(xa, "xa_k", [P, KT, MEM])
        v = K.buf(xa, "xa_v", [P, 2, D])
        o = K.buf(xa, "xa_o", [P, KT, S])
        arrived = K.sem("mem_arrived")
        with K.stage() as block:
            @block.sync
            def _(sp):
                sp.dma_start(mem[:], ins["mem"]).then_inc(arrived, 16)
                sp.wait_ge(arrived, 16)
        norm_stage(K, lambda i: mem[:, i, :], lambda i: memn[:, i, :], "mem_norm_g", (0, MEM))
        project_stage(K, lambda m: q[:, m, :], lambda j: K.xn[:, j, 0:S], S, "xa_norm_g")
        project_stage(K, lambda m: k[:, m, :], lambda j: memn[:, j, :], MEM)
        token_major_stage(K, lambda i, half: v[:, i, half * 512:(half + 1) * 512], lambda j: memn[:, j, :], 2)
        head_norm_stage(K, [([(t[:, 2 * h + i, :], t[:, 2 * h + i, :], K.vec(gain, i)) for i in range(2)], 1, 4 * HD, times)
                            for t, gain, times in ((q, "xa_q_norm", 4 * HD), (k, "xa_k_norm", 1)) for h in range(4)])

        def scores(unit, part, lo, hi, to):
            h, i, _ = unit
            nc.tensor.matmul(to, q[:, 2 * h, i * P:(i + 1) * P], k[:, 2 * h, lo:hi], start=True, stop=False)
            return nc.tensor.matmul(to, q[:, 2 * h + 1, i * P:(i + 1) * P], k[:, 2 * h + 1, lo:hi], start=False, stop=True)

        attention_stage(K, [(h, i, 2) for h in range(4) for i in range(4)], P, scores,
                        lambda h, t, d: v[:, t, h * 256 + d * P:h * 256 + (d + 1) * P],
                        lambda unit, d: o[:, 2 * unit[0] + d, unit[1] * P:(unit[1] + 1) * P], width=256)
        residual_stage(K, lambda j: o[:, j, :], KT)


def conv_ffn_1(K):
    nc = K.nc
    with ExitStack() as ffn:
        hidden = K.buf(ffn, "ffn_hidden", [P, FT, S])
        a = K.buf(ffn, "ffn_a", [P, 4, 2 + S])
        up = K.buf(ffn, "ffn_b", [P, 4, S])
        c = K.buf(ffn, "ffn_c", [P, 4, S])
        filled, b_ready, a_ready, conv, gelu, chain, multiplied = (K.sem(n) for n in ("up_filled", "b_ready", "a_ready", "conv_done", "gelu_done", "conv_chain", "ffn_multiplied"))
        sizes = [4] * (FT // 4) + [FT % 4] * (FT % 4 > 0)
        feed = Feed(K, ffn, KT * len(sizes), lambda i: K.xn[:, i % KT, 0:S], [S], residual_norm(K, ffn, "ffn_norm_g", (0, S)))
        groups, before = [], 0
        for g, n in enumerate(sizes):
            groups.append(Group(feed, 2 * n, KT * g, KT, filled, before))
            before += 2 * n - 1
        starts = [sum(sizes[:g]) for g in range(len(sizes))]
        with K.stage() as block:
            @block.sync
            def _(sp):
                feed.refill(sp)

            @block.tensor
            def _(pe):
                for g, n in enumerate(sizes):
                    def free(e, b, g=g):
                        e.wait_ge(a_ready, starts[g - 1] + min(b, 3) + 1)
                        if b >= 4:
                            e.wait_ge(b_ready, starts[g - 1] + b - 3)
                    groups[g].products(pe, features_product(K, feed, S), free if g else None)

            @block.scalar
            def _(act):
                feed.start_hi(act)
                for g, n in enumerate(sizes):
                    feed.ahead_hi(act, groups[g].body)
                    for i in range(n):
                        f = starts[g] + i
                        groups[g].bank_ready(act, i)
                        if f >= 4:
                            act.wait_ge(conv, f - 3)
                        nc.scalar.activation(a[:, f % 4, 2:2 + S], K.ps[:, i, :], ACT.Copy).then_inc(a_ready, 1)
                    for i in range(n):
                        f = starts[g] + i
                        groups[g].bank_ready(act, n + i)
                        if f >= 4:
                            act.wait_ge(multiplied, f - 3)
                        nc.scalar.activation(up[:, f % 4, :], K.ps[:, n + i, :], ACT.Copy).then_inc(b_ready, 1)
                    feed.ahead_hi(act, groups[g].end)
                    for i in range(n):
                        f = starts[g] + i
                        act.wait_ge(conv, f + 1)
                        nc.scalar.activation(hidden[:, f, :], c[:, f % 4, :], ACT.Gelu).then_inc(gelu, 1)

            @block.vector
            def _(dve):
                link = Chain(dve, chain)
                link(nc.vector.memset(a[:, :, 0:2], 0.0))
                feed.start_lo(dve)
                for g, n in enumerate(sizes):
                    feed.ahead_lo(dve, groups[g].body)
                    for i in range(n):
                        f = starts[g] + i
                        dve.wait_ge(a_ready, f + 1)
                        if f >= 4:
                            dve.wait_ge(gelu, f - 3)
                        at, to = a[:, f % 4, :], c[:, f % 4, :]
                        link(nc.vector.tensor_scalar(to, at[:, 0:S], K.vec("ffn_conv_w", f), K.vec("ffn_conv_b", f), ALU.mult, ALU.add))
                        link(nc.vector.scalar_tensor_tensor(out=to, in0=at[:, 1:1 + S], scalar=K.vec("ffn_conv_w", FT + f), in1=to, op0=ALU.mult, op1=ALU.add))
                        nc.vector.scalar_tensor_tensor(out=to, in0=at[:, 2:2 + S], scalar=K.vec("ffn_conv_w", 2 * FT + f), in1=to, op0=ALU.mult, op1=ALU.add).then_inc(conv, 1)
                        if i == n - 2:
                            feed.ahead_lo(dve, groups[g].end)

            @block.gpsimd
            def _(pool):
                for f in range(FT):
                    pool.wait_ge(gelu, f + 1)
                    pool.wait_ge(b_ready, f + 1)
                    nc.gpsimd.tensor_tensor(hidden[:, f, :], hidden[:, f, :], up[:, f % 4, :], ALU.mult).then_inc(multiplied, 1)
        residual_stage(K, lambda j: hidden[:, j, :], FT)


def block_1(K, ins):
    mixer_1(K, ins)
    cross_attention(K, ins)
    conv_ffn_1(K)


def block_2_slabs(a):
    w = a["w_in_2"]
    parts = [wide(w, [(0, 1024)]), wide(w, [(1024, 1536), (2048, 2560)]), wide(w, [(1536, 2048), (2560, 3072)]),
             wide(w, [(3144, 4168)]), wide(w, [(4168, 5192)]), wide(a["w_out_a_2"], [(0, D)]),
             wide(a["w_out_b_2"], [(0, D)]), wide(a["w_o_2"], [(0, D)])]
    parts += [wide(a["w_ff_in_2"], [(f, f + D)]) for f in range(0, FF2, D)]
    return parts + [wide(a["w_ff_out_2"], [(0, D)])]


def block_2_inputs(i):
    w = i["w_in_2"][0]
    index = np.concatenate([w[:, 3072:3136], w[:, 3072:3136], w[:, 3136:3144]], axis=1)
    return dict(
        index_w=np.ascontiguousarray(index.reshape(KT, P, -1).transpose(1, 0, 2)),
        sgu_w=np.ascontiguousarray(i["w_s_2"][0].transpose(2, 0, 1)),
        sgu_b=np.ascontiguousarray(np.broadcast_to(np.tile(i["b_s_2"][0], (1, 4)), (P, 4, S))),
        sgu_ln=np.ascontiguousarray(np.broadcast_to(np.stack([i["sgu_ln_g_2"][0], i["sgu_ln_b_2"][0]]), (P, 2, S))))


def mix_in_2_stage(K, u, vg, q, v, k, qi, ki, wi, gates, ins):
    nc = K.nc
    filled, drained, arrived, index_filled = K.sem("proj_filled"), K.sem("proj_drained"), K.sem("index_w_arrived"), K.sem("index_filled")
    with ExitStack() as local:
        feed = Feed(K, local, 5 * KT, lambda i: K.xn[:, i % KT, 0:S], [S], residual_norm(K, local, "norm1_g_2", (0, S)))
        groups = [Group(feed, 8, g * KT, KT, filled, 7 * g) for g in range(5)]
        w = K.buf(local, "index_w", [P, KT, 2 * HD + 8])
        with K.stage() as block:
            @block.sync
            def _(sp):
                sp.dma_start(w[:], ins["index_w"]).then_inc(arrived, 16)
                feed.refill(sp)

            @block.tensor
            def _(pe):
                for g, group in enumerate(groups):
                    def product(i, b, start, stop, g=g):
                        if g < 2 and b >= 4:
                            return exact(nc, K.ps[:, b, :], cut(feed.acts(i), (b - 4) * P, (b - 3) * P), cut(feed.slab(i), 512, 1024), start, stop)
                        return features_product(K, feed, S)(i, b, start, stop)
                    group.products(pe, product, (lambda e, b, g=g: e.wait_ge(drained, 8 * (g - 1) + b + 1)) if g else None)
                pe.wait_ge(arrived, 16)
                pe.wait_ge(drained, 8 * 4 + 2)
                for j in range(KT):
                    last = nc.tensor.matmul(K.ps[:, 0, :], w[:, j, 0:P], K.xn[:, j, 0:S], start=j == 0, stop=j == KT - 1)
                last.then_inc(index_filled, 1)
                for i in range(4):
                    for j in range(KT):
                        last = nc.tensor.matmul(K.ps[:, 1, i * 8:(i + 1) * 8], K.xn[:, j, i * P:(i + 1) * P], w[:, j, P:P + 8], start=j == 0, stop=j == KT - 1)
                last.then_inc(index_filled, 1)

            @block.scalar
            def _(act):
                places = [(u, vg), (q, v), (k, qi), (gates[:, 0:4], gates[:, 4:8]), (gates[:, 8:12], gates[:, 12:16])]
                feed.start_hi(act)
                for g, group in enumerate(groups):
                    feed.ahead_hi(act, group.body)
                    func = ACT.Gelu_apprx_tanh if g == 0 else ACT.Sigmoid if g >= 3 else ACT.Copy
                    for b in range(8):
                        group.bank_ready(act, b)
                        nc.scalar.activation(places[g][b // 4][:, b % 4, :], K.ps[:, b, :], func).then_inc(drained, 1)
                    feed.ahead_hi(act, group.end)
                act.wait_ge(index_filled, 2)
                nc.scalar.activation(ki[:], K.ps[:, 0, :], ACT.Copy)
                nc.scalar.activation(wi[:].rearrange("p i h -> p (i h)"), K.ps[:, 1, 0:32], ACT.Copy, scale=float(64.0 ** -0.5 * 8.0 ** -0.5))

            @block.vector
            def _(dve):
                feed.start_lo(dve)
                feed.ahead_lo(dve, range(5 * KT))


def sgu_stage(K, u, vg, ya, ins):
    nc = K.nc
    with ExitStack() as local:
        w = K.buf(local, "sgu_w", [P, 4, P])
        b = K.buf(local, "sgu_b", [P, 4, S])
        ln = K.buf(local, "sgu_ln", [P, 2, S])
        stats = K.buf(local, "sgu_stats", [P, 4, 6])
        moments = K.buf(local, "sgu_moments", [P, 4, 2])
        arrived, chain, rooted, v_ready, w_ready, filled = (K.sem(n) for n in ("sgu_arrived", "sgu_chain", "sgu_rooted", "sgu_v_ready", "sgu_w_ready", "sgu_filled"))
        moments_ready, rstd_ready = K.sem("moments_ready"), K.sem("sgu_rstd_ready")
        with K.stage() as block:
            @block.sync
            def _(sp):
                for to, src in ((w, "sgu_w"), (b, "sgu_b"), (ln, "sgu_ln")):
                    sp.dma_start(to[:], ins[src]).then_inc(arrived, 16)

            @block.vector
            def _(dve):
                link = Chain(dve, chain)
                for c in range(4):
                    link(nc.vector.bn_stats(stats[:, c, :], vg[:, c, :]))
                    link(nc.vector.bn_aggr(moments[:, c, :], stats[:, c, :]))
                nc.vector.tensor_copy(stats[:, :, 0:1], moments[:, :, 1:2]).then_inc(moments_ready, 1)
                dve.wait_ge(arrived, 48)
                nc.vector.tensor_tensor(w[:], w[:], K.upper.unsqueeze(1).to_broadcast((P, 4, P)), ALU.mult).then_inc(w_ready, 1)
                dve.wait_ge(rooted, 1)
                nc.vector.reciprocal(stats[:, :, 2:3], stats[:, :, 1:2]).then_inc(rstd_ready, 1)
                dve.wait_ge(rstd_ready, 1)
                for c in range(4):
                    link(nc.vector.tensor_scalar(vg[:, c, :], vg[:, c, :], moments[:, c, 0:1], stats[:, c, 2:3], ALU.subtract, ALU.mult))
                    link(nc.vector.tensor_tensor(vg[:, c, :], vg[:, c, :], ln[:, 0, :], ALU.mult))
                    nc.vector.tensor_tensor(vg[:, c, :], vg[:, c, :], ln[:, 1, :], ALU.add).then_inc(v_ready, 1)
                for g in range(4):
                    dve.wait_ge(filled, g + 1)
                    link(nc.vector.tensor_tensor(ya[:, g, :], K.ps[:, g, :], b[:, g, :], ALU.add))
                    nc.vector.tensor_tensor(ya[:, g, :], ya[:, g, :], u[:, g, :], ALU.mult)

            @block.scalar
            def _(act):
                act.wait_ge(moments_ready, 1)
                nc.scalar.activation(stats[:, :, 1:2], stats[:, :, 0:1], ACT.Sqrt, bias=K.eps_col).then_inc(rooted, 1)

            @block.tensor
            def _(pe):
                pe.wait_ge(w_ready, 1)
                pe.wait_ge(v_ready, 4)
                for g in range(4):
                    for c in range(4):
                        last = nc.tensor.matmul(K.ps[:, g, c * P:(c + 1) * P], vg[:, c, g * P:(g + 1) * P], w[:, g, :], start=True, stop=True)
                    last.then_inc(filled, 1)


def rope_stage(K, tiles, ins):
    nc = K.nc
    with ExitStack() as local:
        table = K.buf(local, "rope_table", [P, 2, 2, S])
        part = K.buf(local, "rope_part", [P, 2, S])
        arrived, scaled, turned, chain, cos_done, drained = (K.sem(n) for n in ("rope_arrived", "rope_scaled", "rope_turned", "rope_chain", "rope_cos_done", "rope_drained"))
        with K.stage() as block:
            @block.sync
            def _(sp):
                sp.dma_start(table[:, 0, 0, :], ins["c_cos"]).then_inc(arrived, 16)
                sp.dma_start(table[:, 0, 1, :], ins["c_sin"]).then_inc(arrived, 16)

            @block.tensor
            def _(pe):
                for n, (x, _) in enumerate(tiles):
                    if n >= 8:
                        pe.wait_ge(drained, n - 7)
                    nc.tensor.matmul(K.ps[:, n % 8, :], K.rot, x, start=True, stop=True).then_inc(turned, 1)

            @block.gpsimd
            def _(pool):
                pool.wait_ge(scaled, 1)
                for n, (x, small) in enumerate(tiles):
                    pool.wait_ge(turned, n + 1)
                    nc.gpsimd.tensor_tensor(x, x, table[:, small, 0, :], ALU.mult).then_inc(cos_done, 1)

            @block.vector
            def _(dve):
                link = Chain(dve, chain)
                dve.wait_ge(arrived, 32)
                nc.vector.tensor_scalar(table[:, 1], table[:, 0], HD ** -0.5, None, ALU.mult).then_inc(scaled, 1)
                dve.wait_ge(scaled, 1)
                for n, (x, small) in enumerate(tiles):
                    dve.wait_ge(turned, n + 1)
                    nc.vector.tensor_tensor(part[:, n % 2, :], K.ps[:, n % 8, :], table[:, small, 1, :], ALU.mult).then_inc(drained, 1)
                    dve.wait_ge(drained, n + 1)
                    dve.wait_ge(cos_done, n + 1)
                    link(nc.vector.tensor_tensor(x, x, part[:, n % 2, :], ALU.add))


def select_stage(K, qi, ki, wi, mask, ins):
    nc = K.nc
    heads = 8
    with ExitStack() as local:
        causal = K.buf(local, "causal", [P, P])
        pos = K.buf(local, "relu_logits", [P, 2, S])
        score = K.buf(local, "index_score", [P, S])
        work = K.buf(local, "index_work", [P, S])
        top = K.buf(local, "index_top", [P, 8])
        above = K.buf(local, "index_above", [P, S])
        equal = K.buf(local, "index_equal", [P, S])
        count = K.buf(local, "index_count", [P, 2])
        one = K.buf(local, "index_ones", [P, S])
        arrived, chain, filled, relu, summed = (K.sem(n) for n in ("causal_arrived", "select_chain", "logits_filled", "logits_relu", "logits_summed"))
        with K.stage() as block:
            @block.sync
            def _(sp):
                sp.dma_start(causal[:], ins["c_causal"]).then_inc(arrived, 16)

            @block.tensor
            def _(pe):
                for n in range(3 * heads):
                    i, h = 1 + n // heads, n % heads
                    keys = (i + 1) * P
                    rows = slice((h % 2) * HD, (h % 2 + 1) * HD)
                    if n >= 8:
                        pe.wait_ge(relu, n - 7)
                    nc.tensor.matmul(K.ps[:, n % 8, 0:keys], qi[rows, h // 2, i * P:(i + 1) * P], ki[rows, 0:keys], start=True, stop=True).then_inc(filled, 1)

            @block.scalar
            def _(act):
                for n in range(3 * heads):
                    keys = (2 + n // heads) * P
                    act.wait_ge(filled, n + 1)
                    if n >= 2:
                        act.wait_ge(summed, n - 1)
                    nc.scalar.activation(pos[:, n % 2, 0:keys], K.ps[:, n % 8, 0:keys], ACT.Relu).then_inc(relu, 1)

            @block.vector
            def _(dve):
                link = Chain(dve, chain)
                link(nc.vector.memset(one[:], 1.0))
                dve.wait_ge(arrived, 16)
                nc.vector.tensor_copy(mask[:, 0, 0:P], causal[:])
                for i in range(1, 4):
                    keys = (i + 1) * P
                    sc, wk = score[:, 0:keys], work[:, 0:keys]
                    for h in range(heads):
                        n = (i - 1) * heads + h
                        dve.wait_ge(relu, n + 1)
                        if h == 0:
                            ins_ = nc.vector.tensor_scalar(sc, pos[:, n % 2, 0:keys], wi[:, i, 0:1], None, ALU.mult)
                        else:
                            ins_ = nc.vector.scalar_tensor_tensor(out=sc, in0=pos[:, n % 2, 0:keys], scalar=wi[:, i, h:h + 1], in1=sc, op0=ALU.mult, op1=ALU.add)
                        ins_.then_inc(summed, 1)
                        dve.wait_ge(summed, n + 1)
                    link(nc.vector.tensor_tensor(score[:, i * P:keys], score[:, i * P:keys], causal[:], ALU.add))
                    for n in range(TOPK // 8):
                        link(nc.vector.max(top[:], sc if n == 0 else wk))
                        if n < TOPK // 8 - 1:
                            link(nc.vector.match_replace(wk, top[:], sc if n == 0 else wk, LOWEST))
                    last = top[:, 7:8]
                    link(nc.vector.tensor_scalar(above[:, 0:keys], sc, last, 0.0, ALU.is_gt, ALU.add, accum_out=count[:, 0:1]))
                    link(nc.vector.tensor_scalar(equal[:, 0:keys], sc, last, None, ALU.is_equal))
                    link(nc.vector.tensor_scalar(count[:, 1:2], count[:, 0:1], -1.0, float(TOPK), ALU.mult, ALU.add))
                    link(nc.vector.tensor_tensor_scan(wk, one[:, 0:keys], equal[:, 0:keys], 0.0, ALU.mult, ALU.add))
                    link(nc.vector.scalar_tensor_tensor(out=wk, in0=wk, scalar=count[:, 1:2], in1=equal[:, 0:keys], op0=ALU.is_le, op1=ALU.mult))
                    link(nc.vector.tensor_tensor(wk, wk, above[:, 0:keys], ALU.add))
                    link(nc.vector.tensor_scalar(mask[:, i, 0:keys], wk, -NEG, NEG, ALU.mult, ALU.add))


def merge_stage(K, ya, yb, gates, merged):
    nc = K.nc
    filled, drained, chain = K.sem("merge_filled"), K.sem("merge_drained"), K.sem("merge_chain")
    with ExitStack() as local:
        part = K.buf(local, "merge_part", [P, 2, S])
        feed = Feed(K, local, KT, lambda i: (ya, yb)[i // 4][:, i % 4, :], [S])
        groups = [Group(feed, KT, 4 * g, 4, filled, 7 * g) for g in range(2)]
        with K.stage() as block:
            @block.sync
            def _(sp):
                feed.refill(sp)

            @block.tensor
            def _(pe):
                for g, group in enumerate(groups):
                    group.products(pe, features_product(K, feed, S), (lambda e, b: e.wait_ge(drained, b + 1)) if g else None)

            @block.scalar
            def _(act):
                feed.start_hi(act)
                feed.ahead_hi(act, range(KT))

            @block.vector
            def _(dve):
                link = Chain(dve, chain)
                feed.start_lo(dve)
                feed.ahead_lo(dve, groups[0].body)
                for m in range(KT):
                    groups[0].bank_ready(dve, m)
                    nc.vector.tensor_tensor(merged(m), K.ps[:, m, :], gates[:, m, :], ALU.mult).then_inc(drained, 1)
                feed.ahead_lo(dve, groups[0].end)
                feed.ahead_lo(dve, groups[1].body)
                dve.wait_ge(drained, KT)
                for m in range(KT):
                    groups[1].bank_ready(dve, m)
                    link(nc.vector.tensor_tensor(part[:, m % 2, :], K.ps[:, m, :], gates[:, KT + m, :], ALU.mult))
                    nc.vector.tensor_tensor(merged(m), merged(m), part[:, m % 2, :], ALU.add)


def ffn_2(K):
    nc = K.nc
    turns = FF2 // D
    with ExitStack() as ffn:
        hidden = K.buf(ffn, "ff_hidden", [P, FF2 // P, S])
        filled, drained = K.sem("ff_filled"), K.sem("ff_drained")
        with ExitStack() as local:
            feed = Feed(K, local, turns * KT, lambda i: K.xn[:, i % KT, 0:S], [S], residual_norm(K, local, "norm2_g_2", (0, S)))
            group = Group(feed, KT, 0, KT, filled)
            with K.stage() as block:
                @block.sync
                def _(sp):
                    feed.refill(sp)

                @block.tensor
                def _(pe):
                    product = features_product(K, feed, S)
                    group.products(pe, product)
                    with pe.Fori(1, turns) as turn:
                        group.products(pe, product, lambda e, b: e.wait_ge(drained, turn * KT), turn)

                @block.scalar
                def _(act):
                    def drain(m, turn):
                        group.bank_ready(act, m, turn)
                        nc.scalar.activation(hidden[:, bass.ds(turn * KT + m, 1), :], K.ps[:, m:m + 1, :], ACT.Relu).then_inc(drained, 1)

                    feed.start_hi(act)
                    with act.Fori(0, turns - 1) as turn:
                        feed.ahead_hi(act, group.body, turn)
                        for m in range(KT):
                            drain(m, turn)
                        feed.ahead_hi(act, group.end, turn)
                    feed.ahead_hi(act, range((turns - 1) * KT, turns * KT - 1))
                    for m in range(KT):
                        drain(m, turns - 1)

                @block.vector
                def _(dve):
                    feed.start_lo(dve)
                    with dve.Fori(0, turns - 1) as turn:
                        feed.ahead_lo(dve, range(KT), turn)
                    feed.ahead_lo(dve, range((turns - 1) * KT, turns * KT))

                @block.gpsimd
                def _(pool):
                    with pool.Fori(0, turns) as turn:
                        for m in range(KT):
                            pool.wait_ge(drained, turn * KT + (m + 1))
                            at = hidden[:, bass.ds(turn * KT + m, 1), :]
                            nc.gpsimd.tensor_tensor(at, at, at, ALU.mult)
        residual_stage(K, lambda j: hidden[:, j, :], FF2 // P)


def block_2(K, ins):
    with ExitStack() as mix:
        ya, yb, u, vg, q, v, k, qi = (K.buf(mix, n, [P, 4, S]) for n in ("sgu_y", "dsa_y", "sgu_u", "sgu_v", "dsa_q", "dsa_v", "dsa_k", "index_q"))
        ki = K.buf(mix, "index_k", [P, S])
        wi = K.buf(mix, "index_weights", [P, 4, 8])
        gates = K.buf(mix, "branch_gates", [P, 16, S])
        mix_in_2_stage(K, u, vg, q, v, k, qi, ki, wi, gates, ins)
        sgu_stage(K, u, vg, ya, ins)
        rope_stage(K, [(x[:, t, :], s) for x, s in ((qi, 0), (k, 0), (q, 1)) for t in range(4)] + [(ki[:], 0)], ins)
        with ExitStack() as att:
            mask = K.buf(att, "dsa_mask", [P, 4, S])
            select_stage(K, qi, ki, wi, mask, ins)

            def scores(unit, part, lo, hi, to):
                h, i, _ = unit
                rows = slice((h % 2) * HD, (h % 2 + 1) * HD)
                return K.nc.tensor.matmul(to, q[rows, h // 2, i * P:(i + 1) * P], k[rows, h // 2, lo:hi], start=True, stop=True)

            attention_stage(K, [(h, i, i + 1) for h in range(8) for i in range(4)], P, scores,
                            lambda h, t, d: v[:, t, h * HD:(h + 1) * HD],
                            lambda unit, d: yb[(unit[0] % 2) * HD:(unit[0] % 2 + 1) * HD, unit[0] // 2, unit[1] * P:(unit[1] + 1) * P],
                            bias=lambda unit: mask[:, unit[1], 0:unit[2] * P])
        merge_stage(K, ya, yb, gates, lambda m: K.xn[:, m, 0:S])
    residual_stage(K, lambda j: K.xn[:, j, 0:S], KT)
    ffn_2(K)
    norm_stage(K, lambda k: K.h[:, k, 0:S], lambda k: K.xn[:, k, META:T3], "norm_f_g_2", (0, S))
    K.h, K.xn = K.xn, K.h


FOX_HEADS = 8
GDN_HEADS = 8
QUAD = 4


def block_3_slabs(a):
    w = a["w_in_3"]
    parts = [paired(w, [(lo, lo + 512)]) for lo in (1544, 2056, 2568, 0, 512, 1024, 3080, 3608, 4120, 4632, 5144)]
    for lo in (0, 512):
        parts += [paired(a["w_branch_fox_3"], [(lo, lo + 512)]), paired(a["w_branch_gdn_3"], [(lo, lo + 512)])]
    parts += [paired(a["w_out_3"], [(lo, lo + 512)]) for lo in (0, 512)]
    parts += [paired(a["ffn_w_up_3"], [(f, f + 256), (FF + f, FF + f + 256)]) for f in range(0, FF, 256)]
    return parts + [wide(a["ffn_w_down_3"], [(0, D)])]


def block_3_inputs(i):
    w = i["w_in_3"][0]
    small = np.concatenate([w[:, 1536:1544], w[:, 3592:3600], w[:, 3600:3608]], axis=1)
    return dict(head_w=np.ascontiguousarray(small.reshape(KT, P, 24).transpose(1, 0, 2)))


def half_product(K, feed):
    def product(i, b, start, stop):
        lo, hi = HALVES[b % 2]
        for k in range(2):
            at = k * 512 + (b // 2) * P
            mm = exact(K.nc, K.ps[:, b, 0:hi - lo], cut(feed.slab(i), at, at + P), [x[:, k, lo:hi] for x in feed.acts(i)],
                       start and k == 0, stop and k == 1)
        return mm
    return product


def pairs_of(x):
    n = x.shape[1] // 2
    return lambda i: x[:, 2 * (i % n):2 * (i % n) + 2, :]


def mix_in_3_stage(K, fq, fk, fv, gin, heads, sums, ins):
    nc = K.nc
    filled, drained, arrived, head_filled, padded, conv, done, chain = (K.sem(n) for n in (
        "proj3_filled", "proj3_drained", "head_w_arrived", "heads_filled", "fox_padded", "gdn_conv_done", "gdn_silu_done", "gdn_conv_chain"))
    with ExitStack() as local:
        feed = Feed(K, local, 24, pairs_of(K.xn), [2, T3], residual_norm(K, local, "norm_mix_w_3", (0, T3)))
        groups, before = [], 0
        for g in range(6):
            groups.append(Group(feed, NC3 if g == 5 else 8, 4 * g, 4, filled, before))
            before += groups[-1].banks - 1
        out_before = [sum(x.banks for x in groups[:g]) for g in range(7)]
        w = K.buf(local, "head_w", [P, KT, 24])
        mixed = K.buf(local, "gdn_conv", [P, 2, T3])
        with K.stage() as block:
            @block.sync
            def _(sp):
                sp.dma_start(w[:], ins["head_w"]).then_inc(arrived, 16)
                feed.refill(sp)

            @block.tensor
            def _(pe):
                for g, group in enumerate(groups):
                    def token_major(i, b, start, stop):
                        for k in range(2):
                            mm = exact(nc, K.ps[0:C3, b, :], [x[:, k, b * C3:(b + 1) * C3] for x in feed.acts(i)],
                                       cut(feed.slab(i), k * 512, (k + 1) * 512), start and k == 0, stop and k == 1)
                        return mm

                    def free(e, b, g=g):
                        e.wait_ge(drained, out_before[g - 1] + min(b + 1, groups[g - 1].banks))
                    group.products(pe, token_major if g == 5 else half_product(K, feed), free if g else None)
                pe.wait_ge(arrived, 16)
                pe.wait_ge(drained, out_before[6])
                for n in range(3):
                    for c, (lo, hi) in enumerate(HALVES):
                        for j in range(KT):
                            last = nc.tensor.matmul(K.ps[0:8, 2 * n + c, 0:hi - lo], w[:, j, n * 8:(n + 1) * 8], K.xn[:, j, lo:hi], start=j == 0, stop=j == KT - 1)
                last.then_inc(head_filled, 1)

            @block.scalar
            def _(act):
                def silu(t):
                    act.wait_ge(conv, t + 1)
                    nc.scalar.activation(gin[:, t, 3:3 + T3], mixed[:, t % 2, :], ACT.Silu).then_inc(done, 1)

                def ahead(steps):
                    for i in steps:
                        feed.ahead_hi(act, [i])
                        if 0 <= i - 5 < 12:
                            silu(i - 5)

                feed.start_hi(act)
                for g, group in enumerate(groups):
                    ahead(group.body)
                    for b in range(group.banks):
                        group.bank_ready(act, b)
                        (lo, hi), t = HALVES[b % 2], b // 2
                        if g == 5:
                            if b == 0:
                                act.wait_ge(padded, 3)
                            ins_ = nc.scalar.activation(fv[0:C3, b, :], K.ps[0:C3, b, :], ACT.Copy)
                        elif g == 3:
                            if b == 0:
                                act.wait_ge(padded, 2)
                            for o in range(2):
                                rows = slice(o * HD, (o + 1) * HD)
                                ins_ = nc.scalar.activation(fq[rows, 2 * t + o, lo:hi], K.ps[rows, b, 0:hi - lo], ACT.Copy, scale=HD ** -0.5)
                        else:
                            to = fk[:, t, lo:hi] if g == 4 else gin[:, 4 * g + t, 3 + lo:3 + hi]
                            ins_ = nc.scalar.activation(to, K.ps[:, b, 0:hi - lo], ACT.Copy)
                        ins_.then_inc(drained, 1)
                    ahead(group.end)
                act.wait_ge(head_filled, 1)
                for n in range(3):
                    for c, (lo, hi) in enumerate(HALVES):
                        nc.scalar.activation(heads[:, n, lo:hi], K.ps[0:8, 2 * n + c, 0:hi - lo], ACT.Copy)

            @block.vector
            def _(dve):
                feed.start_lo(dve)
                for o in range(2):
                    nc.vector.memset(fq[o * HD:(o + 1) * HD, 1 - o:FOX_HEADS:2, :], 0.0).then_inc(padded, 1)
                nc.vector.memset(fv[HD:P], 0.0).then_inc(padded, 1)
                nc.vector.memset(sums[:], 0.0)
                nc.vector.memset(gin[:, :, 0:3], 0.0).then_inc(padded, 1)
                dve.wait_ge(padded, 4)
                link = Chain(dve, chain)
                for i in range(24):
                    feed.ahead_lo(dve, [i])
                    t = i - 4
                    if 0 <= t < 12:
                        dve.wait_ge(drained, 2 * t + 2)
                        if t >= 2:
                            dve.wait_ge(done, t - 1)
                        to = mixed[:, t % 2, :]
                        link(nc.vector.tensor_scalar(to, gin[:, t, 0:T3], K.vec("gdn_conv_w_3", t), None, ALU.mult))
                        for tap in range(1, 4):
                            ins_ = nc.vector.scalar_tensor_tensor(out=to, in0=gin[:, t, tap:tap + T3], scalar=K.vec("gdn_conv_w_3", 12 * tap + t), in1=to, op0=ALU.mult, op1=ALU.add)
                            if tap < 3:
                                link(ins_)
                        ins_.then_inc(conv, 1)


def gate_3_stage(K, z, gates):
    nc = K.nc
    filled, drained = K.sem("gates3_filled"), K.sem("gates3_drained")
    with ExitStack() as local:
        feed = Feed(K, local, 20, pairs_of(K.xn), [2, T3])
        groups = [Group(feed, 8, 4 * g, 4, filled, 7 * g) for g in range(5)]
        with K.stage() as block:
            @block.sync
            def _(sp):
                feed.refill(sp)

            @block.tensor
            def _(pe):
                for g, group in enumerate(groups):
                    group.products(pe, half_product(K, feed), (lambda e, b, g=g: e.wait_ge(drained, 8 * (g - 1) + b + 1)) if g else None)

            @block.scalar
            def _(act):
                feed.start_hi(act)
                for g, group in enumerate(groups):
                    feed.ahead_hi(act, group.body)
                    for b in range(8):
                        group.bank_ready(act, b)
                        (lo, hi), t = HALVES[b % 2], b // 2
                        src = K.ps[:, b, 0:hi - lo]
                        if g == 0:
                            nc.scalar.activation(z[:, t, lo:hi], src, ACT.Silu).then_inc(drained, 1)
                        else:
                            m = 4 * (g - 1) + t
                            nc.scalar.activation(gates[:, m, lo:hi], src, ACT.Sigmoid, bias=K.vec("gate_bias_3", m)).then_inc(drained, 1)
                    feed.ahead_hi(act, group.end)

            @block.vector
            def _(dve):
                feed.start_lo(dve)
                feed.ahead_lo(dve, range(20))


def head_rates_stage(K, heads, sums, keep):
    nc = K.nc
    with ExitStack() as local:
        x = K.buf(local, "rate_x", [8, 2, T3])
        e = K.buf(local, "rate_e", [8, 2, T3])
        rate = K.buf(local, "gdn_rate", [8, 2])
        chain, e_ready, log_ready, rate_ready, summed = (K.sem(n) for n in ("rate_chain", "e_ready", "log_ready", "rate_ready", "gc_summed"))
        with K.stage() as block:
            @block.vector
            def _(dve):
                link = Chain(dve, chain)
                link(nc.vector.tensor_scalar(x[:, 0, :], heads[:, 0, :], K.vec("fgt_bias_3")[0:8, :], None, ALU.add))
                link(nc.vector.tensor_scalar(x[:, 1, :], heads[:, 2, :], K.vec("gdn_dt_bias_3")[0:8, :], None, ALU.add))
                link(nc.vector.tensor_scalar(e[:], x[:], -1.0, None, ALU.mult))
                nc.vector.tensor_tensor(e[:], e[:], x[:], ALU.min).then_inc(e_ready, 1)
                dve.wait_ge(e_ready, 1)
                dve.wait_ge(log_ready, 1)
                link(nc.vector.tensor_scalar(heads[:, 3, :], x[:, 0, :], 0.0, None, ALU.min))
                link(nc.vector.tensor_tensor(x[:, 0, :], e[:, 0, :], heads[:, 3, :], ALU.subtract))
                link(nc.vector.memset(heads[:, 3, :], 1.0))
                link(nc.vector.tensor_tensor_scan(sums[0:8, :], heads[:, 3, :], x[:, 0, :], 0.0, ALU.mult, ALU.add))
                link(nc.vector.scalar_tensor_tensor(out=x[:, 1, :], in0=x[:, 1, :], scalar=0.0, in1=e[:, 1, :], op0=ALU.max, op1=ALU.add))
                dve.wait_ge(rate_ready, 1)
                link(nc.vector.tensor_scalar(x[:, 1, :], x[:, 1, :], rate[:, 0:1], -1.0, ALU.mult, ALU.mult))
                nc.vector.tensor_tensor_scan(heads[:, 2, :], keep, x[:, 1, :], 0.0, ALU.mult, ALU.add).then_inc(summed, 1)

            @block.scalar
            def _(act):
                nc.scalar.activation(rate[:, 0:1], K.vec("gdn_a_log_3")[0:8, :], ACT.Exp).then_inc(rate_ready, 1)
                act.wait_ge(e_ready, 1)
                nc.scalar.activation(e[:], e[:], ACT.Exp).then_inc(e_ready, 1)
                act.wait_ge(e_ready, 2)
                nc.scalar.activation(e[:], e[:], ACT.Ln, bias=K.one_col[0:8, :]).then_inc(log_ready, 1)
                act.wait_ge(summed, 1)
                nc.scalar.activation(heads[:, 3, :], heads[:, 2, :], ACT.Exp)
                nc.scalar.activation(heads[:, 1, :], heads[:, 1, :], ACT.Sigmoid)


def gdn_rates_stage(K, heads, q, q0, tok, last_decay):
    nc = K.nc
    with ExitStack() as local:
        turned, turned_out, spread, chain, exped, q_filled, q_out, last_in = (K.sem(n) for n in ("rates_turned", "rates_out", "rates_spread", "rates_chain", "rates_exped", "q_filled", "q_out", "last_in"))
        last_sum = K.buf(local, "last_sum", [8, NC3])
        with K.stage() as block:
            @block.tensor
            def _(pe):
                for n, row in enumerate((1, 2, 3)):
                    for c in range(NC3):
                        last = nc.tensor.transpose(K.ps[0:C3, n, c * 8:(c + 1) * 8], heads[:, row, c * C3:(c + 1) * C3], K.ident[0:8, 0:8])
                last.then_inc(turned, 1)
                pe.wait_ge(last_in, 1)
                for h in range(GDN_HEADS):
                    last = nc.tensor.matmul(K.ps[:, 3, h * NC3:(h + 1) * NC3], K.pick(h, P), last_sum[:], start=True, stop=True)
                last.then_inc(spread, 1)
                for h in range(GDN_HEADS):
                    for c, (lo, hi) in enumerate(HALVES):
                        n = 2 * h + c
                        if n >= 4:
                            pe.wait_ge(q_out, n - 3)
                        nc.tensor.matmul(K.ps[:, 4 + n % 4, 0:hi - lo], K.pick(h, P), heads[:, 3, lo:hi], start=True, stop=True).then_inc(q_filled, 1)

            @block.vector
            def _(dve):
                link = Chain(dve, chain)
                nc.vector.tensor_copy(last_sum[:], heads[:, 2, :].rearrange("h (c i) -> h c i", i=C3)[:, :, C3 - 1]).then_inc(last_in, 1)
                dve.wait_ge(turned, 1)
                flat = tok[:].rearrange("p n c h -> p n (c h)")
                for n in range(3):
                    link(nc.vector.tensor_copy(flat[:, n, :], K.ps[0:C3, n, 0:NC3 * 8]))
                link(nc.vector.tensor_tensor(flat[:, 2, :], flat[:, 2, :], flat[:, 0, :], ALU.mult))
                dve.wait_ge(spread, 1)
                sums = K.ps[0:C3, 3, 0:NC3 * 8].rearrange("p (h c) -> p c h", c=NC3)
                nc.vector.tensor_tensor(tok[:, 3], sums, tok[:, 1], ALU.subtract).then_inc(turned_out, 1)
                for h in range(GDN_HEADS):
                    rows = slice((h % 2) * HD, (h % 2 + 1) * HD)
                    for c, (lo, hi) in enumerate(HALVES):
                        n = 2 * h + c
                        dve.wait_ge(q_filled, n + 1)
                        nc.vector.tensor_tensor(q0[:, h, lo:hi], K.ps[rows, 4 + n % 4, 0:hi - lo], q[rows, h // 2, lo:hi], ALU.mult).then_inc(q_out, 1)

            @block.scalar
            def _(act):
                act.wait_ge(turned_out, 1)
                nc.scalar.activation(tok[:, 3], tok[:, 3], ACT.Exp)
                nc.scalar.activation(last_decay[:].rearrange("p h c -> p (h c)"), K.ps[0:HD, 3, 0:NC3 * 8], ACT.Exp)


def gdn_chunk_stage(K, gin, heads, tok, k_tok, v_tok, out, ins):
    nc = K.nc
    (kcdT, value, attnT) = out
    SH = [C3, QUAD, C3]
    LV = LEVELS_G - 1
    with ExitStack() as local:
        masks_in = K.buf(local, "gdn_masks", [C3, LEVELS_G + 5, C3])
        wide_prod, wide_amask, wide_inv, wide_invT = wides = [K.buf(local, n, [P, 2, QUAD, C3]) for n in ("gdn_prod", "gdn_A_level", "gdn_inv", "gdn_invT")]
        wide_bv, wide_bk = wide_rhs = [K.buf(local, n, [P, 2, QUAD, HD]) for n in ("gdn_beta_v", "gdn_beta_k")]
        prod, amask, inv, invT, bv, bk = (t[0:C3] for t in wides + wide_rhs)
        amat = K.buf(local, "gdn_A", [C3, 2, QUAD, C3])
        arrived, chain, pool_chain, padded = (K.sem(n) for n in ("gdn_masks_arrived", "gdn_chain", "gdn_pool_chain", "gdn_padded"))
        (sums_filled, keys_filled, queries_filled, split, exped, first, attn_out, firstT_filled, firstT, masked, turned, inv_out,
         z_filled, z_out, d_filled, d_added, x_filled, x_out, rhs_ready) = ([K.sem(f"gdn_{n}_{q}") for q in range(2)] for n in (
            "sums_filled", "keys_filled", "queries_filled", "split", "exped", "first", "attn_out", "firstT_filled", "firstT", "masked", "turned",
            "inv_out", "z_filled", "z_out", "d_filled", "d_added", "x_filled", "x_out", "rhs_ready"))

        def mask(n):
            return masks_in[:, n:n + 1, :].to_broadcast(SH)

        def over(n, c, q, width):
            return tok[:, n, c, q:GDN_HEADS:2].unsqueeze(2).to_broadcast((C3, QUAD, width))

        def own(t, c, q):
            return t[:, c, q:GDN_HEADS:2, :]

        def bank(q, b):
            return K.ps[0:C3, 4 * q + b, 0:QUAD * C3].rearrange("p (h i) -> p h i", i=C3)

        def head(base, h, c):
            rows = slice((h % 2) * HD, (h % 2 + 1) * HD)
            return gin[rows, base + h // 2, 3 + c * C3:3 + (c + 1) * C3]

        PAIRS, TRIANGLE, TURN = range(3)
        RESULT = TURN + 1 + 2 * LV
        STEPS = RESULT + 1

        def run(**step):
            for n in range(NC3 * STEPS + STEPS // 2):
                for q in range(2):
                    c, at = divmod(n - q * (STEPS // 2), STEPS)
                    if not 0 <= c < NC3:
                        continue
                    if at in (PAIRS, TRIANGLE, TURN, RESULT):
                        name = {PAIRS: "pairs", TRIANGLE: "triangle", TURN: "turn", RESULT: "result"}[at]
                        if name in step:
                            step[name](c, q)
                    else:
                        l, second = divmod(at - TURN - 1, 2)
                        step["add" if second else "product"](c, q, l, c * LV + l)

        with K.stage() as block:
            @block.sync
            def _(sp):
                sp.dma_start(masks_in[:], ins["c_levels_g"][0:C3]).then_inc(arrived, 16)

            @block.tensor
            def _(pe):
                def pairs(c, q):
                    for i in range(QUAD):
                        last = nc.tensor.matmul(bank(q, 0)[:, i, :], K.pick(2 * i + q, C3), heads[:, 2, c * C3:(c + 1) * C3], start=True, stop=True)
                    last.then_inc(sums_filled[q], 1)
                    for i in range(QUAD):
                        h = 2 * i + q
                        last = nc.tensor.matmul(bank(q, 1)[:, i, :], head(4, h, c), head(4, h, c), start=True, stop=True)
                    last.then_inc(keys_filled[q], 1)
                    if c:
                        pe.wait_ge(x_out[q], 2 * c)
                    for i in range(QUAD):
                        h = 2 * i + q
                        last = nc.tensor.matmul(bank(q, 2)[:, i, :], head(4, h, c), head(0, h, c), start=True, stop=True)
                    last.then_inc(queries_filled[q], 1)

                def turn(c, q):
                    pe.wait_ge(first[q], c + 1)
                    for i in range(QUAD):
                        last = nc.tensor.transpose(bank(q, 3)[:, i, :], inv[:, q, i, :], K.ident[0:C3, 0:C3])
                    last.then_inc(firstT_filled[q], 1)

                def product(c, q, l, n):
                    if l == 0:
                        pe.wait_ge(firstT[q], c + 1)
                    else:
                        pe.wait_ge(d_added[q], n)
                        pe.wait_ge(attn_out[q], c + 1)
                        for i in range(QUAD):
                            last = nc.tensor.transpose(bank(q, 2)[:, i, :], invT[:, q, i, :], K.ident[0:C3, 0:C3])
                        last.then_inc(turned[q], 1)
                    pe.wait_ge(masked[q], n + 1)
                    for i in range(QUAD):
                        last = nc.tensor.matmul(bank(q, 0)[:, i, :], wide_amask[:, q, i, :], wide_invT[:, q, i, :], start=True, stop=True)
                    last.then_inc(z_filled[q], 1)

                def add(c, q, l, n):
                    pe.wait_ge(z_out[q], n + 1)
                    if l:
                        pe.wait_ge(inv_out[q], c * (LV - 1) + l)
                    for i in range(QUAD):
                        last = nc.tensor.matmul(bank(q, 1)[:, i, :], wide_inv[:, q, i, :], wide_prod[:, q, i, :], start=True, stop=True)
                    last.then_inc(d_filled[q], 1)

                def result(c, q):
                    pe.wait_ge(d_added[q], LV * (c + 1))
                    pe.wait_ge(rhs_ready[q], c + 1)
                    for i in range(QUAD):
                        last = nc.tensor.matmul(K.ps[0:HD, 4 * q + 2, i * C3:(i + 1) * C3], wide_bk[:, q, i, :], wide_invT[:, q, i, :], start=True, stop=True)
                    last.then_inc(x_filled[q], 1)
                    for i in range(QUAD):
                        last = nc.tensor.matmul(K.ps[0:C3, 4 * q + 3, i * HD:(i + 1) * HD], wide_invT[:, q, i, :], wide_bv[:, q, i, :], start=True, stop=True)
                    last.then_inc(x_filled[q], 1)

                pe.wait_ge(padded, len(wides + wide_rhs))
                run(pairs=pairs, turn=turn, product=product, add=add, result=result)

            @block.vector
            def _(dve):
                link = Chain(dve, chain)

                def pairs(c, q):
                    dve.wait_ge(sums_filled[q], c + 1)
                    if c:
                        dve.wait_ge(masked[q], LV * c)
                    link(nc.vector.tensor_tensor(amask[:, q], bank(q, 0), over(1, c, q, C3), ALU.subtract))
                    nc.vector.tensor_scalar(amat[:, q], amask[:, q], 0.0, None, ALU.max).then_inc(split[q], 1)
                    nc.vector.tensor_scalar(own(attnT, c, q), amask[:, q], 0.0, None, ALU.min).then_inc(split[q], 1)

                def triangle(c, q):
                    dve.wait_ge(keys_filled[q], c + 1)
                    dve.wait_ge(exped[q], 2 * c + 1)
                    link(nc.vector.tensor_tensor(amat[:, q], bank(q, 1), amat[:, q], ALU.mult))
                    link(nc.vector.scalar_tensor_tensor(out=amat[:, q], in0=amat[:, q], scalar=-1.0, in1=over(0, c, q, C3), op0=ALU.mult, op1=ALU.mult))
                    link(nc.vector.tensor_tensor(amat[:, q], amat[:, q], mask(LEVELS_G + 2), ALU.mult))
                    link(nc.vector.tensor_tensor(inv[:, q], amat[:, q], mask(0), ALU.mult))
                    nc.vector.tensor_tensor(inv[:, q], inv[:, q], mask(LEVELS_G + 1), ALU.add).then_inc(first[q], 1)

                def turn(c, q):
                    dve.wait_ge(queries_filled[q], c + 1)
                    dve.wait_ge(exped[q], 2 * c + 2)
                    at = own(attnT, c, q)
                    link(nc.vector.tensor_tensor(at, bank(q, 2), at, ALU.mult))
                    nc.vector.tensor_tensor(at, at, mask(LEVELS_G + 4), ALU.mult).then_inc(attn_out[q], 1)

                def product(c, q, l, n):
                    pass

                def add(c, q, l, n):
                    dve.wait_ge(d_filled[q], n + 1)
                    dve.wait_ge(firstT[q], c + 1)
                    nc.vector.tensor_tensor(invT[:, q], bank(q, 1), invT[:, q], ALU.add).then_inc(d_added[q], 1)

                for t in wides + wide_rhs:
                    nc.vector.memset(t[HD:P], 0.0).then_inc(padded, 1)
                dve.wait_ge(padded, len(wides + wide_rhs))
                dve.wait_ge(arrived, 16)
                run(pairs=pairs, triangle=triangle, turn=turn, product=product, add=add)

            @block.scalar
            def _(act):
                def pairs(c, q):
                    act.wait_ge(split[q], 2 * c + 1)
                    nc.scalar.activation(amat[:, q], amat[:, q], ACT.Exp, scale=-1.0).then_inc(exped[q], 1)
                    act.wait_ge(split[q], 2 * c + 2)
                    nc.scalar.activation(own(attnT, c, q), own(attnT, c, q), ACT.Exp).then_inc(exped[q], 1)

                def turn(c, q):
                    act.wait_ge(firstT_filled[q], c + 1)
                    if c:
                        act.wait_ge(x_filled[q], 2 * c)
                    nc.scalar.activation(invT[:, q], bank(q, 3), ACT.Copy).then_inc(firstT[q], 1)

                def product(c, q, l, n):
                    if l:
                        act.wait_ge(turned[q], c * (LV - 1) + l)
                        nc.scalar.activation(inv[:, q], bank(q, 2), ACT.Copy).then_inc(inv_out[q], 1)
                    act.wait_ge(z_filled[q], n + 1)
                    nc.scalar.activation(prod[:, q], bank(q, 0), ACT.Copy).then_inc(z_out[q], 1)

                def add(c, q, l, n):
                    pass

                def result(c, q):
                    act.wait_ge(x_filled[q], 2 * c + 1)
                    nc.scalar.activation(own(kcdT, c, q), K.ps[0:HD, 4 * q + 2, 0:QUAD * C3].rearrange("p (h i) -> p h i", i=C3), ACT.Copy).then_inc(x_out[q], 1)
                    act.wait_ge(x_filled[q], 2 * c + 2)
                    nc.scalar.activation(own(value, c, q), K.ps[0:C3, 4 * q + 3, 0:QUAD * HD].rearrange("p (h i) -> p h i", i=HD), ACT.Copy).then_inc(x_out[q], 1)

                run(pairs=pairs, turn=turn, product=product, add=add, result=result)

            @block.gpsimd
            def _(pool):
                link = Chain(pool, pool_chain)

                def triangle(c, q):
                    pool.wait_ge(first[q], c + 1)
                    nc.gpsimd.tensor_tensor(amask[:, q], amat[:, q], mask(1), ALU.mult).then_inc(masked[q], 1)

                def turn(c, q):
                    if c:
                        pool.wait_ge(x_filled[q], 2 * c)
                    keys, values = (own(t[:].rearrange("p c (h i) -> p c h i", i=HD), c, q) for t in (k_tok, v_tok))
                    link(nc.gpsimd.tensor_tensor(bv[:, q], values, over(0, c, q, HD), ALU.mult))
                    link(nc.gpsimd.tensor_tensor(bk[:, q], keys, over(2, c, q, HD), ALU.mult))
                    nc.gpsimd.tensor_tensor(keys, keys, over(3, c, q, HD), ALU.mult).then_inc(rhs_ready[q], 1)

                def product(c, q, l, n):
                    if l < LV - 1:
                        pool.wait_ge(z_filled[q], n + 1)
                        nc.gpsimd.tensor_tensor(amask[:, q], amat[:, q], mask(l + 2), ALU.mult).then_inc(masked[q], 1)

                def add(c, q, l, n):
                    pass

                pool.wait_ge(padded, len(wides + wide_rhs))
                pool.wait_ge(arrived, 16)
                run(triangle=triangle, turn=turn, product=product, add=add)


def gdn_scan_stage(K, mats, k_tail, q0, last_decay, y):
    nc = K.nc
    (kcdT, value, attnT) = mats
    H = GDN_HEADS
    with ExitStack() as local:
        state = K.buf(local, "gdn_state", [HD, 2, H, HD])
        kept = K.buf(local, "gdn_kept", [HD, H, HD])
        vn = K.buf(local, "gdn_new_values", [C3, 2, H, HD])
        cleared, v_filled, v_ready, s_filled, s_ready, y_filled, y_out, chain = (K.sem(n) for n in (
            "gdn_cleared", "gdn_v_filled", "gdn_v_ready", "gdn_s_filled", "gdn_s_ready", "gdn_y_filled", "gdn_y_out", "gdn_scan_chain"))

        def grid(rows, b, i):
            return K.ps[0:rows, b, 0:H * HD].rearrange("p (h i) -> p h i", i=i)

        with K.stage() as block:
            @block.tensor
            def _(pe):
                pe.wait_ge(cleared, 1)
                for c in range(NC3):
                    s = state[:, c % 2]
                    if c:
                        pe.wait_ge(s_ready, c)
                    for h in range(H):
                        last = nc.tensor.matmul(grid(C3, c % 2, HD)[:, h, :], kcdT[:, c, h, :], s[:, h, :], start=True, stop=True)
                    last.then_inc(v_filled, 1)
                    pe.wait_ge(v_ready, c + 1)
                    for h in range(H):
                        last = nc.tensor.matmul(grid(HD, 2 + c % 2, HD)[:, h, :], k_tail[:, c, h * HD:(h + 1) * HD], vn[:, c % 2, h, :], start=True, stop=True)
                    last.then_inc(s_filled, 1)
                    if c >= 2:
                        pe.wait_ge(y_out, 4 * (c - 1))
                    for h in range(H):
                        b = 4 + 2 * (c % 2) + h // QUAD
                        to = K.ps[0:HD, b, (h % QUAD) * C3:(h % QUAD + 1) * C3]
                        nc.tensor.matmul(to, s[:, h, :], q0[:, h, c * C3:(c + 1) * C3], start=True, stop=False)
                        last = nc.tensor.matmul(to, vn[:, c % 2, h, :], attnT[:, c, h, :], start=False, stop=True)
                    last.then_inc(y_filled, 1)

            @block.vector
            def _(dve):
                link = Chain(dve, chain)
                nc.vector.memset(state[:, 0], 0.0).then_inc(cleared, 1)
                dve.wait_ge(cleared, 1)
                for c in range(NC3):
                    dve.wait_ge(v_filled, c + 1)
                    if c >= 2:
                        dve.wait_ge(y_filled, c - 1)
                    nc.vector.scalar_tensor_tensor(out=vn[:, c % 2], in0=grid(C3, c % 2, HD), scalar=-1.0, in1=value[:, c], op0=ALU.mult, op1=ALU.add).then_inc(v_ready, 1)
                    link(nc.vector.tensor_tensor(kept[:], state[:, c % 2], last_decay[:, :, c:c + 1].to_broadcast((HD, H, HD)), ALU.mult))
                    dve.wait_ge(s_filled, c + 1)
                    if c:
                        dve.wait_ge(y_filled, c)
                    nc.vector.tensor_tensor(state[:, (c + 1) % 2], grid(HD, 2 + c % 2, HD), kept[:], ALU.add).then_inc(s_ready, 1)
                    dve.wait_ge(s_ready, c + 1)

            @block.scalar
            def _(act):
                for c in range(NC3):
                    act.wait_ge(y_filled, c + 1)
                    for half in range(2):
                        src = K.ps[0:HD, 4 + 2 * (c % 2) + half, 0:QUAD * C3].rearrange("p (t o i) -> p t o i", o=2, i=C3)
                        for odd in range(2):
                            nc.scalar.activation(y[odd * HD:(odd + 1) * HD, 2 * half:2 * half + 2, c * C3:(c + 1) * C3], src[:, :, odd, :], ACT.Copy).then_inc(y_out, 1)


def multiply_stage(K, dst, other):
    with K.stage() as block:
        @block.vector
        def _(dve):
            K.nc.vector.tensor_tensor(dst, dst, other, ALU.mult)


def merge_3_stage(K, yf, yg, gates, merged):
    nc = K.nc
    filled, drained, chain = K.sem("merge3_filled"), K.sem("merge3_drained"), K.sem("merge3_chain")
    with ExitStack() as local:
        part = K.buf(local, "merge3_part", [P, 2, T3 // 2])
        feed = Feed(K, local, 8, lambda i: (yf, yg)[(i // 2) % 2][:, 2 * (i % 2):2 * (i % 2) + 2, :], [2, T3])
        groups = [Group(feed, 8, 2 * g, 2, filled, 7 * g) for g in range(4)]
        with K.stage() as block:
            @block.sync
            def _(sp):
                feed.refill(sp)

            @block.tensor
            def _(pe):
                for g, group in enumerate(groups):
                    group.products(pe, half_product(K, feed), (lambda e, b, g=g: e.wait_ge(drained, 8 * (g - 1) + b + 1)) if g else None)

            @block.scalar
            def _(act):
                feed.start_hi(act)
                feed.ahead_hi(act, range(8))

            @block.vector
            def _(dve):
                link = Chain(dve, chain)
                feed.start_lo(dve)
                for g, group in enumerate(groups):
                    feed.ahead_lo(dve, group.body)
                    for b in range(8):
                        (lo, hi), m = HALVES[b % 2], 4 * (g // 2) + b // 2
                        group.bank_ready(dve, b)
                        gate, src = gates[:, KT * (g % 2) + m, lo:hi], K.ps[:, b, 0:hi - lo]
                        if g % 2 == 0:
                            nc.vector.tensor_tensor(merged(m)[:, lo:hi], src, gate, ALU.mult).then_inc(drained, 1)
                        else:
                            nc.vector.tensor_tensor(part[:, b % 2, :], src, gate, ALU.mult).then_inc(drained, 1)
                            dve.wait_ge(drained, 8 * g + b + 1)
                            link(nc.vector.tensor_tensor(merged(m)[:, lo:hi], merged(m)[:, lo:hi], part[:, b % 2, :], ALU.add))
                    feed.ahead_lo(dve, group.end)


def residual_3_stage(K, x):
    nc = K.nc
    filled, drained = K.sem("out3_filled"), K.sem("out3_drained")
    with ExitStack() as local:
        feed = Feed(K, local, 8, pairs_of(x), [2, T3])
        groups = [Group(feed, 8, 4 * g, 4, filled, 7 * g) for g in range(2)]
        with K.stage() as block:
            @block.sync
            def _(sp):
                feed.refill(sp)

            @block.tensor
            def _(pe):
                for g, group in enumerate(groups):
                    group.products(pe, half_product(K, feed), (lambda e, b: e.wait_ge(drained, b + 1)) if g else None)

            @block.scalar
            def _(act):
                feed.start_hi(act)
                feed.ahead_hi(act, range(8))

            @block.vector
            def _(dve):
                feed.start_lo(dve)
                for g, group in enumerate(groups):
                    feed.ahead_lo(dve, group.body)
                    for b in range(8):
                        (lo, hi), m = HALVES[b % 2], 4 * g + b // 2
                        group.bank_ready(dve, b)
                        nc.vector.tensor_tensor(K.h[:, m, lo:hi], K.ps[:, b, 0:hi - lo], K.h[:, m, lo:hi], ALU.add).then_inc(drained, 1)
                    feed.ahead_lo(dve, group.end)


def conv_ffn_3(K):
    nc = K.nc
    with ExitStack() as ffn:
        hidden = K.buf(ffn, "ffn3_hidden", [P, FT, S])
        raw = K.buf(ffn, "ffn3_raw", [P, 2, 4, T3])
        c = K.buf(ffn, "ffn3_conv", [P, 2, 4, S])
        filled, drained, conv, silu, chain, multiplied = (K.sem(n) for n in ("up3_filled", "up3_drained", "conv3_done", "silu_done", "conv3_chain", "ffn3_multiplied"))
        G = FT // 2
        feed = Feed(K, ffn, 4 * G, pairs_of(K.xn), [2, T3], residual_norm(K, ffn, "norm_ffn_w_3", (0, T3)))
        groups = [Group(feed, 8, 4 * g, 4, filled, 7 * g) for g in range(G)]
        with K.stage() as block:
            @block.sync
            def _(sp):
                feed.refill(sp)

            @block.tensor
            def _(pe):
                for g, group in enumerate(groups):
                    group.products(pe, half_product(K, feed),
                                   (lambda e, b, g=g: e.wait_ge(drained, 8 * (g - 1) + b + 1)) if g else None)

            @block.scalar
            def _(act):
                feed.start_hi(act)
                for g, group in enumerate(groups):
                    feed.ahead_hi(act, group.body)
                    if g >= 2:
                        act.wait_ge(conv, 4 * (g - 1))
                    for b in range(8):
                        lo, hi = HALVES[b % 2]
                        group.bank_ready(act, b)
                        nc.scalar.activation(raw[:, g % 2, b // 2, lo:hi], K.ps[:, b, 0:hi - lo], ACT.Copy).then_inc(drained, 1)
                    feed.ahead_hi(act, group.end)
                    for i in range(2):
                        act.wait_ge(conv, 4 * g + i + 1)
                        nc.scalar.activation(hidden[:, 2 * g + i, :], c[:, g % 2, i, :], ACT.Silu).then_inc(silu, 1)

            @block.vector
            def _(dve):
                link = Chain(dve, chain)
                feed.start_lo(dve)
                for g in range(G):
                    feed.ahead_lo(dve, groups[g].body if g == 0 else [])
                    for i in range(4):
                        f = 2 * g + i if i < 2 else FT + 2 * g + i - 2
                        dve.wait_ge(drained, 8 * g + 2 * i + 2)
                        if g >= 2:
                            dve.wait_ge(silu, 2 * (g - 1))
                            dve.wait_ge(multiplied, 2 * (g - 1))
                        x, to = raw[:, g % 2, i, :], c[:, g % 2, i, :]
                        link(nc.vector.tensor_scalar(to, x[:, META - 2:T3 - 2], K.vec("ffn_conv_w_3", f), K.vec("ffn_conv_b_3", f), ALU.mult, ALU.add))
                        link(nc.vector.scalar_tensor_tensor(out=to, in0=x[:, META - 1:T3 - 1], scalar=K.vec("ffn_conv_w_3", 2 * FT + f), in1=to, op0=ALU.mult, op1=ALU.add))
                        nc.vector.scalar_tensor_tensor(out=to, in0=x[:, META:T3], scalar=K.vec("ffn_conv_w_3", 4 * FT + f), in1=to, op0=ALU.mult, op1=ALU.add).then_inc(conv, 1)
                        feed.ahead_lo(dve, range(4 * g + 3 + i, min(4 * g + 4 + i, 4 * G)))

            @block.gpsimd
            def _(pool):
                for g in range(G):
                    for i in range(2):
                        pool.wait_ge(silu, 2 * g + i + 1)
                        pool.wait_ge(conv, 4 * g + 2 + i + 1)
                        at = hidden[:, 2 * g + i, :]
                        nc.gpsimd.tensor_tensor(at, at, c[:, g % 2, 2 + i, :], ALU.mult).then_inc(multiplied, 1)
        residual_stage(K, lambda j: hidden[:, j, :], FT, (META, T3))


def load_meta_stage(K, ins, keep, causal):
    nc = K.nc
    arrived = K.sem("meta_arrived")
    with K.stage() as block:
        @block.sync
        def _(sp):
            sp.dma_start(K.h[:, :, 0:META], ins["meta"]).then_inc(arrived, 16)
            sp.dma_start(keep[:], ins["c_gdn_keep"][0:8, :]).then_inc(arrived, 16)
            sp.dma_start(causal[:], ins["c_causal88"][0:C3, 0:C3]).then_inc(arrived, 16)
            sp.wait_ge(arrived, 48)


def block_3(K, ins):
    with ExitStack() as mix:
        heads = K.buf(mix, "head_rates", [8, 4, T3])
        yf = K.buf(mix, "fox_y", [P, 4, T3])
        gin = K.buf(mix, "gdn_in", [P, 12, 3 + T3])
        yg = gin[:, 0:4, 3:3 + T3]
        with ExitStack() as fox:
            keep = K.buf(fox, "gdn_keep", [8, T3])
            causal = K.buf(fox, "causal88", [C3, C3])
            load_meta_stage(K, ins, keep, causal)
            fq = K.buf(fox, "fox_q", [P, FOX_HEADS, T3])
            fk = K.buf(fox, "fox_k", [P, 4, T3])
            fv = K.buf(fox, "fox_v", [P, NC3, 512])
            sums = K.buf(fox, "fox_sums", [P, T3])
            mix_in_3_stage(K, fq, fk, fv, gin, heads, sums, ins)
            head_rates_stage(K, heads, sums, keep[:])

            def scores(unit, part, lo, hi, to):
                h, i, _ = unit
                K.nc.tensor.matmul(to, fq[:, h, i * C3:(i + 1) * C3], fk[:, h // 2, lo:hi], start=True, stop=False)
                return K.nc.tensor.matmul(to, K.pick(h, C3, P), sums[:, lo:hi], start=False, stop=True)

            attention_stage(K, [(h, i, i + 1) for h in range(FOX_HEADS) for i in range(NC3)], C3, scores,
                            lambda h, t, d: fv[:, t, h * HD:(h + 1) * HD],
                            lambda unit, d: yf[(unit[0] % 2) * HD:(unit[0] % 2 + 1) * HD, unit[0] // 2, unit[1] * C3:(unit[1] + 1) * C3],
                            diagonal=causal[:], value_rows=P)
        head_norm_stage(K, [([(gin[:, t, 3:3 + T3], gin[:, t, 3:3 + T3], None)], 2, 1, HD if t < 4 else 1) for t in range(8)])
        with ExitStack() as gdn:
            q0 = K.buf(gdn, "gdn_q0", [HD, GDN_HEADS, T3])
            tok = K.buf(gdn, "gdn_tok_rates", [C3, 4, NC3, 8])
            last_decay = K.buf(gdn, "gdn_last_decay", [HD, GDN_HEADS, NC3])
            k_tok, v_tok = (K.buf(gdn, n, [C3, NC3, 512]) for n in ("gdn_k_tok", "gdn_v_tok"))
            kcdT = K.buf(gdn, "gdn_kcdT", [HD, NC3, GDN_HEADS, C3])
            value = v_tok[:].rearrange("p c (h i) -> p c h i", i=HD)
            gdn_rates_stage(K, heads, gin[:, 0:4, 3:3 + T3], q0, tok, last_decay)
            token_tiles_stage(K, [(gin[:, b + t, 3:3 + T3], (lambda c, n, to=to, t=t: to[:, c:c + n, t * P:(t + 1) * P]))
                                  for b, to in ((4, k_tok), (8, v_tok)) for t in range(4)], C3, NC3)
            attnT = K.buf(gdn, "gdn_attnT", [C3, NC3, GDN_HEADS, C3])
            mats = (kcdT, value, attnT)
            gdn_chunk_stage(K, gin, heads, tok, k_tok, v_tok, mats, ins)
            gdn_scan_stage(K, mats, k_tok, q0, last_decay, yg)
        head_norm_stage(K, [([(yg[:, t, :], yg[:, t, :], K.vec("gdn_norm_w_3"))], 2, HD, 1) for t in range(4)])
        gates = K.buf(mix, "branch3_gates", [P, 16, T3])
        z = K.buf(mix, "gdn_z", [P, 4, T3])
        gate_3_stage(K, z, gates)
        multiply_stage(K, yg, z[:])
        merge_3_stage(K, yf, yg, gates, lambda m: K.xn[:, m, :])
    residual_3_stage(K, K.xn)
    conv_ffn_3(K)
    norm_stage(K, lambda k: K.h[:, k, :], lambda k: K.xn[:, k, :], "norm_final_w_3", (META, T3))


def device_inputs(i):
    vec = {}
    for name, (at, n) in VEC_COLS.items():
        v = i[name]
        if v.size < HD:
            vec[name] = short_column(v)
        elif v.size == HD:
            vec[name] = columns(np.concatenate([v.reshape(-1)] * 2))
        else:
            vec[name] = columns(v)
    arrays = shape_constants()
    pool_w = np.zeros((P, 2, P), np.float32)
    for g in range(4):
        r = slice((g % 2) * HD, (g % 2 + 1) * HD)
        pool_w[r, g // 2, r] = i["pool_w"][0, g]
    lora = np.stack([np.concatenate([i["rwkv_w2"][0], i["rwkv_a2"][0]]), i["rwkv_g2"][0]], axis=1)
    lam = np.stack([i[n][0] for n in ("diff_lq1", "diff_lk1", "diff_lq2", "diff_lk2")])
    arrays.update(
        stream=weight_stream(i), x=features(i["x"][0]), mem=features(i["mem"][0]), meta=features(i["meta_tokens_3"]),
        vecs=np.ascontiguousarray(np.concatenate([vec[n] for n in VEC_COLS], axis=1)),
        pool_w=pool_w, rwkv_lora=np.ascontiguousarray(lora),
        diff_lambda=np.ascontiguousarray(np.broadcast_to(lam, (P, 4, HD))))
    arrays.update(block_2_inputs(i))
    arrays.update(block_3_inputs(i))
    return arrays


def build(nc, ins, out, total):
    with ExitStack() as ctx:
        K = Core(nc, ctx, ins["stream"], total)
        load_stage(K, ins)
        block_1(K, ins)
        block_2(K, ins)
        block_3(K, ins)
        store_stage(K, out)


def store_stage(K, out):
    nc = K.nc
    stored = K.sem("stored")
    with K.stage() as block:
        @block.sync
        def _(sp):
            sp.dma_start(out, K.xn[:, :, META:T3]).then_inc(stored, 16)
            sp.wait_ge(stored, 16)


def features(a):
    a = a.reshape(a.shape[-2], -1)
    return np.ascontiguousarray(a.T.reshape(-1, P, a.shape[0]).transpose(1, 0, 2))


def columns(a):
    return a.reshape(-1, P).T


def short_column(a):
    out = np.zeros((P, 1), a.dtype)
    out[:a.size, 0] = a.reshape(-1)
    return out


def wide(w, cols):
    w = np.concatenate([w[:, lo:hi] for lo, hi in cols], axis=1)
    w = w.reshape(-1, P, w.shape[1])
    if w.shape[2] == D:
        return w
    out = np.zeros((w.shape[0], P, D), w.dtype)
    out[:, :, :w.shape[2]] = w
    return out


def paired(w, cols):
    w = np.concatenate([w[:, lo:hi] for lo, hi in cols], axis=1)
    n = w.shape[1]
    if n < 512:
        w = np.concatenate([w, np.zeros((w.shape[0], 512 - n), w.dtype)], axis=1)
    return np.ascontiguousarray(w.reshape(-1, 2, P, 512).transpose(0, 2, 1, 3)).reshape(-1, P, D)


def weight_stream(i):
    a = {k: v[0] for k, v in i.items() if v.ndim == 3}
    w = a["w_in"]
    parts = [wide(w, [(0, 1024)]), wide(w, [(1024, 2048)]), wide(w, [(2048, 2816)]), wide(a["w_out"], [(0, D)]),
             wide(a["xa_wq"], [(0, D)]), wide(a["xa_wk"], [(0, D)]), wide(a["xa_wv"], [(0, D)]), wide(a["xa_wo"], [(0, D)])]
    for f in range(0, FF, 512):
        e = min(FF, f + 512)
        parts.append(wide(a["ffn_w_up"], [(f, e), (FF + f, FF + e)]))
    parts.append(wide(a["ffn_w_down"], [(0, D)]))
    parts += block_2_slabs(a) + block_3_slabs(a)
    return np.concatenate(parts)


def kernel(**inputs):
    import concourse.bacc as bacc
    from concourse.bass_utils import run_bass_kernel_spmd

    i = {k: np.asarray(v) for k, v in inputs.items()}
    arrays = device_inputs(i)
    nc = bacc.Bacc("TRN2", target_bir_lowering=False, num_devices=1)
    aps = {k: nc.dram_tensor(f"in_{k}", v.shape, F32, kind="ExternalInput").ap() for k, v in arrays.items()}
    out = nc.dram_tensor("out_features", (P, KT, S), F32, kind="ExternalOutput").ap()
    build(nc, aps, out, arrays["stream"].shape[0])
    r = run_bass_kernel_spmd(nc, [{f"in_{k}": v for k, v in arrays.items()}], core_ids=[0])
    got = r.results[0]["out_features"]
    return np.ascontiguousarray(got.transpose(1, 0, 2).reshape(D, S).T).reshape(1, S, D)
```

```python
from contextlib import ExitStack, contextmanager

import numpy as np

import concourse.bass as bass
from concourse import mybir

F32 = mybir.dt.float32
F32R = mybir.dt.float32r
ALU = mybir.AluOpType
ACT = mybir.ActivationFunctionType
AX = mybir.AxisListType.X

P = 128
D = 1024
KT = D // P
S = 512
META = 16
T3 = S + META
MEM = 256
FF = 2816
FT = FF // P
FF2 = 4096
CH = 64
NCH = S // CH
HD = 64
C3 = 88
NC3 = T3 // C3
SLOTS = 4
PARTS = 2
EPS = 1e-6
GN_EPS = 64e-5
LAMBDA_INIT = 0.2
SUBLN = (1.0 - LAMBDA_INIT) ** -2
TOPK = 128
NEG = -1.0e30
LOWEST = -3.0e38
HALVES = [(0, T3 // 2), (T3 // 2, T3)]

VEC_COLS = {}


def _vec(name, n):
    VEC_COLS[name] = (sum(c for _, c in VEC_COLS.values()), n)


for _n, _c in [("mix_norm_g", KT), ("pool_scale", 2), ("rwkv_mu", 8), ("rwkv_w0", 2), ("rwkv_a0", 2),
               ("rwkv_k_k", 2), ("rwkv_k_a", 2), ("rwkv_r_k", 2), ("rwkv_ln_w", 2), ("rwkv_ln_b", 2),
               ("diff_q_norm", 1), ("diff_k_norm", 1), ("diff_subln", 1), ("xa_norm_g", KT),
               ("mem_norm_g", KT), ("xa_q_norm", 2), ("xa_k_norm", 2), ("ffn_norm_g", KT),
               ("ffn_conv_w", 3 * FT), ("ffn_conv_b", FT),
               ("norm1_g_2", KT), ("norm2_g_2", KT), ("norm_f_g_2", KT),
               ("fgt_bias_3", 1), ("gdn_a_log_3", 1), ("gdn_dt_bias_3", 1), ("gdn_conv_w_3", 4 * 12),
               ("gdn_norm_w_3", 1), ("gate_bias_3", 16), ("norm_mix_w_3", KT), ("norm_ffn_w_3", KT),
               ("ffn_conv_w_3", 3 * 2 * FT), ("ffn_conv_b_3", 2 * FT), ("norm_final_w_3", KT)]:
    _vec(_n, _c)
NVEC = sum(c for _, c in VEC_COLS.values())

LEVELS_R = 6
LEVELS_G = 7


def shape_constants():
    i = np.arange(P)
    ident = np.eye(P)
    ones = np.ones((P, P))
    blk = (i[:, None] // HD == i[None, :] // HD) * 1.0
    half = HD // 2
    rot = np.zeros((P, P))
    for p in range(P):
        if p % HD < half:
            rot[p + half, p] = -1.0
        else:
            rot[p - half, p] = 1.0
    upper = (i[:, None] <= i[None, :]) * 1.0
    sq = np.concatenate([ident, ones, blk, rot, upper], axis=1)

    def level(n, l):
        a = np.arange(n)
        return ((a[:, None] >> (l + 1) == a[None, :] >> (l + 1)) & (a[:, None] >> l & 1 == 1)
                & (a[None, :] >> l & 1 == 0)) * 1.0

    c = np.arange(CH)
    pair = [c[:, None] > c[None, :], c[:, None] < c[None, :], c[:, None] <= c[None, :], level(CH, 0).T]
    lr = np.concatenate([np.tile(m, (2, 1)) for m in pair] + [np.kron(np.eye(2), level(CH, l)) for l in range(1, LEVELS_R)], axis=1)
    lg = np.zeros((P, LEVELS_G + 5, C3))
    c = np.arange(C3)
    for l in range(LEVELS_G):
        lg[:C3, l] = level(C3, l)
    lg[:C3, LEVELS_G] = level(C3, 0).T
    lg[:C3, LEVELS_G + 1] = np.eye(C3)
    lg[:C3, LEVELS_G + 2] = c[:, None] > c[None, :]
    lg[:C3, LEVELS_G + 3] = c[:, None] < c[None, :]
    lg[:C3, LEVELS_G + 4] = c[:, None] <= c[None, :]
    t = np.arange(S)
    win = np.array([2, 4, 8, 16])[(np.arange(256) // 64)]
    recip_count = (1.0 / np.minimum(t[None, :] + 1, win[:, None])).reshape(2, P, S).transpose(1, 0, 2)
    chunk_keep = np.broadcast_to((t % CH != 0) * 1.0, (P, S))
    gdn_keep = np.broadcast_to((np.arange(T3) % C3 != 0) * 1.0, (P, T3))
    j = np.arange(S) - 3 * P
    dist = np.abs(i[:, None] - j[None, :]).astype(np.float64)
    dist[(j[None, :] // 64) > (i[:, None] // 64)] = 1.0e32
    pos = np.arange(S, dtype=np.float32)
    inv = np.float32(10000.0) ** (-np.arange(0, HD, 2, dtype=np.float32) / np.float32(HD))
    ang = (pos[None, :] * inv[:, None]).astype(np.float32)
    cos, sin = (np.tile(f(ang), (4, 1)) for f in (np.cos, np.sin))
    causal = np.where(i[None, :] <= i[:, None], 0.0, NEG)
    causal88 = np.zeros((P, 2 * C3))
    causal88[:C3, :C3] = np.where(np.arange(C3)[None, :] <= np.arange(C3)[:, None], 0.0, NEG)
    parts = {"c_square": sq, "c_levels_r": lr, "c_levels_g": lg, "c_recip_count": recip_count,
             "c_chunk_keep": chunk_keep, "c_gdn_keep": gdn_keep, "c_dist": dist, "c_cos": cos, "c_sin": sin,
             "c_causal": causal, "c_causal88": causal88}
    return {k: np.ascontiguousarray(v, dtype=np.float32) for k, v in parts.items()}


class Slabs:

    def __init__(self, nc, ctx, stream, total):
        self.nc = nc
        self.ring = ctx.enter_context(nc.sbuf_tensor("ring", [P, SLOTS, D], F32))
        self.hi = ctx.enter_context(nc.sbuf_tensor("slab_hi", [P, PARTS, D], F32R))
        self.lo = ctx.enter_context(nc.sbuf_tensor("slab_lo", [P, PARTS, D], F32R))
        self.loaded = [ctx.enter_context(nc.semaphore(f"slab_loaded_{j}")) for j in range(SLOTS)]
        self.hi_ready, self.lo_ready, self.used = (ctx.enter_context(nc.semaphore(f"slabs_{n}"))
                                                   for n in ("hi_ready", "lo_ready", "used"))
        self.stream, self.total, self.n = stream, total, 0

    def parts(self, n):
        return self.hi[:, n % PARTS, :], self.lo[:, n % PARTS, :]

    def first(self, sp):
        for n in range(SLOTS):
            sp.dma_start(self.ring[:, n, :], self.stream[n]).then_inc(self.loaded[n], 16)

    def split_hi(self, act, n, turn=0):
        if n >= PARTS:
            act.wait_ge(self.used, turn * KT + (n - PARTS + 1))
        act.wait_ge(self.loaded[n % SLOTS], turn * (16 * KT // SLOTS) + 16 * (n // SLOTS + 1))
        self.nc.scalar.activation(self.hi[:, n % PARTS, :], self.ring[:, n % SLOTS, :], ACT.Copy).then_inc(self.hi_ready, 1)

    def split_lo(self, eng, n, turn=0):
        eng.wait_ge(self.hi_ready, turn * KT + (n + 1))
        eng.tensor_tensor(self.lo[:, n % PARTS, :], self.ring[:, n % SLOTS, :], self.hi[:, n % PARTS, :].bitcast(F32),
                                     ALU.subtract).then_inc(self.lo_ready, 1)

    def refill(self, sp, first, count):
        count = min(count, self.total - SLOTS - first)
        turns = count // SLOTS
        if turns > 1:
            with sp.Fori(0, turns) as turn:
                for j in range(SLOTS):
                    n = first + j
                    sp.wait_ge(self.lo_ready, turn * SLOTS + (n + 1))
                    sp.dma_start(self.ring[:, n % SLOTS:n % SLOTS + 1, :],
                                 self.stream[bass.ds(turn * SLOTS + (n + SLOTS), 1)].rearrange("o p n -> p o n")
                                 ).then_inc(self.loaded[n % SLOTS], 16)
        else:
            turns = 0
        for n in range(first + turns * SLOTS, first + count):
            sp.wait_ge(self.lo_ready, n + 1)
            sp.dma_start(self.ring[:, n % SLOTS, :], self.stream[n + SLOTS]).then_inc(self.loaded[n % SLOTS], 16)


class Feed:

    def __init__(self, K, ctx, steps, rows, shape, norm=None):
        self.norm, self.tiles = norm, shape[0] if len(shape) > 1 else 1
        self.nc, self.slabs, self.rows, self.steps, self.n0 = K.nc, K.slabs, rows, steps, K.slabs.n
        K.slabs.n += steps
        self.hi, self.lo = (K.buf(ctx, f"rows_{n}", [P, PARTS] + shape, F32R) for n in ("hi", "lo"))
        self.hi_ready, self.lo_ready = K.sem("rows_hi_ready"), K.sem("rows_lo_ready")

    def slab(self, i):
        return self.slabs.parts(self.n0 + i)

    def acts(self, i):
        return self.hi[:, i % PARTS], self.lo[:, i % PARTS]

    def refill(self, sp):
        self.slabs.refill(sp, self.n0 + 1, self.steps)

    def _rows_hi(self, act, i, turn=0):
        if i >= PARTS:
            act.wait_ge(self.slabs.used, turn * KT + (self.n0 + i - PARTS + 1))
        if self.norm and (i + 1) * self.tiles <= KT:
            act.wait_ge(self.norm.normed, (i + 1) * self.tiles)
        self.nc.scalar.activation(self.hi[:, i % PARTS], self.rows(i), ACT.Copy).then_inc(self.hi_ready, 1)

    def _rows_lo(self, eng, i, turn=0):
        eng.wait_ge(self.hi_ready, turn * KT + (i + 1))
        eng.tensor_tensor(self.lo[:, i % PARTS], self.rows(i), self.hi[:, i % PARTS].bitcast(F32),
                                     ALU.subtract).then_inc(self.lo_ready, 1)

    def start_hi(self, act):
        if self.norm:
            self.norm.scalar(act)
        self._rows_hi(act, 0)
        self.slabs.split_hi(act, self.n0 + 1)
        self._rows_hi(act, 1)

    def start_lo(self, dve):
        if self.norm:
            self.norm.vector(dve, range(2 * self.tiles))
        self._rows_lo(dve, 0)
        self.slabs.split_lo(dve, self.n0 + 1)
        self._rows_lo(dve, 1)
        if self.norm:
            self.norm.vector(dve, range(2 * self.tiles, KT))

    def ahead_hi(self, act, steps, turn=0):
        for i in steps:
            if i + 2 <= self.steps and self.n0 + i + 2 < self.slabs.total:
                self.slabs.split_hi(act, self.n0 + i + 2, turn)
            if i + 2 < self.steps:
                self._rows_hi(act, i + 2, turn)

    def ahead_lo(self, dve, steps, turn=0):
        for i in steps:
            if i + 2 <= self.steps and self.n0 + i + 2 < self.slabs.total:
                self.slabs.split_lo(dve, self.n0 + i + 2, turn)
            if i + 2 < self.steps:
                self._rows_lo(dve, i + 2, turn)

    def wait(self, pe, i, turn=0):
        pe.wait_ge(self.slabs.lo_ready, turn * KT + (self.n0 + i + 1))
        pe.wait_ge(self.lo_ready, turn * KT + (i + 1))


def cut(pair, lo, hi):
    return tuple(part[:, lo:hi] for part in pair)


def exact(nc, to, lhsT, rhs, start, stop):
    nc.tensor.matmul(to, lhsT[0], rhs[0], start=start, stop=False)
    nc.tensor.matmul(to, lhsT[0], rhs[1], start=False, stop=False)
    return nc.tensor.matmul(to, lhsT[1], rhs[0], start=False, stop=stop)


class Chain:

    def __init__(self, eng, sem):
        self.eng, self.sem, self.n = eng, sem, 0

    def __call__(self, ins):
        self.n += 1
        ins.then_inc(self.sem, 1)
        self.eng.wait_ge(self.sem, self.n)


class Core:

    def __init__(self, nc, ctx, stream, total):
        self.nc, self.ctx = nc, ctx
        self.ps = ctx.enter_context(nc.psum_tensor("ps", [P, 8, 512], F32))
        self.slabs = Slabs(nc, ctx, stream, total)
        self.vecs = ctx.enter_context(nc.sbuf_tensor("vecs", [P, NVEC], F32))
        self.sq = ctx.enter_context(nc.sbuf_tensor("square_constants", [P, 5 * P], F32))
        self.h = ctx.enter_context(nc.sbuf_tensor("h", [P, KT, T3], F32))
        self.xn = ctx.enter_context(nc.sbuf_tensor("xn", [P, KT, T3], F32))
        self.eps = ctx.enter_context(nc.sbuf_tensor("eps", [P, 6], F32))
        self.ident, self.ones, self.blk, self.rot, self.upper = (self.sq[:, n * P:(n + 1) * P] for n in range(5))
        self.eps_col, self.gn_eps_col, self.one_col = self.eps[:, 0:1], self.eps[:, 1:2], self.eps[:, 2:3]
        self.eps_times = {1: self.eps_col, HD: self.eps[:, 3:4], 4 * HD: self.eps[:, 4:5], SUBLN: self.eps[:, 5:6]}
        self.x_arrived = [ctx.enter_context(nc.semaphore(f"x_arrived_{k}")) for k in range(KT)]
        self.count, self.in_use, self.cleared = 0, [], []

    def sem(self, name):
        self.count += 1
        self.in_use.append(self.nc.alloc_semaphore(name=f"{name}_{self.count}"))
        return self.in_use[-1]

    @contextmanager
    def stage(self):
        with self.nc.Block() as block:
            yield block
        for s in self.cleared:
            self.nc.release_semaphore(s)
        for s in self.in_use:
            self.nc.sync.sem_clear(s)
        self.cleared, self.in_use = self.in_use, []

    def vec(self, name, n=0):
        c = VEC_COLS[name][0] + n
        return self.vecs[:, c:c + 1]

    def pick(self, h, n, rows=8):
        return self.ident[0:rows, h:h + 1].to_broadcast((rows, n))

    def buf(self, ctx, name, shape, dtype=F32):
        self.count += 1
        return ctx.enter_context(self.nc.sbuf_tensor(f"{name}_{self.count}", shape, dtype))


def load_stage(K, ins):
    nc = K.nc
    arrived, set_up = K.sem("inputs_arrived"), K.sem("eps_set")
    with K.stage() as block:
        @block.sync
        def _(sp):
            sp.dma_start(K.sq[:], ins["c_square"]).then_inc(arrived, 16)
            sp.dma_start(K.vecs[:], ins["vecs"]).then_inc(arrived, 16)
            for k in range(KT):
                sp.dma_start(K.h[:, k, 0:S], ins["x"][:, k, :]).then_inc(K.x_arrived[k], 16)
            K.slabs.first(sp)
            K.slabs.refill(sp, 0, 1)
            sp.wait_ge(arrived, 32)

        @block.scalar
        def _(act):
            K.slabs.split_hi(act, 0)

        @block.vector
        def _(dve):
            K.slabs.split_lo(dve, 0)
            nc.vector.memset(K.eps[:, 0:1], EPS).then_inc(set_up, 1)
            nc.vector.memset(K.eps[:, 1:2], GN_EPS).then_inc(set_up, 1)
            nc.vector.memset(K.eps[:, 2:3], 1.0).then_inc(set_up, 1)
            nc.vector.memset(K.eps[:, 3:4], EPS * HD).then_inc(set_up, 1)
            nc.vector.memset(K.eps[:, 4:5], EPS * 4 * HD).then_inc(set_up, 1)
            nc.vector.memset(K.eps[:, 5:6], EPS * SUBLN).then_inc(set_up, 1)


class Norm:

    def __init__(self, K, ctx, src, dst, gain, cols, arrived=None):
        self.arrived = arrived
        self.K, self.src, self.dst, self.gain, (self.lo, self.hi) = K, src, dst, gain, cols
        self.n = self.hi - self.lo
        self.tiles = [(a, min(a + P, self.n)) for a in range(0, self.n, P)]
        self.square = K.buf(ctx, "norm_square", [P, KT, self.n])
        self.rstd = K.buf(ctx, "norm_rstd", [P, len(self.tiles)])
        self.squared, self.added, self.summed, self.rooted, self.inverted, self.spread, self.normed = (
            K.sem(n) for n in ("squared", "added", "summed", "rooted", "inverted", "spread", "normed"))
        full = self.n // P
        self.lots = [(P, 0, full)] + ([(self.n % P, full, full + 1)] if self.n % P else [])

    def scalar(self, act):
        K, nc = self.K, self.K.nc
        for k in range(KT):
            if self.arrived:
                act.wait_ge(self.arrived[k], 16)
            nc.scalar.activation(self.square[:, k, :], self.src(k)[:, self.lo:self.hi], ACT.Square).then_inc(self.squared, 1)
        act.wait_ge(self.summed, 1)
        for rows, a, b in self.lots:
            nc.scalar.activation(self.rstd[0:rows, a:b], K.ps[0:rows, 3 + a:3 + b, 0], ACT.Sqrt, bias=K.eps_col[0:rows, :], scale=1.0 / D).then_inc(self.rooted, 1)

    def tensor(self, pe):
        K, nc = self.K, self.K.nc
        pe.wait_ge(self.added, KT - 1)
        for i, (a, b) in enumerate(self.tiles):
            last = nc.tensor.matmul(K.ps[0:b - a, 3 + i, 0:1], self.square[:, 0, a:b], K.ones[:, 0:1], start=True, stop=True)
        last.then_inc(self.summed, 1)
        pe.wait_ge(self.inverted, len(self.lots))
        for i, (a, b) in enumerate(self.tiles):
            last = nc.tensor.matmul(K.ps[:, 6 + a // 512, a % 512:a % 512 + b - a], self.rstd[0:b - a, i:i + 1].to_broadcast((b - a, P)),
                                    K.ident[0:b - a, 0:b - a], start=True, stop=True)
        last.then_inc(self.spread, 1)

    def vector(self, dve, ks):
        K, nc = self.K, self.K.nc
        spread = K.ps[:].rearrange("p b n -> p (b n)")[:, 6 * 512:6 * 512 + self.n]
        for k in ks:
            if k == 0:
                for j in range(1, KT):
                    dve.wait_ge(self.squared, j + 1)
                    nc.vector.tensor_tensor(self.square[:, 0, :], self.square[:, 0, :], self.square[:, j, :], ALU.add).then_inc(self.added, 1)
                    dve.wait_ge(self.added, j)
                dve.wait_ge(self.rooted, len(self.lots))
                for rows, a, b in self.lots:
                    nc.vector.reciprocal(self.rstd[0:rows, a:b], self.rstd[0:rows, a:b]).then_inc(self.inverted, 1)
                dve.wait_ge(self.spread, 1)
            nc.vector.scalar_tensor_tensor(out=self.dst(k)[:, self.lo:self.hi], in0=self.src(k)[:, self.lo:self.hi], scalar=K.vec(self.gain, k),
                                           in1=spread, op0=ALU.mult, op1=ALU.mult).then_inc(self.normed, 1)

    def free(self, e, b):
        if b >= 6:
            e.wait_ge(self.normed, KT)


def norm_stage(K, src, dst, gain, cols, transfers=None):
    with ExitStack() as local:
        norm = Norm(K, local, src, dst, gain, cols)
        with K.stage() as block:
            @block.sync
            def _(sp):
                if transfers:
                    transfers(sp, norm.normed)

            @block.scalar
            def _(act):
                norm.scalar(act)

            @block.tensor
            def _(pe):
                norm.tensor(pe)

            @block.vector
            def _(dve):
                norm.vector(dve, range(KT))


def residual_norm(K, ctx, gain, cols, arrived=None):
    return Norm(K, ctx, lambda k: K.h[:, k, :], lambda k: K.xn[:, k, :], gain, cols, arrived)


class Group:

    def __init__(self, feed, banks, first, steps, filled, filled_before=0):
        self.feed, self.banks, self.first, self.steps, self.filled = feed, banks, first, steps, filled
        self.before = filled_before
        self.body = range(first, first + steps - 1)
        self.end = range(first + steps - 1, first + steps)

    def bank_ready(self, eng, b, turn=0):
        if b < self.banks - 1:
            eng.wait_ge(self.filled, turn * (self.banks - 1) + (self.before + b + 1))
        else:
            eng.wait_ge(self.feed.slabs.used, turn * self.steps + (self.feed.n0 + self.first + self.steps))

    def products(self, pe, product, drained=None, turn=0):
        if self.first == 0 and self.feed.norm and drained is None:
            drained = self.feed.norm.free
            self.feed.norm.tensor(pe)
        for j in range(self.steps):
            self.feed.wait(pe, self.first + j, turn)
            for b in range(self.banks):
                if j == 0 and drained is not None:
                    drained(pe, b)
                mm = product(self.first + j, b, j == 0, j == self.steps - 1)
                if b == self.banks - 1:
                    mm.then_inc(self.feed.slabs.used, 1)
                elif j == self.steps - 1:
                    mm.then_inc(self.filled, 1)


def features_product(K, feed, cols):
    return lambda i, b, start, stop: exact(K.nc, K.ps[:, b, 0:cols], cut(feed.slab(i), b * P, (b + 1) * P), feed.acts(i), start, stop)


def residual_stage(K, rhs, steps, cols=(0, S)):
    nc, (lo, hi) = K.nc, cols
    filled = K.sem("out_filled")
    with ExitStack() as local:
        feed = Feed(K, local, steps, rhs, [hi - lo])
        group = Group(feed, KT, 0, steps, filled)
        with K.stage() as block:
            @block.sync
            def _(sp):
                feed.refill(sp)

            @block.tensor
            def _(pe):
                group.products(pe, features_product(K, feed, hi - lo))

            @block.scalar
            def _(act):
                feed.start_hi(act)
                feed.ahead_hi(act, group.body)

            @block.vector
            def _(dve):
                feed.start_lo(dve)
                feed.ahead_lo(dve, group.body)
                for m in range(KT):
                    group.bank_ready(dve, m)
                    nc.vector.tensor_tensor(K.h[:, m, lo:hi], K.ps[:, m, 0:hi - lo], K.h[:, m, lo:hi], ALU.add)


def project_stage(K, dst, rhs, cols, gain=None):
    nc = K.nc
    filled = K.sem("projection_filled")
    with ExitStack() as local:
        feed = Feed(K, local, KT, rhs, [cols], residual_norm(K, local, gain, (0, cols)) if gain else None)
        group = Group(feed, KT, 0, KT, filled)
        with K.stage() as block:
            @block.sync
            def _(sp):
                feed.refill(sp)

            @block.tensor
            def _(pe):
                group.products(pe, features_product(K, feed, cols))

            @block.scalar
            def _(act):
                feed.start_hi(act)
                feed.ahead_hi(act, group.body)
                for m in range(KT):
                    group.bank_ready(act, m)
                    nc.scalar.activation(dst(m), K.ps[:, m, 0:cols], ACT.Copy)

            @block.vector
            def _(dve):
                feed.start_lo(dve)
                feed.ahead_lo(dve, group.body)


def token_major_stage(K, dst, rows, tiles):
    nc = K.nc
    filled = K.sem("token_major_filled")
    with ExitStack() as local:
        feed = Feed(K, local, KT, rows, [tiles * P])
        group = Group(feed, 2 * tiles, 0, KT, filled)
        with K.stage() as block:
            @block.sync
            def _(sp):
                feed.refill(sp)

            @block.tensor
            def _(pe):
                group.products(pe, lambda i, b, start, stop: exact(
                    nc, K.ps[:, b, :], cut(feed.acts(i), b // 2 * P, (b // 2 + 1) * P),
                    cut(feed.slab(i), (b % 2) * 512, (b % 2 + 1) * 512), start, stop))

            @block.scalar
            def _(act):
                feed.start_hi(act)
                feed.ahead_hi(act, group.body)
                for b in range(2 * tiles):
                    group.bank_ready(act, b)
                    nc.scalar.activation(dst(b // 2, b % 2), K.ps[:, b, :], ACT.Copy)

            @block.vector
            def _(dve):
                feed.start_lo(dve)
                feed.ahead_lo(dve, group.body)


def mix_in_stage(K, pool_u, rwkv_z, diff_qk, diff_v, tables):
    nc = K.nc
    filled, drained = K.sem("z_filled"), K.sem("z_drained")

    def place(i):
        if i < 2:
            return pool_u[:, i, 16:16 + S]
        if i < 10:
            return rwkv_z[:, i - 2, 1:1 + S]
        return diff_qk[:, i - 10, :]

    with ExitStack() as local:
        feed = Feed(K, local, 3 * KT, lambda i: K.xn[:, i % KT, 0:S], [S], residual_norm(K, local, "mix_norm_g", (0, S), K.x_arrived))
        groups = [Group(feed, banks, g * KT, KT, filled, 7 * g) for g, banks in enumerate((8, 8, 6))]
        tables.buffers(local)
        with K.stage() as block:
            @block.sync
            def _(sp):
                tables.sync(sp)
                feed.refill(sp)

            @block.tensor
            def _(pe):
                features = features_product(K, feed, S)

                def last(i, b, start, stop):
                    if b < 2:
                        return features(i, b, start, stop)
                    return exact(nc, K.ps[:, b, :], cut(feed.acts(i), (b - 2) * P, (b - 1) * P),
                                 cut(feed.slab(i), 2 * P, 2 * P + 512), start, stop)

                groups[0].products(pe, features)
                groups[1].products(pe, features, lambda e, b: e.wait_ge(drained, b + 1))
                groups[2].products(pe, last, lambda e, b: e.wait_ge(drained, 8 + b + 1))

            @block.scalar
            def _(act):
                feed.start_hi(act)
                for g, group in enumerate(groups):
                    feed.ahead_hi(act, group.body)
                    if g == 1:
                        tables.scalar(act)
                    for b in range(group.banks):
                        group.bank_ready(act, b)
                        to = place(8 * g + b) if 8 * g + b < 18 else diff_v[:, b - 2, :]
                        nc.scalar.activation(to, K.ps[:, b, :], ACT.Copy).then_inc(drained, 1)
                    feed.ahead_hi(act, group.end)

            @block.vector
            def _(dve):
                nc.vector.memset(pool_u[:, :, 0:16], 0.0)
                nc.vector.memset(rwkv_z[:, :, 0:1], 0.0)
                feed.start_lo(dve)
                feed.ahead_lo(dve, range(KT))
                tables.sums(dve)
                feed.ahead_lo(dve, range(KT, 2 * KT))
                tables.vector(dve)
                feed.ahead_lo(dve, range(2 * KT, 3 * KT))


class Pool:

    def __init__(self, K, ctx, pool_u, y, ins):
        self.K, self.u, self.y, self.ins = K, pool_u, y, ins
        self.recip = K.buf(ctx, "pool_recip", [P, 2, S])
        self.w = K.buf(ctx, "pool_w", [P, 2, P])
        self.sums = K.buf(ctx, "pool_sums", [P, 2, 2, 16 + S])
        self.diff = K.buf(ctx, "pool_diff", [P, 2, S])
        self.arrived, self.chain, self.ready, self.filled = (K.sem(n) for n in ("pool_arrived", "pool_chain", "pool_ready", "pool_filled"))

    def sync(self, sp):
        sp.dma_start(self.recip[:], self.ins["c_recip_count"]).then_inc(self.arrived, 16)
        sp.dma_start(self.w[:], self.ins["pool_w"]).then_inc(self.arrived, 16)

    def gpsimd(self, pool):
        nc, sums, diff = self.K.nc, self.sums, self.diff
        link = Chain(pool, self.chain)
        src = self.u
        link(nc.gpsimd.memset(sums[:, :, :, 0:16], 0.0))
        pool.wait_ge(self.arrived, 32)
        for n, shift in enumerate((1, 2, 4, 8)):
            s = sums[:, n % 2]
            link(nc.gpsimd.tensor_tensor(s[:, :, 16:16 + S], src[:, :, 16:16 + S], src[:, :, 16 - shift:16 - shift + S], ALU.add))
            part, tile = (n % 2) * HD, n // 2
            rows = slice(part, part + HD)
            link(nc.gpsimd.tensor_tensor(diff[rows, tile, :], s[rows, tile, 16:16 + S], self.recip[rows, tile, :], ALU.mult))
            src = s
        nc.gpsimd.tensor_tensor(diff[:], diff[:], self.u[:, :, 16:16 + S], ALU.subtract).then_inc(self.ready, 1)

    def tensor(self, pe):
        K = self.K
        pe.wait_ge(self.ready, 1)
        pe.wait_ge(self.arrived, 32)
        for t in range(2):
            K.nc.tensor.matmul(K.ps[:, t, :], self.w[:, t, :], self.diff[:, t, :], start=True, stop=True).then_inc(self.filled, 1)

    def scalar(self, act):
        K = self.K
        for t in range(2):
            act.wait_ge(self.filled, t + 1)
            K.nc.scalar.activation(self.y[:, t, :], K.ps[:, t, :], ACT.Copy, scale=K.vec("pool_scale", t))


def rwkv_prepare_stage(K, z, zm, V, ins):
    nc = K.nc
    (gate, a_t, b_t, k_t, r_t, bonus, p_end) = V
    with ExitStack() as local:
        lora = K.buf(local, "rwkv_lora", [P, 2, 256])
        keep = K.buf(local, "rwkv_keep", [P, S])
        diff = K.xn[:, :, 0:S]
        tanh_w = K.buf(local, "rwkv_tanh", [P, S])
        sig_g = K.buf(local, "rwkv_sig_g", [P, S])
        logw, iclr, kk, cum, p_now, p_before, p_inv, k2 = (
            K.buf(local, n, [P, 2, S]) for n in ("logw", "iclr", "kk", "cum", "p_now", "p_before", "p_inv", "k2"))
        arrived, mixed, gates_in, filled, sig_ready, kk_sq, kk_sum, kk_root, cum_ready, less_ready, decays, chain, \
            rk_ready, rk_sum = (K.sem(n) for n in (
                "rwkv_arrived", "mixed", "gates_in", "lora_filled", "sig_ready", "kk_sq", "kk_sum", "kk_root",
                "cum_ready", "less_ready", "decays", "rwkv_chain", "rk_ready", "rk_sum"))
        with K.stage() as block:
            @block.sync
            def _(sp):
                sp.dma_start(lora[:], ins["rwkv_lora"]).then_inc(arrived, 16)
                sp.dma_start(keep[:], ins["c_chunk_keep"]).then_inc(arrived, 16)

            @block.vector
            def _(dve):
                link = Chain(dve, chain)
                link(nc.vector.tensor_tensor(diff, z[:, :, 0:S], z[:, :, 1:1 + S], ALU.subtract))
                for i in (6, 7, 0, 1, 2, 3, 4, 5):
                    nc.vector.scalar_tensor_tensor(out=zm[:, i, :], in0=diff[:, i, :], scalar=K.vec("rwkv_mu", i),
                                                   in1=z[:, i, 1:1 + S], op0=ALU.mult, op1=ALU.add).then_inc(mixed, 1)
                dve.wait_ge(mixed, 8)
                r, k, v = zm[:, 0:2, :], zm[:, 2:4, :], zm[:, 4:6, :]
                for t in range(2):
                    link(nc.vector.tensor_scalar(kk[:, t, :], k[:, t, :], K.vec("rwkv_k_k", t), None, ALU.mult))
                nc.vector.tensor_tensor(k2[:], kk[:], kk[:], ALU.mult).then_inc(kk_sq, 1)
                dve.wait_ge(kk_root, 2)
                link(nc.vector.tensor_scalar(p_inv[:], p_inv[:], 1e-12, None, ALU.max))
                link(nc.vector.reciprocal(p_inv[:], p_inv[:]))
                link(nc.vector.tensor_tensor(kk[:], kk[:], p_inv[:], ALU.mult))
                dve.wait_ge(sig_ready, 2)
                dve.wait_ge(arrived, 32)
                link(nc.vector.tensor_scalar(logw[:], logw[:], -float(np.exp(-0.5)), None, ALU.mult))
                for t in range(2):
                    nc.vector.tensor_tensor_scan(cum[:, t, :], keep[:], logw[:, t, :], 0.0, ALU.mult, ALU.add).then_inc(cum_ready, 1)
                dve.wait_ge(cum_ready, 2)
                nc.vector.tensor_tensor(p_before[:], cum[:], logw[:], ALU.subtract).then_inc(less_ready, 1)
                dve.wait_ge(sig_ready, 4)
                for t in range(2):
                    link(nc.vector.tensor_scalar(k2[:, t, :], iclr[:, t, :], -1.0, K.vec("rwkv_k_a", t), ALU.add, ALU.mult))
                    link(nc.vector.scalar_tensor_tensor(out=k2[:, t, :], in0=k2[:, t, :], scalar=1.0, in1=k[:, t, :],
                                                        op0=ALU.add, op1=ALU.mult))
                    nc.vector.scalar_tensor_tensor(out=diff[:, t, :], in0=r[:, t, :], scalar=K.vec("rwkv_r_k", t),
                                                   in1=k2[:, t, :], op0=ALU.mult, op1=ALU.mult).then_inc(rk_ready, 1)
                link(nc.vector.tensor_tensor(b_t[:], kk[:], iclr[:], ALU.mult))
                dve.wait_ge(decays, 3)
                nc.vector.scalar_tensor_tensor(out=a_t[:], in0=kk[:], scalar=-1.0, in1=p_before[:], op0=ALU.mult, op1=ALU.mult)
                nc.vector.tensor_tensor(b_t[:], b_t[:], p_inv[:], ALU.mult)
                nc.vector.tensor_tensor(k_t[:], k2[:], p_inv[:], ALU.mult)
                nc.vector.tensor_tensor(r_t[:], r, p_now[:], ALU.mult)
                nc.vector.tensor_copy(p_end[:], p_now[:].rearrange("p t (c i) -> p t c i", i=CH)[:, :, :, CH - 1])
                for t in range(2):
                    dve.wait_ge(rk_sum, t + 1)
                    nc.vector.tensor_tensor(bonus[:, t, :], K.ps[:, t, :], v[:, t, :], ALU.mult)

            @block.scalar
            def _(act):
                act.wait_ge(mixed, 2)
                nc.scalar.activation(tanh_w[0:64, :], zm[0:64, 6, :], ACT.Tanh).then_inc(gates_in, 1)
                nc.scalar.activation(sig_g[:], zm[:, 7, :], ACT.Sigmoid).then_inc(gates_in, 1)
                for t in range(2):
                    act.wait_ge(filled, t + 1)
                    nc.scalar.activation(logw[:, t, :], K.ps[:, t, :], ACT.Sigmoid, bias=K.vec("rwkv_w0", t)).then_inc(sig_ready, 1)
                for t in range(2):
                    act.wait_ge(filled, 2 + t + 1)
                    nc.scalar.activation(iclr[:, t, :], K.ps[:, 2 + t, :], ACT.Sigmoid, bias=K.vec("rwkv_a0", t)).then_inc(sig_ready, 1)
                for t in range(2):
                    act.wait_ge(filled, 4 + t + 1)
                    nc.scalar.activation(gate[:, t, :], K.ps[:, 4 + t, :], ACT.Copy)
                for t in range(2):
                    act.wait_ge(kk_sum, t + 1)
                    nc.scalar.activation(p_inv[:, t, :], K.ps[:, 6 + t, :], ACT.Sqrt).then_inc(kk_root, 1)
                act.wait_ge(cum_ready, 2)
                nc.scalar.activation(p_now[:], cum[:], ACT.Exp).then_inc(decays, 1)
                act.wait_ge(less_ready, 1)
                nc.scalar.activation(p_before[:], p_before[:], ACT.Exp).then_inc(decays, 1)
                nc.scalar.activation(p_inv[:], cum[:], ACT.Exp, scale=-1.0).then_inc(decays, 1)

            @block.tensor
            def _(pe):
                pe.wait_ge(arrived, 32)
                pe.wait_ge(gates_in, 2)
                for t in range(2):
                    nc.tensor.matmul(K.ps[:, t, :], lora[0:64, 0, t * P:(t + 1) * P], tanh_w[0:64, :], start=True, stop=True).then_inc(filled, 1)
                for t in range(2):
                    nc.tensor.matmul(K.ps[:, 2 + t, :], lora[64:128, 0, t * P:(t + 1) * P], zm[64:128, 6, :], start=True, stop=True).then_inc(filled, 1)
                for t in range(2):
                    nc.tensor.matmul(K.ps[:, 4 + t, :], lora[:, 1, t * P:(t + 1) * P], sig_g[:], start=True, stop=True).then_inc(filled, 1)
                pe.wait_ge(kk_sq, 1)
                for t in range(2):
                    nc.tensor.matmul(K.ps[:, 6 + t, :], K.blk, k2[:, t, :], start=True, stop=True).then_inc(kk_sum, 1)
                pe.wait_ge(sig_ready, 2)
                for t in range(2):
                    pe.wait_ge(rk_ready, t + 1)
                    nc.tensor.matmul(K.ps[:, t, :], K.blk, diff[:, t, :], start=True, stop=True).then_inc(rk_sum, 1)


def token_tiles_stage(K, jobs, rows, tiles):
    nc = K.nc
    ready, drained = K.sem("turned"), K.sem("turned_out")
    lots = [(src, place, t, min(4, tiles - t)) for src, place in jobs for t in range(0, tiles, 4)]
    with K.stage() as block:
        @block.tensor
        def _(pe):
            for n, (src, place, t0, k) in enumerate(lots):
                if n >= 8:
                    pe.wait_ge(drained, n - 7)
                for i in range(k):
                    last = nc.tensor.transpose(K.ps[0:rows, n % 8, i * P:(i + 1) * P],
                                               src[:, (t0 + i) * rows:(t0 + i + 1) * rows], K.ident)
                last.then_inc(ready, 1)

        @block.scalar
        def _(act):
            for n, (src, place, t0, k) in enumerate(lots):
                act.wait_ge(ready, n + 1)
                nc.scalar.activation(place(t0, k), K.ps[0:rows, n % 8, 0:k * P].rearrange("p (i c) -> p i c", c=P),
                                     ACT.Copy).then_inc(drained, 1)


def rwkv_chunk_stage(K, V, tok, out, ins):
    nc = K.nc
    (_, a_t, b_t, k_t, r_t, _, _) = V
    (a_tok, v_tok) = tok
    (x1, x2, rbk) = out
    rb, rk = rbk[0:CH], rbk[CH:P]
    PAIRS, LV = 2, LEVELS_R - 1
    with ExitStack() as local:
        masks_in = K.buf(local, "rwkv_masks", [P, 4 * CH + LV * P])
        spare = K.xn[:].rearrange("p k t -> p (k t)")
        amat, prod = (spare[:, n * PAIRS * NCH * P:(n + 1) * PAIRS * NCH * P].rearrange("p (q c i) -> p q c i", q=PAIRS, c=NCH) for n in range(2))
        inv, invT, amask = (K.buf(local, n, [P, PAIRS, NCH, P]) for n in ("rwkv_inv", "rwkv_invT", "rwkv_A_level"))
        a_blocks, b_blocks, k_blocks = prod, amask, inv
        akT = K.buf(local, "rwkv_akT", [P, 2, NCH, CH])[CH:P]
        low = [amat[0:CH, q].rearrange("p c i -> p (c i)").rearrange("p (o c i) -> p o c i", o=2, c=NCH) for q in range(PAIRS)]
        arrived, zeroed, zeroed_too, chain, a_ready, b_ready, k_ready = (K.sem(n) for n in (
            "masks_arrived", "blocks_zeroed", "A_zeroed", "chunk_chain", "a_blocks_ready", "b_blocks_ready", "k_blocks_ready"))
        filled, drained, w_filled, w_out, firstT, masked, turned, inv_out, z_filled, z_out, d_filled, d_added, x_filled = (
            [K.sem(f"rwkv_{n}_{q}") for q in range(PAIRS)] for n in (
                "pairs_filled", "pairs_drained", "w_filled", "w_out", "firstT", "masked", "turned", "inv_out", "z_filled", "z_out", "d_filled", "d_added", "x_filled"))
        half = [slice(o * CH, (o + 1) * CH) for o in range(2)]

        def mask(n, o):
            return masks_in[half[o], n * CH:(n + 1) * CH].unsqueeze(1).to_broadcast((CH, NCH, CH))

        def level(l):
            return masks_in[:, 4 * CH + l * P:4 * CH + (l + 1) * P].unsqueeze(1).to_broadcast((P, NCH, P))

        def bank(q, b):
            return K.ps[:, 4 * q + b, :].rearrange("p (c i) -> p c i", i=CH)

        def two_banks(q, b):
            return K.ps[:, 4 * q + b:4 * q + b + 2, :].rearrange("p b (c i) -> p (b c) i", i=P)

        def blocks(t, q, o):
            return t[half[o], q, :, half[o]]

        def vectors(t, q, o):
            return t[half[o], q, :].rearrange("p (c i) -> p c i", i=CH)

        products = ((a_blocks, b_t, a_ready), (b_blocks, a_t, b_ready), (k_blocks, a_t, k_ready), (b_blocks, r_t, b_ready), (k_blocks, r_t, k_ready))
        with K.stage() as block:
            @block.sync
            def _(sp):
                sp.dma_start(masks_in[:], ins["c_levels_r"]).then_inc(arrived, 16)

            @block.gpsimd
            def _(pool):
                nc.gpsimd.memset(a_blocks, 0.0).then_inc(zeroed, 1)
                nc.gpsimd.memset(k_blocks[:], 0.0).then_inc(zeroed, 1)
                nc.gpsimd.memset(invT[:], 0.0).then_inc(zeroed, 1)

            @block.tensor
            def _(pe):
                for q in range(PAIRS):
                    for n, (lhs, rhs, ready) in enumerate(products):
                        pe.wait_ge(ready, 2 * (q + 1))
                        if n == 4:
                            pe.wait_ge(drained[q], 2)
                        for c in range(NCH):
                            last = nc.tensor.matmul(bank(q, n % 4)[:, c, :], lhs[:, q, c, :], rhs[:, q, c * CH:(c + 1) * CH], start=True, stop=True)
                        last.then_inc(filled[q], 1)
                for q in range(PAIRS):
                    pe.wait_ge(drained[q], 8)
                    for o in range(2):
                        h = 2 * q + o
                        for c in range(NCH):
                            last = nc.tensor.matmul(bank(q, 1 + 2 * o)[0:CH, c, :], akT[:, o, c, :], v_tok[:, c, h * HD:(h + 1) * HD], start=True, stop=True)
                        last.then_inc(w_filled[q], 1)
                    pe.wait_ge(firstT[q], 1)
                    pe.wait_ge(drained[q], 10)
                    pe.wait_ge(w_out[q], 2)
                for l in range(LV):
                    for q in range(PAIRS):
                        if l:
                            pe.wait_ge(d_added[q], l)
                        for c in range(NCH):
                            last = nc.tensor.transpose(two_banks(q, 2)[:, c, :], invT[:, q, c, :], K.ident)
                        last.then_inc(turned[q], 1)
                        pe.wait_ge(masked[q], l + 1)
                        for c in range(NCH):
                            last = nc.tensor.matmul(two_banks(q, 0)[:, c, :], amask[:, q, c, :], invT[:, q, c, :], start=True, stop=True)
                        last.then_inc(z_filled[q], 1)
                    for q in range(PAIRS):
                        pe.wait_ge(z_out[q], l + 1)
                        pe.wait_ge(inv_out[q], l + 1)
                        for c in range(NCH):
                            last = nc.tensor.matmul(two_banks(q, 0)[:, c, :], inv[:, q, c, :], prod[:, q, c, :], start=True, stop=True)
                        last.then_inc(d_filled[q], 1)
                for q in range(PAIRS):
                    pe.wait_ge(d_added[q], LV + 1)
                    for o in range(2):
                        h = 2 * q + o
                        for c in range(NCH):
                            last = nc.tensor.matmul(bank(q, 2 * o)[0:CH, c, :], a_tok[:, c, h * HD:(h + 1) * HD], low[q][:, o, c, :], start=True, stop=True)
                        last.then_inc(x_filled[q], 1)
                        for c in range(NCH):
                            last = nc.tensor.matmul(bank(q, 2 * o + 1)[0:CH, c, :], low[q][:, o, c, :], x2[:, h, c, :], start=True, stop=True)
                        last.then_inc(x_filled[q], 1)

            @block.vector
            def _(dve):
                link = Chain(dve, chain)
                nc.vector.memset(b_blocks[:], 0.0).then_inc(zeroed_too, 1)
                nc.vector.memset(amat, 0.0).then_inc(zeroed_too, 1)
                dve.wait_ge(zeroed_too, 2)
                dve.wait_ge(zeroed, 3)
                dve.wait_ge(arrived, 16)
                for q in range(PAIRS):
                    for n, m in enumerate((0, 3, 1, 2, 2)):
                        dve.wait_ge(filled[q], n + 1)
                        if n == 2 and q:
                            dve.wait_ge(w_filled[q - 1], 2)
                        for o in range(2):
                            to = (blocks(amat, q, o), blocks(invT, q, o), akT[:, o], rb[:, 2 * q + o], rk[:, 2 * q + o])[n]
                            nc.vector.tensor_tensor(to, bank(q, n % 4)[half[o]], mask(m, o), ALU.mult).then_inc(drained[q], 1)
                    dve.wait_ge(drained[q], 10)
                    nc.vector.tensor_tensor(invT[:, q], invT[:, q], K.ident.unsqueeze(1).to_broadcast((P, NCH, P)), ALU.add).then_inc(firstT[q], 1)
                    nc.vector.tensor_tensor(amask[:, q], amat[:, q], level(0), ALU.mult).then_inc(masked[q], 1)
                for l in range(LV):
                    for q in range(PAIRS):
                        if l < LV - 1:
                            dve.wait_ge(z_filled[q], l + 1)
                            nc.vector.tensor_tensor(amask[:, q], amat[:, q], level(l + 1), ALU.mult).then_inc(masked[q], 1)
                    for q in range(PAIRS):
                        dve.wait_ge(d_filled[q], l + 1)
                        dve.wait_ge(firstT[q], 1)
                        if l < LV - 1:
                            nc.vector.tensor_tensor(invT[:, q], two_banks(q, 0), invT[:, q], ALU.add).then_inc(d_added[q], 1)
                        else:
                            for o in range(2):
                                nc.vector.tensor_tensor(low[q][:, o], two_banks(q, 0)[half[o], :, half[o]], blocks(invT, q, o), ALU.add).then_inc(d_added[q], 1)

            @block.scalar
            def _(act):
                for to, src, ready, zero, count in ((a_blocks, a_t, a_ready, zeroed, 1), (b_blocks, b_t, b_ready, zeroed_too, 1), (k_blocks, k_t, k_ready, zeroed, 2)):
                    act.wait_ge(zero, count)
                    for q in range(PAIRS):
                        for o in range(2):
                            nc.scalar.activation(blocks(to, q, o), vectors(src, q, o), ACT.Copy).then_inc(ready, 1)
                for q in range(PAIRS):
                    for o in range(2):
                        act.wait_ge(w_filled[q], o + 1)
                        nc.scalar.activation(x2[:, 2 * q + o], bank(q, 1 + 2 * o)[0:CH], ACT.Copy).then_inc(w_out[q], 1)
                for l in range(LV):
                    for q in range(PAIRS):
                        act.wait_ge(turned[q], l + 1)
                        nc.scalar.activation(inv[:, q], two_banks(q, 2), ACT.Copy).then_inc(inv_out[q], 1)
                        act.wait_ge(z_filled[q], l + 1)
                        nc.scalar.activation(prod[:, q], two_banks(q, 0), ACT.Copy).then_inc(z_out[q], 1)
                for q in range(PAIRS):
                    for o in range(2):
                        act.wait_ge(x_filled[q], 2 * o + 1)
                        nc.scalar.activation(x1[half[o], q], bank(q, 2 * o)[0:CH], ACT.Copy)
                        act.wait_ge(x_filled[q], 2 * o + 2)
                        nc.scalar.activation(x2[:, 2 * q + o], bank(q, 2 * o + 1)[0:CH], ACT.Copy)


def rwkv_scan_stage(K, V, tok, mats, y):
    nc = K.nc
    (gate, _, _, _, r_t, bonus, p_end) = V
    (bk_tok, uv_tok) = tok
    (x1, x2, rbk) = mats
    PAIRS = 2
    with ExitStack() as local:
        state = K.buf(local, "rwkv_state", [P, 2, PAIRS, P])
        kept = K.buf(local, "rwkv_kept", [P, PAIRS, HD])
        yraw = K.buf(local, "rwkv_y", [P, 2, S])
        ysq = K.buf(local, "rwkv_ysq", [P, 2, S])
        var = K.buf(local, "rwkv_var", [P, 2, S])
        u_filled, u_ready, s_filled, s_ready, y_filled, y_out, chain, cleared = (K.sem(n) for n in (
            "u_filled", "u_ready", "s_filled", "s_ready", "y_filled", "y_out", "scan_chain", "state_cleared"))
        mean_filled, centred, var_filled, rooted, weighed, gain_chain, inverted = (K.sem(n) for n in (
            "mean_filled", "centred", "var_filled", "rwkv_rooted", "rwkv_weighed", "rwkv_gain_chain", "rwkv_inverted"))
        half = [slice(o * HD, (o + 1) * HD) for o in range(2)]

        def pairs(rows, b, i):
            return K.ps[0:rows, b, 0:PAIRS * i].rearrange("p (q i) -> p q i", i=i)

        with K.stage() as block:
            @block.scalar
            def _(act):
                for c in range(NCH):
                    act.wait_ge(y_filled, c + 1)
                    nc.scalar.activation(yraw[:, :, c * CH:(c + 1) * CH], pairs(P, 4 + c % 2, CH), ACT.Copy).then_inc(y_out, 1)
                for t in range(2):
                    act.wait_ge(var_filled, t + 1)
                    nc.scalar.activation(var[:, t, :], K.ps[:, 6 + t, :], ACT.Sqrt, bias=K.gn_eps_col, scale=1.0 / HD).then_inc(rooted, 1)

            @block.tensor
            def _(pe):
                pe.wait_ge(cleared, 1)
                for c in range(NCH):
                    s = state[:, c % 2]
                    if c:
                        pe.wait_ge(s_ready, 4 * c)
                    for q in range(PAIRS):
                        last = nc.tensor.matmul(pairs(CH, c % 2, P)[:, q, :], x1[:, q, c, :], s[:, q, :], start=True, stop=True)
                    last.then_inc(u_filled, 1)
                    pe.wait_ge(u_ready, c + 1)
                    for q in range(PAIRS):
                        cols = slice(q * P, (q + 1) * P)
                        last = nc.tensor.matmul(pairs(P, 2 + c % 2, P)[:, q, :], bk_tok[:, c, cols], uv_tok[:, c, cols], start=True, stop=True)
                    last.then_inc(s_filled, 1)
                    if c >= 2:
                        pe.wait_ge(y_out, c - 1)
                    for q in range(PAIRS):
                        to = pairs(P, 4 + c % 2, CH)[:, q, :]
                        nc.tensor.matmul(to, s[:, q, :], r_t[:, q, c * CH:(c + 1) * CH], start=True, stop=False)
                        for o in range(2):
                            h = 2 * q + o
                            last = nc.tensor.matmul(to[half[o]], uv_tok[:, c, h * HD:(h + 1) * HD], rbk[:, h, c, :], start=False, stop=True)
                    last.then_inc(y_filled, 1)
                pe.wait_ge(y_out, NCH)
                for t in range(2):
                    nc.tensor.matmul(K.ps[:, t, :], K.blk, yraw[:, t, :], start=True, stop=True).then_inc(mean_filled, 1)
                for t in range(2):
                    pe.wait_ge(centred, t + 1)
                    nc.tensor.matmul(K.ps[:, 6 + t, :], K.blk, ysq[:, t, :], start=True, stop=True).then_inc(var_filled, 1)

            @block.vector
            def _(dve):
                link = Chain(dve, chain)
                nc.vector.memset(state[:], 0.0).then_inc(cleared, 1)
                dve.wait_ge(cleared, 1)
                for c in range(NCH):
                    dve.wait_ge(u_filled, c + 1)
                    grid = K.ps[0:CH, c % 2, 0:4 * HD].rearrange("p (h i) -> p h i", i=HD)
                    nc.vector.tensor_tensor(uv_tok[0:CH, c, :].rearrange("p (h i) -> p h i", i=HD), grid, x2[:, :, c, :], ALU.add).then_inc(u_ready, 1)
                    for o in range(2):
                        link(nc.vector.tensor_tensor(kept[half[o]], state[half[o], c % 2, :, half[o]], p_end[half[o], :, c:c + 1].to_broadcast((HD, PAIRS, HD)), ALU.mult))
                    dve.wait_ge(s_filled, c + 1)
                    if c >= 1:
                        dve.wait_ge(y_filled, c)
                    for q in range(PAIRS):
                        for o in range(2):
                            nc.vector.scalar_tensor_tensor(out=state[half[o], (c + 1) % 2, q, half[o]], in0=pairs(P, 2 + c % 2, P)[half[o], q, half[o]],
                                                           scalar=p_end[half[o], q, c:c + 1], in1=kept[half[o], q, :], op0=ALU.mult, op1=ALU.add).then_inc(s_ready, 1)
                    dve.wait_ge(s_ready, 4 * (c + 1))
                for t in range(2):
                    dve.wait_ge(mean_filled, t + 1)
                    link(nc.vector.scalar_tensor_tensor(out=yraw[:, t, :], in0=K.ps[:, t, :], scalar=-1.0 / HD, in1=yraw[:, t, :], op0=ALU.mult, op1=ALU.add))
                    nc.vector.tensor_tensor(ysq[:, t, :], yraw[:, t, :], yraw[:, t, :], ALU.mult).then_inc(centred, 1)
                dve.wait_ge(weighed, 1)
                for t in range(2):
                    link(nc.vector.tensor_tensor(yraw[:, t, :], yraw[:, t, :], gate[:, t, :], ALU.mult))
                for t in range(2):
                    dve.wait_ge(rooted, t + 1)
                    nc.vector.reciprocal(var[:, t, :], var[:, t, :]).then_inc(inverted, 1)
                dve.wait_ge(inverted, 2)
                link(nc.vector.tensor_tensor(yraw[:, 1, :], yraw[:, 1, :], var[:, 1, :], ALU.mult))
                nc.vector.tensor_tensor(y[:, 3, :], yraw[:, 1, :], bonus[:, 1, :], ALU.add)

            @block.gpsimd
            def _(pool):
                link = Chain(pool, gain_chain)

                for t in range(2):
                    link(nc.gpsimd.tensor_tensor(bonus[:, t, :], bonus[:, t, :], K.vec("rwkv_ln_b", t).to_broadcast((P, S)), ALU.add))
                    link(nc.gpsimd.tensor_tensor(bonus[:, t, :], bonus[:, t, :], gate[:, t, :], ALU.mult))
                    last = nc.gpsimd.tensor_tensor(gate[:, t, :], gate[:, t, :], K.vec("rwkv_ln_w", t).to_broadcast((P, S)), ALU.mult)
                    if t == 0:
                        link(last)
                    else:
                        last.then_inc(weighed, 1)
                pool.wait_ge(inverted, 1)
                link(nc.gpsimd.tensor_tensor(yraw[:, 0, :], yraw[:, 0, :], var[:, 0, :], ALU.mult))
                nc.gpsimd.tensor_tensor(y[:, 2, :], yraw[:, 0, :], bonus[:, 0, :], ALU.add)


def head_norm_stage(K, groups, beside=None):
    nc = K.nc
    G = len(groups)
    firsts = [sum(len(g[0]) for g in groups[:n]) for n in range(G + 1)]
    tokens = [g[0][0][0].shape[-1] for g in groups]
    most = max(tokens)
    flat = K.ps[:].rearrange("p b n -> p (b n)")

    def token_tiles(n):
        return [(a, min(a + P, tokens[n])) for a in range(0, tokens[n], P)]

    def lots(n):
        full, rest, heads = tokens[n] // P, tokens[n] % P, groups[n][1]
        return [(P, 0, full * heads)] * (full > 0) + [(rest, full * heads, (full + 1) * heads)] * (rest > 0)

    with ExitStack() as local:
        square = K.buf(local, "head_square", [P, firsts[G], most])
        rstd = K.buf(local, "head_rstd", [P, G, 2 * ((most + P - 1) // P)])
        pair = K.buf(local, "head_rstd_rows", [P, 2, (most + P - 1) // P, 2, HD])
        squared, squared_too, summed, rooted, inverted, widened, spread, applied = (K.sem(n) for n in (
            "head_squared", "head_squared_too", "head_summed", "head_rooted", "head_inverted", "head_widened", "head_spread", "head_applied"))
        wide_before = [sum(len(lots(m)) for m in range(n) if groups[m][1] == 2) for n in range(G + 1)]
        sources = [src for g in groups for src, _, _ in g[0]]
        other = beside(local) if beside else None

        def sums_at(n, rows, a, b):
            return K.ps[0:rows, n % 2, a:b]

        def spread_at(n, a, b):
            lo = (2 + 2 * (n % 3)) * 512
            return flat[:, lo + a:lo + b]

        with K.stage() as block:
            @block.sync
            def _(sp):
                if other:
                    other.sync(sp)

            @block.gpsimd
            def _(pool):
                if other:
                    other.gpsimd(pool)

            @block.tensor
            def _(pe):
                def sums(n):
                    tiles, heads, _, _ = groups[n]
                    if (firsts[n + 1] + 1) // 2:
                        pe.wait_ge(squared, (firsts[n + 1] + 1) // 2)
                    if firsts[n + 1] // 2:
                        pe.wait_ge(squared_too, firsts[n + 1] // 2)
                    if n >= 2:
                        pe.wait_ge(rooted, sum(len(lots(m)) for m in range(n - 1)))
                    selector = K.ones[:, 0:1] if heads == 1 else K.blk[:, 0:P:HD]
                    for i, (a, b) in enumerate(token_tiles(n)):
                        for j in range(len(tiles)):
                            last = nc.tensor.matmul(sums_at(n, b - a, i * heads, (i + 1) * heads), square[:, firsts[n] + j, a:b], selector, start=j == 0, stop=j == len(tiles) - 1)
                    last.then_inc(summed, 1)

                def spreads(n):
                    heads = groups[n][1]
                    pe.wait_ge(inverted, sum(len(lots(m)) for m in range(n + 1)))
                    if n >= 3:
                        pe.wait_ge(applied, n - 2)
                    if heads == 2:
                        pe.wait_ge(widened, wide_before[n + 1])
                    for i, (a, b) in enumerate(token_tiles(n)):
                        if heads == 1:
                            value = rstd[0:b - a, n, i:i + 1].to_broadcast((b - a, P))
                        else:
                            value = pair[0:b - a, n % 2, i].rearrange("p h r -> p (h r)")
                        last = nc.tensor.matmul(spread_at(n, a, b), value, K.ident[0:b - a, 0:b - a], start=True, stop=True)
                    last.then_inc(spread, 1)

                for n in range(G + 2):
                    if n < G:
                        sums(n)
                    if n >= 2:
                        spreads(n - 2)
                if other:
                    other.tensor(pe)

            @block.scalar
            def _(act):
                for at in range(0, firsts[G], 2):
                    nc.scalar.activation(square[:, at, 0:sources[at].shape[-1]], sources[at], ACT.Square).then_inc(squared, 1)

                def roots(n):
                    _, _, width, times = groups[n]
                    act.wait_ge(summed, n + 1)
                    for rows, a, b in lots(n):
                        nc.scalar.activation(rstd[0:rows, n, a:b], sums_at(n, rows, a, b), ACT.Sqrt, bias=K.eps_times[times][0:rows, :], scale=times / width).then_inc(rooted, 1)

                def widen(n):
                    act.wait_ge(inverted, sum(len(lots(m)) for m in range(n + 1)))
                    if n >= 2:
                        act.wait_ge(spread, n - 1)
                    for rows, a, b in lots(n):
                        to = pair[0:rows, n % 2, a // 2:b // 2].rearrange("p i h r -> p (i h) r")
                        nc.scalar.activation(to, rstd[0:rows, n, a:b].unsqueeze(2).to_broadcast((rows, b - a, HD)), ACT.Copy).then_inc(widened, 1)

                for n in range(G + 1):
                    if n < G:
                        roots(n)
                    if n and groups[n - 1][1] == 2:
                        widen(n - 1)
                if other:
                    other.scalar(act)

            @block.vector
            def _(dve):
                for at in range(1, firsts[G], 2):
                    nc.vector.tensor_tensor(square[:, at, 0:sources[at].shape[-1]], sources[at], sources[at], ALU.mult).then_inc(squared_too, 1)

                def inverses(n):
                    dve.wait_ge(rooted, sum(len(lots(m)) for m in range(n + 1)))
                    for rows, a, b in lots(n):
                        nc.vector.reciprocal(rstd[0:rows, n, a:b], rstd[0:rows, n, a:b]).then_inc(inverted, 1)

                def applications(n):
                    tiles = groups[n][0]
                    dve.wait_ge(spread, n + 1)
                    for i, (src, dst, gain) in enumerate(tiles):
                        if gain is None:
                            ins = nc.vector.tensor_tensor(dst, src, spread_at(n, 0, tokens[n]), ALU.mult)
                        else:
                            ins = nc.vector.scalar_tensor_tensor(out=dst, in0=src, scalar=gain, in1=spread_at(n, 0, tokens[n]), op0=ALU.mult, op1=ALU.mult)
                        if i == len(tiles) - 1:
                            ins.then_inc(applied, 1)

                for n in range(G + 2):
                    if n < G:
                        inverses(n)
                    if n >= 2:
                        applications(n - 2)


def attention_stage(K, units, rows, scores, value, place, bias=None, diagonal=None, parts=1, minus_lambda=None, width=HD, value_rows=None):
    nc = K.nc
    U = len(units)
    units = sorted(units, key=lambda unit: -unit[2])
    kmax = units[0][2]
    value_rows = value_rows or rows
    flat = K.ps[:].rearrange("p b n -> p (b n)")
    dts = (width + P - 1) // P
    drows = min(width, P)
    EXP, NORM, TURN, TURN_OUT, VALUE, OUT = 1, 2, 3, 4, 5, 6
    KEEP = TURN - EXP + 2
    sets = 2 if kmax <= 4 else 1

    def turn(n, lag, step):
        if 0 <= n - lag < U:
            step(n - lag)

    with ExitStack() as local:
        p = K.buf(local, "probs", [P, KEEP, parts, kmax * rows])
        s = K.buf(local, "scores", [P, 2, parts, kmax * rows]) if bias else None
        pT = K.buf(local, "probsT", [P, 2, kmax, rows])
        stat = K.buf(local, "softmax_stats", [P, KEEP, parts, 4])
        padded, p_scaled, scored, maxed, exped, inverted, p_ready, turned, pT_out, o_filled, o_out, chain = (K.sem(n) for n in (
            "att_padded", "p_scaled", "scored", "maxed", "exped", "inverted", "p_ready", "p_turned", "pT_out", "o_filled", "o_out", "att_chain"))

        def bank(u, part, n):
            lo = (u % 2) * 1024 + part * 512
            return flat[0:rows, lo:lo + n]

        def turned_at(u, i, n=1):
            lo = 2048 + (u % sets) * 512 + (i // 4) * 512 + (i % 4) * rows
            return flat[0:rows, lo:lo + n * rows]

        with K.stage() as block:
            @block.tensor
            def _(pe):
                def score(u):
                    keys = units[u][2] * rows
                    if u >= 2:
                        pe.wait_ge(exped if bias is None else maxed, parts * (u - 1))
                    for part in range(parts):
                        for lo in range(0, keys, 512):
                            hi = min(keys, lo + 512)
                            last = scores(units[u], part, lo, hi, bank(u, part, keys)[:, lo:hi])
                    last.then_inc(scored, 1)

                def transposes(u):
                    pe.wait_ge(p_ready, u + 1)
                    if u >= sets:
                        pe.wait_ge(pT_out, u - sets + 1)
                    for t in range(units[u][2]):
                        last = nc.tensor.transpose(turned_at(u, t), p[0:rows, u % KEEP, 0, t * rows:(t + 1) * rows], K.ident[0:rows, 0:rows])
                    last.then_inc(turned, 1)

                def values(u):
                    h, i, kt = units[u]
                    pe.wait_ge(pT_out, u + 1)
                    if u >= 2:
                        pe.wait_ge(o_out, u - 1)
                    for d in range(dts):
                        for t in range(kt):
                            last = nc.tensor.matmul(K.ps[0:drows, 6 + u % 2, d * rows:(d + 1) * rows], value(h, t, d), pT[0:value_rows, u % 2, t, :], start=t == 0, stop=t == kt - 1)
                    last.then_inc(o_filled, 1)

                for n in range(U + VALUE):
                    turn(n, 0, score)
                    turn(n, VALUE, values)
                    turn(n, TURN, transposes)

            @block.vector
            def _(dve):
                link = Chain(dve, chain)

                def maxima(u):
                    keys = units[u][2] * rows
                    if u >= 2:
                        dve.wait_ge(exped, parts * (u - 1))
                    dve.wait_ge(scored, u + 1)
                    for part in range(parts):
                        top = stat[0:rows, u % KEEP, part, 0:1]
                        src = bank(u, part, keys)
                        if bias is not None:
                            link(nc.vector.tensor_tensor_reduce(s[0:rows, u % 2, part, 0:keys], src, bias(units[u]), 1.0, LOWEST, ALU.add, ALU.max, accum_out=top))
                        else:
                            if diagonal is not None:
                                link(nc.vector.tensor_tensor(src[:, keys - rows:keys], src[:, keys - rows:keys], diagonal, ALU.add))
                            link(nc.vector.tensor_reduce(top, src, AX, ALU.max))
                        nc.vector.tensor_scalar(stat[0:rows, u % KEEP, part, 1:2], top, -1.0, None, ALU.mult).then_inc(maxed, 1)

                def inverses(u):
                    dve.wait_ge(exped, parts * (u + 1))
                    for part in range(parts):
                        ins = nc.vector.reciprocal(stat[0:rows, u % KEEP, part, 3:4], stat[0:rows, u % KEEP, part, 2:3])
                        if part == 1:
                            link(ins)
                            ins = nc.vector.tensor_tensor(stat[0:rows, u % KEEP, 1, 3:4], stat[0:rows, u % KEEP, 1, 3:4], minus_lambda[0:rows, :], ALU.mult)
                        ins.then_inc(inverted, 1)

                def joins(u):
                    keys = units[u][2] * rows
                    dve.wait_ge(p_scaled, u + 1)
                    pp = p[0:rows, u % KEEP]
                    nc.vector.scalar_tensor_tensor(out=pp[:, 0, 0:keys], in0=pp[:, 1, 0:keys], scalar=stat[0:rows, u % KEEP, 1, 3:4],
                                                   in1=pp[:, 0, 0:keys], op0=ALU.mult, op1=ALU.add).then_inc(p_ready, 1)

                for n in range(U + TURN):
                    turn(n, NORM, inverses)
                    turn(n, 0, maxima)
                    if parts == 2:
                        turn(n, NORM, joins)

            @block.scalar
            def _(act):
                def exps(u):
                    keys = units[u][2] * rows
                    if u >= KEEP:
                        act.wait_ge(turned, u - KEEP + 1)
                    for part in range(parts):
                        act.wait_ge(maxed, parts * u + part + 1)
                        src = s[0:rows, u % 2, part, 0:keys] if bias is not None else bank(u, part, keys)
                        nc.scalar.activation(p[0:rows, u % KEEP, part, 0:keys], src, ACT.Exp, bias=stat[0:rows, u % KEEP, part, 1:2],
                                             accum_out=stat[0:rows, u % KEEP, part, 2:3]).then_inc(exped, 1)

                def turned_out(u):
                    kt = units[u][2]
                    act.wait_ge(turned, u + 1)
                    if u >= 2:
                        act.wait_ge(o_filled, u - 1)
                    for lo in range(0, kt, 4):
                        k = min(4, kt - lo)
                        ins = nc.scalar.activation(pT[0:rows, u % 2, lo:lo + k, :].rearrange("p t q -> p (t q)"), turned_at(u, lo, k), ACT.Copy)
                    ins.then_inc(pT_out, 1)

                def out(u):
                    act.wait_ge(o_filled, u + 1)
                    for d in range(dts):
                        ins = nc.scalar.activation(place(units[u], d), K.ps[0:drows, 6 + u % 2, d * rows:(d + 1) * rows], ACT.Copy)
                    ins.then_inc(o_out, 1)

                if value_rows > rows:
                    act.wait_ge(padded, 1)
                for n in range(U + OUT):
                    turn(n, EXP, exps)
                    turn(n, TURN_OUT, turned_out)
                    turn(n, OUT, out)

            @block.gpsimd
            def _(pool):
                if value_rows > rows:
                    nc.gpsimd.memset(pT[HD:value_rows], 0.0).then_inc(padded, 1)
                for u in range(U):
                    keys = units[u][2] * rows
                    pool.wait_ge(inverted, parts * (u + 1))
                    pp = p[0:rows, u % KEEP]
                    inv = stat[0:rows, u % KEEP]
                    if parts == 1:
                        nc.gpsimd.tensor_scalar(pp[:, 0, 0:keys], pp[:, 0, 0:keys], inv[:, 0, 3:4], None, ALU.mult).then_inc(p_ready, 1)
                    else:
                        nc.gpsimd.tensor_scalar(pp[:, 0, 0:keys], pp[:, 0, 0:keys], inv[:, 0, 3:4], None, ALU.mult).then_inc(p_scaled, 1)


class DiffTables:

    def __init__(self, K, biases, minus_lambda, ins):
        self.K, self.biases, self.minus_lambda, self.ins = K, biases, minus_lambda, ins

    def buffers(self, ctx):
        K = self.K
        self.dist = K.buf(ctx, "dist", [P, S])
        self.lv = K.buf(ctx, "lambda_vectors", [P, 4, HD])
        self.ls = K.buf(ctx, "lambda_sums", [P, 2])
        self.le = K.buf(ctx, "lambda_exps", [P, 2])
        self.prod = K.buf(ctx, "lambda_products", [P, HD])
        self.arrived, self.summed, self.exped, self.chain = (K.sem(n) for n in ("dist_arrived", "lambda_summed", "lambda_exped", "lambda_chain"))

    def sync(self, sp):
        sp.dma_start(self.dist[:], self.ins["c_dist"]).then_inc(self.arrived, 16)
        sp.dma_start(self.lv[:], self.ins["diff_lambda"]).then_inc(self.arrived, 16)

    def sums(self, dve):
        nc = self.K.nc
        self.link = Chain(dve, self.chain)
        dve.wait_ge(self.arrived, 32)
        for n in range(2):
            self.link(nc.vector.tensor_tensor(self.prod[:], self.lv[:, 2 * n, :], self.lv[:, 2 * n + 1, :], ALU.mult))
            nc.vector.tensor_reduce(self.ls[:, n:n + 1], self.prod[:], AX, ALU.add).then_inc(self.summed, 1)
            dve.wait_ge(self.summed, n + 1)
        for h in range(4):
            nc.vector.tensor_scalar(self.biases[:, h, :], self.dist[:], -float(2.0 ** (-8.0 * (h + 1) / 4)), None, ALU.mult)

    def scalar(self, act):
        act.wait_ge(self.summed, 2)
        self.K.nc.scalar.activation(self.le[:], self.ls[:], ACT.Exp).then_inc(self.exped, 1)

    def vector(self, dve):
        nc = self.K.nc
        dve.wait_ge(self.exped, 1)
        self.link(nc.vector.tensor_tensor(self.minus_lambda[:], self.le[:, 1:2], self.le[:, 0:1], ALU.subtract))
        nc.vector.tensor_scalar(self.minus_lambda[:], self.minus_lambda[:], -LAMBDA_INIT, None, ALU.add)


def mixer_1(K, ins):
    nc = K.nc
    with ExitStack() as mix:
        y = K.buf(mix, "mix_y", [P, KT, S])
        rwkv_z = K.buf(mix, "rwkv_z", [P, 8, 1 + S])
        with ExitStack() as early:
            pool_u = K.buf(early, "pool_u", [P, 2, 16 + S])
            diff_qk = K.buf(early, "diff_qk", [P, 8, S])
            diff_v = K.buf(early, "diff_v", [P, 4, S])
            with ExitStack() as att:
                biases = K.buf(att, "diff_bias", [P, 4, S])
                minus_lambda = K.buf(att, "minus_lambda", [P, 1])
                mix_in_stage(K, pool_u, rwkv_z, diff_qk, diff_v, DiffTables(K, biases, minus_lambda, ins))
                head_norm_stage(K, [([(diff_qk[:, i, :], diff_qk[:, i, :], K.vec("diff_q_norm" if i < 4 else "diff_k_norm"))],
                                     2, HD, HD if i < 4 else 1) for i in range(8)],
                                beside=lambda local: Pool(K, local, pool_u, y, ins))
                units = [(h, i, i + 1) for h in range(4) for i in range(4)]

                def scores(unit, part, lo, hi, to):
                    h, i, _ = unit
                    rows = slice(part * HD, (part + 1) * HD)
                    return nc.tensor.matmul(to, diff_qk[rows, h, i * P:(i + 1) * P], diff_qk[rows, 4 + h, lo:hi], start=True, stop=True)

                attention_stage(K, units, P, scores, lambda h, t, d: diff_v[:, t, h * P:(h + 1) * P],
                                lambda unit, d: y[:, 4 + unit[0], unit[1] * P:(unit[1] + 1) * P],
                                bias=lambda unit: biases[:, unit[0], (3 - unit[1]) * P:4 * P],
                                parts=2, minus_lambda=minus_lambda, width=P)
                head_norm_stage(K, [([(y[:, 4 + h, :], y[:, 4 + h, :], K.vec("diff_subln"))], 1, P, SUBLN) for h in range(4)])
        with ExitStack() as rec:
            V = [K.buf(rec, n, [P, 2, S]) for n in ("rwkv_gate", "rwkv_a", "rwkv_b", "rwkv_k", "rwkv_r", "rwkv_bonus")]
            V.append(K.buf(rec, "rwkv_p_ends", [P, 2, NCH]))
            zm = rwkv_z[:, :, 1:1 + S]
            rwkv_prepare_stage(K, rwkv_z, zm, V, ins)
            a_tok = K.buf(rec, "a_tok", [CH, NCH, 256])
            bk_tok, uv_tok = (K.buf(rec, n, [P, NCH, 256]) for n in ("bk_tok", "uv_tok"))
            jobs = [(src[:, t, :], (lambda c, n, tok=tok, t=t: tok[:, c:c + n, t * P:(t + 1) * P]))
                    for src, tok in zip((V[1], V[2], V[3], zm[:, 4:6, :]), (a_tok, bk_tok[0:CH], bk_tok[CH:P], uv_tok[CH:P])) for t in range(2)]
            token_tiles_stage(K, jobs, CH, NCH)
            spare = rwkv_z[:].rearrange("p k t -> p (k t)")
            x1 = spare[:, 0:2 * S].rearrange("p (q c i) -> p q c i", q=2, c=NCH)
            x2 = spare[0:CH, 2 * S:6 * S].rearrange("p (h c i) -> p h c i", h=4, c=NCH)
            rbk = K.buf(rec, "rbkT", [P, 4, NCH, CH])
            rwkv_chunk_stage(K, V, (a_tok, uv_tok[CH:P]), (x1, x2, rbk), ins)
            rwkv_scan_stage(K, V, (bk_tok, uv_tok), (x1, x2, rbk), y)
        residual_stage(K, lambda j: y[:, j, :], KT)


def cross_attention(K, ins):
    nc = K.nc
    with ExitStack() as xa:
        mem = K.buf(xa, "mem", [P, KT, MEM])
        memn = K.buf(xa, "memn", [P, KT, MEM])
        q = K.buf(xa, "xa_q", [P, KT, S])
        k = K.buf(xa, "xa_k", [P, KT, MEM])
        v = K.buf(xa, "xa_v", [P, 2, D])
        o = K.buf(xa, "xa_o", [P, KT, S])
        arrived = K.sem("mem_arrived")
        with K.stage() as block:
            @block.sync
            def _(sp):
                sp.dma_start(mem[:], ins["mem"]).then_inc(arrived, 16)
                sp.wait_ge(arrived, 16)
        norm_stage(K, lambda i: mem[:, i, :], lambda i: memn[:, i, :], "mem_norm_g", (0, MEM))
        project_stage(K, lambda m: q[:, m, :], lambda j: K.xn[:, j, 0:S], S, "xa_norm_g")
        project_stage(K, lambda m: k[:, m, :], lambda j: memn[:, j, :], MEM)
        token_major_stage(K, lambda i, half: v[:, i, half * 512:(half + 1) * 512], lambda j: memn[:, j, :], 2)
        head_norm_stage(K, [([(t[:, 2 * h + i, :], t[:, 2 * h + i, :], K.vec(gain, i)) for i in range(2)], 1, 4 * HD, times)
                            for t, gain, times in ((q, "xa_q_norm", 4 * HD), (k, "xa_k_norm", 1)) for h in range(4)])

        def scores(unit, part, lo, hi, to):
            h, i, _ = unit
            nc.tensor.matmul(to, q[:, 2 * h, i * P:(i + 1) * P], k[:, 2 * h, lo:hi], start=True, stop=False)
            return nc.tensor.matmul(to, q[:, 2 * h + 1, i * P:(i + 1) * P], k[:, 2 * h + 1, lo:hi], start=False, stop=True)

        attention_stage(K, [(h, i, 2) for h in range(4) for i in range(4)], P, scores,
                        lambda h, t, d: v[:, t, h * 256 + d * P:h * 256 + (d + 1) * P],
                        lambda unit, d: o[:, 2 * unit[0] + d, unit[1] * P:(unit[1] + 1) * P], width=256)
        residual_stage(K, lambda j: o[:, j, :], KT)


def conv_ffn_1(K):
    nc = K.nc
    with ExitStack() as ffn:
        hidden = K.buf(ffn, "ffn_hidden", [P, FT, S])
        a = K.buf(ffn, "ffn_a", [P, 4, 2 + S])
        up = K.buf(ffn, "ffn_b", [P, 4, S])
        c = K.buf(ffn, "ffn_c", [P, 4, S])
        filled, b_ready, a_ready, conv, gelu, chain, multiplied = (K.sem(n) for n in ("up_filled", "b_ready", "a_ready", "conv_done", "gelu_done", "conv_chain", "ffn_multiplied"))
        sizes = [4] * (FT // 4) + [FT % 4] * (FT % 4 > 0)
        feed = Feed(K, ffn, KT * len(sizes), lambda i: K.xn[:, i % KT, 0:S], [S], residual_norm(K, ffn, "ffn_norm_g", (0, S)))
        groups, before = [], 0
        for g, n in enumerate(sizes):
            groups.append(Group(feed, 2 * n, KT * g, KT, filled, before))
            before += 2 * n - 1
        starts = [sum(sizes[:g]) for g in range(len(sizes))]
        with K.stage() as block:
            @block.sync
            def _(sp):
                feed.refill(sp)

            @block.tensor
            def _(pe):
                for g, n in enumerate(sizes):
                    def free(e, b, g=g):
                        e.wait_ge(a_ready, starts[g - 1] + min(b, 3) + 1)
                        if b >= 4:
                            e.wait_ge(b_ready, starts[g - 1] + b - 3)
                    groups[g].products(pe, features_product(K, feed, S), free if g else None)

            @block.scalar
            def _(act):
                feed.start_hi(act)
                for g, n in enumerate(sizes):
                    feed.ahead_hi(act, groups[g].body)
                    for i in range(n):
                        f = starts[g] + i
                        groups[g].bank_ready(act, i)
                        if f >= 4:
                            act.wait_ge(conv, f - 3)
                        nc.scalar.activation(a[:, f % 4, 2:2 + S], K.ps[:, i, :], ACT.Copy).then_inc(a_ready, 1)
                    for i in range(n):
                        f = starts[g] + i
                        groups[g].bank_ready(act, n + i)
                        if f >= 4:
                            act.wait_ge(multiplied, f - 3)
                        nc.scalar.activation(up[:, f % 4, :], K.ps[:, n + i, :], ACT.Copy).then_inc(b_ready, 1)
                    feed.ahead_hi(act, groups[g].end)
                    for i in range(n):
                        f = starts[g] + i
                        act.wait_ge(conv, f + 1)
                        nc.scalar.activation(hidden[:, f, :], c[:, f % 4, :], ACT.Gelu).then_inc(gelu, 1)

            @block.vector
            def _(dve):
                link = Chain(dve, chain)
                link(nc.vector.memset(a[:, :, 0:2], 0.0))
                feed.start_lo(dve)
                for g, n in enumerate(sizes):
                    feed.ahead_lo(dve, groups[g].body)
                    for i in range(n):
                        f = starts[g] + i
                        dve.wait_ge(a_ready, f + 1)
                        if f >= 4:
                            dve.wait_ge(gelu, f - 3)
                        at, to = a[:, f % 4, :], c[:, f % 4, :]
                        link(nc.vector.tensor_scalar(to, at[:, 0:S], K.vec("ffn_conv_w", f), K.vec("ffn_conv_b", f), ALU.mult, ALU.add))
                        link(nc.vector.scalar_tensor_tensor(out=to, in0=at[:, 1:1 + S], scalar=K.vec("ffn_conv_w", FT + f), in1=to, op0=ALU.mult, op1=ALU.add))
                        nc.vector.scalar_tensor_tensor(out=to, in0=at[:, 2:2 + S], scalar=K.vec("ffn_conv_w", 2 * FT + f), in1=to, op0=ALU.mult, op1=ALU.add).then_inc(conv, 1)
                        if i == n - 2:
                            feed.ahead_lo(dve, groups[g].end)

            @block.gpsimd
            def _(pool):
                for f in range(FT):
                    pool.wait_ge(gelu, f + 1)
                    pool.wait_ge(b_ready, f + 1)
                    nc.gpsimd.tensor_tensor(hidden[:, f, :], hidden[:, f, :], up[:, f % 4, :], ALU.mult).then_inc(multiplied, 1)
        residual_stage(K, lambda j: hidden[:, j, :], FT)


def block_1(K, ins):
    mixer_1(K, ins)
    cross_attention(K, ins)
    conv_ffn_1(K)


def block_2_slabs(a):
    w = a["w_in_2"]
    parts = [wide(w, [(0, 1024)]), wide(w, [(1024, 1536), (2048, 2560)]), wide(w, [(1536, 2048), (2560, 3072)]),
             wide(w, [(3144, 4168)]), wide(w, [(4168, 5192)]), wide(a["w_out_a_2"], [(0, D)]),
             wide(a["w_out_b_2"], [(0, D)]), wide(a["w_o_2"], [(0, D)])]
    parts += [wide(a["w_ff_in_2"], [(f, f + D)]) for f in range(0, FF2, D)]
    return parts + [wide(a["w_ff_out_2"], [(0, D)])]


def block_2_inputs(i):
    w = i["w_in_2"][0]
    index = np.concatenate([w[:, 3072:3136], w[:, 3072:3136], w[:, 3136:3144]], axis=1)
    return dict(
        index_w=np.ascontiguousarray(index.reshape(KT, P, -1).transpose(1, 0, 2)),
        sgu_w=np.ascontiguousarray(i["w_s_2"][0].transpose(2, 0, 1)),
        sgu_b=np.ascontiguousarray(np.broadcast_to(np.tile(i["b_s_2"][0], (1, 4)), (P, 4, S))),
        sgu_ln=np.ascontiguousarray(np.broadcast_to(np.stack([i["sgu_ln_g_2"][0], i["sgu_ln_b_2"][0]]), (P, 2, S))))


class Sgu:

    def __init__(self, K, ctx, u, vg, y, ins):
        self.K, self.u, self.vg, self.y, self.ins = K, u, vg, y, ins
        self.w = K.buf(ctx, "sgu_w", [P, 4, P])
        self.b = K.buf(ctx, "sgu_b", [P, 4, S])
        self.ln = K.buf(ctx, "sgu_ln", [P, 2, S])
        self.stats = K.buf(ctx, "sgu_stats", [P, 4, 6])
        self.moments = K.buf(ctx, "sgu_moments", [P, 4, 2])
        self.arrived, self.chain, self.moments_ready, self.rooted = (K.sem(n) for n in ("sgu_arrived", "sgu_chain", "sgu_moments_ready", "sgu_rooted"))

    def start_mix(self):
        self.filled, self.added = self.K.sem("sgu_filled"), self.K.sem("sgu_added")

    def load(self, sp):
        for to, src in ((self.w, "sgu_w"), (self.b, "sgu_b"), (self.ln, "sgu_ln")):
            sp.dma_start(to[:], self.ins[src]).then_inc(self.arrived, 16)

    def take_moments(self, dve):
        nc, stats, moments = self.K.nc, self.stats, self.moments
        self.link = Chain(dve, self.chain)
        for c in range(4):
            self.link(nc.vector.bn_stats(stats[:, c, :], self.vg[:, c, :]))
            self.link(nc.vector.bn_aggr(moments[:, c, :], stats[:, c, :]))
        nc.vector.tensor_copy(stats[:, :, 0:1], moments[:, :, 1:2]).then_inc(self.moments_ready, 1)

    def invert(self, dve):
        nc, w, stats = self.K.nc, self.w, self.stats
        dve.wait_ge(self.arrived, 48)
        nc.vector.tensor_tensor(w[:], w[:], self.K.upper.unsqueeze(1).to_broadcast((P, 4, P)), ALU.mult)
        dve.wait_ge(self.rooted, 1)
        self.link(nc.vector.reciprocal(stats[:, :, 2:3], stats[:, :, 1:2]))

    def norm(self, dve, c):
        nc, vg = self.K.nc, self.vg
        self.link(nc.vector.tensor_scalar(vg[:, c, :], vg[:, c, :], self.moments[:, c, 0:1], self.stats[:, c, 2:3], ALU.subtract, ALU.mult))
        self.link(nc.vector.tensor_tensor(vg[:, c, :], vg[:, c, :], self.ln[:, 0, :], ALU.mult))
        self.link(nc.vector.tensor_tensor(vg[:, c, :], vg[:, c, :], self.ln[:, 1, :], ALU.add))

    def root(self, act):
        act.wait_ge(self.moments_ready, 1)
        self.K.nc.scalar.activation(self.stats[:, :, 1:2], self.stats[:, :, 0:1], ACT.Sqrt, bias=self.K.eps_col).then_inc(self.rooted, 1)

    def tensor(self, pe):
        for g in range(4):
            for c in range(4):
                last = self.K.nc.tensor.matmul(self.K.ps[:, 4 + g, c * P:(c + 1) * P], self.vg[:, c, g * P:(g + 1) * P], self.w[:, g, :], start=True, stop=True)
            last.then_inc(self.filled, 1)

    def vector(self, dve):
        for g in range(4):
            dve.wait_ge(self.filled, g + 1)
            self.K.nc.vector.tensor_tensor(self.y[:, g, :], self.K.ps[:, 4 + g, :], self.b[:, g, :], ALU.add).then_inc(self.added, 1)

    def gpsimd(self, pool):
        for g in range(4):
            pool.wait_ge(self.added, g + 1)
            self.K.nc.gpsimd.tensor_tensor(self.y[:, g, :], self.y[:, g, :], self.u[:, g, :], ALU.mult)


def mix_in_2_stage(K, sgu, u, vg, q, v, k, qi, ki, wi, ins):
    nc = K.nc
    filled, drained, arrived, index_filled = K.sem("proj_filled"), K.sem("proj_drained"), K.sem("index_w_arrived"), K.sem("index_filled")
    with ExitStack() as local:
        feed = Feed(K, local, 3 * KT, lambda i: K.xn[:, i % KT, 0:S], [S], residual_norm(K, local, "norm1_g_2", (0, S)))
        groups = [Group(feed, 8, g * KT, KT, filled, 7 * g) for g in range(3)]
        w = K.buf(local, "index_w", [P, KT, 2 * HD + 8])
        with K.stage() as block:
            @block.sync
            def _(sp):
                sp.dma_start(w[:], ins["index_w"]).then_inc(arrived, 16)
                sgu.load(sp)
                feed.refill(sp)

            @block.tensor
            def _(pe):
                for g, group in enumerate(groups):
                    def product(i, b, start, stop, g=g):
                        if g < 2 and b >= 4:
                            return exact(nc, K.ps[:, b, :], cut(feed.acts(i), (b - 4) * P, (b - 3) * P), cut(feed.slab(i), 512, 1024), start, stop)
                        return features_product(K, feed, S)(i, b, start, stop)
                    group.products(pe, product, (lambda e, b, g=g: e.wait_ge(drained, 8 * (g - 1) + b + 1)) if g else None)
                pe.wait_ge(arrived, 16)
                pe.wait_ge(drained, 8 * 2 + 2)
                for j in range(KT):
                    last = nc.tensor.matmul(K.ps[:, 0, :], w[:, j, 0:P], K.xn[:, j, 0:S], start=j == 0, stop=j == KT - 1)
                last.then_inc(index_filled, 1)
                for i in range(4):
                    for j in range(KT):
                        last = nc.tensor.matmul(K.ps[:, 1, i * 8:(i + 1) * 8], K.xn[:, j, i * P:(i + 1) * P], w[:, j, P:P + 8], start=j == 0, stop=j == KT - 1)
                last.then_inc(index_filled, 1)

            @block.scalar
            def _(act):
                places = [(u, vg), (q, v), (k, qi)]
                feed.start_hi(act)
                for g, group in enumerate(groups):
                    feed.ahead_hi(act, group.body[0:2])
                    if g == 2:
                        sgu.root(act)
                    feed.ahead_hi(act, group.body[2:])
                    func = ACT.Gelu_apprx_tanh if g == 0 else ACT.Copy
                    for b in range(8):
                        group.bank_ready(act, b)
                        nc.scalar.activation(places[g][b // 4][:, b % 4, :], K.ps[:, b, :], func).then_inc(drained, 1)
                    feed.ahead_hi(act, group.end)
                act.wait_ge(index_filled, 2)
                nc.scalar.activation(ki[:], K.ps[:, 0, :], ACT.Copy)
                nc.scalar.activation(wi[:].rearrange("p i h -> p (i h)"), K.ps[:, 1, 0:32], ACT.Copy, scale=float(64.0 ** -0.5 * 8.0 ** -0.5))

            @block.vector
            def _(dve):
                feed.start_lo(dve)
                feed.ahead_lo(dve, range(2 * KT))
                dve.wait_ge(drained, KT)
                feed.ahead_lo(dve, range(2 * KT, 2 * KT + 1))
                sgu.take_moments(dve)
                feed.ahead_lo(dve, range(2 * KT + 1, 2 * KT + 2))
                sgu.invert(dve)
                for c in range(4):
                    feed.ahead_lo(dve, range(2 * KT + 2 + c, 2 * KT + 3 + c))
                    sgu.norm(dve, c)
                feed.ahead_lo(dve, range(2 * KT + 6, 3 * KT))


def rope_stage(K, tiles, sgu, ins):
    nc = K.nc
    sgu.start_mix()
    with ExitStack() as local:
        table = K.buf(local, "rope_table", [P, 2, 2, S])
        part = K.buf(local, "rope_part", [P, 2, S])
        arrived, scaled, turned, chain, cos_done, drained = (K.sem(n) for n in ("rope_arrived", "rope_scaled", "rope_turned", "rope_chain", "rope_cos_done", "rope_drained"))
        with K.stage() as block:
            @block.sync
            def _(sp):
                sp.dma_start(table[:, 0, 0, :], ins["c_cos"]).then_inc(arrived, 16)
                sp.dma_start(table[:, 0, 1, :], ins["c_sin"]).then_inc(arrived, 16)

            @block.tensor
            def _(pe):
                for n, (x, _) in enumerate(tiles):
                    if n == 4:
                        sgu.tensor(pe)
                    if n >= 4:
                        pe.wait_ge(drained, n - 3)
                    nc.tensor.matmul(K.ps[:, n % 4, :], K.rot, x, start=True, stop=True).then_inc(turned, 1)

            @block.gpsimd
            def _(pool):
                pool.wait_ge(scaled, 1)
                for n, (x, small) in enumerate(tiles):
                    pool.wait_ge(turned, n + 1)
                    nc.gpsimd.tensor_tensor(x, x, table[:, small, 0, :], ALU.mult).then_inc(cos_done, 1)
                sgu.gpsimd(pool)

            @block.vector
            def _(dve):
                link = Chain(dve, chain)
                dve.wait_ge(arrived, 32)
                nc.vector.tensor_scalar(table[:, 1], table[:, 0], HD ** -0.5, None, ALU.mult).then_inc(scaled, 1)
                dve.wait_ge(scaled, 1)
                for n, (x, small) in enumerate(tiles):
                    dve.wait_ge(turned, n + 1)
                    nc.vector.tensor_tensor(part[:, n % 2, :], K.ps[:, n % 4, :], table[:, small, 1, :], ALU.mult).then_inc(drained, 1)
                    dve.wait_ge(drained, n + 1)
                    dve.wait_ge(cos_done, n + 1)
                    link(nc.vector.tensor_tensor(x, x, part[:, n % 2, :], ALU.add))
                    if n == len(tiles) - 3:
                        sgu.vector(dve)


def gates_select_stage(K, gates, qi, ki, wi, mask, ins):
    nc = K.nc
    heads = 8
    with ExitStack() as local:
        causal = K.buf(local, "causal", [P, P])
        pos = K.buf(local, "relu_logits", [P, 2, S])
        scores = {i: K.buf(local, "index_score", [P, (i + 1) * P]) for i in range(1, 4)}
        work = K.buf(local, "index_work", [P, S])
        top = K.buf(local, "index_top", [P, 8])
        above = K.buf(local, "index_above", [P, S])
        equal = K.buf(local, "index_equal", [P, S])
        count = K.buf(local, "index_count", [P, 2])
        one = K.buf(local, "index_ones", [P, S])
        arrived, chain, filled, relu, summed, gate_filled, drained = (K.sem(n) for n in (
            "causal_arrived", "select_chain", "logits_filled", "logits_relu", "logits_summed", "gates_filled", "gates_drained"))
        feed = Feed(K, local, 2 * KT, lambda i: K.xn[:, i % KT, 0:S], [S])
        groups = [Group(feed, 8, g * KT, KT, gate_filled, 7 * g) for g in range(2)]
        with K.stage() as block:
            @block.sync
            def _(sp):
                sp.dma_start(causal[:], ins["c_causal"]).then_inc(arrived, 16)
                feed.refill(sp)

            @block.tensor
            def _(pe):
                for n in range(3 * heads):
                    i, h = 1 + n // heads, n % heads
                    keys = (i + 1) * P
                    rows = slice((h % 2) * HD, (h % 2 + 1) * HD)
                    if n >= 8:
                        pe.wait_ge(relu, n - 7)
                    nc.tensor.matmul(K.ps[:, n % 8, 0:keys], qi[rows, h // 2, i * P:(i + 1) * P], ki[rows, 0:keys], start=True, stop=True).then_inc(filled, 1)
                product = features_product(K, feed, S)
                groups[0].products(pe, product, lambda e, b: e.wait_ge(relu, 2 * heads + b + 1))
                groups[1].products(pe, product, lambda e, b: e.wait_ge(drained, b + 1))

            @block.gpsimd
            def _(pool):
                feed.start_lo(pool)
                feed.ahead_lo(pool, range(2 * KT))

            @block.scalar
            def _(act):
                for n in range(3 * heads):
                    keys = (2 + n // heads) * P
                    act.wait_ge(filled, n + 1)
                    if n >= 2:
                        act.wait_ge(summed, n - 1)
                    nc.scalar.activation(pos[:, n % 2, 0:keys], K.ps[:, n % 8, 0:keys], ACT.Relu).then_inc(relu, 1)
                    if n == 2 * heads:
                        feed.start_hi(act)
                for g, group in enumerate(groups):
                    feed.ahead_hi(act, group.body)
                    for b in range(8):
                        group.bank_ready(act, b)
                        nc.scalar.activation(gates[:, 8 * g + b, :], K.ps[:, b, :], ACT.Sigmoid).then_inc(drained, 1)
                    feed.ahead_hi(act, group.end)

            @block.vector
            def _(dve):
                link = Chain(dve, chain)
                link(nc.vector.memset(one[:], 1.0))
                dve.wait_ge(arrived, 16)
                nc.vector.tensor_copy(mask[:, 0, 0:P], causal[:])
                for i in range(1, 4):
                    sc = scores[i][:]
                    for h in range(heads):
                        n = (i - 1) * heads + h
                        dve.wait_ge(relu, n + 1)
                        src = pos[:, n % 2, 0:(i + 1) * P]
                        if h == 0:
                            ins_ = nc.vector.tensor_scalar(sc, src, wi[:, i, 0:1], None, ALU.mult)
                        else:
                            ins_ = nc.vector.scalar_tensor_tensor(out=sc, in0=src, scalar=wi[:, i, h:h + 1], in1=sc, op0=ALU.mult, op1=ALU.add)
                        ins_.then_inc(summed, 1)
                        dve.wait_ge(summed, n + 1)
                    link(nc.vector.tensor_tensor(sc[:, i * P:], sc[:, i * P:], causal[:], ALU.add))
                for i in range(1, 4):
                    keys = (i + 1) * P
                    sc, wk = scores[i][:], work[:, 0:keys]
                    for n in range(TOPK // 8):
                        link(nc.vector.max(top[:], sc if n == 0 else wk))
                        if n < TOPK // 8 - 1:
                            link(nc.vector.match_replace(wk, top[:], sc if n == 0 else wk, LOWEST))
                    last = top[:, 7:8]
                    link(nc.vector.tensor_scalar(above[:, 0:keys], sc, last, 0.0, ALU.is_gt, ALU.add, accum_out=count[:, 0:1]))
                    link(nc.vector.tensor_scalar(equal[:, 0:keys], sc, last, None, ALU.is_equal))
                    link(nc.vector.tensor_scalar(count[:, 1:2], count[:, 0:1], -1.0, float(TOPK), ALU.mult, ALU.add))
                    link(nc.vector.tensor_tensor_scan(wk, one[:, 0:keys], equal[:, 0:keys], 0.0, ALU.mult, ALU.add))
                    link(nc.vector.scalar_tensor_tensor(out=wk, in0=wk, scalar=count[:, 1:2], in1=equal[:, 0:keys], op0=ALU.is_le, op1=ALU.mult))
                    link(nc.vector.tensor_tensor(wk, wk, above[:, 0:keys], ALU.add))
                    link(nc.vector.tensor_scalar(mask[:, i, 0:keys], wk, -NEG, NEG, ALU.mult, ALU.add))


def merge_stage(K, ya, yb, gates, merged):
    nc = K.nc
    filled, drained, gated = K.sem("merge_filled"), K.sem("merge_drained"), K.sem("merge_gated")
    with ExitStack() as local:
        part = K.buf(local, "merge_part", [P, KT, S])
        feed = Feed(K, local, KT, lambda i: (ya, yb)[i // 4][:, i % 4, :], [S])
        groups = [Group(feed, KT, 4 * g, 4, filled, 7 * g) for g in range(2)]

        def add(e, engine, m):
            e.wait_ge(gated, m + 1)
            engine.tensor_tensor(merged(m), merged(m), part[:, m, :], ALU.add)

        with K.stage() as block:
            @block.sync
            def _(sp):
                feed.refill(sp)

            @block.tensor
            def _(pe):
                for g, group in enumerate(groups):
                    group.products(pe, features_product(K, feed, S), (lambda e, b: e.wait_ge(drained, b + 1)) if g else None)

            @block.scalar
            def _(act):
                feed.start_hi(act)
                feed.ahead_hi(act, range(KT))

            @block.vector
            def _(dve):
                feed.start_lo(dve)
                feed.ahead_lo(dve, groups[0].body)
                for m in range(KT):
                    groups[0].bank_ready(dve, m)
                    nc.vector.tensor_tensor(merged(m), K.ps[:, m, :], gates[:, m, :], ALU.mult).then_inc(drained, 1)
                feed.ahead_lo(dve, groups[0].end)
                feed.ahead_lo(dve, groups[1].body)
                dve.wait_ge(drained, KT)
                for m in range(KT):
                    groups[1].bank_ready(dve, m)
                    nc.vector.tensor_tensor(part[:, m, :], K.ps[:, m, :], gates[:, KT + m, :], ALU.mult).then_inc(gated, 1)
                    if m % 2:
                        add(dve, nc.vector, m)

            @block.gpsimd
            def _(pool):
                for m in range(0, KT, 2):
                    add(pool, nc.gpsimd, m)


def ffn_2(K):
    nc = K.nc
    turns = FF2 // D
    with ExitStack() as ffn:
        hidden = K.buf(ffn, "ff_hidden", [P, FF2 // P, S])
        filled, drained = K.sem("ff_filled"), K.sem("ff_drained")
        with ExitStack() as local:
            feed = Feed(K, local, turns * KT, lambda i: K.xn[:, i % KT, 0:S], [S], residual_norm(K, local, "norm2_g_2", (0, S)))
            group = Group(feed, KT, 0, KT, filled)

            def square(e, engine, m, turn):
                e.wait_ge(drained, turn * KT + (m + 1))
                at = hidden[:, bass.ds(turn * KT + m, 1), :]
                engine.tensor_tensor(at, at, at, ALU.mult)

            with K.stage() as block:
                @block.sync
                def _(sp):
                    feed.refill(sp)

                @block.tensor
                def _(pe):
                    product = features_product(K, feed, S)
                    group.products(pe, product)
                    with pe.Fori(1, turns) as turn:
                        group.products(pe, product, lambda e, b: e.wait_ge(drained, turn * KT), turn)

                @block.scalar
                def _(act):
                    def drain(m, turn):
                        group.bank_ready(act, m, turn)
                        nc.scalar.activation(hidden[:, bass.ds(turn * KT + m, 1), :], K.ps[:, m:m + 1, :], ACT.Relu).then_inc(drained, 1)

                    feed.start_hi(act)
                    with act.Fori(0, turns - 1) as turn:
                        feed.ahead_hi(act, group.body, turn)
                        for m in range(KT):
                            drain(m, turn)
                        feed.ahead_hi(act, group.end, turn)
                    feed.ahead_hi(act, range((turns - 1) * KT, turns * KT - 1))
                    for m in range(KT):
                        drain(m, turns - 1)

                @block.vector
                def _(dve):
                    feed.start_lo(dve)
                    with dve.Fori(0, turns - 1) as turn:
                        feed.ahead_lo(dve, range(KT), turn)
                    feed.ahead_lo(dve, range((turns - 1) * KT, turns * KT))
                    for m in range(1, KT, 2):
                        square(dve, nc.vector, m, turns - 1)

                @block.gpsimd
                def _(pool):
                    with pool.Fori(0, turns - 1) as turn:
                        for m in range(KT):
                            square(pool, nc.gpsimd, m, turn)
                    for m in range(0, KT, 2):
                        square(pool, nc.gpsimd, m, turns - 1)
        residual_stage(K, lambda j: hidden[:, j, :], FF2 // P)


def block_2(K, ins):
    with ExitStack() as mix:
        ya, yb, u, vg, q, v, k, qi = (K.buf(mix, n, [P, 4, S]) for n in ("sgu_y", "dsa_y", "sgu_u", "sgu_v", "dsa_q", "dsa_v", "dsa_k", "index_q"))
        ki = K.buf(mix, "index_k", [P, S])
        wi = K.buf(mix, "index_weights", [P, 4, 8])
        with ExitStack() as first:
            sgu = Sgu(K, first, u, vg, ya, ins)
            mix_in_2_stage(K, sgu, u, vg, q, v, k, qi, ki, wi, ins)
            rope_stage(K, [(x[:, t, :], s) for x, s in ((qi, 0), (k, 0), (q, 1)) for t in range(4)] + [(ki[:], 0)], sgu, ins)
        gates = K.buf(mix, "branch_gates", [P, 16, S])
        with ExitStack() as att:
            mask = K.buf(att, "dsa_mask", [P, 4, S])
            gates_select_stage(K, gates, qi, ki, wi, mask, ins)

            def scores(unit, part, lo, hi, to):
                h, i, _ = unit
                rows = slice((h % 2) * HD, (h % 2 + 1) * HD)
                return K.nc.tensor.matmul(to, q[rows, h // 2, i * P:(i + 1) * P], k[rows, h // 2, lo:hi], start=True, stop=True)

            attention_stage(K, [(h, i, i + 1) for h in range(8) for i in range(4)], P, scores,
                            lambda h, t, d: v[:, t, h * HD:(h + 1) * HD],
                            lambda unit, d: yb[(unit[0] % 2) * HD:(unit[0] % 2 + 1) * HD, unit[0] // 2, unit[1] * P:(unit[1] + 1) * P],
                            bias=lambda unit: mask[:, unit[1], 0:unit[2] * P])
        merge_stage(K, ya, yb, gates, lambda m: K.xn[:, m, 0:S])
    residual_stage(K, lambda j: K.xn[:, j, 0:S], KT)
    ffn_2(K)
    meta_arrived = K.sem("meta_arrived")

    def load_meta(sp, normed):
        sp.dma_start(K.xn[:, :, 0:META], ins["meta"]).then_inc(meta_arrived, 16)
        sp.wait_ge(meta_arrived, 16)

    norm_stage(K, lambda k: K.h[:, k, 0:S], lambda k: K.xn[:, k, META:T3], "norm_f_g_2", (0, S), load_meta)
    K.h, K.xn = K.xn, K.h


FOX_HEADS = 8
GDN_HEADS = 8
QUAD = 4


def block_3_slabs(a):
    w = a["w_in_3"]
    parts = [paired(w, [(lo, lo + 512)]) for lo in (1544, 2056, 2568, 0, 512, 1024, 3080, 3608, 4120, 4632, 5144)]
    for lo in (0, 512):
        parts += [paired(a["w_branch_fox_3"], [(lo, lo + 512)]), paired(a["w_branch_gdn_3"], [(lo, lo + 512)])]
    parts += [paired(a["w_out_3"], [(lo, lo + 512)]) for lo in (0, 512)]
    parts += [paired(a["ffn_w_up_3"], [(f, f + 256), (FF + f, FF + f + 256)]) for f in range(0, FF, 256)]
    return parts + [wide(a["ffn_w_down_3"], [(0, D)])]


def block_3_inputs(i):
    w = i["w_in_3"][0]
    small = np.concatenate([w[:, 1536:1544], w[:, 3592:3600], w[:, 3600:3608]], axis=1)
    return dict(head_w=np.ascontiguousarray(small.reshape(KT, P, 24).transpose(1, 0, 2)))


def half_product(K, feed):
    def product(i, b, start, stop):
        lo, hi = HALVES[b % 2]
        for k in range(2):
            at = k * 512 + (b // 2) * P
            mm = exact(K.nc, K.ps[:, b, 0:hi - lo], cut(feed.slab(i), at, at + P), [x[:, k, lo:hi] for x in feed.acts(i)],
                       start and k == 0, stop and k == 1)
        return mm
    return product


def pairs_of(x):
    n = x.shape[1] // 2
    return lambda i: x[:, 2 * (i % n):2 * (i % n) + 2, :]


def mix_in_3_stage(K, fq, fk, fv, gin, heads, keep, causal, ins):
    nc = K.nc
    filled, drained, arrived, head_filled, padded, zeroed, conv, done, chain = (K.sem(n) for n in (
        "proj3_filled", "proj3_drained", "head_w_arrived", "heads_filled", "fox_padded", "fox_zeroed", "gdn_conv_done", "gdn_silu_done", "gdn_conv_chain"))
    with ExitStack() as local:
        feed = Feed(K, local, 24, pairs_of(K.xn), [2, T3], residual_norm(K, local, "norm_mix_w_3", (0, T3)))
        groups, before = [], 0
        for g in range(6):
            groups.append(Group(feed, NC3 if g == 5 else 8, 4 * g, 4, filled, before))
            before += groups[-1].banks - 1
        out_before = [sum(x.banks for x in groups[:g]) for g in range(7)]
        w = K.buf(local, "head_w", [P, KT, 24])
        mixed = K.buf(local, "gdn_conv", [P, 2, T3])
        with K.stage() as block:
            @block.sync
            def _(sp):
                sp.dma_start(w[:], ins["head_w"]).then_inc(arrived, 16)
                sp.dma_start(keep[:], ins["c_gdn_keep"][0:8, :]).then_inc(arrived, 16)
                sp.dma_start(causal[:], ins["c_causal88"][0:C3, 0:C3]).then_inc(arrived, 16)
                feed.refill(sp)

            @block.gpsimd
            def _(pool):
                for o in range(2):
                    other = slice((1 - o) * HD, (2 - o) * HD)
                    nc.gpsimd.memset(fk[other, o:FOX_HEADS:2, :], 0.0)
                    nc.gpsimd.memset(fq[other, o:FOX_HEADS:2, :], 0.0).then_inc(zeroed, 1)
                pool.wait_ge(zeroed, 2)
                for o in range(2):
                    nc.gpsimd.memset(fq[(1 - o) * HD:(1 - o) * HD + 1, o:FOX_HEADS:2, :], 1.0)

            @block.tensor
            def _(pe):
                for g, group in enumerate(groups):
                    def token_major(i, b, start, stop):
                        for k in range(2):
                            mm = exact(nc, K.ps[0:C3, b, :], [x[:, k, b * C3:(b + 1) * C3] for x in feed.acts(i)],
                                       cut(feed.slab(i), k * 512, (k + 1) * 512), start and k == 0, stop and k == 1)
                        return mm

                    def free(e, b, g=g):
                        e.wait_ge(drained, out_before[g - 1] + min(b + 1, groups[g - 1].banks))
                    group.products(pe, token_major if g == 5 else half_product(K, feed), free if g else None)
                pe.wait_ge(arrived, 48)
                pe.wait_ge(drained, out_before[6])
                for n in range(3):
                    for c, (lo, hi) in enumerate(HALVES):
                        for j in range(KT):
                            last = nc.tensor.matmul(K.ps[0:8, 2 * n + c, 0:hi - lo], w[:, j, n * 8:(n + 1) * 8], K.xn[:, j, lo:hi], start=j == 0, stop=j == KT - 1)
                last.then_inc(head_filled, 1)

            @block.scalar
            def _(act):
                def silu(t):
                    act.wait_ge(conv, t + 1)
                    nc.scalar.activation(gin[:, t, 3:3 + T3], mixed[:, t % 2, :], ACT.Silu).then_inc(done, 1)

                def ahead(steps):
                    for i in steps:
                        feed.ahead_hi(act, [i])
                        if 0 <= i - 5 < 12:
                            silu(i - 5)

                feed.start_hi(act)
                for g, group in enumerate(groups):
                    ahead(group.body)
                    for b in range(group.banks):
                        group.bank_ready(act, b)
                        (lo, hi), t = HALVES[b % 2], b // 2
                        if g == 5:
                            if b == 0:
                                act.wait_ge(padded, 1)
                            ins_ = nc.scalar.activation(fv[0:C3, b, :], K.ps[0:C3, b, :], ACT.Copy)
                        elif g >= 3:
                            for o in range(2):
                                rows = slice(o * HD, (o + 1) * HD)
                                ins_ = nc.scalar.activation((fq, fk)[g - 3][rows, 2 * t + o, lo:hi], K.ps[rows, b, 0:hi - lo], ACT.Copy,
                                                            scale=HD ** -0.5 if g == 3 else 1.0)
                        else:
                            ins_ = nc.scalar.activation(gin[:, 4 * g + t, 3 + lo:3 + hi], K.ps[:, b, 0:hi - lo], ACT.Copy)
                        ins_.then_inc(drained, 1)
                    ahead(group.end)
                act.wait_ge(head_filled, 1)
                for n in range(3):
                    for c, (lo, hi) in enumerate(HALVES):
                        nc.scalar.activation(heads[:, n, lo:hi], K.ps[0:8, 2 * n + c, 0:hi - lo], ACT.Copy)

            @block.vector
            def _(dve):
                feed.start_lo(dve)
                nc.vector.memset(fv[HD:P], 0.0).then_inc(padded, 1)
                nc.vector.memset(gin[:, :, 0:3], 0.0).then_inc(padded, 1)
                dve.wait_ge(padded, 2)
                link = Chain(dve, chain)
                for i in range(24):
                    feed.ahead_lo(dve, [i])
                    t = i - 4
                    if 0 <= t < 12:
                        dve.wait_ge(drained, 2 * t + 2)
                        if t >= 2:
                            dve.wait_ge(done, t - 1)
                        to = mixed[:, t % 2, :]
                        link(nc.vector.tensor_scalar(to, gin[:, t, 0:T3], K.vec("gdn_conv_w_3", t), None, ALU.mult))
                        for tap in range(1, 4):
                            ins_ = nc.vector.scalar_tensor_tensor(out=to, in0=gin[:, t, tap:tap + T3], scalar=K.vec("gdn_conv_w_3", 12 * tap + t), in1=to, op0=ALU.mult, op1=ALU.add)
                            if tap < 3:
                                link(ins_)
                        ins_.then_inc(conv, 1)


def gate_3_stage(K, z, yg, gates):
    nc = K.nc
    filled, drained = K.sem("gates3_filled"), K.sem("gates3_drained")
    with ExitStack() as local:
        feed = Feed(K, local, 20, pairs_of(K.xn), [2, T3])
        groups = [Group(feed, 8, 4 * g, 4, filled, 7 * g) for g in range(5)]
        with K.stage() as block:
            @block.sync
            def _(sp):
                feed.refill(sp)

            @block.tensor
            def _(pe):
                for g, group in enumerate(groups):
                    group.products(pe, half_product(K, feed), (lambda e, b, g=g: e.wait_ge(drained, 8 * (g - 1) + b + 1)) if g else None)

            @block.scalar
            def _(act):
                feed.start_hi(act)
                for g, group in enumerate(groups):
                    feed.ahead_hi(act, group.body)
                    for b in range(8):
                        group.bank_ready(act, b)
                        (lo, hi), t = HALVES[b % 2], b // 2
                        src = K.ps[:, b, 0:hi - lo]
                        if g == 0:
                            nc.scalar.activation(z[:, t, lo:hi], src, ACT.Silu).then_inc(drained, 1)
                        else:
                            m = 4 * (g - 1) + t
                            nc.scalar.activation(gates[:, m, lo:hi], src, ACT.Sigmoid, bias=K.vec("gate_bias_3", m)).then_inc(drained, 1)
                    feed.ahead_hi(act, group.end)

            @block.vector
            def _(dve):
                feed.start_lo(dve)
                feed.ahead_lo(dve, range(20))

            @block.gpsimd
            def _(pool):
                pool.wait_ge(drained, 8)
                nc.gpsimd.tensor_tensor(yg, yg, z[:], ALU.mult)


def head_rates_stage(K, heads, fk, keep):
    nc = K.nc
    with ExitStack() as local:
        x = K.buf(local, "rate_x", [8, 2, T3])
        e = K.buf(local, "rate_e", [8, 2, T3])
        rate = K.buf(local, "gdn_rate", [8, 2])
        chain, e_ready, log_ready, rate_ready, summed, f_summed, rows_arrived = (K.sem(n) for n in (
            "rate_chain", "e_ready", "log_ready", "rate_ready", "gc_summed", "f_summed", "fox_rows_arrived"))
        with K.stage() as block:
            @block.vector
            def _(dve):
                link = Chain(dve, chain)
                link(nc.vector.tensor_scalar(x[:, 0, :], heads[:, 0, :], K.vec("fgt_bias_3")[0:8, :], None, ALU.add))
                link(nc.vector.tensor_scalar(x[:, 1, :], heads[:, 2, :], K.vec("gdn_dt_bias_3")[0:8, :], None, ALU.add))
                link(nc.vector.tensor_scalar(e[:], x[:], -1.0, None, ALU.mult))
                nc.vector.tensor_tensor(e[:], e[:], x[:], ALU.min).then_inc(e_ready, 1)
                dve.wait_ge(e_ready, 1)
                dve.wait_ge(log_ready, 1)
                link(nc.vector.tensor_scalar(heads[:, 3, :], x[:, 0, :], 0.0, None, ALU.min))
                link(nc.vector.tensor_tensor(x[:, 0, :], e[:, 0, :], heads[:, 3, :], ALU.subtract))
                link(nc.vector.memset(heads[:, 3, :], 1.0))
                nc.vector.tensor_tensor_scan(heads[:, 0, :], heads[:, 3, :], x[:, 0, :], 0.0, ALU.mult, ALU.add).then_inc(f_summed, 1)
                dve.wait_ge(f_summed, 1)
                link(nc.vector.scalar_tensor_tensor(out=x[:, 1, :], in0=x[:, 1, :], scalar=0.0, in1=e[:, 1, :], op0=ALU.max, op1=ALU.add))
                dve.wait_ge(rate_ready, 1)
                link(nc.vector.tensor_scalar(x[:, 1, :], x[:, 1, :], rate[:, 0:1], -1.0, ALU.mult, ALU.mult))
                nc.vector.tensor_tensor_scan(heads[:, 2, :], keep, x[:, 1, :], 0.0, ALU.mult, ALU.add).then_inc(summed, 1)

            @block.scalar
            def _(act):
                nc.scalar.activation(rate[:, 0:1], K.vec("gdn_a_log_3")[0:8, :], ACT.Exp).then_inc(rate_ready, 1)
                act.wait_ge(e_ready, 1)
                nc.scalar.activation(e[:], e[:], ACT.Exp).then_inc(e_ready, 1)
                act.wait_ge(e_ready, 2)
                nc.scalar.activation(e[:], e[:], ACT.Ln, bias=K.one_col[0:8, :]).then_inc(log_ready, 1)
                act.wait_ge(summed, 1)
                nc.scalar.activation(heads[:, 3, :], heads[:, 2, :], ACT.Exp)
                nc.scalar.activation(heads[:, 1, :], heads[:, 1, :], ACT.Sigmoid)

            @block.sync
            def _(sp):
                sp.wait_ge(f_summed, 1)
                for h in range(FOX_HEADS):
                    row = (1 - h % 2) * HD
                    sp.dma_start(fk[row:row + 1, h, :], heads[h:h + 1, 0, :]).then_inc(rows_arrived, 16)
                sp.wait_ge(rows_arrived, 16 * FOX_HEADS)


def gdn_rates_stage(K, heads, q, q0, tok, last_decay, zeroed):
    nc = K.nc
    with ExitStack() as local:
        turned, turned_out, spread, chain, exped, q_filled, q_out, last_in = (K.sem(n) for n in ("rates_turned", "rates_out", "rates_spread", "rates_chain", "rates_exped", "q_filled", "q_out", "last_in"))
        last_sum = K.buf(local, "last_sum", [8, NC3])
        with K.stage() as block:
            @block.tensor
            def _(pe):
                for n, row in enumerate((1, 2, 3)):
                    for c in range(NC3):
                        last = nc.tensor.transpose(K.ps[0:C3, n, c * 8:(c + 1) * 8], heads[:, row, c * C3:(c + 1) * C3], K.ident[0:8, 0:8])
                last.then_inc(turned, 1)
                pe.wait_ge(last_in, 1)
                for h in range(GDN_HEADS):
                    last = nc.tensor.matmul(K.ps[:, 3, h * NC3:(h + 1) * NC3], K.pick(h, P), last_sum[:], start=True, stop=True)
                last.then_inc(spread, 1)
                for h in range(GDN_HEADS):
                    for c, (lo, hi) in enumerate(HALVES):
                        n = 2 * h + c
                        if n >= 4:
                            pe.wait_ge(q_out, n - 3)
                        nc.tensor.matmul(K.ps[:, 4 + n % 4, 0:hi - lo], K.pick(h, P), heads[:, 3, lo:hi], start=True, stop=True).then_inc(q_filled, 1)

            @block.vector
            def _(dve):
                link = Chain(dve, chain)
                nc.vector.tensor_copy(last_sum[:], heads[:, 2, :].rearrange("h (c i) -> h c i", i=C3)[:, :, C3 - 1]).then_inc(last_in, 1)
                dve.wait_ge(turned, 1)
                flat = tok[:].rearrange("p n c h -> p n (c h)")
                for n in range(3):
                    link(nc.vector.tensor_copy(flat[:, n, :], K.ps[0:C3, n, 0:NC3 * 8]))
                link(nc.vector.tensor_tensor(flat[:, 2, :], flat[:, 2, :], flat[:, 0, :], ALU.mult))
                dve.wait_ge(spread, 1)
                sums = K.ps[0:C3, 3, 0:NC3 * 8].rearrange("p (h c) -> p c h", c=NC3)
                nc.vector.tensor_tensor(tok[:, 3], sums, tok[:, 1], ALU.subtract).then_inc(turned_out, 1)
                for h in range(GDN_HEADS):
                    rows = slice((h % 2) * HD, (h % 2 + 1) * HD)
                    for c, (lo, hi) in enumerate(HALVES):
                        n = 2 * h + c
                        dve.wait_ge(q_filled, n + 1)
                        nc.vector.tensor_tensor(q0[rows, h // 2, lo:hi], K.ps[rows, 4 + n % 4, 0:hi - lo], q[rows, h // 2, lo:hi], ALU.mult).then_inc(q_out, 1)

            @block.scalar
            def _(act):
                act.wait_ge(turned_out, 1)
                nc.scalar.activation(tok[:, 3], tok[:, 3], ACT.Exp)
                for o in range(2):
                    rows = slice(o * HD, (o + 1) * HD)
                    src = K.ps[rows, 3, 0:NC3 * 8].rearrange("p (i o c) -> p i o c", o=2, c=NC3)[:, :, o, :]
                    nc.scalar.activation(last_decay[rows], src, ACT.Exp)

            @block.gpsimd
            def _(pool):
                for t in zeroed:
                    nc.gpsimd.memset(t[HD:P], 0.0)


def gdn_chunk_stage(K, gin, heads, tok, k_tok, v_tok, out, ins):
    nc = K.nc
    (kcdT, value, attnT) = out
    SH = [C3, QUAD, C3]
    LV = LEVELS_G - 1
    with ExitStack() as local:
        masks_in = K.buf(local, "gdn_masks", [C3, LEVELS_G + 5, C3])
        wide_prod, wide_amask, wide_inv, wide_invT = wides = [K.buf(local, n, [P, 2, QUAD, C3]) for n in ("gdn_prod", "gdn_A_level", "gdn_inv", "gdn_invT")]
        wide_bv, wide_bk = wide_rhs = [K.buf(local, n, [P, 2, QUAD, HD]) for n in ("gdn_beta_v", "gdn_beta_k")]
        prod, amask, inv, invT, bv, bk = (t[0:C3] for t in wides + wide_rhs)
        amat, beta_mask = (K.buf(local, n, [C3, 2, QUAD, C3]) for n in ("gdn_A", "gdn_beta_mask"))
        arrived, chain, pool_chain, padded = (K.sem(n) for n in ("gdn_masks_arrived", "gdn_chain", "gdn_pool_chain", "gdn_padded"))
        (sums_filled, keys_filled, queries_filled, split, exped, weighted, first, attn_out, firstT_filled, firstT, masked, turned, inv_out,
         z_filled, z_out, d_filled, d_added, x_filled, x_out, rhs_ready) = ([K.sem(f"gdn_{n}_{q}") for q in range(2)] for n in (
            "sums_filled", "keys_filled", "queries_filled", "split", "exped", "weighted", "first", "attn_out", "firstT_filled", "firstT", "masked", "turned",
            "inv_out", "z_filled", "z_out", "d_filled", "d_added", "x_filled", "x_out", "rhs_ready"))

        def mask(n):
            return masks_in[:, n:n + 1, :].to_broadcast(SH)

        def over(n, c, q, width):
            return tok[:, n, c, q:GDN_HEADS:2].unsqueeze(2).to_broadcast((C3, QUAD, width))

        def own(t, c, q):
            return t[0:C3, c, q:GDN_HEADS:2, :]

        def bank(q, b):
            return K.ps[0:C3, 4 * q + b, 0:QUAD * C3].rearrange("p (h i) -> p h i", i=C3)

        def head(base, h, c):
            rows = slice((h % 2) * HD, (h % 2 + 1) * HD)
            return gin[rows, base + h // 2, 3 + c * C3:3 + (c + 1) * C3]

        PAIRS, TRIANGLE, TURN = range(3)
        RESULT = TURN + 1 + 2 * LV
        STEPS = RESULT + 1

        APART = STEPS // 2 - 1

        def run(**step):
            for n in range(NC3 * STEPS + APART):
                for q in range(2):
                    c, at = divmod(n - q * APART, STEPS)
                    if not 0 <= c < NC3:
                        continue
                    if at in (PAIRS, TRIANGLE, TURN, RESULT):
                        name = {PAIRS: "pairs", TRIANGLE: "triangle", TURN: "turn", RESULT: "result"}[at]
                        if name in step:
                            step[name](c, q)
                    else:
                        l, second = divmod(at - TURN - 1, 2)
                        step["add" if second else "product"](c, q, l, c * LV + l)

        with K.stage() as block:
            @block.sync
            def _(sp):
                sp.dma_start(masks_in[:], ins["c_levels_g"][0:C3]).then_inc(arrived, 16)

            @block.tensor
            def _(pe):
                def pairs(c, q):
                    for i in range(QUAD):
                        last = nc.tensor.matmul(bank(q, 0)[:, i, :], K.pick(2 * i + q, C3), heads[:, 2, c * C3:(c + 1) * C3], start=True, stop=True)
                    last.then_inc(sums_filled[q], 1)
                    for i in range(QUAD):
                        h = 2 * i + q
                        last = nc.tensor.matmul(bank(q, 1)[:, i, :], head(4, h, c), head(4, h, c), start=True, stop=True)
                    last.then_inc(keys_filled[q], 1)
                    if c:
                        pe.wait_ge(x_out[q], 2 * c)
                    for i in range(QUAD):
                        h = 2 * i + q
                        last = nc.tensor.matmul(bank(q, 2)[:, i, :], head(4, h, c), head(0, h, c), start=True, stop=True)
                    last.then_inc(queries_filled[q], 1)

                def turn(c, q):
                    pe.wait_ge(first[q], c + 1)
                    for i in range(QUAD):
                        last = nc.tensor.transpose(bank(q, 3)[:, i, :], inv[:, q, i, :], K.ident[0:C3, 0:C3])
                    last.then_inc(firstT_filled[q], 1)

                def product(c, q, l, n):
                    if l == 0:
                        pe.wait_ge(firstT[q], c + 1)
                    else:
                        pe.wait_ge(d_added[q], n)
                        pe.wait_ge(attn_out[q], c + 1)
                        for i in range(QUAD):
                            last = nc.tensor.transpose(bank(q, 2)[:, i, :], invT[:, q, i, :], K.ident[0:C3, 0:C3])
                        last.then_inc(turned[q], 1)
                    pe.wait_ge(masked[q], n + 1)
                    for i in range(QUAD):
                        last = nc.tensor.matmul(bank(q, 0)[:, i, :], wide_amask[:, q, i, :], wide_invT[:, q, i, :], start=True, stop=True)
                    last.then_inc(z_filled[q], 1)

                def add(c, q, l, n):
                    pe.wait_ge(z_out[q], n + 1)
                    if l:
                        pe.wait_ge(inv_out[q], c * (LV - 1) + l)
                    for i in range(QUAD):
                        last = nc.tensor.matmul(bank(q, 1)[:, i, :], wide_inv[:, q, i, :], wide_prod[:, q, i, :], start=True, stop=True)
                    last.then_inc(d_filled[q], 1)

                def result(c, q):
                    pe.wait_ge(d_added[q], LV * (c + 1))
                    pe.wait_ge(rhs_ready[q], c + 1)
                    for i in range(QUAD):
                        last = nc.tensor.matmul(K.ps[0:HD, 4 * q + 2, i * C3:(i + 1) * C3], wide_bk[:, q, i, :], wide_invT[:, q, i, :], start=True, stop=True)
                    last.then_inc(x_filled[q], 1)
                    for i in range(QUAD):
                        last = nc.tensor.matmul(K.ps[0:C3, 4 * q + 3, i * HD:(i + 1) * HD], wide_invT[:, q, i, :], wide_bv[:, q, i, :], start=True, stop=True)
                    last.then_inc(x_filled[q], 1)

                pe.wait_ge(padded, len(wides + wide_rhs))
                run(pairs=pairs, turn=turn, product=product, add=add, result=result)

            @block.vector
            def _(dve):
                link = Chain(dve, chain)

                def pairs(c, q):
                    dve.wait_ge(sums_filled[q], c + 1)
                    if c:
                        dve.wait_ge(masked[q], LV * c)
                    link(nc.vector.tensor_tensor(amask[:, q], bank(q, 0), over(1, c, q, C3), ALU.subtract))
                    nc.vector.tensor_scalar(amat[:, q], amask[:, q], 0.0, None, ALU.max).then_inc(split[q], 1)
                    nc.vector.tensor_scalar(own(attnT, c, q), amask[:, q], 0.0, None, ALU.min).then_inc(split[q], 1)

                def triangle(c, q):
                    dve.wait_ge(keys_filled[q], c + 1)
                    dve.wait_ge(exped[q], 2 * c + 1)
                    link(nc.vector.scalar_tensor_tensor(out=amat[:, q], in0=bank(q, 1), scalar=-1.0, in1=amat[:, q], op0=ALU.mult, op1=ALU.mult))
                    dve.wait_ge(weighted[q], c + 1)
                    link(nc.vector.tensor_tensor(amat[:, q], amat[:, q], beta_mask[:, q], ALU.mult))
                    link(nc.vector.tensor_tensor(inv[:, q], amat[:, q], mask(0), ALU.mult))
                    nc.vector.tensor_tensor(inv[:, q], inv[:, q], mask(LEVELS_G + 1), ALU.add).then_inc(first[q], 1)

                def turn(c, q):
                    dve.wait_ge(queries_filled[q], c + 1)
                    dve.wait_ge(exped[q], 2 * c + 2)
                    at = own(attnT, c, q)
                    nc.vector.tensor_tensor(at, bank(q, 2), at, ALU.mult).then_inc(attn_out[q], 1)

                def product(c, q, l, n):
                    pass

                def add(c, q, l, n):
                    dve.wait_ge(d_filled[q], n + 1)
                    dve.wait_ge(firstT[q], c + 1)
                    nc.vector.tensor_tensor(invT[:, q], bank(q, 1), invT[:, q], ALU.add).then_inc(d_added[q], 1)

                for t in wides + wide_rhs:
                    nc.vector.memset(t[HD:P], 0.0).then_inc(padded, 1)
                dve.wait_ge(padded, len(wides + wide_rhs))
                dve.wait_ge(arrived, 16)
                run(pairs=pairs, triangle=triangle, turn=turn, product=product, add=add)

            @block.scalar
            def _(act):
                def pairs(c, q):
                    act.wait_ge(split[q], 2 * c + 1)
                    nc.scalar.activation(amat[:, q], amat[:, q], ACT.Exp, scale=-1.0).then_inc(exped[q], 1)
                    act.wait_ge(split[q], 2 * c + 2)
                    nc.scalar.activation(own(attnT, c, q), own(attnT, c, q), ACT.Exp).then_inc(exped[q], 1)

                def turn(c, q):
                    act.wait_ge(firstT_filled[q], c + 1)
                    if c:
                        act.wait_ge(x_filled[q], 2 * c)
                    nc.scalar.activation(invT[:, q], bank(q, 3), ACT.Copy).then_inc(firstT[q], 1)

                def product(c, q, l, n):
                    if l:
                        act.wait_ge(turned[q], c * (LV - 1) + l)
                        nc.scalar.activation(inv[:, q], bank(q, 2), ACT.Copy).then_inc(inv_out[q], 1)
                    act.wait_ge(z_filled[q], n + 1)
                    nc.scalar.activation(prod[:, q], bank(q, 0), ACT.Copy).then_inc(z_out[q], 1)

                def add(c, q, l, n):
                    pass

                def result(c, q):
                    act.wait_ge(x_filled[q], 2 * c + 1)
                    nc.scalar.activation(kcdT[q * HD:(q + 1) * HD, c], K.ps[0:HD, 4 * q + 2, 0:QUAD * C3].rearrange("p (h i) -> p h i", i=C3), ACT.Copy).then_inc(x_out[q], 1)
                    act.wait_ge(x_filled[q], 2 * c + 2)
                    nc.scalar.activation(own(value, c, q), K.ps[0:C3, 4 * q + 3, 0:QUAD * HD].rearrange("p (h i) -> p h i", i=HD), ACT.Copy).then_inc(x_out[q], 1)

                run(pairs=pairs, turn=turn, product=product, add=add, result=result)

            @block.gpsimd
            def _(pool):
                link = Chain(pool, pool_chain)

                def pairs(c, q):
                    if c:
                        pool.wait_ge(first[q], c)
                    nc.gpsimd.tensor_tensor(beta_mask[:, q], over(0, c, q, C3), mask(LEVELS_G + 2), ALU.mult).then_inc(weighted[q], 1)

                def triangle(c, q):
                    pool.wait_ge(first[q], c + 1)
                    nc.gpsimd.tensor_tensor(amask[:, q], amat[:, q], mask(1), ALU.mult).then_inc(masked[q], 1)


                def result(c, q):
                    pool.wait_ge(attn_out[q], c + 1)
                    nc.gpsimd.tensor_tensor(own(attnT, c, q), own(attnT, c, q), mask(LEVELS_G + 4), ALU.mult)

                def product(c, q, l, n):
                    if l < LV - 1:
                        pool.wait_ge(z_filled[q], n + 1)
                        nc.gpsimd.tensor_tensor(amask[:, q], amat[:, q], mask(l + 2), ALU.mult).then_inc(masked[q], 1)

                def add(c, q, l, n):
                    keys, values = (own(t.rearrange("p c (h i) -> p c h i", i=HD), c, q) for t in (k_tok, v_tok[:]))
                    if l == 0:
                        if c:
                            pool.wait_ge(x_filled[q], 2 * c)
                        link(nc.gpsimd.tensor_tensor(bv[:, q], values, over(0, c, q, HD), ALU.mult))
                    elif l == 1:
                        link(nc.gpsimd.tensor_tensor(bk[:, q], keys, over(2, c, q, HD), ALU.mult))
                    elif l == 2:
                        nc.gpsimd.tensor_tensor(keys, keys, over(3, c, q, HD), ALU.mult).then_inc(rhs_ready[q], 1)

                pool.wait_ge(padded, len(wides + wide_rhs))
                pool.wait_ge(arrived, 16)
                run(pairs=pairs, triangle=triangle, product=product, add=add, result=result)


def gdn_scan_stage(K, mats, k_tail, q0, last_decay, y):
    nc = K.nc
    (kcdT, value, attnT) = mats
    H = GDN_HEADS
    with ExitStack() as local:
        state = K.buf(local, "gdn_state", [P, 2, QUAD, P])
        kept = K.buf(local, "gdn_kept", [P, QUAD, HD])
        vn = K.buf(local, "gdn_new_values", [P, 2, H, HD])
        cleared, v_filled, v_ready, s_filled, s_ready, y_filled, y_out, chain = (K.sem(n) for n in (
            "gdn_cleared", "gdn_v_filled", "gdn_v_ready", "gdn_s_filled", "gdn_s_ready", "gdn_y_filled", "gdn_y_out", "gdn_scan_chain"))
        half = [slice(o * HD, (o + 1) * HD) for o in range(2)]

        def pairs(rows, b, i):
            return K.ps[0:rows, b, 0:QUAD * i].rearrange("p (h i) -> p h i", i=i)

        with K.stage() as block:
            @block.tensor
            def _(pe):
                pe.wait_ge(cleared, 2)
                for c in range(NC3):
                    s = state[:, c % 2]
                    if c:
                        pe.wait_ge(s_ready, 2 * c)
                    for i in range(QUAD):
                        last = nc.tensor.matmul(pairs(C3, c % 2, P)[:, i, :], kcdT[:, c, i, :], s[:, i, :], start=True, stop=True)
                    last.then_inc(v_filled, 1)
                    pe.wait_ge(v_ready, c + 1)
                    for i in range(QUAD):
                        last = nc.tensor.matmul(pairs(P, 2 + c % 2, P)[:, i, :], k_tail[:, c, i * P:(i + 1) * P],
                                                vn[:, c % 2, 2 * i:2 * i + 2, :].rearrange("p o v -> p (o v)"), start=True, stop=True)
                    last.then_inc(s_filled, 1)
                    if c >= 2:
                        pe.wait_ge(y_out, c - 1)
                    for i in range(QUAD):
                        to = pairs(P, 4 + c % 2, C3)[:, i, :]
                        nc.tensor.matmul(to, s[:, i, :], q0[:, i, c * C3:(c + 1) * C3], start=True, stop=False)
                        for o in range(2):
                            last = nc.tensor.matmul(to[half[o]], vn[:, c % 2, 2 * i + o, :], attnT[:, c, 2 * i + o, :], start=False, stop=True)
                    last.then_inc(y_filled, 1)

            @block.vector
            def _(dve):
                link = Chain(dve, chain)
                nc.vector.memset(state[:], 0.0).then_inc(cleared, 1)
                nc.vector.memset(vn[HD:P], 0.0).then_inc(cleared, 1)
                dve.wait_ge(cleared, 2)
                for c in range(NC3):
                    dve.wait_ge(v_filled, c + 1)
                    if c >= 2:
                        dve.wait_ge(y_filled, c - 1)
                    grid = K.ps[0:C3, c % 2, 0:H * HD].rearrange("p (h i) -> p h i", i=HD)
                    nc.vector.scalar_tensor_tensor(out=vn[0:C3, c % 2], in0=grid, scalar=-1.0, in1=value[:, c], op0=ALU.mult, op1=ALU.add).then_inc(v_ready, 1)
                    for o in range(2):
                        link(nc.vector.tensor_tensor(kept[half[o]], state[half[o], c % 2, :, half[o]], last_decay[half[o], :, c:c + 1].to_broadcast((HD, QUAD, HD)), ALU.mult))
                    dve.wait_ge(s_filled, c + 1)
                    if c:
                        dve.wait_ge(y_filled, c)
                    for o in range(2):
                        nc.vector.tensor_tensor(state[half[o], (c + 1) % 2, :, half[o]], pairs(P, 2 + c % 2, P)[half[o], :, half[o]], kept[half[o]], ALU.add).then_inc(s_ready, 1)
                    dve.wait_ge(s_ready, 2 * (c + 1))

            @block.scalar
            def _(act):
                for c in range(NC3):
                    act.wait_ge(y_filled, c + 1)
                    nc.scalar.activation(y[:, :, c * C3:(c + 1) * C3], pairs(P, 4 + c % 2, C3), ACT.Copy).then_inc(y_out, 1)


def merge_3_stage(K, yf, yg, gates, merged):
    nc = K.nc
    filled, drained, gated = K.sem("merge3_filled"), K.sem("merge3_drained"), K.sem("merge3_gated")
    with ExitStack() as local:
        part = K.buf(local, "merge3_part", [P, 2, 8, T3 // 2])
        feed = Feed(K, local, 8, lambda i: (yf, yg)[(i // 2) % 2][:, 2 * (i % 2):2 * (i % 2) + 2, :], [2, T3])
        groups = [Group(feed, 8, 2 * g, 2, filled, 7 * g) for g in range(4)]

        def add(e, engine, g, b):
            (lo, hi), at = HALVES[b % 2], merged(4 * (g // 2) + b // 2)
            e.wait_ge(gated, 8 * (g // 2) + b + 1)
            engine.tensor_tensor(at[:, lo:hi], at[:, lo:hi], part[:, g // 2, b, :], ALU.add)

        def taken(e, g, b):
            e.wait_ge((drained, gated)[g % 2], 8 * (g // 2) + b + 1)

        with K.stage() as block:
            @block.sync
            def _(sp):
                feed.refill(sp)

            @block.tensor
            def _(pe):
                for g, group in enumerate(groups):
                    group.products(pe, half_product(K, feed), (lambda e, b, g=g: taken(e, g - 1, b)) if g else None)

            @block.scalar
            def _(act):
                feed.start_hi(act)
                feed.ahead_hi(act, range(8))

            @block.vector
            def _(dve):
                feed.start_lo(dve)
                for g, group in enumerate(groups):
                    feed.ahead_lo(dve, group.body)
                    if g % 2:
                        dve.wait_ge(drained, 8 * (g // 2 + 1))
                    for b in range(8):
                        (lo, hi), m = HALVES[b % 2], 4 * (g // 2) + b // 2
                        group.bank_ready(dve, b)
                        gate, src = gates[:, KT * (g % 2) + m, lo:hi], K.ps[:, b, 0:hi - lo]
                        if g % 2 == 0:
                            nc.vector.tensor_tensor(merged(m)[:, lo:hi], src, gate, ALU.mult).then_inc(drained, 1)
                        else:
                            nc.vector.tensor_tensor(part[:, g // 2, b, :], src, gate, ALU.mult).then_inc(gated, 1)
                            if b % 2:
                                add(dve, nc.vector, g, b)
                    feed.ahead_lo(dve, group.end)

            @block.gpsimd
            def _(pool):
                for g in (1, 3):
                    for b in range(0, 8, 2):
                        add(pool, nc.gpsimd, g, b)


def residual_3_stage(K, x):
    nc = K.nc
    filled, drained = K.sem("out3_filled"), K.sem("out3_drained")
    with ExitStack() as local:
        feed = Feed(K, local, 8, pairs_of(x), [2, T3])
        groups = [Group(feed, 8, 4 * g, 4, filled, 7 * g) for g in range(2)]
        with K.stage() as block:
            @block.sync
            def _(sp):
                feed.refill(sp)

            @block.tensor
            def _(pe):
                for g, group in enumerate(groups):
                    group.products(pe, half_product(K, feed), (lambda e, b: e.wait_ge(drained, b + 1)) if g else None)

            @block.scalar
            def _(act):
                feed.start_hi(act)
                feed.ahead_hi(act, range(8))

            @block.vector
            def _(dve):
                feed.start_lo(dve)
                for g, group in enumerate(groups):
                    feed.ahead_lo(dve, group.body)
                    for b in range(8):
                        (lo, hi), m = HALVES[b % 2], 4 * g + b // 2
                        group.bank_ready(dve, b)
                        nc.vector.tensor_tensor(K.h[:, m, lo:hi], K.ps[:, b, 0:hi - lo], K.h[:, m, lo:hi], ALU.add).then_inc(drained, 1)
                    feed.ahead_lo(dve, group.end)


def conv_ffn_3(K):
    nc = K.nc
    with ExitStack() as ffn:
        hidden = K.buf(ffn, "ffn3_hidden", [P, FT, S])
        raw = K.buf(ffn, "ffn3_raw", [P, 2, 4, T3])
        c = K.buf(ffn, "ffn3_conv", [P, 2, 4, S])
        filled, drained, conv, silu, chain, multiplied = (K.sem(n) for n in ("up3_filled", "up3_drained", "conv3_done", "silu_done", "conv3_chain", "ffn3_multiplied"))
        G = FT // 2
        feed = Feed(K, ffn, 4 * G, pairs_of(K.xn), [2, T3], residual_norm(K, ffn, "norm_ffn_w_3", (0, T3)))
        groups = [Group(feed, 8, 4 * g, 4, filled, 7 * g) for g in range(G)]
        with K.stage() as block:
            @block.sync
            def _(sp):
                feed.refill(sp)

            @block.tensor
            def _(pe):
                for g, group in enumerate(groups):
                    group.products(pe, half_product(K, feed),
                                   (lambda e, b, g=g: e.wait_ge(drained, 8 * (g - 1) + b + 1)) if g else None)

            @block.scalar
            def _(act):
                feed.start_hi(act)
                for g, group in enumerate(groups):
                    feed.ahead_hi(act, group.body)
                    if g >= 2:
                        act.wait_ge(conv, 4 * (g - 1))
                    for b in range(8):
                        lo, hi = HALVES[b % 2]
                        group.bank_ready(act, b)
                        nc.scalar.activation(raw[:, g % 2, b // 2, lo:hi], K.ps[:, b, 0:hi - lo], ACT.Copy).then_inc(drained, 1)
                    feed.ahead_hi(act, group.end)
                    for i in range(2):
                        act.wait_ge(conv, 4 * g + i + 1)
                        nc.scalar.activation(hidden[:, 2 * g + i, :], c[:, g % 2, i, :], ACT.Silu).then_inc(silu, 1)

            @block.vector
            def _(dve):
                link = Chain(dve, chain)
                feed.start_lo(dve)
                for g in range(G):
                    feed.ahead_lo(dve, groups[g].body if g == 0 else [])
                    for i in range(4):
                        f = 2 * g + i if i < 2 else FT + 2 * g + i - 2
                        dve.wait_ge(drained, 8 * g + 2 * i + 2)
                        if g >= 2:
                            dve.wait_ge(silu, 2 * (g - 1))
                            dve.wait_ge(multiplied, 2 * (g - 1))
                        x, to = raw[:, g % 2, i, :], c[:, g % 2, i, :]
                        link(nc.vector.tensor_scalar(to, x[:, META - 2:T3 - 2], K.vec("ffn_conv_w_3", f), K.vec("ffn_conv_b_3", f), ALU.mult, ALU.add))
                        link(nc.vector.scalar_tensor_tensor(out=to, in0=x[:, META - 1:T3 - 1], scalar=K.vec("ffn_conv_w_3", 2 * FT + f), in1=to, op0=ALU.mult, op1=ALU.add))
                        nc.vector.scalar_tensor_tensor(out=to, in0=x[:, META:T3], scalar=K.vec("ffn_conv_w_3", 4 * FT + f), in1=to, op0=ALU.mult, op1=ALU.add).then_inc(conv, 1)
                        feed.ahead_lo(dve, range(4 * g + 3 + i, min(4 * g + 4 + i, 4 * G)))

            @block.gpsimd
            def _(pool):
                for g in range(G):
                    for i in range(2):
                        pool.wait_ge(silu, 2 * g + i + 1)
                        pool.wait_ge(conv, 4 * g + 2 + i + 1)
                        at = hidden[:, 2 * g + i, :]
                        nc.gpsimd.tensor_tensor(at, at, c[:, g % 2, 2 + i, :], ALU.mult).then_inc(multiplied, 1)
        residual_stage(K, lambda j: hidden[:, j, :], FT, (META, T3))


def block_3(K, ins, out):
    with ExitStack() as mix:
        heads = K.buf(mix, "head_rates", [8, 4, T3])
        yf = K.buf(mix, "fox_y", [P, 4, T3])
        gin = K.buf(mix, "gdn_in", [P, 12, 3 + T3])
        yg = gin[:, 0:4, 3:3 + T3]
        with ExitStack() as fox:
            keep = K.buf(fox, "gdn_keep", [8, T3])
            causal = K.buf(fox, "causal88", [C3, C3])
            fq, fk = (K.buf(fox, n, [P, FOX_HEADS, T3]) for n in ("fox_q", "fox_k"))
            fv = K.buf(fox, "fox_v", [P, NC3, 512])
            mix_in_3_stage(K, fq, fk, fv, gin, heads, keep, causal, ins)
            head_rates_stage(K, heads, fk, keep[:])

            def scores(unit, part, lo, hi, to):
                h, i, _ = unit
                return K.nc.tensor.matmul(to, fq[:, h, i * C3:(i + 1) * C3], fk[:, h, lo:hi], start=True, stop=True)

            attention_stage(K, [(h, i, i + 1) for h in range(FOX_HEADS) for i in range(NC3)], C3, scores,
                            lambda h, t, d: fv[:, t, h * HD:(h + 1) * HD],
                            lambda unit, d: yf[(unit[0] % 2) * HD:(unit[0] % 2 + 1) * HD, unit[0] // 2, unit[1] * C3:(unit[1] + 1) * C3],
                            diagonal=causal[:], value_rows=P)
        head_norm_stage(K, [([(gin[:, t, 3:3 + T3], gin[:, t, 3:3 + T3], None)], 2, 1, HD if t < 4 else 1) for t in range(8)])
        with ExitStack() as gdn:
            q0 = K.buf(gdn, "gdn_q0", [P, 4, T3])
            tok = K.buf(gdn, "gdn_tok_rates", [C3, 4, NC3, 8])
            last_decay = K.buf(gdn, "gdn_last_decay", [P, QUAD, NC3])
            wide_k = K.buf(gdn, "gdn_k_tok", [P, NC3, 512])
            k_tok, v_tok = wide_k[0:C3], K.buf(gdn, "gdn_v_tok", [C3, NC3, 512])
            kcdT = K.buf(gdn, "gdn_kcdT", [P, NC3, QUAD, C3])
            attnT = K.buf(gdn, "gdn_attnT", [P, NC3, GDN_HEADS, C3])
            value = v_tok[:].rearrange("p c (h i) -> p c h i", i=HD)
            gdn_rates_stage(K, heads, gin[:, 0:4, 3:3 + T3], q0, tok, last_decay, (wide_k, attnT))
            token_tiles_stage(K, [(gin[:, b + t, 3:3 + T3], (lambda c, n, to=to, t=t: to[:, c:c + n, t * P:(t + 1) * P]))
                                  for b, to in ((4, k_tok), (8, v_tok)) for t in range(4)], C3, NC3)
            mats = (kcdT, value, attnT)
            gdn_chunk_stage(K, gin, heads, tok, k_tok, v_tok, mats, ins)
            gdn_scan_stage(K, mats, wide_k, q0, last_decay, yg)
        head_norm_stage(K, [([(yg[:, t, :], yg[:, t, :], K.vec("gdn_norm_w_3"))], 2, HD, 1) for t in range(4)])
        gates = K.buf(mix, "branch3_gates", [P, 16, T3])
        z = K.buf(mix, "gdn_z", [P, 4, T3])
        gate_3_stage(K, z, yg, gates)
        merge_3_stage(K, yf, yg, gates, lambda m: K.xn[:, m, :])
    residual_3_stage(K, K.xn)
    conv_ffn_3(K)
    stored = K.sem("stored")

    def store(sp, normed):
        for k in range(KT):
            sp.wait_ge(normed, k + 1)
            sp.dma_start(out[:, k, :], K.xn[:, k, META:T3]).then_inc(stored, 16)
        sp.wait_ge(stored, 16 * KT)

    norm_stage(K, lambda k: K.h[:, k, :], lambda k: K.xn[:, k, :], "norm_final_w_3", (META, T3), store)


def device_inputs(i):
    vec = {}
    for name, (at, n) in VEC_COLS.items():
        v = i[name]
        if v.size < HD:
            vec[name] = short_column(v)
        elif v.size == HD:
            vec[name] = columns(np.concatenate([v.reshape(-1)] * 2))
        else:
            vec[name] = columns(v)
    arrays = shape_constants()
    pool_w = np.zeros((P, 2, P), np.float32)
    for g in range(4):
        r = slice((g % 2) * HD, (g % 2 + 1) * HD)
        pool_w[r, g // 2, r] = i["pool_w"][0, g]
    lora = np.stack([np.concatenate([i["rwkv_w2"][0], i["rwkv_a2"][0]]), i["rwkv_g2"][0]], axis=1)
    lam = np.stack([i[n][0] for n in ("diff_lq1", "diff_lk1", "diff_lq2", "diff_lk2")])
    arrays.update(
        stream=weight_stream(i), x=features(i["x"][0]), mem=features(i["mem"][0]), meta=features(i["meta_tokens_3"]),
        vecs=np.ascontiguousarray(np.concatenate([vec[n] for n in VEC_COLS], axis=1)),
        pool_w=pool_w, rwkv_lora=np.ascontiguousarray(lora),
        diff_lambda=np.ascontiguousarray(np.broadcast_to(lam, (P, 4, HD))))
    arrays.update(block_2_inputs(i))
    arrays.update(block_3_inputs(i))
    return arrays


def build(nc, ins, out, total):
    with ExitStack() as ctx:
        K = Core(nc, ctx, ins["stream"], total)
        load_stage(K, ins)
        block_1(K, ins)
        block_2(K, ins)
        block_3(K, ins, out)


def features(a):
    a = a.reshape(a.shape[-2], -1)
    return np.ascontiguousarray(a.T.reshape(-1, P, a.shape[0]).transpose(1, 0, 2))


def columns(a):
    return a.reshape(-1, P).T


def short_column(a):
    out = np.zeros((P, 1), a.dtype)
    out[:a.size, 0] = a.reshape(-1)
    return out


def wide(w, cols):
    w = np.concatenate([w[:, lo:hi] for lo, hi in cols], axis=1)
    w = w.reshape(-1, P, w.shape[1])
    if w.shape[2] == D:
        return w
    out = np.zeros((w.shape[0], P, D), w.dtype)
    out[:, :, :w.shape[2]] = w
    return out


def paired(w, cols):
    w = np.concatenate([w[:, lo:hi] for lo, hi in cols], axis=1)
    n = w.shape[1]
    if n < 512:
        w = np.concatenate([w, np.zeros((w.shape[0], 512 - n), w.dtype)], axis=1)
    return np.ascontiguousarray(w.reshape(-1, 2, P, 512).transpose(0, 2, 1, 3)).reshape(-1, P, D)


def weight_stream(i):
    a = {k: v[0] for k, v in i.items() if v.ndim == 3}
    w = a["w_in"]
    parts = [wide(w, [(0, 1024)]), wide(w, [(1024, 2048)]), wide(w, [(2048, 2816)]), wide(a["w_out"], [(0, D)]),
             wide(a["xa_wq"], [(0, D)]), wide(a["xa_wk"], [(0, D)]), wide(a["xa_wv"], [(0, D)]), wide(a["xa_wo"], [(0, D)])]
    for f in range(0, FF, 512):
        e = min(FF, f + 512)
        parts.append(wide(a["ffn_w_up"], [(f, e), (FF + f, FF + e)]))
    parts.append(wide(a["ffn_w_down"], [(0, D)]))
    parts += block_2_slabs(a) + block_3_slabs(a)
    return np.concatenate(parts)


def kernel(**inputs):
    import concourse.bacc as bacc
    from concourse.bass_utils import run_bass_kernel_spmd

    i = {k: np.asarray(v) for k, v in inputs.items()}
    arrays = device_inputs(i)
    nc = bacc.Bacc("TRN2", target_bir_lowering=False, num_devices=1)
    aps = {k: nc.dram_tensor(f"in_{k}", v.shape, F32, kind="ExternalInput").ap() for k, v in arrays.items()}
    out = nc.dram_tensor("out_features", (P, KT, S), F32, kind="ExternalOutput").ap()
    build(nc, aps, out, arrays["stream"].shape[0])
    r = run_bass_kernel_spmd(nc, [{f"in_{k}": v for k, v in arrays.items()}], core_ids=[0])
    got = r.results[0]["out_features"]
    return np.ascontiguousarray(got.transpose(1, 0, 2).reshape(D, S).T).reshape(1, S, D)
```
